# Optimizing a Trainium2 kernel written in Bass

```python
import math
import jax, jax.numpy as jnp
from jax import lax
import numpy as np
import functools

D_MODEL = 1024
BATCH = 1
SEQ = 512
DEPTH = 1

D_SC = 512
SC_KERNEL = 3
D_POOL = 512
POOL_WINDOWS = (2, 4, 8, 16)
N_POOL_GROUPS = 4
POOL_GROUP = D_POOL // N_POOL_GROUPS
POOL_OUT_GROUP = D_MODEL // N_POOL_GROUPS
D_CONF = 512
CONF_KERNEL = 31
N_DIFF_HEADS = 4
DIFF_HEAD_DIM = 64
D_DIFF_QK = N_DIFF_HEADS * 2 * DIFF_HEAD_DIM
D_DIFF_V = N_DIFF_HEADS * 2 * DIFF_HEAD_DIM
Q_BLOCK = 128
N_BRANCHES = 4
N_IN = 3 * D_SC + D_POOL + 2 * D_CONF + 2 * D_DIFF_QK + D_DIFF_V + N_BRANCHES * D_MODEL
D_FF = 2816
FFN_KERNEL = 3
EPS = 1e-6


def rms_norm(x, g):
    xf = x.astype(jnp.float32)
    y = xf * lax.rsqrt(jnp.mean(xf * xf, axis=-1, keepdims=True) + EPS)
    return (y * g.astype(jnp.float32)).astype(x.dtype)

def layer_norm(x, g, b):
    xf = x.astype(jnp.float32)
    mu = jnp.mean(xf, axis=-1, keepdims=True)
    var = jnp.mean(jnp.square(xf - mu), axis=-1, keepdims=True)
    y = (xf - mu) * lax.rsqrt(var + EPS)
    return (y * g.astype(jnp.float32) + b.astype(jnp.float32)).astype(x.dtype)

def causal_dwconv(x, w):
    ksz, ch = w.shape
    rhs = w.astype(x.dtype)[:, None, :]
    return lax.conv_general_dilated(
        x, rhs, window_strides=(1,), padding=[(ksz - 1, 0)],
        dimension_numbers=("NWC", "WIO", "NWC"), feature_group_count=ch)

def pool_mixer(xp, w_pool, scale):
    b, s, _ = xp.shape
    xg = xp.astype(jnp.float32).reshape(b, s, N_POOL_GROUPS, POOL_GROUP)
    cs = jnp.cumsum(xg, axis=1)
    t = jnp.arange(s)
    outs = []
    for g, w in enumerate(POOL_WINDOWS):
        csg = cs[:, :, g]
        lag = jnp.pad(csg, ((0, 0), (w, 0), (0, 0)))[:, :s]
        count = jnp.minimum(t + 1, w).astype(jnp.float32)[None, :, None]
        outs.append((csg - lag) / count - xg[:, :, g])
    pooled = jnp.stack(outs, axis=2).astype(xp.dtype)
    y = jnp.einsum("bsgc,gco->bsgo", pooled, w_pool.astype(xp.dtype))
    return y.reshape(b, s, D_MODEL) * scale.astype(xp.dtype)

def conformer_conv(u, conv_w, conv_b, ln_g, ln_b, w_out):
    a, gate = jnp.split(u, 2, axis=-1)
    y = a * jax.nn.sigmoid(gate)
    y = causal_dwconv(y, conv_w) + conv_b.astype(y.dtype)
    y = layer_norm(y, ln_g, ln_b)
    y = jax.nn.silu(y)
    return y @ w_out.astype(y.dtype)

def diff_attention(q, k, v, q_norm, k_norm, lq1, lk1, lq2, lk2, subln, lam_init):
    b, s, _ = q.shape
    hd = DIFF_HEAD_DIM
    q = rms_norm(q.reshape(b, s, N_DIFF_HEADS, 2, hd), q_norm) * (hd ** -0.5)
    k = rms_norm(k.reshape(b, s, N_DIFF_HEADS, 2, hd), k_norm)
    v = v.reshape(b, s, N_DIFF_HEADS, 2 * hd)
    qt = jnp.transpose(q, (0, 2, 3, 1, 4))
    kt = jnp.transpose(k, (0, 2, 3, 1, 4))
    vt = jnp.transpose(v, (0, 2, 1, 3))
    lam = (jnp.exp(jnp.sum(lq1.astype(jnp.float32) * lk1.astype(jnp.float32)))
           - jnp.exp(jnp.sum(lq2.astype(jnp.float32) * lk2.astype(jnp.float32)))
           + lam_init)
    nb = s // Q_BLOCK
    q_blocks = jnp.moveaxis(qt.reshape(b, N_DIFF_HEADS, 2, nb, Q_BLOCK, hd), 3, 0)
    starts = jnp.arange(nb, dtype=jnp.int32) * Q_BLOCK
    kpos = jnp.arange(s, dtype=jnp.int32)

    def attend(args):
        qb, start = args
        sc = jnp.einsum("bhmqd,bhmkd->bhmqk", qb, kt).astype(jnp.float32)
        qpos = start + jnp.arange(Q_BLOCK, dtype=jnp.int32)
        mask = kpos[None, :] <= qpos[:, None]
        p = jax.nn.softmax(jnp.where(mask, sc, -jnp.inf), axis=-1)
        a = (p[:, :, 0] - lam * p[:, :, 1]).astype(vt.dtype)
        return jnp.einsum("bhqk,bhkv->bhqv", a, vt)

    o = lax.map(attend, (q_blocks, starts))
    o = jnp.transpose(o, (1, 0, 3, 2, 4)).reshape(b, s, N_DIFF_HEADS, 2 * hd)
    o = rms_norm(o, subln) * (1.0 - lam_init)
    return o.reshape(b, s, D_DIFF_V)

def conv_glu_ffn(h, w_up, conv_w, w_down):
    u = causal_dwconv(h @ w_up.astype(h.dtype), conv_w)
    gate, up = jnp.split(u, 2, axis=-1)
    return (jax.nn.silu(gate) * up) @ w_down.astype(h.dtype)

def first_inputs(seed: int = 0) -> dict:
    key = jax.random.key(seed)
    ks = jax.random.split(key, 32)
    L = DEPTH
    f32 = jnp.float32

    def nrm(k, shape, scale):
        return jax.random.normal(k, shape, f32) * scale

    def gain(k, shape):
        return 1.0 + 0.02 * jax.random.normal(k, shape, f32)

    return {
        "x": nrm(ks[0], (BATCH, SEQ, D_MODEL), 1.0),
        "mix_norm": gain(ks[1], (L, D_MODEL)),
        "w_in": nrm(ks[2], (L, D_MODEL, N_IN), D_MODEL ** -0.5),
        "sc_conv": nrm(ks[3], (L, SC_KERNEL, D_SC), SC_KERNEL ** -0.5),
        "sc_out": nrm(ks[4], (L, D_SC, D_MODEL), D_SC ** -0.5),
        "pool_w": nrm(ks[5], (L, N_POOL_GROUPS, POOL_GROUP, POOL_OUT_GROUP), POOL_GROUP ** -0.5),
        "pool_scale": 1.0 + 0.1 * jax.random.normal(ks[6], (L, D_MODEL), f32),
        "conf_conv": nrm(ks[7], (L, CONF_KERNEL, D_CONF), CONF_KERNEL ** -0.5),
        "conf_conv_b": nrm(ks[8], (L, D_CONF), 0.02),
        "conf_ln_g": gain(ks[9], (L, D_CONF)),
        "conf_ln_b": nrm(ks[10], (L, D_CONF), 0.02),
        "conf_out": nrm(ks[11], (L, D_CONF, D_MODEL), D_CONF ** -0.5),
        "q_norm": gain(ks[12], (L, DIFF_HEAD_DIM)),
        "k_norm": gain(ks[13], (L, DIFF_HEAD_DIM)),
        "lambda_q1": nrm(ks[14], (L, DIFF_HEAD_DIM), 0.1),
        "lambda_k1": nrm(ks[15], (L, DIFF_HEAD_DIM), 0.1),
        "lambda_q2": nrm(ks[16], (L, DIFF_HEAD_DIM), 0.1),
        "lambda_k2": nrm(ks[17], (L, DIFF_HEAD_DIM), 0.1),
        "diff_subln": gain(ks[18], (L, 2 * DIFF_HEAD_DIM)),
        "diff_out": nrm(ks[19], (L, D_DIFF_V, D_MODEL), D_DIFF_V ** -0.5),
        "w_o": nrm(ks[20], (L, D_MODEL, D_MODEL), D_MODEL ** -0.5),
        "ffn_norm": gain(ks[21], (L, D_MODEL)),
        "ffn_up": nrm(ks[22], (L, D_MODEL, 2 * D_FF), D_MODEL ** -0.5),
        "ffn_conv": nrm(ks[23], (L, FFN_KERNEL, 2 * D_FF), FFN_KERNEL ** -0.5),
        "ffn_down": nrm(ks[24], (L, D_FF, D_MODEL), D_FF ** -0.5),
    }

def first_block(x, mix_norm, w_in, sc_conv, sc_out, pool_w, pool_scale, conf_conv, conf_conv_b,
              conf_ln_g, conf_ln_b, conf_out, q_norm, k_norm, lambda_q1, lambda_k1, lambda_q2,
              lambda_k2, diff_subln, diff_out, w_o, ffn_norm, ffn_up, ffn_conv, ffn_down):
    b, s, _ = x.shape
    widths = [D_SC, D_SC, D_SC, D_POOL, 2 * D_CONF, D_DIFF_QK, D_DIFF_QK, D_DIFF_V,
              N_BRANCHES * D_MODEL]
    offsets = [int(o) for o in np.cumsum(widths)[:-1]]
    for l in range(DEPTH):
        lam_init = 0.8 - 0.6 * math.exp(-0.3 * l)
        h = rms_norm(x, mix_norm[l])
        z = h @ w_in[l].astype(h.dtype)
        sc_b, sc_c, sc_x, pool_in, conf_in, q, k, v, gate_logits = jnp.split(z, offsets, axis=-1)
        y_sc = (sc_b * causal_dwconv(sc_c * sc_x, sc_conv[l])) @ sc_out[l].astype(h.dtype)
        y_pool = pool_mixer(pool_in, pool_w[l], pool_scale[l])
        y_conf = conformer_conv(conf_in, conf_conv[l], conf_conv_b[l], conf_ln_g[l],
                                conf_ln_b[l], conf_out[l])
        y_diff = diff_attention(q, k, v, q_norm[l], k_norm[l], lambda_q1[l], lambda_k1[l],
                                lambda_q2[l], lambda_k2[l], diff_subln[l], lam_init)
        y_diff = y_diff @ diff_out[l].astype(h.dtype)
        gates = jax.nn.sigmoid(gate_logits.astype(jnp.float32)).reshape(b, s, N_BRANCHES, D_MODEL)
        ys = jnp.stack([y_sc, y_pool, y_conf, y_diff], axis=2)
        merged = jnp.sum(gates.astype(ys.dtype) * ys, axis=2)
        x = x + merged @ w_o[l].astype(h.dtype)
        h2 = rms_norm(x, ffn_norm[l])
        x = x + conv_glu_ffn(h2, ffn_up[l], ffn_conv[l], ffn_down[l])
    return x


_first_inputs = first_inputs


def first_inputs(seed=0):
    import zlib

    import numpy as np

    out = dict(_first_inputs(seed))
    spreads = {}
    factors = {'conf_conv_b': 5.331,
     'conf_ln_g': 8.0,
     'conf_ln_b': 8.0,
     'q_norm': 8.0,
     'k_norm': 7.813,
     'lambda_q1': 8.0,
     'diff_subln': 8.0,
     'ffn_norm': 4.487}
    for name, (base, spread) in spreads.items():
        noise = np.random.default_rng([zlib.crc32(name.encode()), seed]).standard_normal(out[name].shape)
        drawn = base * np.exp(spread * noise) if base else spread * noise
        out[name] = __import__('jax').numpy.asarray(drawn.astype(out[name].dtype))
    for name, factor in factors.items():
        out[name] = (out[name] * factor).astype(out[name].dtype)
    return out


_narrow_inputs = first_inputs


def first_inputs(seed=0):

    out = dict(_narrow_inputs(seed))
    wider = {'pool_scale': 4.48, 'conf_ln_g': 3.67, 'conf_ln_b': 3.41, 'diff_subln': 3.37}
    for name, times in wider.items():
        mean = out[name].mean()
        out[name] = (mean + times * (out[name] - mean)).astype(out[name].dtype)
    return out


GDN_HEADS = 8
GDN_HEAD_DIM = 64
GDN_WIDTH = GDN_HEADS * GDN_HEAD_DIM
GDN_CONV = 4
GDN_CHUNK = 64
RWKV_HEADS = 8
RWKV_HEAD_DIM = 64
RWKV_WIDTH = RWKV_HEADS * RWKV_HEAD_DIM
DECAY_LORA = 64
ICLR_LORA = 64
GATE_LORA = 160
RWKV_COLS = 3 * RWKV_WIDTH + DECAY_LORA + ICLR_LORA + GATE_LORA
IN_SIZES = (3 * GDN_WIDTH, GDN_WIDTH, GDN_HEADS, GDN_HEADS, RWKV_COLS, D_MODEL, D_MODEL)
D_IN = 3 * GDN_WIDTH + GDN_WIDTH + 2 * GDN_HEADS + RWKV_COLS + 2 * D_MODEL
FFN_CONV = 3
NORM_EPS = 1e-6
LNX_EPS = 64e-5


def rms_norm_2(x, w, eps=NORM_EPS):
    xf = x.astype(jnp.float32)
    y = xf * lax.rsqrt(jnp.mean(xf * xf, axis=-1, keepdims=True) + eps)
    return (y * w.astype(jnp.float32)).astype(x.dtype)

def l2_normalize(x, eps=1e-6):
    xf = x.astype(jnp.float32)
    return xf * lax.rsqrt(jnp.sum(xf * xf, axis=-1, keepdims=True) + eps)

def split_cols(p, sizes):
    out, start = [], 0
    for s in sizes:
        out.append(p[..., start:start + s])
        start += s
    return out

def token_shift(p):
    return jnp.pad(p, ((0, 0), (1, 0), (0, 0)))[:, :-1]

def causal_depthwise_conv(x, w):
    k = w.shape[0]
    return lax.conv_general_dilated(
        x, w[:, None, :].astype(x.dtype), window_strides=(1,), padding=((k - 1, 0),),
        dimension_numbers=('NWC', 'WIO', 'NWC'), feature_group_count=x.shape[-1])

def chunk_gated_delta_rule(q, k, v, g, beta):
    B, T, H, dk = q.shape
    dv = v.shape[-1]
    C = GDN_CHUNK
    n = T // C
    to_chunks = lambda t: t.reshape(B, n, C, H, -1).transpose(0, 3, 1, 2, 4)
    q, k, v = to_chunks(q), to_chunks(k), to_chunks(v)
    g = g.reshape(B, n, C, H).transpose(0, 3, 1, 2)
    beta = beta.reshape(B, n, C, H).transpose(0, 3, 1, 2)
    g_cum = jnp.cumsum(g, axis=-1)
    causal = jnp.tril(jnp.ones((C, C), dtype=bool))
    strict = jnp.tril(jnp.ones((C, C), dtype=bool), -1)
    diff = g_cum[..., :, None] - g_cum[..., None, :]
    decay = jnp.where(causal, jnp.exp(jnp.where(causal, diff, 0.0)), 0.0)
    k_beta = k * beta[..., None]
    v_beta = v * beta[..., None]
    lower = jnp.where(strict, jnp.einsum('bhncd,bhnsd->bhncs', k_beta, k) * decay, 0.0)
    eye = jnp.eye(C, dtype=q.dtype)
    t_mat = lax.linalg.triangular_solve(lower + eye, jnp.broadcast_to(eye, lower.shape),
                                        left_side=True, lower=True, unit_diagonal=True)
    u = jnp.matmul(t_mat, v_beta)
    w = jnp.matmul(t_mat, k_beta * jnp.exp(g_cum)[..., None])
    attn = jnp.where(causal, jnp.einsum('bhncd,bhnsd->bhncs', q, k) * decay, 0.0)

    def step(S, inp):
        q_i, k_i, u_i, w_i, a_i, gc_i = inp
        v_new = u_i - jnp.matmul(w_i, S)
        o_i = jnp.matmul(q_i * jnp.exp(gc_i)[..., None], S) + jnp.matmul(a_i, v_new)
        g_last = gc_i[..., -1]
        k_dec = k_i * jnp.exp(g_last[..., None] - gc_i)[..., None]
        S = S * jnp.exp(g_last)[..., None, None] + jnp.einsum('bhcd,bhce->bhde', k_dec, v_new)
        return S, o_i

    mv = lambda t: jnp.moveaxis(t, 2, 0)
    S0 = jnp.zeros((B, H, dk, dv), dtype=q.dtype)
    _, o = lax.scan(step, S0, (mv(q), mv(k), mv(u), mv(w), mv(attn), mv(g_cum)))
    return o.transpose(1, 0, 3, 2, 4).reshape(B, T, H, dv)

def gated_deltanet(qkv, z, b_logit, a_logit, conv_w, a_log, dt_bias, onorm_w):
    B, T, _ = qkv.shape
    qkv = jax.nn.silu(causal_depthwise_conv(qkv, conv_w)).astype(jnp.float32)
    q, k, v = jnp.split(qkv, 3, axis=-1)
    heads = lambda t: t.reshape(B, T, GDN_HEADS, GDN_HEAD_DIM)
    q = l2_normalize(heads(q)) * (GDN_HEAD_DIM ** -0.5)
    k = l2_normalize(heads(k))
    v = heads(v)
    beta = jax.nn.sigmoid(b_logit.astype(jnp.float32))
    g = -jnp.exp(a_log.astype(jnp.float32)) * jax.nn.softplus(
        a_logit.astype(jnp.float32) + dt_bias.astype(jnp.float32))
    o = chunk_gated_delta_rule(q, k, v, g, beta)
    o = rms_norm_2(o, onorm_w) * jax.nn.silu(heads(z).astype(jnp.float32))
    return o.reshape(B, T, GDN_WIDTH)

def rwkv7_scan(r, decay, k, v, a, b):
    B, T, H, N = r.shape

    def step(S, inp):
        r_t, w_t, k_t, v_t, a_t, b_t = inp
        sa = jnp.einsum('bhvk,bhk->bhv', S, a_t)
        S = S * w_t[:, :, None, :] + sa[..., None] * b_t[:, :, None, :] + v_t[..., None] * k_t[:, :, None, :]
        return S, jnp.einsum('bhvk,bhk->bhv', S, r_t)

    tm = lambda t: jnp.moveaxis(t, 1, 0)
    S0 = jnp.zeros((B, H, N, N), dtype=jnp.float32)
    _, y = lax.scan(step, S0, (tm(r), tm(decay), tm(k), tm(v), tm(a), tm(b)))
    return jnp.moveaxis(y, 0, 1)

def rwkv7_time_mix(pb, mu, w0, w2, a0, a2, g2, k_k, k_a, r_k, lnx_w, lnx_b):
    f32 = lambda t: t.astype(jnp.float32)
    B, T, _ = pb.shape
    pb = f32(pb)
    pb = pb + (token_shift(pb) - pb) * f32(mu)
    r, k, v, w_lo, a_lo, g_lo = split_cols(
        pb, (RWKV_WIDTH, RWKV_WIDTH, RWKV_WIDTH, DECAY_LORA, ICLR_LORA, GATE_LORA))
    w = -jax.nn.softplus(-(f32(w0) + jnp.tanh(w_lo) @ f32(w2))) - 0.5
    decay = jnp.exp(-jnp.exp(w))
    a = jax.nn.sigmoid(f32(a0) + a_lo @ f32(a2))
    g = jax.nn.sigmoid(g_lo) @ f32(g2)
    heads = lambda t: t.reshape(B, T, RWKV_HEADS, RWKV_HEAD_DIM)
    kk = l2_normalize(heads(k * f32(k_k)))
    k = k * (1.0 + (a - 1.0) * f32(k_a))
    r, k, v, a, decay = heads(r), heads(k), heads(v), heads(a), heads(decay)
    y = rwkv7_scan(r, decay, k, v, -kk, kk * a)
    mean = jnp.mean(y, axis=-1, keepdims=True)
    var = jnp.mean(jnp.square(y - mean), axis=-1, keepdims=True)
    y = ((y - mean) * lax.rsqrt(var + LNX_EPS)).reshape(B, T, RWKV_WIDTH) * f32(lnx_w) + f32(lnx_b)
    bonus = jnp.sum(r * k * f32(r_k), axis=-1, keepdims=True) * v
    return (y + bonus.reshape(B, T, RWKV_WIDTH)) * g

def conv_glu(h, w_in, conv_w, w_out):
    gate, up = jnp.split(h @ w_in, 2, axis=-1)
    gate = causal_depthwise_conv(gate, conv_w)
    return (jax.nn.silu(gate) * up) @ w_out

def second_inputs(seed: int = 0) -> dict:
    key = jax.random.key(seed)
    ks = iter(jax.random.split(key, 40))
    nrm = lambda shape, scale: jax.random.normal(next(ks), shape, jnp.float32) * scale
    uni = lambda shape, lo, hi: jax.random.uniform(next(ks), shape, jnp.float32, minval=lo, maxval=hi)
    L = DEPTH
    x = nrm((BATCH, SEQ, D_MODEL), 1.0)
    c = nrm((BATCH, D_MODEL), 1.0)
    w_ada = nrm((L, D_MODEL, 6 * D_MODEL), D_MODEL ** -0.5)
    b_ada = nrm((L, 6 * D_MODEL), 0.02)
    norm1_w = 1.0 + nrm((L, D_MODEL), 0.02)
    w_in = nrm((L, D_MODEL, D_IN), D_MODEL ** -0.5)
    conv_gdn = nrm((L, GDN_CONV, 3 * GDN_WIDTH), GDN_CONV ** -0.5)
    a_log = jnp.log(uni((L, GDN_HEADS), 1.0, 16.0))
    dt = jnp.exp(uni((L, GDN_HEADS), math.log(1e-3), math.log(1e-1)))
    dt_bias = dt + jnp.log(-jnp.expm1(-dt))
    onorm_gdn = 1.0 + nrm((L, GDN_HEAD_DIM), 0.02)
    w_branch_gdn = nrm((L, GDN_WIDTH, D_MODEL), GDN_WIDTH ** -0.5)
    mu_rwkv = uni((L, RWKV_COLS), 0.0, 1.0)
    w0 = uni((L, RWKV_WIDTH), -6.5, -1.5)
    w2 = nrm((L, DECAY_LORA, RWKV_WIDTH), 0.5 * DECAY_LORA ** -0.5)
    a0 = nrm((L, RWKV_WIDTH), 0.1)
    a2 = nrm((L, ICLR_LORA, RWKV_WIDTH), 0.5 * ICLR_LORA ** -0.5)
    g2 = nrm((L, GATE_LORA, RWKV_WIDTH), GATE_LORA ** -0.5)
    k_k = 0.85 + nrm((L, RWKV_WIDTH), 0.02)
    k_a = 1.0 + nrm((L, RWKV_WIDTH), 0.02)
    r_k = nrm((L, RWKV_HEADS, RWKV_HEAD_DIM), 0.1)
    lnx_w = 1.0 + nrm((L, RWKV_WIDTH), 0.02)
    lnx_b = nrm((L, RWKV_WIDTH), 0.02)
    w_branch_rwkv = nrm((L, RWKV_WIDTH, D_MODEL), RWKV_WIDTH ** -0.5)
    w_out = nrm((L, D_MODEL, D_MODEL), D_MODEL ** -0.5)
    norm2_w = 1.0 + nrm((L, D_MODEL), 0.02)
    w_ffn_in = nrm((L, D_MODEL, 2 * D_FF), D_MODEL ** -0.5)
    conv_ffn = nrm((L, FFN_CONV, D_FF), FFN_CONV ** -0.5)
    w_ffn_out = nrm((L, D_FF, D_MODEL), D_FF ** -0.5)
    norm_f_w = 1.0 + nrm((D_MODEL,), 0.02)
    return {"x": x, "c": c, "w_ada": w_ada, "b_ada": b_ada, "norm1_w": norm1_w, "w_in": w_in,
            "conv_gdn": conv_gdn, "a_log": a_log, "dt_bias": dt_bias, "onorm_gdn": onorm_gdn,
            "w_branch_gdn": w_branch_gdn, "mu_rwkv": mu_rwkv, "w0": w0, "w2": w2, "a0": a0, "a2": a2,
            "g2": g2, "k_k": k_k, "k_a": k_a, "r_k": r_k, "lnx_w": lnx_w, "lnx_b": lnx_b,
            "w_branch_rwkv": w_branch_rwkv, "w_out": w_out, "norm2_w": norm2_w, "w_ffn_in": w_ffn_in,
            "conv_ffn": conv_ffn, "w_ffn_out": w_ffn_out, "norm_f_w": norm_f_w}

def second_block(x, c, w_ada, b_ada, norm1_w, w_in, conv_gdn, a_log, dt_bias, onorm_gdn, w_branch_gdn,
              mu_rwkv, w0, w2, a0, a2, g2, k_k, k_a, r_k, lnx_w, lnx_b, w_branch_rwkv, w_out,
              norm2_w, w_ffn_in, conv_ffn, w_ffn_out, norm_f_w):
    cond = jax.nn.silu(c)
    for i in range(DEPTH):
        mod = cond @ w_ada[i] + b_ada[i]
        shift1, scale1, gate1, shift2, scale2, gate2 = jnp.split(mod[:, None, :], 6, axis=-1)
        h = rms_norm_2(x, norm1_w[i]) * (1.0 + scale1) + shift1
        p = h @ w_in[i]
        qkv_a, z_a, b_a, a_a, p_b, gl_a, gl_b = split_cols(p, IN_SIZES)
        y_a = gated_deltanet(qkv_a, z_a, b_a, a_a, conv_gdn[i], a_log[i], dt_bias[i], onorm_gdn[i])
        y_b = rwkv7_time_mix(p_b, mu_rwkv[i], w0[i], w2[i], a0[i], a2[i], g2[i], k_k[i], k_a[i],
                             r_k[i], lnx_w[i], lnx_b[i])
        y_a = y_a.astype(x.dtype) @ w_branch_gdn[i]
        y_b = y_b.astype(x.dtype) @ w_branch_rwkv[i]
        merged = jax.nn.sigmoid(gl_a) * y_a + jax.nn.sigmoid(gl_b) * y_b
        x = x + gate1 * (merged @ w_out[i])
        h = rms_norm_2(x, norm2_w[i]) * (1.0 + scale2) + shift2
        x = x + gate2 * conv_glu(h, w_ffn_in[i], conv_ffn[i], w_ffn_out[i])
    return rms_norm_2(x, norm_f_w)


_first_inputs_2 = second_inputs


def second_inputs(seed=0):
    import zlib

    import numpy as np

    out = dict(_first_inputs_2(seed))
    spreads = {}
    factors = {'norm1_w': 4.663,
     'onorm_gdn': 47.007,
     'w2': 14.797,
     'a0': 7.089,
     'k_k': 32.912,
     'k_a': 4.245,
     'lnx_w': 64.0,
     'lnx_b': 64.0,
     'norm2_w': 27.922,
     'norm_f_w': 7.446}
    for name, (base, spread) in spreads.items():
        noise = np.random.default_rng([zlib.crc32(name.encode()), seed]).standard_normal(out[name].shape)
        drawn = base * np.exp(spread * noise) if base else spread * noise
        out[name] = __import__('jax').numpy.asarray(drawn.astype(out[name].dtype))
    for name, factor in factors.items():
        out[name] = (out[name] * factor).astype(out[name].dtype)
    return out


_narrow_inputs_2 = second_inputs


def second_inputs(seed=0):

    out = dict(_narrow_inputs_2(seed))
    wider = {'k_k': 12.0, 'k_a': 3.66, 'lnx_w': 11.56, 'lnx_b': 11.86, 'norm_f_w': 3.02}
    for name, times in wider.items():
        mean = out[name].mean()
        out[name] = (mean + times * (out[name] - mean)).astype(out[name].dtype)
    return out


GRID_W = 64
CTX_LEN = 256

GLA_HEADS = 4
GLA_DK = D_MODEL // 2 // GLA_HEADS
GLA_DV = D_MODEL // GLA_HEADS
GLA_QK = GLA_HEADS * GLA_DK
GLA_V = GLA_HEADS * GLA_DV
GLA_RANK = 16
GLA_TAU = 16.0
GLA_CHUNK = 64

SSM_INNER = 2 * D_MODEL
SSM_HEADDIM = 64
SSM_HEADS = SSM_INNER // SSM_HEADDIM
SSM_GROUPS = 4
SSM_HPG = SSM_HEADS // SSM_GROUPS
SSM_STATE = 128
SSM_BC = SSM_GROUPS * SSM_STATE
SSM_CONV = 4
CONV_LEFT = 2
SSM_CONV_DIM = SSM_INNER + 2 * SSM_BC
SSM_CHUNK = 128

D_FF_3 = ((8 * D_MODEL // 3 + 255) // 256) * 256

IN_WIDTHS = (GLA_QK, GLA_QK, GLA_V, GLA_V, GLA_RANK, GLA_RANK,
             SSM_INNER, SSM_INNER, SSM_BC, SSM_BC, SSM_HEADS, SSM_HEADS,
             D_MODEL, D_MODEL)
D_IN_3 = sum(IN_WIDTHS)


def rms_norm_3(x, w):
    xf = x.astype(jnp.float32)
    y = xf * lax.rsqrt(jnp.mean(xf * xf, axis=-1, keepdims=True) + EPS)
    return (y * w.astype(jnp.float32)).astype(x.dtype)

def modulate(h, shift, scale):
    return h * (1 + scale) + shift

def _split_in(proj):
    idx = np.cumsum(IN_WIDTHS)[:-1].tolist()
    return jnp.split(proj, idx, axis=-1)

def _chunks(t, size):
    Bn, L = t.shape[:2]
    return jnp.moveaxis(t.reshape(Bn, L // size, size, *t.shape[2:]), 1, 0)

def _unchunks(t):
    n, Bn, C = t.shape[:3]
    return jnp.moveaxis(t, 0, 1).reshape(Bn, n * C, *t.shape[3:])

def _dwconv_centred(u, w, b):
    W = u.shape[1]
    up = jnp.pad(u, ((0, 0), (CONV_LEFT, SSM_CONV - 1 - CONV_LEFT), (0, 0)))
    out = b + up[:, 0:W] * w[0]
    for j in range(1, SSM_CONV):
        out = out + up[:, j:j + W] * w[j]
    return out

def _seq_conv(u, w, b):
    return _dwconv_centred(u, w, b)

def _row_conv(u, w, b, rows):
    Bn, L, Cc = u.shape
    return _dwconv_centred(u.reshape(Bn * rows, GRID_W, Cc), w, b).reshape(Bn, L, Cc)

def _gla_scan(q, k, v, log_g, s0):
    out_dtype = v.dtype
    f32 = jnp.float32
    qc, kc, vc, gc = (_chunks(t.astype(f32), GLA_CHUNK) for t in (q, k, v, log_g))
    mask = jnp.tril(jnp.ones((GLA_CHUNK, GLA_CHUNK), bool))[None, :, :, None, None]

    def step(S, inp):
        qi, ki, vi, gi = inp
        b = jnp.cumsum(gi, axis=1)
        b_last = b[:, -1]
        diff = b[:, :, None] - b[:, None, :]
        decay = jnp.exp(jnp.where(mask, diff, -jnp.inf))
        att = jnp.einsum('bthk,bshk,btshk->bhts', qi, ki, decay)
        o = jnp.einsum('bhts,bshv->bthv', att, vi) + jnp.einsum('bthk,bhkv->bthv', qi * jnp.exp(b), S)
        S_new = jnp.exp(b_last)[..., None] * S + jnp.einsum(
            'bshk,bshv->bhkv', ki * jnp.exp(b_last[:, None] - b), vi)
        return S_new, o

    S_fin, o = lax.scan(step, s0, (qc, kc, vc, gc))
    return _unchunks(o).astype(out_dtype), S_fin

def _gla_state(k, v, log_g):
    b = jnp.cumsum(log_g.astype(jnp.float32), axis=1)
    return jnp.einsum('blhk,blhv->bhkv', k.astype(jnp.float32) * jnp.exp(b[:, -1:] - b), v.astype(jnp.float32))

def _ssd_scan(x, bm, cm, a, s0):
    out_dtype = bm.dtype
    f32 = jnp.float32
    xc, bc, cc, ac = (_chunks(t.astype(f32), SSM_CHUNK) for t in (x, bm, cm, a))
    mask = jnp.tril(jnp.ones((SSM_CHUNK, SSM_CHUNK), bool))[None, :, :, None, None]

    def step(S, inp):
        xi, bi, ci, ai = inp
        cum = jnp.cumsum(ai, axis=1)
        seg = cum[:, :, None] - cum[:, None, :]
        Lm = jnp.exp(jnp.where(mask, seg, -jnp.inf))
        cb = jnp.einsum('btgn,bsgn->btsg', ci, bi)
        y = jnp.einsum('btsg,btsge,bsgep->btgep', cb, Lm, xi)
        y = y + jnp.einsum('btgn,bgenp->btgep', ci, S) * jnp.exp(cum)[..., None]
        S_new = jnp.exp(cum[:, -1])[..., None, None] * S + jnp.einsum(
            'bsgn,bsge,bsgep->bgenp', bi, jnp.exp(cum[:, -1:] - cum), xi)
        return S_new, y

    S_fin, y = lax.scan(step, s0, (xc, bc, cc, ac))
    return _unchunks(y).astype(out_dtype), S_fin

def _ssd_state(x, bm, a):
    cum = jnp.cumsum(a.astype(jnp.float32), axis=1)
    return jnp.einsum('blgn,blge,blgep->bgenp', bm.astype(jnp.float32),
                      jnp.exp(cum[:, -1:] - cum), x.astype(jnp.float32))

def _flip(t):
    return jnp.flip(t, axis=1)

def _bidir(scan_fn, fwd_in, bwd_in, s_f, s_b):
    o_f, st_f = scan_fn(*fwd_in, s_f)
    o_b, st_b = scan_fn(*[_flip(t) for t in bwd_in], s_b)
    return o_f + _flip(o_b), st_f, st_b

def _gla_features(q, k, v, lr_f, lr_b, lp):
    Bn, L, _ = q.shape
    heads = lambda t, d: t.reshape(Bn, L, GLA_HEADS, d)
    q = heads(q, GLA_DK) * (GLA_DK ** -0.5)
    k = heads(k, GLA_DK)
    v = heads(v, GLA_DV)

    def log_gate(lr, up, bias):
        pre = (lr @ up + bias).astype(jnp.float32)
        return heads(jax.nn.log_sigmoid(pre) / GLA_TAU, GLA_DK)

    return (q, k, v, log_gate(lr_f, lp['gla_up_f'], lp['gla_bias_f']),
            log_gate(lr_b, lp['gla_up_b'], lp['gla_bias_b']))

def _ssm_features(xs, bm, cm, dt_f, dt_b, lp, conv_fn):
    xbc = jax.nn.silu(conv_fn(jnp.concatenate([xs, bm, cm], axis=-1), lp['conv_w'], lp['conv_b']))
    xs, bm, cm = jnp.split(xbc, [SSM_INNER, SSM_INNER + SSM_BC], axis=-1)
    Bn, L, _ = xs.shape
    xh = xs.reshape(Bn, L, SSM_GROUPS, SSM_HPG, SSM_HEADDIM)
    bm = bm.reshape(Bn, L, SSM_GROUPS, SSM_STATE)
    cm = cm.reshape(Bn, L, SSM_GROUPS, SSM_STATE)

    def direction(dt_raw, dt_bias, a_log):
        dt = jax.nn.softplus((dt_raw + dt_bias).astype(jnp.float32)).reshape(Bn, L, SSM_GROUPS, SSM_HPG)
        a = -jnp.exp(a_log.astype(jnp.float32)).reshape(SSM_GROUPS, SSM_HPG) * dt
        return xh * dt[..., None], a

    return (xh, bm, cm, direction(dt_f, lp['dt_bias_f'], lp['a_log_f']),
            direction(dt_b, lp['dt_bias_b'], lp['a_log_b']))

def _mixer(parts, lp, init, conv_fn):
    q, k, v, r, lr_f, lr_b, z, xs, bm, cm, dt_f, dt_b, gate_a, gate_b = parts
    Bn, L, _ = q.shape
    gq, gk, gv, lg_f, lg_b = _gla_features(q, k, v, lr_f, lr_b, lp)
    o_a, st_af, st_ab = _bidir(_gla_scan, (gq, gk, gv, lg_f), (gq, gk, gv, lg_b), init[0], init[1])
    o_a = rms_norm_3(o_a, lp['gla_norm_w']) * jax.nn.silu(r).reshape(Bn, L, GLA_HEADS, GLA_DV)
    y_a = o_a.reshape(Bn, L, GLA_V) @ lp['w_pa']
    xh, sb, sc, (x_f, a_f), (x_b, a_b) = _ssm_features(xs, bm, cm, dt_f, dt_b, lp, conv_fn)
    o_b, st_bf, st_bb = _bidir(_ssd_scan, (x_f, sb, sc, a_f), (x_b, sb, sc, a_b), init[2], init[3])
    o_b = o_b + lp['d_skip'].reshape(SSM_GROUPS, SSM_HPG, 1) * xh
    o_b = o_b.reshape(Bn, L, SSM_INNER) * jax.nn.silu(z)
    o_b = rms_norm_3(o_b.reshape(Bn, L, SSM_GROUPS, SSM_INNER // SSM_GROUPS),
                   lp['ssm_norm_w'].reshape(SSM_GROUPS, SSM_INNER // SSM_GROUPS)).reshape(Bn, L, SSM_INNER)
    y_b = o_b @ lp['w_pb']
    merged = jax.nn.sigmoid(gate_a) * y_a + jax.nn.sigmoid(gate_b) * y_b
    return merged @ lp['w_out'], (st_af, st_ab, st_bf, st_bb)

def _context_states(parts, lp):
    k, v, lr_f, lr_b = parts[1], parts[2], parts[4], parts[5]
    xs, bm, cm, dt_f, dt_b = parts[7], parts[8], parts[9], parts[10], parts[11]
    _, gk, gv, lg_f, lg_b = _gla_features(parts[0], k, v, lr_f, lr_b, lp)
    _, sb, _, (x_f, a_f), (x_b, a_b) = _ssm_features(xs, bm, cm, dt_f, dt_b, lp, _seq_conv)
    return (_gla_state(gk, gv, lg_f), _gla_state(_flip(gk), _flip(gv), _flip(lg_b)),
            _ssd_state(x_f, sb, a_f), _ssd_state(_flip(x_b), _flip(sb), _flip(a_b)))

def _zero_states(Bn):
    f32 = jnp.float32
    g = jnp.zeros((Bn, GLA_HEADS, GLA_DK, GLA_DV), f32)
    s = jnp.zeros((Bn, SSM_GROUPS, SSM_HPG, SSM_STATE, SSM_HEADDIM), f32)
    return (g, g, s, s)

def _swiglu(h, w_gate, w_up, w_down):
    return (jax.nn.silu(h @ w_gate) * (h @ w_up)) @ w_down

def third_inputs(seed: int = 0) -> dict:
    key = jax.random.key(seed)
    ks = iter(jax.random.split(key, 40))
    nrm = lambda shape, s: jax.random.normal(next(ks), shape, jnp.float32) * s
    L_ = DEPTH
    dt = jnp.exp(jax.random.uniform(next(ks), (2, L_, SSM_HEADS), jnp.float32,
                                    np.log(1e-3), np.log(1e-1)))
    dt_bias = dt + jnp.log(-jnp.expm1(-dt))
    a_log = jnp.log(jax.random.uniform(next(ks), (2, L_, SSM_HEADS), jnp.float32, 1.0, 16.0))
    return {
        'x': nrm((BATCH, SEQ, D_MODEL), 1.0),
        'c': nrm((BATCH, D_MODEL), 1.0),
        'ctx': nrm((BATCH, CTX_LEN, D_MODEL), 1.0),
        'c_ctx': nrm((D_MODEL,), 1.0),
        'w_ada': nrm((L_, D_MODEL, 6 * D_MODEL), 0.02),
        'b_ada': nrm((L_, 6 * D_MODEL), 0.01),
        'norm1_w': 1.0 + nrm((L_, D_MODEL), 0.02),
        'w_in': nrm((L_, D_MODEL, D_IN_3), D_MODEL ** -0.5),
        'gla_up_f': nrm((L_, GLA_RANK, GLA_QK), GLA_RANK ** -0.5),
        'gla_bias_f': nrm((L_, GLA_QK), 0.1),
        'gla_up_b': nrm((L_, GLA_RANK, GLA_QK), GLA_RANK ** -0.5),
        'gla_bias_b': nrm((L_, GLA_QK), 0.1),
        'gla_norm_w': 1.0 + nrm((L_, GLA_DV), 0.02),
        'conv_w': nrm((L_, SSM_CONV, SSM_CONV_DIM), SSM_CONV ** -0.5),
        'conv_b': nrm((L_, SSM_CONV_DIM), 0.02),
        'dt_bias_f': dt_bias[0],
        'dt_bias_b': dt_bias[1],
        'a_log_f': a_log[0],
        'a_log_b': a_log[1],
        'd_skip': 1.0 + nrm((L_, SSM_HEADS), 0.02),
        'ssm_norm_w': 1.0 + nrm((L_, SSM_INNER), 0.02),
        'w_pa': nrm((L_, GLA_V, D_MODEL), GLA_V ** -0.5),
        'w_pb': nrm((L_, SSM_INNER, D_MODEL), SSM_INNER ** -0.5),
        'w_out': nrm((L_, D_MODEL, D_MODEL), D_MODEL ** -0.5),
        'norm2_w': 1.0 + nrm((L_, D_MODEL), 0.02),
        'w_gate': nrm((L_, D_MODEL, D_FF_3), D_MODEL ** -0.5),
        'w_up': nrm((L_, D_MODEL, D_FF_3), D_MODEL ** -0.5),
        'w_down': nrm((L_, D_FF_3, D_MODEL), D_FF_3 ** -0.5),
        'final_norm_w': 1.0 + nrm((D_MODEL,), 0.02),
    }

def third_block(x, c, ctx, c_ctx, w_ada, b_ada, norm1_w, w_in, gla_up_f, gla_bias_f, gla_up_b, gla_bias_b,
              gla_norm_w, conv_w, conv_b, dt_bias_f, dt_bias_b, a_log_f, a_log_b, d_skip, ssm_norm_w,
              w_pa, w_pb, w_out, norm2_w, w_gate, w_up, w_down, final_norm_w):
    rows = x.shape[1] // GRID_W
    latent_conv = functools.partial(_row_conv, rows=rows)
    h_lat, h_ctx = x, ctx
    for layer in range(DEPTH):
        lp = {
            'gla_up_f': gla_up_f[layer], 'gla_bias_f': gla_bias_f[layer],
            'gla_up_b': gla_up_b[layer], 'gla_bias_b': gla_bias_b[layer],
            'gla_norm_w': gla_norm_w[layer], 'conv_w': conv_w[layer], 'conv_b': conv_b[layer],
            'dt_bias_f': dt_bias_f[layer], 'dt_bias_b': dt_bias_b[layer],
            'a_log_f': a_log_f[layer], 'a_log_b': a_log_b[layer], 'd_skip': d_skip[layer],
            'ssm_norm_w': ssm_norm_w[layer], 'w_pa': w_pa[layer], 'w_pb': w_pb[layer], 'w_out': w_out[layer],
        }
        ada = jax.nn.silu(c)[:, None, :] @ w_ada[layer] + b_ada[layer]
        sh1, sc1, g1, sh2, sc2, g2 = jnp.split(ada, 6, axis=-1)
        ada_c = jax.nn.silu(c_ctx) @ w_ada[layer] + b_ada[layer]
        csh1, csc1, cg1, csh2, csc2, cg2 = jnp.split(ada_c, 6, axis=-1)

        parts_c = _split_in(modulate(rms_norm_3(h_ctx, norm1_w[layer]), csh1, csc1) @ w_in[layer])
        if layer == DEPTH - 1:
            states = _context_states(parts_c, lp)
        else:
            mix_c, states = _mixer(parts_c, lp, _zero_states(h_ctx.shape[0]), _seq_conv)
            h_ctx = h_ctx + cg1 * mix_c
            h_ctx = h_ctx + cg2 * _swiglu(modulate(rms_norm_3(h_ctx, norm2_w[layer]), csh2, csc2),
                                          w_gate[layer], w_up[layer], w_down[layer])

        parts = _split_in(modulate(rms_norm_3(h_lat, norm1_w[layer]), sh1, sc1) @ w_in[layer])
        mix, _ = _mixer(parts, lp, states, latent_conv)
        h_lat = h_lat + g1 * mix
        h_lat = h_lat + g2 * _swiglu(modulate(rms_norm_3(h_lat, norm2_w[layer]), sh2, sc2),
                                     w_gate[layer], w_up[layer], w_down[layer])
    return rms_norm_3(h_lat, final_norm_w)


_first_inputs_3 = third_inputs


def third_inputs(seed=0):
    import zlib

    import numpy as np

    out = dict(_first_inputs_3(seed))
    spreads = {}
    factors = {'ctx': 3.033,
     'b_ada': 4.475,
     'norm1_w': 7.876,
     'gla_up_f': 3.213,
     'gla_bias_f': 8.0,
     'gla_bias_b': 8.0,
     'gla_norm_w': 8.0,
     'conv_b': 8.0,
     'd_skip': 8.0,
     'ssm_norm_w': 8.0,
     'norm2_w': 7.309,
     'final_norm_w': 2.784}
    for name, (base, spread) in spreads.items():
        noise = np.random.default_rng([zlib.crc32(name.encode()), seed]).standard_normal(out[name].shape)
        drawn = base * np.exp(spread * noise) if base else spread * noise
        out[name] = __import__('jax').numpy.asarray(drawn.astype(out[name].dtype))
    for name, factor in factors.items():
        out[name] = (out[name] * factor).astype(out[name].dtype)
    return out


_narrow_inputs_3 = third_inputs


def third_inputs(seed=0):

    out = dict(_narrow_inputs_3(seed))
    wider = {'conv_b': 12.0, 'd_skip': 12.0, 'ssm_norm_w': 12.0, 'final_norm_w': 3.03}
    for name, times in wider.items():
        mean = out[name].mean()
        out[name] = (mean + times * (out[name] - mean)).astype(out[name].dtype)
    return out


def setup_inputs(seed=0):
    out = dict(first_inputs(seed))
    for name, value in second_inputs(seed + 1).items():
        if name != "x":
            out[name + "_2"] = value
    for name, value in third_inputs(seed + 2).items():
        if name != "x":
            out[name + "_3"] = value
    return out


def reference(
    x, mix_norm, w_in, sc_conv, sc_out, pool_w, pool_scale, conf_conv, conf_conv_b, conf_ln_g,
    conf_ln_b, conf_out, q_norm, k_norm, lambda_q1, lambda_k1, lambda_q2, lambda_k2, diff_subln,
    diff_out, w_o, ffn_norm, ffn_up, ffn_conv, ffn_down, c_2, w_ada_2, b_ada_2, norm1_w_2,
    w_in_2, conv_gdn_2, a_log_2, dt_bias_2, onorm_gdn_2, w_branch_gdn_2, mu_rwkv_2, w0_2, w2_2,
    a0_2, a2_2, g2_2, k_k_2, k_a_2, r_k_2, lnx_w_2, lnx_b_2, w_branch_rwkv_2, w_out_2,
    norm2_w_2, w_ffn_in_2, conv_ffn_2, w_ffn_out_2, norm_f_w_2, c_3, ctx_3, c_ctx_3, w_ada_3,
    b_ada_3, norm1_w_3, w_in_3, gla_up_f_3, gla_bias_f_3, gla_up_b_3, gla_bias_b_3,
    gla_norm_w_3, conv_w_3, conv_b_3, dt_bias_f_3, dt_bias_b_3, a_log_f_3, a_log_b_3, d_skip_3,
    ssm_norm_w_3, w_pa_3, w_pb_3, w_out_3, norm2_w_3, w_gate_3, w_up_3, w_down_3,
    final_norm_w_3,
):
    x = first_block(
        x, mix_norm, w_in, sc_conv, sc_out, pool_w, pool_scale, conf_conv, conf_conv_b,
        conf_ln_g, conf_ln_b, conf_out, q_norm, k_norm, lambda_q1, lambda_k1, lambda_q2,
        lambda_k2, diff_subln, diff_out, w_o, ffn_norm, ffn_up, ffn_conv, ffn_down,
    )
    x = second_block(
        x, c_2, w_ada_2, b_ada_2, norm1_w_2, w_in_2, conv_gdn_2, a_log_2, dt_bias_2,
        onorm_gdn_2, w_branch_gdn_2, mu_rwkv_2, w0_2, w2_2, a0_2, a2_2, g2_2, k_k_2, k_a_2,
        r_k_2, lnx_w_2, lnx_b_2, w_branch_rwkv_2, w_out_2, norm2_w_2, w_ffn_in_2, conv_ffn_2,
        w_ffn_out_2, norm_f_w_2,
    )
    return third_block(
        x, c_3, ctx_3, c_ctx_3, w_ada_3, b_ada_3, norm1_w_3, w_in_3, gla_up_f_3, gla_bias_f_3,
        gla_up_b_3, gla_bias_b_3, gla_norm_w_3, conv_w_3, conv_b_3, dt_bias_f_3, dt_bias_b_3,
        a_log_f_3, a_log_b_3, d_skip_3, ssm_norm_w_3, w_pa_3, w_pb_3, w_out_3, norm2_w_3,
        w_gate_3, w_up_3, w_down_3, final_norm_w_3,
    )


_drawn_inputs = setup_inputs


def setup_inputs(seed=0):
    import zlib

    import numpy as np

    out = dict(_drawn_inputs(seed))
    spreads = {}
    factors = {'gla_norm_w_3': 7.984,
     'a_log_f_3': 15.733,
     'd_skip_3': 64.0,
     'conv_b_3': 3.526,
     'dt_bias_f_3': 6.243,
     'dt_bias_b_3': 5.582,
     'a_log_b_3': 6.359,
     'ssm_norm_w_3': 3.505,
     'norm2_w_3': 4.302}
    for name, (base, spread) in spreads.items():
        noise = np.random.default_rng([zlib.crc32(name.encode()), seed]).standard_normal(out[name].shape)
        drawn = base * np.exp(spread * noise) if base else spread * noise
        out[name] = __import__('jax').numpy.asarray(drawn.astype(out[name].dtype))
    for name, factor in factors.items():
        out[name] = (out[name] * factor).astype(out[name].dtype)
    return out
```

```python
import math
from contextlib import ExitStack

import numpy as np

import concourse.bass as bass
from concourse import mybir

F32 = mybir.dt.float32
I32 = mybir.dt.int32
ALU = mybir.AluOpType
ACT = mybir.ActivationFunctionType
AX_X = mybir.AxisListType.X

P = 128
T = 512
D = 1024
DT = D // P
WCOLS = 256
EPS = 1e-6
D_FF = 2816
FT = D_FF // P
CTX = 256
C64 = 64
HN = 64
NC64 = T // C64
GATE_ROWS = 4096
LAM_INIT = 0.8 - 0.6 * math.exp(0.0)


class Steps:

    def __init__(self, eng, sem):
        self.eng, self.sem, self.n = eng, sem, 0

    def mark(self, ins):
        ins.then_inc(self.sem, 1)
        self.n += 1

    def wait(self):
        self.eng.wait_ge(self.sem, self.n)

    def __call__(self, ins):
        self.mark(ins)
        self.wait()


class Scope:

    def __init__(self, nc, ctx, name):
        self.nc, self.ctx, self.name = nc, ctx, name
        self.sems = []
        ctx.callback(self.close)

    def close(self):
        for sem in self.sems:
            self.nc.gpsimd.sem_clear(sem)
            self.nc.release_semaphore(sem)

    def sb(self, name, shape, dt=F32):
        return self.ctx.enter_context(self.nc.sbuf_tensor(f"{self.name}_{name}", shape, dt))

    def ps(self, name, shape):
        return self.ctx.enter_context(self.nc.psum_tensor(f"{self.name}_{name}", shape, F32))

    def sem(self, name):
        self.sems.append(self.nc.alloc_semaphore(f"{self.name}_{name}"))
        return self.sems[-1]


class Core:

    def __init__(self, nc, ctx, dram, vec_at, vec_cols):
        def sb(name, shape, dt=F32):
            return ctx.enter_context(nc.sbuf_tensor(name, shape, dt))

        self.dram, self.vec_at, self.count = dram, vec_at, 0
        self.vec = sb("vec", [P, vec_cols])
        self.ident = sb("ident", [P, P])
        self.ones = sb("ones", [P, P])
        self.halves = sb("halves", [P, P])
        self.x = sb("x_res", [P, DT, T])
        self.h = sb("h_norm", [P, DT, T])

    def v(self, name, k=0, n=1):
        at = self.vec_at[name] + k
        return self.vec[:, at:at + n]

    def scope(self, nc, ctx, name):
        self.count += 1
        return Scope(nc, ctx, f"{name}{self.count}")


def rows(ap):
    return ap.rearrange("(j p) t -> p j t", p=P)




def stage_start(nc, core):
    with ExitStack() as ctx:
        s = core.scope(nc, ctx, "start")
        loaded, made = s.sem("loaded"), s.sem("made")
        with nc.Block() as block:
            @block.sync
            def _(sp):
                sp.dma_start(core.vec[:], core.dram["vecs"]).then_inc(loaded, 16)
                sp.dma_start(core.x[:], rows(core.dram["xT"])).then_inc(loaded, 16)
                sp.wait_ge(loaded, 32)

            @block.gpsimd
            def _(pool):
                done = Steps(pool, made)
                done(nc.gpsimd.memset(core.ones[:], 1.0))
                done(nc.gpsimd.memset(core.halves[:], 0.0))
                done(nc.gpsimd.memset(core.halves[0:64, 0:64], 1.0))
                done(nc.gpsimd.memset(core.halves[64:128, 64:128], 1.0))
                done(nc.gpsimd.memset(core.ident[:], 0.0))
                done(nc.gpsimd.affine_select(out=core.ident[:], in_=core.ident[:], pattern=[[-1, P]],
                                             compare_op=ALU.not_equal, fill=1.0, base=0, channel_multiplier=1))


def stage_rstd(nc, core, src, dst, per, ones, count, eps, toks=T):
    n = src.shape[1]
    with ExitStack() as ctx:
        s = core.scope(nc, ctx, "rstd")
        sq = s.sb("sq", [P, n, toks])
        acc = s.ps("acc", [P, 4, 512])
        squared, summed, freed, inverted, step = (s.sem(x) for x in
                                                  ("squared", "summed", "freed", "inverted", "step"))
        with nc.Block() as block:
            @block.scalar
            def _(act):
                for k in range(n):
                    nc.scalar.activation(sq[:, k], src[:, k], ACT.Square).then_inc(squared, 1)
                for g in range(n // per):
                    act.wait_ge(inverted, g + 1)
                    nc.scalar.activation(dst[:, g], dst[:, g], ACT.Sqrt).then_inc(step, 1)

            @block.tensor
            def _(pe):
                for g in range(n // per):
                    if g >= 4:
                        pe.wait_ge(freed, g - 3)
                    for k in range(per):
                        pe.wait_ge(squared, g * per + k + 1)
                        last = nc.tensor.matmul(acc[:, g % 4, :toks], ones[:], sq[:, g * per + k],
                                                start=k == 0, stop=k == per - 1)
                    last.then_inc(summed, 1)

            @block.vector
            def _(dve):
                for g in range(n // per):
                    dve.wait_ge(summed, g + 1)
                    nc.vector.tensor_scalar(dst[:, g], acc[:, g % 4, :toks], 1.0 / count, eps,
                                            ALU.mult, ALU.add).then_inc(freed, 1)
                    dve.wait_ge(freed, g + 1)
                    nc.vector.reciprocal(dst[:, g], dst[:, g]).then_inc(inverted, 1)


def stage_centre(nc, core, src, per, ones, count):
    n = src.shape[1]
    with ExitStack() as ctx:
        s = core.scope(nc, ctx, "centre")
        mean = s.sb("mean", [P, 4, T])
        acc = s.ps("acc", [P, 4, 512])
        summed, freed, done = s.sem("summed"), s.sem("freed"), s.sem("done")
        with nc.Block() as block:
            @block.tensor
            def _(pe):
                for g in range(n // per):
                    if g >= 4:
                        pe.wait_ge(freed, g - 3)
                    for k in range(per):
                        last = nc.tensor.matmul(acc[:, g % 4, :], ones[:], src[:, g * per + k],
                                                start=k == 0, stop=k == per - 1)
                    last.then_inc(summed, 1)

            @block.vector
            def _(dve):
                for g in range(n // per):
                    dve.wait_ge(summed, g + 1)
                    nc.vector.tensor_scalar(mean[:, g % 4], acc[:, g % 4, :], 1.0 / count, None,
                                            ALU.mult).then_inc(freed, 1)
                    dve.wait_ge(freed, g + 1)
                    for k in range(per):
                        nc.vector.tensor_tensor(src[:, g * per + k], src[:, g * per + k], mean[:, g % 4],
                                                ALU.subtract).then_inc(done, 1)


def stage_norm(nc, core, src, dst, gain, mod=None, toks=T):
    with ExitStack() as ctx:
        s = core.scope(nc, ctx, "norm")
        rstd = s.sb("rstd", [P, 1, toks])
        stage_rstd(nc, core, src, rstd, DT, core.ones, D, EPS, toks)
        full = s.sb("full", [P, DT])
        ready, scaled = s.sem("ready"), s.sem("scaled")
        with nc.Block() as block:
            @block.vector
            def _(dve):
                g = core.v(gain, 0, DT)
                if mod is not None:
                    nc.vector.scalar_tensor_tensor(out=full[:], in0=mod[0], scalar=1.0, in1=g,
                                                   op0=ALU.add, op1=ALU.mult).then_inc(ready, 1)
                    dve.wait_ge(ready, 1)
                    g = full[:]
                for k in range(DT):
                    nc.vector.scalar_tensor_tensor(out=dst[:, k], in0=src[:, k], scalar=g[:, k:k + 1],
                                                   in1=rstd[:, 0], op0=ALU.mult,
                                                   op1=ALU.mult).then_inc(scaled, 1)

            @block.scalar
            def _(act):
                if mod is not None:
                    for k in range(DT):
                        act.wait_ge(scaled, k + 1)
                        nc.scalar.activation(dst[:, k], dst[:, k], ACT.Identity, bias=mod[1][:, k:k + 1])


def stage_rows(nc, core, segments, tails=(), toks=T, rhs=None):
    rhs = core.h if rhs is None else rhs
    with ExitStack() as ctx:
        s = core.scope(nc, ctx, "rows")
        w = s.sb("w", [P, 2, DT, WCOLS])
        out = s.sb("out", [P, 2, 2, toks])
        tail_w = s.sb("tail_w", [P, DT, P])
        tail_out = s.sb("tail_out", [P, toks])
        acc = s.ps("acc", [P, 4, 512])
        tail_acc = s.ps("tail_acc", [P, 512])
        loaded = [s.sem(f"loaded{n}") for n in range(2)]
        product = [s.sem(f"product{n}") for n in range(2)]
        copied_act = [s.sem(f"copied_act{n}") for n in range(2)]
        copied_dve = [s.sem(f"copied_dve{n}") for n in range(2)]
        stored = [s.sem(f"stored{n}") for n in range(2)]
        tail_loaded, tail_done, tail_copied, tail_stored = (
            s.sem(x) for x in ("tail_loaded", "tail_done", "tail_copied", "tail_stored"))
        turns = [seg[0].shape[0] // 2 for seg in segments]
        base = [sum(turns[:n]) for n in range(len(turns))]
        with nc.Block() as block:
            @block.sync
            def _(sp):
                for (wt, _, _), at, n in zip(segments, base, turns):
                    with sp.Fori(0, n) as i:
                        for k in range(2):
                            sp.wait_ge(product[k], (i + at) * 2)
                            sp.dma_start(w[:, k], wt[bass.ds(i * 2 + k, 1)].rearrange(
                                "a p k n -> p (a k) n")).then_inc(loaded[k], 16)
                for n, (wt, _) in enumerate(tails):
                    if n:
                        sp.wait_ge(tail_done, n)
                    sp.dma_start(tail_w[:, :, :wt.shape[2]], wt).then_inc(tail_loaded, 16)

            @block.tensor
            def _(pe):
                for (_, _, _), at, n in zip(segments, base, turns):
                    with pe.Fori(0, n) as i:
                        for k in range(2):
                            pe.wait_ge(loaded[k], (i + at) * 16 + 16)
                            pe.wait_ge(copied_act[k], i + at)
                            pe.wait_ge(copied_dve[k], i + at)
                            for j in range(2):
                                for c in range(DT):
                                    last = nc.tensor.matmul(acc[:, 2 * k + j, :toks],
                                                            w[:, k, c, j * P:(j + 1) * P], rhs[:, c],
                                                            start=c == 0, stop=c == DT - 1)
                                last.then_inc(product[k], 1)
                for n, (wt, _) in enumerate(tails):
                    pe.wait_ge(tail_loaded, 16 * (n + 1))
                    if n:
                        pe.wait_ge(tail_copied, n)
                    for c in range(DT):
                        last = nc.tensor.matmul(tail_acc[:wt.shape[2], :toks], tail_w[:, c, :wt.shape[2]],
                                                rhs[:, c], start=c == 0, stop=c == DT - 1)
                    last.then_inc(tail_done, 1)

            @block.scalar
            def _(act):
                for (_, dst, func), at, n in zip(segments, base, turns):
                    with act.Fori(0, n) as i:
                        for k in range(2):
                            act.wait_ge(product[k], (i + at) * 2 + 1)
                            act.wait_ge(stored[k], (i + at) * 16)
                            nc.scalar.activation(out[:, k, 0], acc[:, 2 * k, :toks],
                                                 func).then_inc(copied_act[k], 1)
                            if func != ACT.Copy:
                                act.wait_ge(product[k], (i + at) * 2 + 2)
                                nc.scalar.activation(out[:, k, 1], acc[:, 2 * k + 1, :toks],
                                                     func).then_inc(copied_dve[k], 1)
                            act.wait_ge(copied_act[k], i + at + 1)
                            act.wait_ge(copied_dve[k], i + at + 1)
                            act.dma_start(rows(dst[bass.ds(i * 2 * WCOLS + k * WCOLS, WCOLS), :]),
                                          out[:, k]).then_inc(stored[k], 16)
                for n, (wt, dst) in enumerate(tails):
                    act.wait_ge(tail_done, n + 1)
                    if n:
                        act.wait_ge(tail_stored, 16 * n)
                    nc.scalar.activation(tail_out[:wt.shape[2]], tail_acc[:wt.shape[2], :toks],
                                         ACT.Copy).then_inc(tail_copied, 1)
                    act.wait_ge(tail_copied, n + 1)
                    act.dma_start(dst, tail_out[:wt.shape[2]]).then_inc(tail_stored, 16)
                if tails:
                    act.wait_ge(tail_stored, 16 * len(tails))
                for k in range(2):
                    act.wait_ge(stored[k], 16 * sum(turns))

            @block.vector
            def _(dve):
                for (_, _, func), at, n in zip(segments, base, turns):
                    if func != ACT.Copy:
                        continue
                    with dve.Fori(0, n) as i:
                        for k in range(2):
                            dve.wait_ge(product[k], (i + at) * 2 + 2)
                            dve.wait_ge(stored[k], (i + at) * 16)
                            nc.vector.tensor_copy(out[:, k, 1],
                                                  acc[:, 2 * k + 1, :toks]).then_inc(copied_dve[k], 1)


def stage_tokens(nc, core, wt, dst, toks=T, rhs=None):
    rhs = core.h if rhs is None else rhs
    chunks = wt.shape[0]
    with ExitStack() as ctx:
        s = core.scope(nc, ctx, "tokens")
        w = s.sb("w", [P, 2, DT, 512])
        acc = s.ps("acc", [P, 4, 512])
        loaded, product, copied = s.sem("loaded"), s.sem("product"), s.sem("copied")
        with nc.Block() as block:
            @block.sync
            def _(sp):
                for c in range(chunks):
                    sp.dma_start(w[:, c % 2], wt[c]).then_inc(loaded, 16)

            @block.tensor
            def _(pe):
                for n in range(chunks * (toks // P)):
                    c, t = n // (toks // P), n % (toks // P)
                    pe.wait_ge(loaded, 16 * (c + 1) if chunks == 1 else 16 * chunks)
                    if n >= 4:
                        pe.wait_ge(copied, n - 3)
                    for k in range(DT):
                        last = nc.tensor.matmul(acc[:, n % 4], rhs[:, k, t * P:(t + 1) * P], w[:, c % 2, k],
                                                start=k == 0, stop=k == DT - 1)
                    last.then_inc(product, 1)

            @block.vector
            def _(dve):
                for n in range(chunks * (toks // P)):
                    c, t = n // (toks // P), n % (toks // P)
                    dve.wait_ge(product, n + 1)
                    nc.vector.tensor_copy(dst[:, t, c * 512:(c + 1) * 512], acc[:, n % 4]).then_inc(copied, 1)


def stage_project(nc, core, wt, y, kt, dst, gates=None, first=False, scale=None, groups=False):
    with ExitStack() as ctx:
        s = core.scope(nc, ctx, "project")
        w = s.sb("w", [P, 2, kt, P])
        gate = s.sb("gate", [P, DT, T]) if gates is not None else None
        part = s.sb("part", [P, 2, T])
        acc = s.ps("acc", [P, 2, 512])
        gate_loaded, used, product, freed, step = (
            s.sem(x) for x in ("gate_loaded", "used", "product", "freed", "step"))
        loaded = [s.sem(f"loaded{n}") for n in range(2)]
        with nc.Block() as block:
            @block.sync
            def _(sp):
                for m in range(DT):
                    if m >= 2:
                        sp.wait_ge(product, m - 1)
                    sp.dma_start(w[:, m % 2], wt[m]).then_inc(loaded[m % 2], 16)
                    if m == 0 and gates is not None:
                        sp.dma_start(gate[:], rows(gates)).then_inc(gate_loaded, 16)

            @block.tensor
            def _(pe):
                for m in range(DT):
                    pe.wait_ge(loaded[m % 2], 16 * (m // 2 + 1))
                    if m >= 2:
                        pe.wait_ge(freed, m - 1)
                    for k in range(kt):
                        last = nc.tensor.matmul(acc[:, m % 2], w[:, m % 2, k], y[:, m // 2 if groups else k],
                                                start=k == 0, stop=k == kt - 1)
                    last.then_inc(product, 1)

            @block.vector
            def _(dve):
                for m in range(DT):
                    by = 1.0 if scale is None else scale[:, m:m + 1]
                    dve.wait_ge(product, m + 1)
                    if gates is None:
                        nc.vector.scalar_tensor_tensor(out=dst[:, m], in0=acc[:, m % 2], scalar=by, in1=dst[:, m],
                                                       op0=ALU.mult, op1=ALU.add).then_inc(freed, 1)
                        continue
                    if m == 0:
                        dve.wait_ge(gate_loaded, 16)
                    to = dst[:, m] if first else part[:, m % 2]
                    nc.vector.scalar_tensor_tensor(out=to, in0=acc[:, m % 2], scalar=by, in1=gate[:, m],
                                                   op0=ALU.mult, op1=ALU.mult).then_inc(freed, 1)
                    if not first:
                        dve.wait_ge(freed, m + 1)
                        nc.vector.tensor_tensor(dst[:, m], dst[:, m], part[:, m % 2], ALU.add).then_inc(step, 1)


def stage_ffn(nc, core, up, down, conv=None, conv_up=False, scale=None):
    with ExitStack() as ctx:
        s0 = core.scope(nc, ctx, "ffn")
        mid = s0.sb("mid", [P, FT, T])
        with ExitStack() as inner:
            s = core.scope(nc, inner, "up")
            w = s.sb("w", [P, 2, 2, DT, P])
            gate = s.sb("gate", [P, 2, T])
            lift = s.sb("lift", [P, 2, T])
            acc = s.ps("acc", [P, 4, 512])
            loaded = [s.sem(f"loaded{n}") for n in range(2)]
            product = [s.sem(f"product{n}") for n in range(2)]
            tapped = [s.sem(f"tapped{n}") for n in range(2)]
            convolved = [s.sem(f"convolved{n}") for n in range(2)]
            gated = [s.sem(f"gated{n}") for n in range(2)]
            made = [s.sem(f"made{n}") for n in range(2)]
            sides = 2 if conv_up else 1
            kinds = 3 if conv is not None else 0
            with nc.Block() as block:
                @block.sync
                def _(sp):
                    with sp.Fori(0, FT // 2) as i:
                        for k in range(2):
                            sp.wait_ge(product[k], i * 2)
                            sp.dma_start(w[:, k], up[bass.ds(i * 2 + k, 1)].rearrange(
                                "a p g k n -> p (a g) k n")).then_inc(loaded[k], 16)

                @block.tensor
                def _(pe):
                    with pe.Fori(0, FT // 2) as i:
                        for k in range(2):
                            pe.wait_ge(loaded[k], i * 16 + 16)
                            pe.wait_ge(made[k], i)
                            for g in range(2):
                                for c in range(DT):
                                    last = nc.tensor.matmul(acc[:, 2 * k + g], w[:, k, g, c], core.h[:, c],
                                                            start=c == 0, stop=c == DT - 1)
                                last.then_inc(product[k], 1)

                @block.scalar
                def _(act):
                    with act.Fori(0, FT // 2) as i:
                        for k in range(2):
                            act.wait_ge(made[k], i)
                            if conv is None:
                                act.wait_ge(product[k], i * 2 + 1)
                                nc.scalar.activation(gate[:, k], acc[:, 2 * k], ACT.Silu).then_inc(gated[k], 1)
                                continue
                            for g in range(sides):
                                act.wait_ge(product[k], i * 2 + g + 1)
                                tap = conv[:, bass.ds(i * 6 + (3 * k + 2 + g * 3 * FT), 1)]
                                nc.scalar.activation((gate, lift)[g][:, k], acc[:, 2 * k + g], ACT.Copy,
                                                     scale=tap).then_inc(tapped[k], 1)
                            act.wait_ge(convolved[k], i * (2 * sides) + 2)
                            nc.scalar.activation(gate[:, k], gate[:, k], ACT.Silu).then_inc(gated[k], 1)

                @block.vector
                def _(dve):
                    with dve.Fori(0, FT // 2) as i:
                        for k in range(2):
                            if kinds:
                                for g in range(sides):
                                    dve.wait_ge(tapped[k], i * sides + g + 1)
                                    buf = (gate, lift)[g]
                                    for lag in (1, 2):
                                        tap = conv[:, bass.ds(i * 6 + (3 * k + 2 - lag + g * 3 * FT), 1)]
                                        nc.vector.scalar_tensor_tensor(
                                            out=buf[:, k, lag:], in0=acc[:, 2 * k + g, :T - lag], scalar=tap,
                                            in1=buf[:, k, lag:], op0=ALU.mult, op1=ALU.add
                                        ).then_inc(convolved[k], 1)
                                        dve.wait_ge(convolved[k], i * (2 * sides) + (2 * g + lag))
                            dve.wait_ge(product[k], i * 2 + 2)
                            dve.wait_ge(gated[k], i + 1)
                            second = lift[:, k] if conv_up else acc[:, 2 * k + 1]
                            nc.vector.tensor_tensor(mid[:, bass.ds(i * 2 + k, 1), :],
                                                    gate[:, k:k + 1], second.unsqueeze(1),
                                                    ALU.mult).then_inc(made[k], 1)
        stage_project(nc, core, down, mid, FT, core.x, scale=scale)



Z1 = {"b": 0, "c": 512, "x": 1024, "pool": 1536, "conf": 2048, "q": 3072, "k": 3584}


def stage_short_conv(nc, core, z, y):
    with ExitStack() as ctx:
        s = core.scope(nc, ctx, "short")
        part = {n: s.sb(n, [P, 4, T]) for n in "bcx"}
        loaded, step = s.sem("loaded"), s.sem("step")
        with nc.Block() as block:
            @block.sync
            def _(sp):
                for n in "cxb":
                    sp.dma_start(part[n][:], rows(z[Z1[n]:Z1[n] + 512])).then_inc(loaded, 16)

            @block.vector
            def _(dve):
                done = Steps(dve, step)
                prod = part["c"]
                dve.wait_ge(loaded, 48)
                done(nc.vector.tensor_tensor(prod[:], prod[:], part["x"][:], ALU.mult))
                for j in range(4):
                    done.mark(nc.vector.tensor_scalar(y[:, j], prod[:, j], core.v("sc_conv", 3 * j + 2), None,
                                                      ALU.mult))
                done.wait()
                for lag in (1, 2):
                    for j in range(4):
                        done.mark(nc.vector.scalar_tensor_tensor(
                            out=y[:, j, lag:], in0=prod[:, j, :T - lag], scalar=core.v("sc_conv", 3 * j + 2 - lag),
                            in1=y[:, j, lag:], op0=ALU.mult, op1=ALU.add))
                    done.wait()
                done(nc.vector.tensor_tensor(y[:], y[:], part["b"][:], ALU.mult))


def stage_pool(nc, core, z, y):
    with ExitStack() as ctx:
        s = core.scope(nc, ctx, "pool")
        src = s.sb("src", [P, 4, T])
        even = s.sb("even", [P, 4, T])
        odd = s.sb("odd", [P, 4, T])
        inv = s.sb("inv", [P, 4, 16])
        loaded, step = s.sem("loaded"), s.sem("step")
        with nc.Block() as block:
            @block.sync
            def _(sp):
                sp.dma_start(src[:], rows(z[Z1["pool"]:Z1["pool"] + 512])).then_inc(loaded, 16)

            @block.vector
            def _(dve):
                done = Steps(dve, step)
                for g in range(4):
                    for t in range(2 << g):
                        done.mark(nc.vector.memset(inv[:, g, t:t + 1], 1.0 / (t + 1)))
                dve.wait_ge(loaded, 16)
                now = src
                for r in range(4):
                    nxt = even if r % 2 == 0 else odd
                    lag = 1 << r
                    done.mark(nc.vector.tensor_tensor(nxt[:, r:, lag:], now[:, r:, lag:], now[:, r:, :T - lag],
                                                      ALU.add))
                    done(nc.vector.tensor_copy(nxt[:, r:, :lag], now[:, r:, :lag]))
                    w = 2 << r
                    done.mark(nc.vector.scalar_tensor_tensor(out=y[:, r, w:], in0=nxt[:, r, w:], scalar=1.0 / w,
                                                             in1=src[:, r, w:], op0=ALU.mult, op1=ALU.subtract))
                    done(nc.vector.tensor_tensor(y[:, r, :w], nxt[:, r, :w], inv[:, r, :w], ALU.mult))
                    done(nc.vector.tensor_tensor(y[:, r, :w], y[:, r, :w], src[:, r, :w], ALU.subtract))
                    now = nxt


def stage_conformer(nc, core, z, y):
    taps = 31
    with ExitStack() as ctx:
        s = core.scope(nc, ctx, "conf")
        pad = s.sb("pad", [P, 4, taps - 1 + T])
        gate = s.sb("gate", [P, 4, T])
        loaded, sig, glu, step = s.sem("loaded"), s.sem("sig"), s.sem("glu"), s.sem("step")
        diag = s.sb("diag", [P, 4, P])
        acc = s.ps("acc", [P, 4, 512])
        diag_made, conv_done = s.sem("diag_made"), s.sem("conv_done")
        pe_taps = 14
        with nc.Block() as block:
            @block.sync
            def _(sp):
                at = Z1["conf"]
                sp.dma_start(pad[:, :, taps - 1:], rows(z[at:at + 512])).then_inc(loaded, 16)
                sp.dma_start(gate[:], rows(z[at + 512:at + 1024])).then_inc(loaded, 16)

            @block.scalar
            def _(act):
                act.wait_ge(loaded, 32)
                nc.scalar.activation(gate[:], gate[:], ACT.Sigmoid).then_inc(sig, 1)
                for n in range(4 * pe_taps):
                    if n >= 4:
                        act.wait_ge(conv_done, n - 3)
                    nc.scalar.activation(diag[:, n % 4], core.ident[:], ACT.Copy,
                                         scale=core.v("conf_conv", taps * (n // pe_taps) + n % pe_taps)
                                         ).then_inc(diag_made, 1)

            @block.tensor
            def _(pe):
                pe.wait_ge(glu, 1)
                for n in range(4 * pe_taps):
                    j, i = n // pe_taps, n % pe_taps
                    pe.wait_ge(diag_made, n + 1)
                    nc.tensor.matmul(acc[:, j], diag[:, n % 4], pad[:, j, i:i + T],
                                     start=i == 0, stop=i == pe_taps - 1).then_inc(conv_done, 1)

            @block.vector
            def _(dve):
                done = Steps(dve, step)
                done.mark(nc.vector.memset(pad[:, :, :taps - 1], 0.0))
                dve.wait_ge(sig, 1)
                nc.vector.tensor_tensor(pad[:, :, taps - 1:], pad[:, :, taps - 1:], gate[:],
                                        ALU.mult).then_inc(glu, 1)
                dve.wait_ge(glu, 1)
                done.wait()
                for j in range(4):
                    done.mark(nc.vector.tensor_scalar(y[:, j], pad[:, j, taps - 1:],
                                                      core.v("conf_conv", taps * j + taps - 1),
                                                      core.v("conf_conv_b", j), ALU.mult, ALU.add))
                for i in range(pe_taps, taps - 1):
                    done.wait()
                    for j in range(4):
                        done.mark(nc.vector.scalar_tensor_tensor(
                            out=y[:, j], in0=pad[:, j, i:i + T], scalar=core.v("conf_conv", taps * j + i),
                            in1=y[:, j], op0=ALU.mult, op1=ALU.add))
                done.wait()
                dve.wait_ge(conv_done, 4 * pe_taps)
                done(nc.vector.tensor_tensor(y[:], y[:], acc[:], ALU.add))
        stage_centre(nc, core, y, 4, core.ones, 512)
        rstd = gate[:, 0:1]
        stage_rstd(nc, core, y, rstd, 4, core.ones, 512, EPS)
        ready = s.sem("ready")
        with nc.Block() as block:
            @block.vector
            def _(dve):
                for j in range(4):
                    nc.vector.tensor_tensor(y[:, j], y[:, j], rstd[:, 0], ALU.mult).then_inc(ready, 1)

            @block.scalar
            def _(act):
                for j in range(4):
                    act.wait_ge(ready, j + 1)
                    nc.scalar.activation(y[:, j], y[:, j], ACT.Silu, bias=core.v("conf_ln_b", j),
                                         scale=core.v("conf_ln_g", j))


def stage_attention(nc, core, z, v_tok, y):
    with ExitStack() as ctx:
        s = core.scope(nc, ctx, "attn")
        q = s.sb("q", [P, 4, T])
        k = s.sb("k", [P, 4, T])
        rq = s.sb("rq", [P, 4, T])
        rk = s.sb("rk", [P, 4, T])
        loaded = s.sem("loaded")
        with nc.Block() as block:
            @block.sync
            def _(sp):
                sp.dma_start(q[:], rows(z[Z1["q"]:Z1["q"] + 512])).then_inc(loaded, 16)
                sp.dma_start(k[:], rows(z[Z1["k"]:Z1["k"] + 512])).then_inc(loaded, 16)
                sp.wait_ge(loaded, 32)
        stage_rstd(nc, core, q, rq, 1, core.halves, 64, EPS)
        stage_rstd(nc, core, k, rk, 1, core.halves, 64, EPS)
        with ExitStack() as inner:
            s = core.scope(nc, inner, "heads")
            mask = s.sb("mask", [P, P])
            probs = s.sb("probs", [P, 2, 2, T])
            attn = s.sb("attn", [P, 2, T])
            attn_t = s.sb("attn_t", [P, 2, 4, P])
            small = s.sb("small", [P, 2, 8])
            lam = s.sb("lam", [P, 8])
            scores = s.ps("scores", [P, 2, 2, 512])
            turned = s.ps("turned", [P, 2, 4, P])
            acc_o = s.ps("acc_o", [P, 2, 512])
            names = ("q_ready", "k_ready", "masked", "lam_in", "lam_sum", "lam_exp", "scored", "max_ready",
                     "exped", "mixed", "turned_ready", "turned_copied", "out_ready", "out_copied", "step", "made")
            (q_ready, k_ready, masked, lam_in, lam_sum, lam_exp, scored, max_ready, exped, mixed, turned_ready,
             turned_copied, out_ready, out_copied, step, made) = (s.sem(x) for x in names)
            units = [(h, b) for h in range(4) for b in range(4)]
            with nc.Block() as block:
                @block.gpsimd
                def _(pool):
                    nc.gpsimd.memset(mask[:], 0.0).then_inc(made, 1)
                    pool.wait_ge(made, 1)
                    nc.gpsimd.affine_select(out=mask[:], in_=mask[:], pattern=[[-1, P]], compare_op=ALU.is_ge,
                                            fill=-1e30, base=0, channel_multiplier=1).then_inc(made, 1)

                @block.tensor
                def _(pe):
                    pe.wait_ge(lam_in, 1)
                    nc.tensor.matmul(acc_o[:, 0, 0:2], core.ones[0:64, :], lam[0:64, 0:2], start=True,
                                     stop=True).then_inc(lam_sum, 1)
                    pe.wait_ge(q_ready, 4)
                    pe.wait_ge(k_ready, 4)

                    def score(n):
                        h, b = units[n]
                        if n >= 2:
                            pe.wait_ge(exped, 2 * (n - 1))
                        for m in range(2):
                            at = slice(64 * m, 64 * m + 64)
                            nc.tensor.matmul(scores[:, n % 2, m, :(b + 1) * P], q[at, h, b * P:(b + 1) * P],
                                             k[at, h, :(b + 1) * P], start=True, stop=True).then_inc(scored, 1)

                    def mix(n):
                        h, b = units[n]
                        pe.wait_ge(mixed, n + 1)
                        if n >= 2:
                            pe.wait_ge(turned_copied, n - 1)
                        for c in range(b + 1):
                            last = nc.tensor.transpose(turned[:, n % 2, c], attn[:, n % 2, c * P:(c + 1) * P],
                                                       core.ident[:])
                        last.then_inc(turned_ready, 1)
                        pe.wait_ge(turned_copied, n + 1)
                        if n >= 2:
                            pe.wait_ge(out_copied, n - 1)
                        for c in range(b + 1):
                            last = nc.tensor.matmul(acc_o[:, n % 2, :P], v_tok[:, c, h * P:(h + 1) * P],
                                                    attn_t[:, n % 2, c], start=c == 0, stop=c == b)
                        last.then_inc(out_ready, 1)

                    pe.wait_ge(lam_exp, 1)
                    score(0)
                    for n in range(len(units)):
                        if n + 1 < len(units):
                            score(n + 1)
                        mix(n)

                @block.scalar
                def _(act):
                    act.wait_ge(lam_sum, 1)
                    nc.scalar.activation(lam[:, 2:4], acc_o[:, 0, 0:2], ACT.Exp).then_inc(lam_exp, 1)
                    for n, (h, b) in enumerate(units):
                        if n >= 2:
                            act.wait_ge(mixed, n - 1)
                        for m in range(2):
                            act.wait_ge(max_ready, 2 * n + m + 1)
                            nc.scalar.activation(probs[:, n % 2, m, :(b + 1) * P], scores[:, n % 2, m, :(b + 1) * P],
                                                 ACT.Exp, scale=0.125, bias=small[:, n % 2, 2 + m:3 + m],
                                                 accum_out=small[:, n % 2, 4 + m:5 + m]).then_inc(exped, 1)

                @block.vector
                def _(dve):
                    done = Steps(dve, step)
                    nc.vector.tensor_tensor(lam[:, 0:2], core.v("lam_q", 0, 2), core.v("lam_k", 0, 2),
                                            ALU.mult).then_inc(lam_in, 1)
                    for h in range(4):
                        nc.vector.scalar_tensor_tensor(out=q[:, h], in0=q[:, h], scalar=core.v("q_norm"), in1=rq[:, h],
                                                       op0=ALU.mult, op1=ALU.mult).then_inc(q_ready, 1)
                        nc.vector.scalar_tensor_tensor(out=k[:, h], in0=k[:, h], scalar=core.v("k_norm"), in1=rk[:, h],
                                                       op0=ALU.mult, op1=ALU.mult).then_inc(k_ready, 1)
                    dve.wait_ge(lam_exp, 1)
                    done(nc.vector.tensor_tensor(lam[:, 4:5], lam[:, 3:4], lam[:, 2:3], ALU.subtract))
                    done(nc.vector.tensor_scalar(lam[:, 5:6], lam[:, 4:5], -LAM_INIT, None, ALU.add))
                    dve.wait_ge(made, 2)

                    def top(n):
                        h, b = units[n]
                        for m in range(2):
                            dve.wait_ge(scored, 2 * n + m + 1)
                            sc = scores[:, n % 2, m]
                            done(nc.vector.tensor_tensor(sc[:, b * P:(b + 1) * P], sc[:, b * P:(b + 1) * P], mask[:],
                                                         ALU.add))
                            done(nc.vector.reduce_max(small[:, n % 2, m:m + 1], sc[:, :(b + 1) * P], AX_X))
                            nc.vector.tensor_scalar(small[:, n % 2, 2 + m:3 + m], small[:, n % 2, m:m + 1], -0.125,
                                                    None, ALU.mult).then_inc(max_ready, 1)

                    top(0)
                    for n, (h, b) in enumerate(units):
                        if n + 1 < len(units):
                            top(n + 1)
                        w = (b + 1) * P
                        dve.wait_ge(exped, 2 * n + 2)
                        if n >= 2:
                            dve.wait_ge(turned_ready, n - 1)
                        inv = small[:, n % 2, 6:8]
                        done(nc.vector.reciprocal(inv, small[:, n % 2, 4:6]))
                        done(nc.vector.tensor_scalar(inv[:, 1:2], inv[:, 1:2], lam[:, 5:6], None, ALU.mult))
                        done(nc.vector.tensor_scalar(attn[:, n % 2, :w], probs[:, n % 2, 0, :w], inv[:, 0:1], None,
                                                     ALU.mult))
                        nc.vector.scalar_tensor_tensor(out=attn[:, n % 2, :w], in0=probs[:, n % 2, 1, :w],
                                                       scalar=inv[:, 1:2], in1=attn[:, n % 2, :w], op0=ALU.mult,
                                                       op1=ALU.add).then_inc(mixed, 1)
                        dve.wait_ge(turned_ready, n + 1)
                        if n >= 2:
                            dve.wait_ge(out_ready, n - 1)
                        nc.vector.tensor_copy(attn_t[:, n % 2, :b + 1], turned[:, n % 2, :b + 1]).then_inc(
                            turned_copied, 1)
                        dve.wait_ge(out_ready, n + 1)
                        nc.vector.tensor_copy(y[:, h, b * P:(b + 1) * P], acc_o[:, n % 2, :P]).then_inc(out_copied, 1)
        stage_rstd(nc, core, y, rq, 1, core.ones, P, EPS)
        s = core.scope(nc, ctx, "subln")
        with nc.Block() as block:
            @block.vector
            def _(dve):
                done = Steps(dve, s.sem("scaled"))
                for h in range(4):
                    done.mark(nc.vector.scalar_tensor_tensor(out=y[:, h], in0=y[:, h], scalar=core.v("diff_subln"),
                                                             in1=rq[:, h], op0=ALU.mult, op1=ALU.mult))
                done.wait()
                done(nc.vector.tensor_scalar(y[:], y[:], 1.0 - LAM_INIT, None, ALU.mult))


def first_block(nc, core):
    dram = core.dram
    z = dram["z"]
    stage_norm(nc, core, core.x, core.h, "mix_norm")
    stage_rows(nc, core, [(dram["w_in_a"], z[0:4096], ACT.Copy), (dram["w_in_g"], dram["gates"], ACT.Sigmoid)])
    with ExitStack() as ctx:
        s = core.scope(nc, ctx, "first")
        v_tok = s.sb("v_tok", [P, 4, 512])
        y = s.sb("y", [P, 4, T])
        stage_tokens(nc, core, dram["w_in_v"], v_tok)
        merged = core.h
        g = dram["gates"]
        stage_short_conv(nc, core, z, y)
        stage_project(nc, core, dram["sc_out"], y, 4, merged, gates=g[0:D], first=True)
        stage_pool(nc, core, z, y)
        stage_project(nc, core, dram["pool_w"], y, 1, merged, gates=g[D:2 * D], groups=True,
                      scale=core.v("pool_scale", 0, DT))
        stage_conformer(nc, core, z, y)
        stage_project(nc, core, dram["conf_out"], y, 4, merged, gates=g[2 * D:3 * D])
        stage_attention(nc, core, z, v_tok, y)
        stage_project(nc, core, dram["diff_out"], y, 4, merged, gates=g[3 * D:4 * D])
        stage_project(nc, core, dram["w_o"], merged, DT, core.x)
    stage_norm(nc, core, core.x, core.h, "ffn_norm")
    stage_ffn(nc, core, dram["ffn_up"], dram["ffn_down"], conv=core.v("ffn_conv", 0, 6 * FT), conv_up=True)



def stage_ada(nc, core, wt, cond, bias, dst):
    m = dst.shape[1]
    with ExitStack() as ctx:
        s = core.scope(nc, ctx, "ada")
        w = s.sb("w", [P, 3, DT, 512])
        act_c = s.sb("act_c", [P, DT, m])
        acc = s.ps("acc", [P, 48, m])
        ready, product, added = s.sem("ready"), s.sem("product"), s.sem("added")
        loaded = [s.sem(f"loaded{n}") for n in range(3)]
        with nc.Block() as block:
            @block.sync
            def _(sp):
                for c in range(12):
                    if c >= 3:
                        sp.wait_ge(product, c - 2)
                    sp.dma_start(w[:, c % 3], wt[c]).then_inc(loaded[c % 3], 16)

            @block.scalar
            def _(act):
                nc.scalar.activation(act_c[:], cond, ACT.Silu).then_inc(ready, 1)

            @block.tensor
            def _(pe):
                pe.wait_ge(ready, 1)
                for c in range(12):
                    pe.wait_ge(loaded[c % 3], 16 * (c // 3 + 1))
                    for j in range(4):
                        for k in range(DT):
                            last = nc.tensor.matmul(acc[:, 4 * c + j], w[:, c % 3, k, j * P:(j + 1) * P],
                                                    act_c[:, k], start=k == 0, stop=k == DT - 1)
                    last.then_inc(product, 1)

            @block.vector
            def _(dve):
                dve.wait_ge(product, 12)
                for n in range(m):
                    nc.vector.tensor_tensor(dst[:, n], acc[:, :, n], bias, ALU.add).then_inc(added, 1)


def stage_softplus(nc, core, x, parts, n):
    with ExitStack() as ctx:
        s = core.scope(nc, ctx, "softplus")
        u, low, series = s.sb("u", [P, n]), s.sb("low", [P, n]), s.sb("series", [P, n])
        exped, negated, step = s.sem("exped"), s.sem("negated"), s.sem("step")
        with nc.Block() as block:
            @block.scalar
            def _(act):
                act.wait_ge(negated, 1)
                nc.scalar.activation(u[:parts], low[:parts], ACT.Exp).then_inc(exped, 1)

            @block.vector
            def _(dve):
                done = Steps(dve, step)
                v = nc.vector
                done(v.tensor_scalar(low[:parts], x[:parts], -1.0, None, ALU.mult))
                v.tensor_tensor(low[:parts], low[:parts], x[:parts], ALU.min).then_inc(negated, 1)
                dve.wait_ge(exped, 1)
                done(v.tensor_scalar(low[:parts], u[:parts], 2.0, None, ALU.add))
                done(v.reciprocal(low[:parts], low[:parts]))
                done(v.tensor_tensor(u[:parts], u[:parts], low[:parts], ALU.mult))
                done(v.tensor_tensor(low[:parts], u[:parts], u[:parts], ALU.mult))
                done(v.tensor_scalar(series[:parts], low[:parts], 2.0 / 15, 2.0 / 13, ALU.mult, ALU.add))
                for odd in (11, 9, 7, 5, 3, 1):
                    done(v.tensor_tensor(series[:parts], series[:parts], low[:parts], ALU.mult))
                    done(v.tensor_scalar(series[:parts], series[:parts], 2.0 / odd, None, ALU.add))
                done(v.tensor_tensor(series[:parts], series[:parts], u[:parts], ALU.mult))
                done(v.scalar_tensor_tensor(out=x[:parts], in0=x[:parts], scalar=0.0, in1=series[:parts],
                                            op0=ALU.max, op1=ALU.add))


F2 = {n: 512 * k for k, n in enumerate(
    ("q", "k", "qg", "kbg", "kd", "vb", "egc", "ra", "rb", "rk", "rr", "rv", "re", "bonus", "rg"))}
Z2 = {"q": 0, "k": 512, "v": 1024, "z": 1536, "pb": 2048, "ba": 3584, "lo": 3600, "glo": 3728}
UNIT = 8 * C64


def feat(core, name):
    at = F2[name]
    return rows(core.dram["feat"][at:at + 512])


def stage_gdn_gates(nc, core, decay_t, beta):
    z = core.dram["z"]
    with ExitStack() as ctx:
        s = core.scope(nc, ctx, "gates")
        g = s.sb("g", [HN, C64])
        keep = s.sb("keep", [HN, 2, C64])
        ones = s.sb("ones", [HN, C64])
        loaded, step0, fin = s.sem("loaded"), s.sem("step0"), s.sem("fin")
        by_unit = "(j q) (n c) -> n q j c"
        with nc.Block() as block:
            @block.sync
            def _(sp):
                for n in range(NC64):
                    for q in range(2):
                        at = n * 8 + q * 4
                        src = z[Z2["ba"]:Z2["ba"] + 8].rearrange(by_unit, q=2, c=C64)[n, q]
                        sp.dma_start(beta[at:at + 4], src).then_inc(loaded, 16)
                        src = z[Z2["ba"] + 8:Z2["ba"] + 16].rearrange(by_unit, q=2, c=C64)[n, q]
                        sp.dma_start(g[at:at + 4], src).then_inc(loaded, 16)
                sp.wait_ge(loaded, 512)

            @block.scalar
            def _(act):
                act.wait_ge(loaded, 512)
                nc.scalar.activation(beta[:], beta[:], ACT.Sigmoid)

            @block.vector
            def _(dve):
                dve.wait_ge(loaded, 512)
                nc.vector.tensor_scalar(g[:], g[:], core.v("dt_bias")[:HN], None, ALU.add)
        stage_softplus(nc, core, g, HN, C64)
        rate = s.sb("rate", [HN, 1])
        rate_ready, diff_ready, exp_done, summed, made, stored = (
            s.sem(x) for x in ("rate_ready", "diff_ready", "exp_done", "summed", "made", "stored"))
        hn = core.dram["hn"]
        with nc.Block() as block:
            @block.scalar
            def _(act):
                nc.scalar.activation(rate[:], core.v("a_log")[:HN], ACT.Exp).then_inc(rate_ready, 1)
                act.wait_ge(summed, 2)
                nc.scalar.activation(keep[:], keep[:], ACT.Exp).then_inc(exp_done, 1)
                act.wait_ge(diff_ready, 1)
                nc.scalar.activation(decay_t[:], decay_t[:], ACT.Exp).then_inc(exp_done, 1)
                act.wait_ge(exp_done, 1)
                act.dma_start(hn[0], beta[:]).then_inc(stored, 16)
                act.dma_start(hn[1:3].rearrange("a p c -> p a c"), keep[:]).then_inc(stored, 16)
                act.wait_ge(made, 1)
                act.dma_start(core.dram["decay"].rearrange("p s c -> p (s c)"),
                              decay_t[:].rearrange("p s c -> p (s c)")).then_inc(stored, 16)
                act.wait_ge(stored, 48)

            @block.vector
            def _(dve):
                done = Steps(dve, step0)
                v = nc.vector
                dve.wait_ge(rate_ready, 1)
                done.mark(v.memset(ones[:], 1.0))
                done(v.tensor_scalar(g[:], g[:], rate[:], -1.0, ALU.mult, ALU.mult))
                v.tensor_tensor_scan(keep[:, 0], ones[:], g[:], 0.0, ALU.mult, ALU.add).then_inc(summed, 1)
                dve.wait_ge(summed, 1)
                gc = g[:]
                done(v.tensor_copy(gc, keep[:, 0]))
                v.tensor_scalar(keep[:, 1], gc, gc[:, C64 - 1:C64], -1.0, ALU.subtract,
                                ALU.mult).then_inc(summed, 1)
                done(v.tensor_tensor(decay_t[:], gc.unsqueeze(1).broadcast_to([HN, C64, C64]),
                                     gc.unsqueeze(2).broadcast_to([HN, C64, C64]), ALU.subtract))
                v.tensor_scalar(decay_t[:], decay_t[:], 0.0, None, ALU.min).then_inc(diff_ready, 1)

            @block.gpsimd
            def _(pool):
                pool.wait_ge(exp_done, 2)
                nc.gpsimd.affine_select(out=decay_t[:], in_=decay_t[:], pattern=[[-1, C64], [1, C64]],
                                        compare_op=ALU.is_ge, fill=0.0, base=0,
                                        channel_multiplier=0).then_inc(made, 1)


def grams(nc, pe, out, lhs, rhs, n):
    at = slice(n * C64, (n + 1) * C64)
    for q in range(2):
        half = slice(64 * q, 64 * q + 64)
        for j in range(4):
            last = nc.tensor.matmul(out[:C64, q, j * C64:(j + 1) * C64], lhs[half, j, at], rhs[half, j, at],
                                    start=True, stop=True)
    return last


def stage_gram(nc, core, lhs, rhs, dst):
    with ExitStack() as ctx:
        s = core.scope(nc, ctx, "gram")
        out = s.sb("out", [C64, NC64, UNIT])
        acc = s.ps("acc", [P, 2, 2, 512])
        product, copied, stored = s.sem("product"), s.sem("copied"), s.sem("stored")
        with nc.Block() as block:
            @block.tensor
            def _(pe):
                for n in range(NC64):
                    if n >= 2:
                        pe.wait_ge(copied, n - 1)
                    grams(nc, pe, acc[:, n % 2], lhs, rhs, n).then_inc(product, 1)

            @block.vector
            def _(dve):
                for n in range(NC64):
                    dve.wait_ge(product, n + 1)
                    nc.vector.tensor_copy(out[:, n].rearrange("p (q c) -> p q c", q=2),
                                          acc[:C64, n % 2, :, :4 * C64]).then_inc(copied, 1)

            @block.sync
            def _(sp):
                for n in range(NC64):
                    sp.wait_ge(copied, n + 1)
                    sp.dma_start(dst[8 * n:8 * n + 8].rearrange("u i j -> i u j"),
                                 out[:, n].rearrange("p (u c) -> p u c", u=8)).then_inc(stored, 16)
                sp.wait_ge(stored, 16 * NC64)


def stage_gdn_prepare(nc, core, decay_t, beta):
    z = core.dram["z"]
    with ExitStack() as ctx:
        s = core.scope(nc, ctx, "gdn")
        raw = s.sb("raw", [P, 12, T])
        qkv = s.sb("qkv", [P, 12, T])
        loaded, step, conved = s.sem("loaded"), s.sem("step"), s.sem("conved")
        with nc.Block() as block:
            @block.sync
            def _(sp):
                sp.dma_start(raw[:], rows(z[0:1536])).then_inc(loaded, 16)

            @block.vector
            def _(dve):
                done = Steps(dve, step)
                dve.wait_ge(loaded, 16)
                for j in range(12):
                    done.mark(nc.vector.tensor_scalar(qkv[:, j], raw[:, j], core.v("conv_gdn", 4 * j + 3), None,
                                                      ALU.mult))
                for lag in (1, 2, 3):
                    done.wait()
                    for j in range(12):
                        ins = nc.vector.scalar_tensor_tensor(
                            out=qkv[:, j, lag:], in0=raw[:, j, :T - lag],
                            scalar=core.v("conv_gdn", 4 * j + 3 - lag), in1=qkv[:, j, lag:],
                            op0=ALU.mult, op1=ALU.add)
                        if lag < 3:
                            done.mark(ins)
                        else:
                            ins.then_inc(conved, 1)

            @block.scalar
            def _(act):
                for j in range(12):
                    act.wait_ge(conved, j + 1)
                    nc.scalar.activation(qkv[:, j], qkv[:, j], ACT.Silu)
        stage_rstd(nc, core, qkv[:, 0:8], raw[:, 0:8], 1, core.halves, 1.0, 1e-6)
        bcast = s.sb("bcast", [P, 3, 4, T])
        half, normed, scaled, stored, step2 = (s.sem(x) for x in ("half", "normed", "scaled", "stored", "step2"))
        spread = s.sem("spread")
        with nc.Block() as block:
            @block.sync
            def _(sp):
                for a in range(3):
                    for q in range(2):
                        for j in range(4):
                            src = core.dram["hn"][a].rearrange("(n q j) c -> q j n c", q=2, j=4)[q, j]
                            sp.dma_start(bcast[64 * q:64 * q + 64, a, j].rearrange("p (n c) -> p n c", c=C64),
                                         src.unsqueeze(0).broadcast_to([64, NC64, C64])).then_inc(spread, 16)
                sp.wait_ge(normed, 2)
                sp.dma_start(feat(core, "q"), qkv[:, 0:4]).then_inc(stored, 16)
                sp.dma_start(feat(core, "k"), qkv[:, 4:8]).then_inc(stored, 16)
                for n, (name, tile) in enumerate((("kd", raw[:, 0:4]), ("qg", raw[:, 4:8]), ("vb", raw[:, 8:12]),
                                                  ("kbg", bcast[:, 0]))):
                    sp.wait_ge(scaled, n + 1)
                    sp.dma_start(feat(core, name), tile).then_inc(stored, 16)
                sp.dma_start(feat(core, "egc"), bcast[:, 1]).then_inc(stored, 16)
                sp.wait_ge(stored, 16 * 7)

            @block.vector
            def _(dve):
                done = Steps(dve, step2)
                v = nc.vector
                v.scalar_tensor_tensor(out=qkv[:, 0:4], in0=qkv[:, 0:4], scalar=0.125, in1=raw[:, 0:4],
                                       op0=ALU.mult, op1=ALU.mult).then_inc(normed, 1)
                v.tensor_tensor(qkv[:, 4:8], qkv[:, 4:8], raw[:, 4:8], ALU.mult).then_inc(normed, 1)
                dve.wait_ge(normed, 2)
                dve.wait_ge(spread, 16 * 24)
                v.tensor_tensor(raw[:, 0:4], qkv[:, 4:8], bcast[:, 2], ALU.mult).then_inc(scaled, 1)
                v.tensor_tensor(raw[:, 4:8], qkv[:, 0:4], bcast[:, 1], ALU.mult).then_inc(scaled, 1)
                v.tensor_tensor(raw[:, 8:12], qkv[:, 8:12], bcast[:, 0], ALU.mult).then_inc(scaled, 1)
                dve.wait_ge(scaled, 3)
                done(v.tensor_tensor(bcast[:, 0], bcast[:, 0], bcast[:, 1], ALU.mult))
                v.tensor_tensor(bcast[:, 0], bcast[:, 0], qkv[:, 4:8], ALU.mult).then_inc(scaled, 1)
        stage_gram(nc, core, qkv[:, 4:8], qkv[:, 4:8], core.dram["gram"][0:HN])


def stage_rwkv_prepare(nc, core):
    z = core.dram["z"]
    with ExitStack() as ctx:
        s = core.scope(nc, ctx, "rwkv")
        r, k, v_ = (s.sb(n, [P, 4, T]) for n in ("r", "k", "v"))
        d = s.sb("d", [P, 4, T])
        lw, a, g = (s.sb(n, [P, 4, T]) for n in ("lw", "a", "g"))
        lo = s.sb("lo", [P, 4, T])
        low = s.sb("low", [P, 4, 512])
        acc = s.ps("acc", [P, 4, 512])
        loaded, step, mixed, bent, product, freed = (
            s.sem(x) for x in ("loaded", "step", "mixed", "bent", "product", "freed"))
        lows = ((0, 64), (1, 64), (2, P), (3, 32))
        with nc.Block() as block:
            @block.sync
            def _(sp):
                for n, at in ((0, 0), (1, 64)):
                    sp.dma_start(lo[:64, n], z[Z2["lo"] + at:Z2["lo"] + at + 64]).then_inc(loaded, 16)
                sp.dma_start(lo[:, 2], z[Z2["glo"]:Z2["glo"] + P]).then_inc(loaded, 16)
                sp.dma_start(lo[:32, 3], z[Z2["glo"] + P:Z2["glo"] + 160]).then_inc(loaded, 16)
                sp.dma_start(low[:64, 0], core.dram["w2"]).then_inc(loaded, 16)
                sp.dma_start(low[:64, 1], core.dram["a2"]).then_inc(loaded, 16)
                sp.dma_start(low[:, 2], core.dram["g2"][0:P]).then_inc(loaded, 16)
                sp.dma_start(low[:32, 3], core.dram["g2"][P:160]).then_inc(loaded, 16)
                for n, tile in enumerate((r, k, v_)):
                    at = Z2["pb"] + 512 * n
                    sp.dma_start(tile[:], rows(z[at:at + 512])).then_inc(loaded, 16)

            @block.vector
            def _(dve):
                done = Steps(dve, step)
                v = nc.vector
                dve.wait_ge(loaded, 16 * 11)
                for n, p in lows:
                    done.mark(v.tensor_tensor(d[:p, n, 1:], lo[:p, n, :T - 1], lo[:p, n, 1:], ALU.subtract))
                    done.mark(v.tensor_scalar(d[:p, n, 0:1], lo[:p, n, 0:1], -1.0, None, ALU.mult))
                done.wait()
                for n, p in lows:
                    v.scalar_tensor_tensor(out=lo[:p, n], in0=d[:p, n], scalar=core.v("mu_lo", n)[:p],
                                           in1=lo[:p, n], op0=ALU.mult, op1=ALU.add).then_inc(mixed, 1)
                dve.wait_ge(mixed, 4)
                for m, tile in enumerate((r, k, v_)):
                    done.mark(v.tensor_tensor(d[:, :, 1:], tile[:, :, :T - 1], tile[:, :, 1:], ALU.subtract))
                    done(v.tensor_scalar(d[:, :, 0:1], tile[:, :, 0:1], -1.0, None, ALU.mult))
                    for j in range(4):
                        done.mark(v.scalar_tensor_tensor(out=tile[:, j], in0=d[:, j],
                                                         scalar=core.v("mu_rkv", 4 * m + j), in1=tile[:, j],
                                                         op0=ALU.mult, op1=ALU.add))
                    done.wait()

            @block.scalar
            def _(act):
                act.wait_ge(mixed, 4)
                nc.scalar.activation(lo[:64, 0], lo[:64, 0], ACT.Tanh).then_inc(bent, 1)
                nc.scalar.activation(lo[:, 2], lo[:, 2], ACT.Sigmoid).then_inc(bent, 1)
                nc.scalar.activation(lo[:32, 3], lo[:32, 3], ACT.Sigmoid).then_inc(bent, 1)
                for n in range(12):
                    which, j = n // 4, n % 4
                    act.wait_ge(product, n + 1)
                    if which == 0:
                        ins = nc.scalar.activation(lw[:, j], acc[:, n % 4], ACT.Sigmoid, bias=core.v("w0", j))
                    elif which == 1:
                        ins = nc.scalar.activation(a[:, j], acc[:, n % 4], ACT.Sigmoid, bias=core.v("a0", j))
                    else:
                        ins = nc.scalar.activation(g[:, j], acc[:, n % 4], ACT.Copy)
                    ins.then_inc(freed, 1)

            @block.tensor
            def _(pe):
                pe.wait_ge(loaded, 16 * 11)
                pe.wait_ge(bent, 3)
                for n in range(12):
                    which, j = n // 4, n % 4
                    if n >= 4:
                        pe.wait_ge(freed, n - 3)
                    at = slice(j * P, (j + 1) * P)
                    if which < 2:
                        nc.tensor.matmul(acc[:, n % 4], low[:64, which, at], lo[:64, which], start=True,
                                         stop=True).then_inc(product, 1)
                    else:
                        nc.tensor.matmul(acc[:, n % 4], low[:, 2, at], lo[:, 2], start=True, stop=False)
                        nc.tensor.matmul(acc[:, n % 4], low[:32, 3, at], lo[:32, 3], start=False,
                                         stop=True).then_inc(product, 1)
        kk, rstd = lo, low
        s = core.scope(nc, ctx, "rwkv_kk")
        step = s.sem("step")
        with nc.Block() as block:
            @block.vector
            def _(dve):
                done = Steps(dve, step)
                v = nc.vector
                for j in range(4):
                    done.mark(v.tensor_scalar(kk[:, j], k[:, j], core.v("k_k", j), None, ALU.mult))
                    done.mark(v.tensor_scalar(d[:, j], a[:, j], -1.0, core.v("k_a", j), ALU.add, ALU.mult))
                done.wait()
                done(v.scalar_tensor_tensor(out=k[:], in0=d[:], scalar=1.0, in1=k[:], op0=ALU.add, op1=ALU.mult))
                done(v.tensor_scalar(lw[:], lw[:], -math.exp(-0.5), None, ALU.mult))
        stage_rstd(nc, core, kk, rstd, 1, core.halves, 1.0, 1e-6)
        s = core.scope(nc, ctx, "rwkv_scale")
        reset = s.sb("reset", [P, T])
        cw, e = s.sb("cw", [P, 4, T]), s.sb("e", [P, 4, T])
        step, summed, exped, ready, stored, sums = (
            s.sem(x) for x in ("step", "summed", "exped", "ready", "stored", "sums"))
        order = ("rv", "rg", "re", "rr", "rb", "rk", "ra", "bonus")
        tiles = {"rv": v_, "rg": g, "re": e, "rr": r, "rb": a, "rk": k, "ra": kk, "bonus": d}
        with nc.Block() as block:
            @block.vector
            def _(dve):
                done = Steps(dve, step)
                v = nc.vector
                done(v.memset(reset[:], 1.0))
                done(v.memset(reset[:].rearrange("p (n c) -> p n c", c=C64)[:, :, 0:1], 0.0))
                for j in range(4):
                    v.tensor_tensor_scan(cw[:, j], reset[:], lw[:, j], 0.0, ALU.mult, ALU.add).then_inc(summed, 1)
                dve.wait_ge(summed, 4)
                v.tensor_tensor(lw[:], cw[:], lw[:], ALU.subtract).then_inc(summed, 1)
                done(v.tensor_tensor(d[:], r[:], k[:], ALU.mult))
                for j in range(4):
                    v.tensor_scalar(d[:, j], d[:, j], core.v("r_k", j), None, ALU.mult).then_inc(ready, 1)
                done(v.tensor_tensor(kk[:], kk[:], rstd[:], ALU.mult))
                done(v.tensor_tensor(a[:], a[:], kk[:], ALU.mult))
                dve.wait_ge(exped, 3)
                v.tensor_tensor(r[:], r[:], e[:], ALU.mult).then_inc(ready, 1)
                v.tensor_tensor(a[:], a[:], cw[:], ALU.mult).then_inc(ready, 1)
                v.tensor_tensor(k[:], k[:], cw[:], ALU.mult).then_inc(ready, 1)
                v.scalar_tensor_tensor(out=kk[:], in0=kk[:], scalar=-1.0, in1=lw[:], op0=ALU.mult,
                                       op1=ALU.mult).then_inc(ready, 1)
                dve.wait_ge(sums, 4)
                v.tensor_tensor(d[:], acc[:], v_[:], ALU.mult).then_inc(ready, 1)

            @block.scalar
            def _(act):
                act.wait_ge(summed, 5)
                nc.scalar.activation(e[:], cw[:], ACT.Exp).then_inc(exped, 1)
                nc.scalar.activation(lw[:], lw[:], ACT.Exp).then_inc(exped, 1)
                act.wait_ge(exped, 2)
                nc.scalar.activation(cw[:], cw[:], ACT.Exp, scale=-1.0).then_inc(exped, 1)

            @block.tensor
            def _(pe):
                pe.wait_ge(ready, 4)
                for j in range(4):
                    nc.tensor.matmul(acc[:, j], core.halves[:], d[:, j], start=True, stop=True).then_inc(sums, 1)

            @block.sync
            def _(sp):
                for n, name in enumerate(order):
                    if n == 2:
                        sp.wait_ge(exped, 1)
                    if n >= 3:
                        sp.wait_ge(ready, 4 + n - 2)
                    sp.dma_start(feat(core, name), tiles[name][:]).then_inc(stored, 16)
                sp.wait_ge(stored, 16 * len(order))
        stage_gram(nc, core, kk, a, core.dram["gram"][HN:2 * HN])


def stage_inverse(nc, core, decay_t, beta):
    with ExitStack() as ctx:
        s = core.scope(nc, ctx, "inverse")
        m = s.sb("m", [P, C64, C64])
        inv = s.sb("inv", [P, C64, C64])
        prod = s.sb("prod", [P, C64, C64])
        loaded, step, stored, made = s.sem("loaded"), s.sem("step"), s.sem("stored"), s.sem("made")
        with nc.Block() as block:
            @block.sync
            def _(sp):
                sp.dma_start(m[:], core.dram["gram"]).then_inc(loaded, 16)
                sp.wait_ge(made, 1)
                sp.dma_start(core.dram["inverse"], inv[:]).then_inc(stored, 16)
                sp.wait_ge(stored, 16)

            @block.vector
            def _(dve):
                done = Steps(dve, step)
                v = nc.vector
                flat = inv[:].rearrange("p s c -> p (s c)")
                done(v.memset(flat, 0.0))
                done(v.memset(flat[:, ::C64 + 1], 1.0))
                dve.wait_ge(loaded, 16)
                low = m[:HN]
                done(v.tensor_tensor(low, low, decay_t[:].rearrange("p s c -> p c s"), ALU.mult))
                done(v.scalar_tensor_tensor(out=low, in0=low, scalar=-1.0,
                                            in1=beta[:].unsqueeze(2).broadcast_to([HN, C64, C64]),
                                            op0=ALU.mult, op1=ALU.mult))
                for i in range(1, C64):
                    done(v.tensor_tensor(prod[:, :i, :i], inv[:, :i, :i],
                                         m[:, i:i + 1, :i].broadcast_to([P, i, i]), ALU.mult))
                    ins = v.tensor_reduce(inv[:, :i, i:i + 1], prod[:, :i, :i], AX_X, ALU.add)
                    if i < C64 - 1:
                        done(ins)
                    else:
                        ins.then_inc(made, 1)


def stage_to_tokens(nc, core, name, dst):
    with ExitStack() as ctx:
        s = core.scope(nc, ctx, "turn")
        src = s.sb("src", [P, 4, T])
        acc = s.ps("acc", [P, 4, 512])
        loaded, turned, copied = s.sem("loaded"), s.sem("turned"), s.sem("copied")
        with nc.Block() as block:
            @block.sync
            def _(sp):
                sp.dma_start(src[:], feat(core, name)).then_inc(loaded, 16)

            @block.tensor
            def _(pe):
                pe.wait_ge(loaded, 16)
                for n in range(NC64):
                    if n >= 4:
                        pe.wait_ge(copied, n - 3)
                    for j in range(4):
                        last = nc.tensor.transpose(acc[:C64, n % 4, j * P:(j + 1) * P],
                                                   src[:, j, n * C64:(n + 1) * C64], core.ident[:])
                    last.then_inc(turned, 1)

            @block.vector
            def _(dve):
                for n in range(NC64):
                    dve.wait_ge(turned, n + 1)
                    nc.vector.tensor_copy(dst[:, n].rearrange("p (q j c) -> p q j c", q=2, j=4),
                                          acc[:C64, n % 4].rearrange("p (j q c) -> p q j c", q=2, j=4)
                                          ).then_inc(copied, 1)


def stage_masked(nc, core, lhs, rhs, dst, weight=None, strict=False):
    with ExitStack() as ctx:
        s = core.scope(nc, ctx, "masked")
        acc = s.ps("acc", [P, 2, 2, 512])
        mask = s.sb("mask", [C64, C64])
        product, copied, made = s.sem("product"), s.sem("copied"), s.sem("made")
        with nc.Block() as block:
            @block.gpsimd
            def _(pool):
                if weight is None:
                    nc.gpsimd.memset(mask[:], 1.0).then_inc(made, 1)
                    pool.wait_ge(made, 1)
                    nc.gpsimd.affine_select(out=mask[:], in_=mask[:], pattern=[[1, C64]], compare_op=ALU.is_ge,
                                            fill=0.0, base=-1 if strict else 0,
                                            channel_multiplier=-1).then_inc(made, 1)

            @block.tensor
            def _(pe):
                for n in range(NC64):
                    if n >= 2:
                        pe.wait_ge(copied, n - 1)
                    grams(nc, pe, acc[:, n % 2], lhs, rhs, n).then_inc(product, 1)

            @block.vector
            def _(dve):
                if weight is None:
                    dve.wait_ge(made, 2)
                for n in range(NC64):
                    dve.wait_ge(product, n + 1)
                    if weight is None:
                        by = mask[:].unsqueeze(1).broadcast_to([C64, 8, C64]).rearrange("p (q j) c -> p q j c", q=2)
                    else:
                        by = weight[:, n].rearrange("p (q j c) -> p q j c", q=2, j=4)
                    nc.vector.tensor_tensor(dst[:, n].rearrange("p (q j c) -> p q j c", q=2, j=4),
                                            acc[:C64, n % 2, :, :4 * C64].rearrange("p q (j c) -> p q j c", c=C64),
                                            by, ALU.mult).then_inc(copied, 1)


def unit(tile, n, q, j):
    at = (q * 4 + j) * C64
    return tile[:, n, at:at + C64]


def by_unit(dram3):
    return dram3.rearrange("(n u) s c -> s n u c", u=8)


def stage_gdn_scan(nc, core, y):
    with ExitStack() as ctx:
        s = core.scope(nc, ctx, "gscan")
        q, kbg, egc = (s.sb(n, [P, 4, T]) for n in ("q", "kbg", "egc"))
        kd_tok, vb_tok, attn, inv = (s.sb(n, [C64, NC64, UNIT]) for n in ("kd_tok", "vb_tok", "attn", "inv"))
        loaded = s.sem("loaded")
        with nc.Block() as block:
            @block.sync
            def _(sp):
                sp.dma_start(q[:], feat(core, "q")).then_inc(loaded, 16)
                sp.dma_start(kbg[:], feat(core, "k")).then_inc(loaded, 16)
                sp.dma_start(egc[:], feat(core, "egc")).then_inc(loaded, 16)
                sp.dma_start(inv[:].rearrange("p n (u c) -> p n u c", c=C64),
                             by_unit(core.dram["decay"])).then_inc(loaded, 16)
                sp.wait_ge(loaded, 64)
        stage_masked(nc, core, kbg, q, attn, weight=inv)
        stage_to_tokens(nc, core, "kd", kd_tok)
        stage_to_tokens(nc, core, "vb", vb_tok)
        s = core.scope(nc, ctx, "gchunks")
        state = s.sb("state", [P, 4, C64])
        r, vn = s.sb("r", [C64, UNIT]), s.sb("vn", [C64, UNIT])
        ks = s.ps("ks", [P, 2, 512])
        tr = s.ps("tr", [P, 512])
        os_ = s.ps("os", [P, 2, 512])
        ov = s.ps("ov", [P, 512])
        up = s.ps("up", [P, 512])
        (loaded, ks_ready, r_ready, tr_ready, vn_ready, os_ready, ov_ready, up_ready, state_ready, o_copied,
         step) = (s.sem(x) for x in ("loaded", "ks_ready", "r_ready", "tr_ready", "vn_ready", "os_ready",
                                     "ov_ready", "up_ready", "state_ready", "o_copied", "step"))
        with nc.Block() as block:
            @block.sync
            def _(sp):
                sp.dma_start(q[:], feat(core, "qg")).then_inc(loaded, 16)
                sp.dma_start(kbg[:], feat(core, "kbg")).then_inc(loaded, 16)
                sp.dma_start(inv[:].rearrange("p n (u c) -> p n u c", c=C64),
                             by_unit(core.dram["inverse"][0:HN])).then_inc(loaded, 16)

            @block.tensor
            def _(pe):
                pe.wait_ge(loaded, 48)
                for n in range(NC64):
                    at = slice(n * C64, (n + 1) * C64)
                    pe.wait_ge(state_ready, n + 1)
                    for h in range(8):
                        c, j = h // 4, h % 4
                        half = slice(64 * c, 64 * c + 64)
                        last = nc.tensor.matmul(ks[:C64, c, j * C64:(j + 1) * C64], kbg[half, j, at],
                                                state[half, j], start=True, stop=True)
                    last.then_inc(ks_ready, 1)
                    if n:
                        pe.wait_ge(o_copied, n)
                    for h in range(8):
                        c, j = h // 4, h % 4
                        half = slice(64 * c, 64 * c + 64)
                        last = nc.tensor.matmul(os_[half, c, j * C64:(j + 1) * C64], state[half, j],
                                                q[half, j, at], start=True, stop=True)
                    last.then_inc(os_ready, 1)
                    pe.wait_ge(r_ready, n + 1)
                    for h in range(8):
                        c, j = h // 4, h % 4
                        last = nc.tensor.matmul(tr[:C64, h * C64:(h + 1) * C64], unit(inv, n, c, j),
                                                r[:, h * C64:(h + 1) * C64], start=True, stop=True)
                    last.then_inc(tr_ready, 1)
                    pe.wait_ge(vn_ready, n + 1)
                    for h in range(8):
                        c, j = h // 4, h % 4
                        half = slice(64 * c, 64 * c + 64)
                        last = nc.tensor.matmul(up[half, j * C64:(j + 1) * C64], unit(kd_tok, n, c, j),
                                                vn[:, h * C64:(h + 1) * C64], start=True, stop=True)
                    last.then_inc(up_ready, 1)
                    for h in range(8):
                        c, j = h // 4, h % 4
                        half = slice(64 * c, 64 * c + 64)
                        last = nc.tensor.matmul(ov[half, j * C64:(j + 1) * C64], vn[:, h * C64:(h + 1) * C64],
                                                unit(attn, n, c, j), start=True, stop=True)
                    last.then_inc(ov_ready, 1)

            @block.scalar
            def _(act):
                for n in range(NC64):
                    act.wait_ge(tr_ready, n + 1)
                    if n:
                        act.wait_ge(ov_ready, n)
                    nc.scalar.activation(vn[:], tr[:C64, :], ACT.Copy).then_inc(vn_ready, 1)

            @block.vector
            def _(dve):
                done = Steps(dve, step)
                v = nc.vector
                v.memset(state[:], 0.0).then_inc(state_ready, 1)
                for n in range(NC64):
                    dve.wait_ge(ks_ready, n + 1)
                    v.tensor_tensor(r[:].rearrange("p (q c) -> p q c", q=2),
                                    vb_tok[:, n].rearrange("p (q c) -> p q c", q=2), ks[:C64, :, :4 * C64],
                                    ALU.subtract).then_inc(r_ready, 1)
                    dve.wait_ge(os_ready, n + 1)
                    last = egc[:, :, n * C64 + C64 - 1:(n + 1) * C64]
                    done(v.tensor_tensor(state[:], state[:], last.broadcast_to([P, 4, C64]), ALU.mult))
                    dve.wait_ge(up_ready, n + 1)
                    v.tensor_tensor(state[:], state[:], up[:, :4 * C64].rearrange("p (j c) -> p j c", j=4),
                                    ALU.add).then_inc(state_ready, 1)
                    dst = y[:, :, n * C64:(n + 1) * C64]
                    for c in range(2):
                        half = slice(64 * c, 64 * c + 64)
                        done.mark(v.tensor_copy(dst[half], os_[half, c, :4 * C64].rearrange(
                            "p (j c) -> p j c", j=4)))
                    done.wait()
                    dve.wait_ge(ov_ready, n + 1)
                    v.tensor_tensor(dst, dst, ov[:, :4 * C64].rearrange("p (j c) -> p j c", j=4),
                                    ALU.add).then_inc(o_copied, 1)


def stage_rwkv_scan(nc, core, y):
    with ExitStack() as ctx:
        s = core.scope(nc, ctx, "rscan")
        ra, rr = s.sb("ra", [P, 4, T]), s.sb("rr", [P, 4, T])
        decay = s.sb("decay", [P, 4, NC64])
        b_tok, k_tok, v_tok, rb, rk, akv = (
            s.sb(n, [C64, NC64, UNIT]) for n in ("b_tok", "k_tok", "v_tok", "rb", "rk", "akv"))
        stage_to_tokens(nc, core, "rv", v_tok)
        with ExitStack() as inner:
            s1 = core.scope(nc, inner, "rmat")
            kb = s1.sb("kb", [P, 4, T])
            loaded, again, product, copied = (s1.sem(x) for x in ("loaded", "again", "product", "copied"))
            with nc.Block() as block:
                @block.sync
                def _(sp):
                    sp.dma_start(ra[:], feat(core, "ra")).then_inc(loaded, 16)
                    sp.dma_start(rr[:], feat(core, "rr")).then_inc(loaded, 16)
                    sp.dma_start(kb[:], feat(core, "rk")).then_inc(loaded, 16)
                    sp.wait_ge(loaded, 48)
            stage_masked(nc, core, kb, ra, b_tok, strict=True)
            stage_masked(nc, core, kb, rr, rk)
            acc = s1.ps("acc", [P, 2, 512])
            with nc.Block() as block:
                @block.sync
                def _(sp):
                    sp.dma_start(kb[:], feat(core, "rb")).then_inc(again, 16)
                    sp.wait_ge(again, 16)

                @block.tensor
                def _(pe):
                    for n in range(NC64):
                        if n >= 2:
                            pe.wait_ge(copied, n - 1)
                        for h in range(8):
                            at = slice(h * C64, (h + 1) * C64)
                            last = nc.tensor.matmul(acc[:C64, n % 2, at], b_tok[:, n, at], v_tok[:, n, at],
                                                    start=True, stop=True)
                        last.then_inc(product, 1)

                @block.vector
                def _(dve):
                    for n in range(NC64):
                        dve.wait_ge(product, n + 1)
                        nc.vector.tensor_copy(akv[:, n], acc[:C64, n % 2]).then_inc(copied, 1)
            stage_masked(nc, core, kb, rr, rb)
            last_loaded, picked = s1.sem("last_loaded"), s1.sem("picked")
            with nc.Block() as block:
                @block.sync
                def _(sp):
                    sp.dma_start(kb[:], feat(core, "re")).then_inc(last_loaded, 16)

                @block.vector
                def _(dve):
                    dve.wait_ge(last_loaded, 16)
                    nc.vector.tensor_copy(decay[:], kb[:].rearrange("p j (n c) -> p j n c", c=C64)[
                        :, :, :, C64 - 1]).then_inc(picked, 1)
        stage_to_tokens(nc, core, "rb", b_tok)
        stage_to_tokens(nc, core, "rk", k_tok)
        s = core.scope(nc, ctx, "rchunks")
        inv = s.sb("inv", [C64, NC64, UNIT])
        state = s.sb("state", [P, 4, C64])
        r, sa = s.sb("r", [C64, UNIT]), s.sb("sa", [C64, UNIT])
        as_ = s.ps("as", [P, 2, 512])
        tr = s.ps("tr", [P, 512])
        ys = s.ps("ys", [P, 2, 512])
        yv = s.ps("yv", [P, 512])
        up = s.ps("up", [P, 512])
        (loaded, as_ready, r_ready, tr_ready, sa_ready, ys_ready, yv_ready, up_ready, state_ready, y_copied,
         step) = (s.sem(x) for x in ("loaded", "as_ready", "r_ready", "tr_ready", "sa_ready", "ys_ready",
                                     "yv_ready", "up_ready", "state_ready", "y_copied", "step"))
        with nc.Block() as block:
            @block.sync
            def _(sp):
                sp.dma_start(inv[:].rearrange("p n (u c) -> p n u c", c=C64),
                             by_unit(core.dram["inverse"][HN:2 * HN])).then_inc(loaded, 16)

            @block.tensor
            def _(pe):
                pe.wait_ge(loaded, 16)
                for n in range(NC64):
                    at = slice(n * C64, (n + 1) * C64)
                    pe.wait_ge(state_ready, n + 1)
                    for h in range(8):
                        c, j = h // 4, h % 4
                        half = slice(64 * c, 64 * c + 64)
                        last = nc.tensor.matmul(as_[:C64, c, j * C64:(j + 1) * C64], ra[half, j, at],
                                                state[half, j], start=True, stop=True)
                    last.then_inc(as_ready, 1)
                    if n:
                        pe.wait_ge(y_copied, n)
                    for h in range(8):
                        c, j = h // 4, h % 4
                        half = slice(64 * c, 64 * c + 64)
                        last = nc.tensor.matmul(ys[half, c, j * C64:(j + 1) * C64], state[half, j],
                                                rr[half, j, at], start=True, stop=True)
                    last.then_inc(ys_ready, 1)
                    pe.wait_ge(r_ready, n + 1)
                    for h in range(8):
                        c, j = h // 4, h % 4
                        last = nc.tensor.matmul(tr[:C64, h * C64:(h + 1) * C64], unit(inv, n, c, j),
                                                r[:, h * C64:(h + 1) * C64], start=True, stop=True)
                    last.then_inc(tr_ready, 1)
                    pe.wait_ge(sa_ready, n + 1)
                    for h in range(8):
                        c, j = h // 4, h % 4
                        half = slice(64 * c, 64 * c + 64)
                        to = up[half, j * C64:(j + 1) * C64]
                        nc.tensor.matmul(to, unit(b_tok, n, c, j), sa[:, h * C64:(h + 1) * C64], start=True,
                                         stop=False)
                        last = nc.tensor.matmul(to, unit(k_tok, n, c, j), unit(v_tok, n, c, j), start=False,
                                                stop=True)
                    last.then_inc(up_ready, 1)
                    for h in range(8):
                        c, j = h // 4, h % 4
                        half = slice(64 * c, 64 * c + 64)
                        to = yv[half, j * C64:(j + 1) * C64]
                        nc.tensor.matmul(to, sa[:, h * C64:(h + 1) * C64], unit(rb, n, c, j), start=True,
                                         stop=False)
                        last = nc.tensor.matmul(to, unit(v_tok, n, c, j), unit(rk, n, c, j), start=False,
                                                stop=True)
                    last.then_inc(yv_ready, 1)

            @block.scalar
            def _(act):
                for n in range(NC64):
                    act.wait_ge(tr_ready, n + 1)
                    if n:
                        act.wait_ge(yv_ready, n)
                    nc.scalar.activation(sa[:], tr[:C64, :], ACT.Copy).then_inc(sa_ready, 1)

            @block.vector
            def _(dve):
                done = Steps(dve, step)
                v = nc.vector
                v.memset(state[:], 0.0).then_inc(state_ready, 1)
                for n in range(NC64):
                    dve.wait_ge(as_ready, n + 1)
                    v.tensor_tensor(r[:].rearrange("p (q c) -> p q c", q=2),
                                    akv[:, n].rearrange("p (q c) -> p q c", q=2), as_[:C64, :, :4 * C64],
                                    ALU.add).then_inc(r_ready, 1)
                    dve.wait_ge(ys_ready, n + 1)
                    dve.wait_ge(up_ready, n + 1)
                    done(v.tensor_tensor(state[:], state[:], up[:, :4 * C64].rearrange("p (j c) -> p j c", j=4),
                                         ALU.add))
                    v.tensor_tensor(state[:], state[:], decay[:, :, n:n + 1].broadcast_to([P, 4, C64]),
                                    ALU.mult).then_inc(state_ready, 1)
                    dst = y[:, :, n * C64:(n + 1) * C64]
                    for c in range(2):
                        half = slice(64 * c, 64 * c + 64)
                        done.mark(v.tensor_copy(dst[half], ys[half, c, :4 * C64].rearrange(
                            "p (j c) -> p j c", j=4)))
                    done.wait()
                    dve.wait_ge(yv_ready, n + 1)
                    v.tensor_tensor(dst, dst, yv[:, :4 * C64].rearrange("p (j c) -> p j c", j=4),
                                    ALU.add).then_inc(y_copied, 1)


def stage_gdn_out(nc, core, y):
    with ExitStack() as ctx:
        s = core.scope(nc, ctx, "gout")
        rstd, zt = s.sb("rstd", [P, 4, T]), s.sb("zt", [P, 4, T])
        loaded, bent, step = s.sem("loaded"), s.sem("bent"), s.sem("step")
        stage_rstd(nc, core, y, rstd, 1, core.halves, 64, EPS)
        with nc.Block() as block:
            @block.sync
            def _(sp):
                sp.dma_start(zt[:], rows(core.dram["z"][Z2["z"]:Z2["z"] + 512])).then_inc(loaded, 16)

            @block.scalar
            def _(act):
                act.wait_ge(loaded, 16)
                nc.scalar.activation(zt[:], zt[:], ACT.Silu).then_inc(bent, 1)

            @block.vector
            def _(dve):
                done = Steps(dve, step)
                done(nc.vector.scalar_tensor_tensor(out=y[:], in0=y[:], scalar=core.v("onorm_gdn"), in1=rstd[:],
                                                    op0=ALU.mult, op1=ALU.mult))
                dve.wait_ge(bent, 1)
                done(nc.vector.tensor_tensor(y[:], y[:], zt[:], ALU.mult))


def stage_rwkv_out(nc, core, y):
    with ExitStack() as ctx:
        s = core.scope(nc, ctx, "rout")
        rstd, bonus, g = (s.sb(n, [P, 4, T]) for n in ("rstd", "bonus", "g"))
        loaded, step = s.sem("loaded"), s.sem("step")
        stage_centre(nc, core, y, 1, core.halves, 64)
        stage_rstd(nc, core, y, rstd, 1, core.halves, 64, 64e-5)
        with nc.Block() as block:
            @block.sync
            def _(sp):
                sp.dma_start(bonus[:], feat(core, "bonus")).then_inc(loaded, 16)
                sp.dma_start(g[:], feat(core, "rg")).then_inc(loaded, 16)

            @block.vector
            def _(dve):
                done = Steps(dve, step)
                v = nc.vector
                for j in range(4):
                    done.mark(v.scalar_tensor_tensor(out=y[:, j], in0=y[:, j], scalar=core.v("lnx_w", j),
                                                     in1=rstd[:, j], op0=ALU.mult, op1=ALU.mult))
                done.wait()
                dve.wait_ge(loaded, 32)
                for j in range(4):
                    done.mark(v.scalar_tensor_tensor(out=y[:, j], in0=y[:, j], scalar=core.v("lnx_b", j),
                                                     in1=bonus[:, j], op0=ALU.add, op1=ALU.add))
                done.wait()
                done(v.tensor_tensor(y[:], y[:], g[:], ALU.mult))


def second_block(nc, core):
    dram = core.dram
    z, gates = dram["z"], dram["gates"]
    with ExitStack() as ctx:
        s = core.scope(nc, ctx, "second")
        mod = s.sb("mod", [P, 1, 48])
        cond = core.v("c_2", 0, DT).unsqueeze(2)
        stage_ada(nc, core, dram["w_ada_2"], cond, core.v("b_ada_2", 0, 48), mod)
        shift1, scale1, gate1, shift2, scale2, gate2 = (mod[:, 0, 8 * n:8 * n + 8] for n in range(6))
        stage_norm(nc, core, core.x, core.h, "norm1_w_2", (scale1, shift1))
        stage_rows(nc, core,
                   [(dram["w_in_2a"], z[0:2048], ACT.Copy), (dram["w_in_2b"], z[2048:3584], ACT.Copy),
                    (dram["w_in_2g"], gates[0:2048], ACT.Sigmoid)],
                   tails=[(dram["w_in_2t0"], z[3584:3600]), (dram["w_in_2t1"], z[3600:3728]),
                          (dram["w_in_2t2"], z[3728:3856]), (dram["w_in_2t3"], z[3856:3888])])
        with ExitStack() as inner:
            s2 = core.scope(nc, inner, "delta")
            decay_t = s2.sb("decay_t", [HN, C64, C64])
            beta = s2.sb("beta", [HN, C64])
            stage_gdn_gates(nc, core, decay_t, beta)
            stage_gdn_prepare(nc, core, decay_t, beta)
            stage_rwkv_prepare(nc, core)
            stage_inverse(nc, core, decay_t, beta)
        merged = core.h
        y = s.sb("y", [P, 4, T])
        stage_gdn_scan(nc, core, y)
        stage_gdn_out(nc, core, y)
        stage_project(nc, core, dram["w_branch_gdn_2"], y, 4, merged, gates=gates[0:D], first=True)
        stage_rwkv_scan(nc, core, y)
        stage_rwkv_out(nc, core, y)
        stage_project(nc, core, dram["w_branch_rwkv_2"], y, 4, merged, gates=gates[D:2 * D])
        stage_project(nc, core, dram["w_out_2"], merged, DT, core.x, scale=gate1)
        stage_norm(nc, core, core.x, core.h, "norm2_w_2", (scale2, shift2))
        stage_ffn(nc, core, dram["ffn_up_2"], dram["ffn_down_2"], conv=core.v("conv_ffn_2", 0, 3 * FT),
                  scale=gate2)
    stage_norm(nc, core, core.x, core.x, "norm_f_w_2")


Z3 = {"q": 0, "k": 512, "r": 1024, "z": 2048, "xbc": 4096, "lr": 7168, "dt": 7200}
ZC = {"k": 0, "xb": 512, "lr": 3072, "dt": 3104}
RANK = 16
GLA_LEVELS = 7
SSM_TILES = 16
SH = 32


def stage_log_gates(nc, core, lr, names, toks, chunk, b):
    with ExitStack() as ctx:
        s = core.scope(nc, ctx, "lgate")
        low = s.sb("low", [RANK, 2, toks])
        up = s.sb("up", [RANK, 2, 512])
        pre, e = s.sb("pre", [P, 4, toks]), s.sb("e", [P, 4, toks])
        reset = s.sb("reset", [P, 2, toks])
        acc = s.ps("acc", [P, 2, 4, 512])
        loaded, product, step, negated, logged, folded, acted = (
            s.sem(x) for x in ("loaded", "product", "step", "negated", "logged", "folded", "acted"))
        with nc.Block() as block:
            @block.sync
            def _(sp):
                for d in range(2):
                    sp.dma_start(low[:, d], lr[RANK * d:RANK * (d + 1)]).then_inc(loaded, 16)
                    sp.dma_start(up[:, d], core.dram[names[d]]).then_inc(loaded, 16)

            @block.tensor
            def _(pe):
                pe.wait_ge(loaded, 64)
                for d in range(2):
                    for j in range(4):
                        last = nc.tensor.matmul(acc[:, d, j, :toks], up[:, d, j * P:(j + 1) * P], low[:, d],
                                                start=True, stop=True)
                    last.then_inc(product, 1)

            @block.scalar
            def _(act):
                for d in range(2):
                    act.wait_ge(negated, d + 1)
                    nc.scalar.activation(e[:], e[:], ACT.Exp).then_inc(acted, 1)
                    act.wait_ge(acted, 2 * d + 1)
                    nc.scalar.activation(e[:], e[:], ACT.Ln, bias=1.0).then_inc(acted, 1)

            @block.vector
            def _(dve):
                done = Steps(dve, step)
                v = nc.vector
                edge = reset[:].rearrange("p d (n c) -> p d n c", c=chunk)
                done(v.memset(reset[:], 1.0))
                done.mark(v.memset(edge[:, 0, :, 0:1], 0.0))
                done(v.memset(edge[:, 1, :, chunk - 1:chunk], 0.0))
                for d in range(2):
                    dve.wait_ge(product, d + 1)
                    for j in range(4):
                        done.mark(v.tensor_scalar(pre[:, j], acc[:, d, j, :toks],
                                                  core.v(("gla_bias_f", "gla_bias_b")[d], j), None, ALU.add))
                    done.wait()
                    v.scalar_tensor_tensor(out=e[:], in0=pre[:], scalar=-1.0, in1=pre[:], op0=ALU.mult,
                                           op1=ALU.min).then_inc(negated, 1)
                    dve.wait_ge(acted, 2 * d + 2)
                    dve.wait_ge(negated, d + 1)
                    done(v.scalar_tensor_tensor(out=pre[:], in0=pre[:], scalar=0.0, in1=e[:], op0=ALU.min,
                                                op1=ALU.subtract))
                    done(v.tensor_scalar(pre[:], pre[:], 1.0 / 16, None, ALU.mult))
                    for j in range(4):
                        way = slice(None, None, -1) if d else slice(None)
                        done.mark(v.tensor_tensor_scan(b[:, d, j][:, way], reset[:, d][:, way], pre[:, j][:, way],
                                                       0.0, ALU.mult, ALU.add))
                    done.wait()


def stage_gla_context(nc, core, v_ctx, start):
    with ExitStack() as ctx:
        s = core.scope(nc, ctx, "gctx")
        b = s.sb("b", [P, 2, 4, CTX])
        stage_log_gates(nc, core, core.dram["zc"][ZC["lr"]:ZC["lr"] + 32], ("gla_up_f", "gla_up_b"), CTX, CTX, b)
        k = s.sb("k", [P, 4, CTX])
        k_tok = s.sb("k_tok", [P, 2, 2, 512])
        turned = s.ps("turned", [P, 2, 2, 512])
        acc = s.ps("acc", [P, 4, 512])
        loaded, diff, exped, weighted, turned_ready, copied, product, step, freed = (
            s.sem(x) for x in ("loaded", "diff", "exped", "weighted", "turned_ready", "copied", "product", "step",
                               "freed"))
        with nc.Block() as block:
            @block.sync
            def _(sp):
                sp.dma_start(k[:], rows(core.dram["zc"][ZC["k"]:ZC["k"] + 512])).then_inc(loaded, 16)

            @block.vector
            def _(dve):
                v = nc.vector
                for d in range(2):
                    at = 0 if d else CTX - 1
                    last = s.sb(f"last{d}", [P, 4, 1])
                    v.tensor_copy(last[:], b[:, d, :, at:at + 1]).then_inc(step, 1)
                    dve.wait_ge(step, d + 1)
                    v.tensor_tensor(b[:, d], last[:].broadcast_to([P, 4, CTX]), b[:, d],
                                    ALU.subtract).then_inc(diff, 1)
                dve.wait_ge(loaded, 16)
                for d in range(2):
                    dve.wait_ge(exped, d + 1)
                    v.tensor_tensor(b[:, d], b[:, d], k[:], ALU.mult).then_inc(weighted, 1)
                for d in range(2):
                    dve.wait_ge(turned_ready, d + 1)
                    v.tensor_copy(k_tok[:, d], turned[:, d]).then_inc(copied, 1)
                for n in range(8):
                    d, h = n // 4, n % 4
                    dve.wait_ge(product, n + 1)
                    v.tensor_copy(start[:, d, h], acc[:, n % 4, :256]).then_inc(freed, 1)

            @block.scalar
            def _(act):
                for d in range(2):
                    act.wait_ge(diff, d + 1)
                    nc.scalar.activation(b[:, d], b[:, d], ACT.Exp).then_inc(exped, 1)

            @block.tensor
            def _(pe):
                for d in range(2):
                    pe.wait_ge(weighted, d + 1)
                    for t in range(2):
                        for h in range(4):
                            last = nc.tensor.transpose(turned[:, d, t, h * P:(h + 1) * P],
                                                       b[:, d, h, t * P:(t + 1) * P], core.ident[:])
                    last.then_inc(turned_ready, 1)
                for n in range(8):
                    d, h = n // 4, n % 4
                    pe.wait_ge(copied, d + 1)
                    if n >= 4:
                        pe.wait_ge(freed, n - 3)
                    for t in range(2):
                        last = nc.tensor.matmul(acc[:, n % 4, :256], k_tok[:, d, t, h * P:(h + 1) * P],
                                                v_ctx[:, t, h * 256:(h + 1) * 256], start=t == 0, stop=t == 1)
                    last.then_inc(product, 1)


def stage_gla_levels(nc, core, q, k, b, attn):
    with ExitStack() as ctx:
        s = core.scope(nc, ctx, "levels")
        x = s.sb("x", [P, 2, 4, T])
        masks = s.sb("masks", [P, 2 * GLA_LEVELS + 1, P], I32)
        acc = s.ps("acc", [P, 2, 4, 512])
        loaded, diffed, exped, weighted, product, taken, cleared, doubled = (
            s.sem(n) for n in ("loaded", "diffed", "exped", "weighted", "product", "taken", "cleared", "doubled"))
        rounds = [(d, n) for d in range(2) for n in range(GLA_LEVELS)]

        def sides(n, tile):
            w = 2 << n
            both = tile.rearrange("p h (m w) -> p (h m) w", w=w)
            return both[:, :, :w // 2], both[:, :, w // 2:]

        with nc.Block() as block:
            @block.sync
            def _(sp):
                sp.dma_start(masks[:], core.dram["masks"]).then_inc(loaded, 16)

            @block.gpsimd
            def _(pool):
                for i, (d, n) in enumerate(rounds):
                    if i >= 2:
                        pool.wait_ge(product, i)
                    left, right = sides(n, x[:, i % 2])
                    bl, br = sides(n, b[:, d])
                    half = 1 << n
                    mid = br[:, :, 0:1] if d else bl[:, :, half - 1:half]
                    mid = mid.broadcast_to(list(bl.shape))
                    if d:
                        nc.gpsimd.tensor_tensor(left, bl, mid, ALU.subtract).then_inc(diffed, 1)
                        nc.gpsimd.tensor_tensor(right, mid, br, ALU.subtract).then_inc(diffed, 1)
                    else:
                        nc.gpsimd.tensor_tensor(left, mid, bl, ALU.subtract).then_inc(diffed, 1)
                        nc.gpsimd.tensor_tensor(right, br, mid, ALU.subtract).then_inc(diffed, 1)

            @block.scalar
            def _(act):
                for i in range(len(rounds)):
                    act.wait_ge(diffed, 2 * i + 2)
                    nc.scalar.activation(x[:, i % 2], x[:, i % 2], ACT.Exp).then_inc(exped, 1)

            @block.vector
            def _(dve):
                v = nc.vector

                def take(i):
                    for h in range(4):
                        dve.wait_ge(product, i + 1)
                        by = masks[:, i:i + 1].broadcast_to([P, 4, P])
                        src = acc[:, (i + 1) % 2, h].rearrange("p (c t) -> p c t", t=P)
                        if i == 0:
                            v.tensor_copy(attn[:, h], src).then_inc(cleared, 1)
                            dve.wait_ge(cleared, h + 1)
                            v.tensor_tensor(attn[:, h], attn[:, h], src, ALU.add).then_inc(taken, 1)
                        else:
                            v.copy_predicated(attn[:, h], by, src).then_inc(taken, 1)
                    dve.wait_ge(taken, 4 * i + 4)

                dve.wait_ge(loaded, 16)
                for i, (d, n) in enumerate(rounds):
                    dve.wait_ge(exped, i + 1)
                    left, right = sides(n, x[:, i % 2])
                    kl, kr = sides(n, k[:])
                    ql, qr = sides(n, q[:])
                    v.tensor_tensor(left, left, ql if d else kl, ALU.mult).then_inc(weighted, 1)
                    v.tensor_tensor(right, right, kr if d else qr, ALU.mult).then_inc(weighted, 1)
                    take(i)
                take(len(rounds))

            @block.tensor
            def _(pe):
                def products(i, lhs, rhs):
                    if i >= 2:
                        pe.wait_ge(taken, 4 * (i - 1))
                    for h in range(4):
                        for c in range(4):
                            at = slice(c * P, (c + 1) * P)
                            last = nc.tensor.matmul(acc[:, (i + 1) % 2, h, at], lhs[:, h, at], rhs[:, h, at],
                                                    start=True, stop=True)
                    last.then_inc(product, 1)

                products(0, k, q)
                for i in range(len(rounds)):
                    pe.wait_ge(weighted, 2 * i + 2)
                    products(i + 1, x[:, i % 2], x[:, i % 2])


def stage_gla_states(nc, core, q, k, b, v_tok, start, states):
    with ExitStack() as ctx:
        s = core.scope(nc, ctx, "gstate")
        kd = s.sb("kd", [P, 2, 4, T])
        edge = s.sb("edge", [P, 2, 4, 4])
        k_tok = s.sb("k_tok", [P, 2, 4, 512])
        turned = s.ps("turned", [P, 2, 512])
        acc = s.ps("acc", [P, 4, 512])
        (picked, diffed, exped, weighted, turned_ready, copied, product, advanced, scaled, step) = (
            s.sem(n) for n in ("picked", "diffed", "exped", "weighted", "turned_ready", "copied", "product",
                               "advanced", "scaled", "step"))
        with nc.Block() as block:
            @block.vector
            def _(dve):
                v = nc.vector
                for d in range(2):
                    at = 0 if d else P - 1
                    view = b[:, d].rearrange("p h (c t) -> p h c t", t=P)
                    v.tensor_copy(edge[:, d], view[:, :, :, at]).then_inc(picked, 1)
                    dve.wait_ge(picked, d + 1)
                    to = kd[:, d].rearrange("p h (c t) -> p h c t", t=P)
                    for h in range(4):
                        v.tensor_tensor(to[:, h], edge[:, d, h].unsqueeze(2).broadcast_to([P, 4, P]), view[:, h],
                                        ALU.subtract).then_inc(diffed, 1)
                for d in range(2):
                    dve.wait_ge(exped, 3 * d + 2)
                    v.tensor_tensor(kd[:, d], kd[:, d], k[:], ALU.mult).then_inc(weighted, 1)
                    dve.wait_ge(exped, 3 * d + 3)
                    v.tensor_tensor(b[:, d], b[:, d], q[:], ALU.mult).then_inc(scaled, 1)
                for n in range(8):
                    d, c = n // 4, n % 4
                    dve.wait_ge(turned_ready, n + 1)
                    v.tensor_copy(k_tok[:, d, c], turned[:, n % 2]).then_inc(copied, 1)
                v.tensor_copy(states[:, 0, :, 0], start[:, 0]).then_inc(step, 1)
                v.tensor_copy(states[:, 1, :, 3], start[:, 1]).then_inc(step, 1)
                dve.wait_ge(step, 2)
                for n in range(24):
                    i, d, h = n // 8, n // 4 % 2, n % 4
                    now, nxt = (3 - i, 2 - i) if d else (i, i + 1)
                    dve.wait_ge(product, n + 1)
                    if n >= 8:
                        dve.wait_ge(advanced, n - 7)
                    v.scalar_tensor_tensor(out=states[:, d, h, nxt], in0=states[:, d, h, now],
                                           scalar=edge[:, d, h, now:now + 1], in1=acc[:, n % 4, :256],
                                           op0=ALU.mult, op1=ALU.add).then_inc(advanced, 1)

            @block.scalar
            def _(act):
                for d in range(2):
                    act.wait_ge(diffed, 4 * d + 4)
                    nc.scalar.activation(edge[:, d], edge[:, d], ACT.Exp).then_inc(exped, 1)
                    nc.scalar.activation(kd[:, d], kd[:, d], ACT.Exp).then_inc(exped, 1)
                    nc.scalar.activation(b[:, d], b[:, d], ACT.Exp).then_inc(exped, 1)

            @block.tensor
            def _(pe):
                for n in range(8):
                    d, c = n // 4, n % 4
                    pe.wait_ge(weighted, d + 1)
                    if n >= 2:
                        pe.wait_ge(copied, n - 1)
                    for h in range(4):
                        last = nc.tensor.transpose(turned[:, n % 2, h * P:(h + 1) * P],
                                                   kd[:, d, h, c * P:(c + 1) * P], core.ident[:])
                    last.then_inc(turned_ready, 1)
                pe.wait_ge(copied, 8)
                for n in range(24):
                    i, d, h = n // 8, n // 4 % 2, n % 4
                    c = 3 - i if d else i
                    if n >= 4:
                        pe.wait_ge(advanced, n - 3)
                    nc.tensor.matmul(acc[:, n % 4, :256], k_tok[:, d, c, h * P:(h + 1) * P],
                                     v_tok[:, c, h * 256:(h + 1) * 256], start=True, stop=True
                                     ).then_inc(product, 1)


def stage_gla_out(nc, core, b, v_tok, states, attn, y):
    with ExitStack() as ctx:
        s = core.scope(nc, ctx, "glaout")
        with ExitStack() as inner:
            s1 = core.scope(nc, inner, "mix")
            acc = s1.ps("acc", [P, 8, 512])
            product, copied = s1.sem("product"), s1.sem("copied")
            with nc.Block() as block:
                @block.tensor
                def _(pe):
                    for n in range(8):
                        h, e = n // 2, n % 2
                        to = slice(h * 256 + e * P, h * 256 + (e + 1) * P)
                        for c in range(4):
                            at = slice(c * P, (c + 1) * P)
                            nc.tensor.matmul(acc[:, n, at], v_tok[:, c, to], attn[:, h, c], start=True, stop=False)
                            for d in range(2):
                                last = nc.tensor.matmul(acc[:, n, at], states[:, d, h, c, e * P:(e + 1) * P],
                                                        b[:, d, h, at], start=False, stop=d == 1)
                        last.then_inc(product, 1)

                @block.vector
                def _(dve):
                    for n in range(8):
                        dve.wait_ge(product, n + 1)
                        nc.vector.tensor_copy(y[:, n], acc[:, n]).then_inc(copied, 1)
        rstd = s.sb("rstd", [P, 4, T])
        stage_rstd(nc, core, y, rstd, 2, core.ones, 256, EPS)
        r = s.sb("r", [P, 8, T])
        loaded, step = s.sem("loaded"), s.sem("step")
        with nc.Block() as block:
            @block.sync
            def _(sp):
                sp.dma_start(r[:], rows(core.dram["z"][Z3["r"]:Z3["r"] + 1024])).then_inc(loaded, 16)

            @block.vector
            def _(dve):
                done = Steps(dve, step)
                for n in range(8):
                    done.mark(nc.vector.scalar_tensor_tensor(out=y[:, n], in0=y[:, n],
                                                             scalar=core.v("gla_norm_w", n % 2),
                                                             in1=rstd[:, n // 2], op0=ALU.mult, op1=ALU.mult))
                done.wait()
                dve.wait_ge(loaded, 16)
                done(nc.vector.tensor_tensor(y[:], y[:], r[:], ALU.mult))


def stage_load(nc, core, pairs):
    with ExitStack() as ctx:
        s = core.scope(nc, ctx, "load")
        loaded = s.sem("loaded")
        with nc.Block() as block:
            @block.sync
            def _(sp):
                for dst, src in pairs:
                    sp.dma_start(dst, src).then_inc(loaded, 16)
                sp.wait_ge(loaded, 16 * len(pairs))


def stage_gla(nc, core, v_tok, v_ctx, y):
    with ExitStack() as ctx:
        s = core.scope(nc, ctx, "gla")
        b = s.sb("b", [P, 2, 4, T])
        start = s.sb("start", [P, 2, 4, 256])
        states = s.sb("states", [P, 2, 4, 4, 256])
        attn = s.sb("attn", [P, 4, 4, P])
        stage_gla_context(nc, core, v_ctx, start)
        z = core.dram["z"]
        stage_log_gates(nc, core, z[Z3["lr"]:Z3["lr"] + 32], ("gla_up_f", "gla_up_b"), T, P, b)
        with ExitStack() as inner:
            s1 = core.scope(nc, inner, "qk")
            q, k = s1.sb("q", [P, 4, T]), s1.sb("k", [P, 4, T])
            scaled = s1.sem("scaled")
            stage_load(nc, core, [(q[:], rows(z[0:512])), (k[:], rows(z[512:1024]))])
            with nc.Block() as block:
                @block.vector
                def _(dve):
                    nc.vector.tensor_scalar(q[:], q[:], float(P) ** -0.5, None, ALU.mult).then_inc(scaled, 1)
            stage_gla_levels(nc, core, q, k, b, attn)
            stage_gla_states(nc, core, q, k, b, v_tok, start, states)
        stage_gla_out(nc, core, b, v_tok, states, attn, y)


def stage_centred_conv(nc, core, src, dst, tiles, toks, width):
    n = tiles // 4
    with ExitStack() as ctx:
        s = core.scope(nc, ctx, "cconv")
        raw, out = s.sb("raw", [P, 2, 4, toks]), s.sb("out", [P, 2, 4, toks])
        loaded, step, conved, bent = (s.sem(x) for x in ("loaded", "step", "conved", "bent"))
        stored = [s.sem(f"stored{i}") for i in range(2)]
        with nc.Block() as block:
            @block.sync
            def _(sp):
                for i in range(n):
                    if i >= 2:
                        sp.wait_ge(conved, 4 * (i - 1))
                    if i:
                        sp.wait_ge(loaded, 16 * i)
                    sp.dma_start(raw[:, i % 2], rows(src[512 * i:512 * (i + 1)])).then_inc(loaded, 16)

            @block.vector
            def _(dve):
                done = Steps(dve, step)
                for i in range(n):
                    dve.wait_ge(loaded, 16 * (i + 1))
                    if i >= 2:
                        dve.wait_ge(stored[i % 2], 16 * (i // 2))
                    for j in range(4):
                        done.mark(nc.vector.tensor_scalar(out[:, i % 2, j], raw[:, i % 2, j],
                                                          core.v("conv_w_3", 4 * (4 * i + j) + 2),
                                                          core.v("conv_b_3", 4 * i + j), ALU.mult, ALU.add))
                    done.wait()
                    for tap, lag in ((0, 2), (1, 1), (3, -1)):
                        for j in range(4):
                            a = raw[:, i % 2, j].rearrange("p (r w) -> p r w", w=width)
                            o = out[:, i % 2, j].rearrange("p (r w) -> p r w", w=width)
                            if lag > 0:
                                a, o = a[:, :, :width - lag], o[:, :, lag:]
                            else:
                                a, o = a[:, :, 1:], o[:, :, :width - 1]
                            ins = nc.vector.scalar_tensor_tensor(
                                out=o, in0=a, scalar=core.v("conv_w_3", 4 * (4 * i + j) + tap), in1=o,
                                op0=ALU.mult, op1=ALU.add)
                            if tap < 3:
                                done.mark(ins)
                            else:
                                ins.then_inc(conved, 1)
                        if tap < 3:
                            done.wait()

            @block.scalar
            def _(act):
                for i in range(n):
                    act.wait_ge(conved, 4 * (i + 1))
                    nc.scalar.activation(out[:, i % 2], out[:, i % 2], ACT.Silu).then_inc(bent, 1)
                    act.wait_ge(bent, i + 1)
                    act.dma_start(rows(dst[512 * i:512 * (i + 1)]), out[:, i % 2]).then_inc(stored[i % 2], 16)
                for i in range(min(n, 2)):
                    act.wait_ge(stored[i], 16 * ((n + 1 - i) // 2))


def stage_steps(nc, core, src, toks, chunk, dt_tok, cum_tok, cum_dram=None, edge_dram=None):
    n = toks // P
    with ExitStack() as ctx:
        s = core.scope(nc, ctx, "steps")
        dt, cum = s.sb("dt", [64, toks]), s.sb("cum", [64, toks])
        reset = s.sb("reset", [64, toks])
        rate = s.sb("rate", [64, 1])
        edges = s.sb("edges", [64, toks // chunk])
        acc = s.ps("acc", [P, 2, 512])
        rated, biased, step, summed, turned, copied, stored = (
            s.sem(x) for x in ("rated", "biased", "step", "summed", "turned", "copied", "stored"))
        stage_load(nc, core, [(dt[:], src)])
        with nc.Block() as block:
            @block.vector
            def _(dve):
                nc.vector.tensor_scalar(dt[:], dt[:], core.v("dt_bias_3")[:64], None, ALU.add).then_inc(biased, 1)
        stage_softplus(nc, core, dt, 64, toks)
        with nc.Block() as block:
            @block.scalar
            def _(act):
                nc.scalar.activation(rate[:], core.v("a_log_3")[:64], ACT.Exp).then_inc(rated, 1)

            @block.vector
            def _(dve):
                done = Steps(dve, step)
                v = nc.vector
                edge = reset[:].rearrange("p (n c) -> p n c", c=chunk)
                view = cum[:].rearrange("p (n c) -> p n c", c=chunk)
                done(v.memset(reset[:], 1.0))
                done.mark(v.memset(edge[:32, :, 0:1], 0.0))
                done.mark(v.memset(edge[32:64, :, chunk - 1:chunk], 0.0))
                dve.wait_ge(rated, 1)
                work = s.sb("work", [64, toks])
                done(v.tensor_scalar(work[:], dt[:], rate[:], -1.0, ALU.mult, ALU.mult))
                v.tensor_tensor_scan(cum[:32], reset[:32], work[:32], 0.0, ALU.mult, ALU.add).then_inc(summed, 1)
                v.tensor_tensor_scan(cum[32:64, ::-1], reset[32:64, ::-1], work[32:64, ::-1], 0.0, ALU.mult,
                                     ALU.add).then_inc(summed, 1)
                dve.wait_ge(summed, 2)
                v.tensor_copy(edges[:32], view[:32, :, chunk - 1]).then_inc(summed, 1)
                v.tensor_copy(edges[32:64], view[32:64, :, 0]).then_inc(summed, 1)
                dve.wait_ge(turned, 1)
                v.tensor_copy(dt_tok[:], acc[:, 0, :64 * n].rearrange("p (c h) -> p c h", h=64)
                              ).then_inc(copied, 1)
                v.tensor_copy(cum_tok[:], acc[:, 1, :64 * n].rearrange("p (c h) -> p c h", h=64)
                              ).then_inc(copied, 1)

            @block.tensor
            def _(pe):
                pe.wait_ge(summed, 2)
                for a, tile in enumerate((dt, cum)):
                    for c in range(n):
                        last = nc.tensor.transpose(acc[:, a, c * 64:(c + 1) * 64], tile[:, c * P:(c + 1) * P],
                                                   core.ident[:64, :64])
                last.then_inc(turned, 1)

            @block.sync
            def _(sp):
                sp.wait_ge(summed, 4)
                sp.dma_start(edge_dram, edges[:]).then_inc(stored, 16)
                if cum_dram is not None:
                    sp.dma_start(cum_dram, cum[:]).then_inc(stored, 16)
                sp.wait_ge(stored, 32 if cum_dram is not None else 16)


def spread(dram2, parts=P):
    shape = list(dram2.shape)
    return dram2.unsqueeze(0).broadcast_to([parts] + shape)


def stage_ssm_context(nc, core):
    dram = core.dram
    with ExitStack() as ctx:
        s = core.scope(nc, ctx, "sctx")
        dt_tok, cum_tok = s.sb("dt_tok", [P, 2, 64]), s.sb("cum_tok", [P, 2, 64])
        total = s.sb("total", [P, 64])
        stage_centred_conv(nc, core, dram["zc"][ZC["xb"]:ZC["xb"] + 2560], dram["xc"], 20, CTX, CTX)
        stage_steps(nc, core, dram["zc"][ZC["dt"]:ZC["dt"] + 64], CTX, CTX, dt_tok, cum_tok,
                    edge_dram=dram["edge_c"])
        w = s.sb("w", [P, 2, 64])
        x = s.sb("x", [P, 4, 5, CTX])
        x_tok = s.sb("x_tok", [P, 2, 2, 5 * P])
        xw = s.sb("xw", [P, 2, 2, 512])
        out = s.sb("out", [P, 2, 512])
        turned = s.ps("turned", [P, 2, 1024])
        acc = s.ps("acc", [P, 2, 512])
        (diffed, exped, ready, turned_ready, copied, weighted, product, saved) = (
            s.sem(n) for n in ("diffed", "exped", "ready", "turned_ready", "copied", "weighted", "product", "saved"))
        stored = s.sem("stored")
        stage_load(nc, core, [(total[:], spread(dram["edge_c"].rearrange("h a -> (h a)")))]
                   + [(x[:, g, :4], rows(dram["xc"][512 * g:512 * (g + 1)])) for g in range(4)]
                   + [(x[:, g, 4], dram["xc"][2048 + P * g:2048 + P * (g + 1)]) for g in range(4)])
        with nc.Block() as block:
            @block.vector
            def _(dve):
                v = nc.vector
                v.tensor_tensor(w[:], total[:].unsqueeze(1).broadcast_to([P, 2, 64]), cum_tok[:],
                                ALU.subtract).then_inc(diffed, 1)
                dve.wait_ge(exped, 1)
                v.tensor_tensor(w[:], w[:], dt_tok[:], ALU.mult).then_inc(ready, 1)
                dve.wait_ge(ready, 1)
                for g in range(4):
                    for t in range(2):
                        n = 2 * g + t
                        dve.wait_ge(turned_ready, n + 1)
                        v.tensor_copy(x_tok[:, g % 2, t], turned[:, t, :5 * P]).then_inc(copied, 1)
                    dve.wait_ge(copied, 2 * g + 2)
                    for d in range(2):
                        if g or d:
                            dve.wait_ge(product, 2 * g + d - 1 if 2 * g + d > 1 else 1)
                        for t in range(2):
                            by = w[:, t, 32 * d + 8 * g:32 * d + 8 * g + 8].unsqueeze(2).broadcast_to([P, 8, 64])
                            v.tensor_tensor(xw[:, d, t].rearrange("p (h c) -> p h c", c=64),
                                            x_tok[:, g % 2, t, :512].rearrange("p (h c) -> p h c", c=64), by,
                                            ALU.mult).then_inc(weighted, 1)

            @block.scalar
            def _(act):
                act.wait_ge(diffed, 1)
                nc.scalar.activation(w[:], w[:], ACT.Exp).then_inc(exped, 1)
                for n in range(8):
                    act.wait_ge(product, n + 1)
                    if n >= 2:
                        act.wait_ge(stored, 16 * (n - 1))
                    nc.scalar.activation(out[:, n % 2], acc[:, n % 2], ACT.Copy).then_inc(saved, 1)
                    act.wait_ge(saved, n + 1)
                    if n:
                        act.wait_ge(stored, 16 * n)
                    act.dma_start(dram["s0"][n % 2, n // 2], out[:, n % 2]).then_inc(stored, 16)
                act.wait_ge(stored, 128)

            @block.tensor
            def _(pe):
                for g in range(4):
                    for t in range(2):
                        if g:
                            pe.wait_ge(copied, 2 * g + t - 1)
                        for j in range(5):
                            last = nc.tensor.transpose(turned[:, t, j * P:(j + 1) * P],
                                                       x[:, g, j, t * P:(t + 1) * P], core.ident[:])
                        last.then_inc(turned_ready, 1)
                    for d in range(2):
                        n = 2 * g + d
                        pe.wait_ge(weighted, 2 * n + 2)
                        if n >= 2:
                            pe.wait_ge(saved, n - 1)
                        for t in range(2):
                            last = nc.tensor.matmul(acc[:, d], x_tok[:, g % 2, t, 512:], xw[:, d, t],
                                                    start=t == 0, stop=t == 1)
                        last.then_inc(product, 1)


def stage_ssm_group(nc, core, g, s, dt_tok, cum_tok, ecum, edges):
    dram = core.dram
    x, bc_ = s["x"], s["bc"]
    x_tok, b_tok = s["x_tok"], s["b_tok"]
    xdt, xw, states, cb, y_tok, y, dts = (s[n] for n in ("xdt", "xw", "states", "cb", "y_tok", "y", "dts"))
    with ExitStack() as ctx:
        o = core.scope(nc, ctx, "sprep")
        turned = o.ps("turned", [P, 2, 1024])
        gram = o.ps("gram", [P, 512])
        acc = o.ps("acc", [P, 2, 512])
        w = o.sb("w", [P, 2, 4, 8])
        heads = [slice(32 * d + 8 * g, 32 * d + 8 * g + 8) for d in range(2)]
        (loaded, turned_ready, copied, grammed, masked, diffed, exped, weighted, product, advanced, step,
         scaled) = (o.sem(n) for n in ("loaded", "turned_ready", "copied", "grammed", "masked", "diffed", "exped",
                                       "weighted", "product", "advanced", "step", "scaled"))
        with nc.Block() as block:
            @block.sync
            def _(sp):
                sp.dma_start(x[:], rows(dram["xbc"][512 * g:512 * (g + 1)])).then_inc(loaded, 16)
                sp.dma_start(bc_[:, 0], dram["xbc"][2048 + P * g:2048 + P * (g + 1)]).then_inc(loaded, 16)
                sp.dma_start(bc_[:, 1], dram["xbc"][2560 + P * g:2560 + P * (g + 1)]).then_inc(loaded, 16)
                sp.dma_start(states[:, 0, 0], dram["s0"][0, g]).then_inc(loaded, 16)
                sp.dma_start(states[:, 1, 3], dram["s0"][1, g]).then_inc(loaded, 16)

            @block.tensor
            def _(pe):
                pe.wait_ge(loaded, 80)
                for c in range(4):
                    at = slice(c * P, (c + 1) * P)
                    last = nc.tensor.matmul(gram[:, at], bc_[:, 0, at], bc_[:, 1, at], start=True, stop=True)
                last.then_inc(grammed, 1)
                for c in range(4):
                    at = slice(c * P, (c + 1) * P)
                    if c >= 2:
                        pe.wait_ge(copied, 2 * (c - 1))
                    for j in range(4):
                        nc.tensor.transpose(turned[:, c % 2, j * P:(j + 1) * P], x[:, j, at], core.ident[:])
                    nc.tensor.transpose(turned[:, c % 2, 512:640], bc_[:, 0, at],
                                        core.ident[:]).then_inc(turned_ready, 1)
                for n in range(6):
                    i, d = n // 2, n % 2
                    c = 3 - i if d else i
                    pe.wait_ge(weighted, 2)
                    if n >= 2:
                        pe.wait_ge(advanced, n - 1)
                    nc.tensor.matmul(acc[:, d], b_tok[:, c], xw[:, d, c], start=True, stop=True
                                     ).then_inc(product, 1)

            @block.scalar
            def _(act):
                for d in range(2):
                    act.wait_ge(diffed, d + 1)
                    nc.scalar.activation(w[:, d], w[:, d], ACT.Exp).then_inc(exped, 1)

            @block.gpsimd
            def _(pool):
                pool.wait_ge(masked, 2)
                for d in range(2):
                    nc.gpsimd.affine_select(out=cb[:, d], in_=cb[:, d],
                                            pattern=[[0, 4], [-1, P] if d else [1, P]], compare_op=ALU.is_ge,
                                            fill=0.0, base=0, channel_multiplier=1 if d else -1
                                            ).then_inc(step, 1)

            @block.vector
            def _(dve):
                v = nc.vector
                for d in range(2):
                    v.tensor_tensor(w[:, d], edges[:, heads[d], :].rearrange("p h c -> p c h"),
                                    cum_tok[:, :, heads[d]], ALU.subtract).then_inc(diffed, 1)
                dve.wait_ge(grammed, 1)
                for d in range(2):
                    v.tensor_copy(cb[:, d].rearrange("p c t -> p (c t)"), gram[:]).then_inc(masked, 1)
                for c in range(4):
                    dve.wait_ge(turned_ready, c + 1)
                    v.tensor_copy(x_tok[:, c], turned[:, c % 2, :512]).then_inc(copied, 1)
                    v.tensor_copy(b_tok[:, c], turned[:, c % 2, 512:640]).then_inc(copied, 1)
                dve.wait_ge(copied, 8)

                def by_head(dst, src, by):
                    return v.tensor_tensor(dst.rearrange("p c (h k) -> p (c h) k", k=64),
                                           src.rearrange("p c (h k) -> p (c h) k", k=64),
                                           by.unsqueeze(2).broadcast_to([P, 32, 64]), ALU.mult)

                for d in range(2):
                    small = dts[:, d]
                    v.tensor_copy(small, dt_tok[:, :, heads[d]]).then_inc(scaled, 1)
                    dve.wait_ge(scaled, 2 * d + 1)
                    by_head(xdt[:, d], x_tok[:], small.rearrange("p c h -> p (c h)")).then_inc(scaled, 1)
                    dve.wait_ge(exped, d + 1)
                    dve.wait_ge(scaled, 2 * d + 2)
                    by_head(xw[:, d], xdt[:, d], w[:, d].rearrange("p c h -> p (c h)")).then_inc(weighted, 1)
                for n in range(6):
                    i, d = n // 2, n % 2
                    now, nxt = (3 - i, 2 - i) if d else (i, i + 1)
                    dve.wait_ge(product, n + 1)
                    by = ecum[:, heads[d], now:now + 1].broadcast_to([P, 8, 64])
                    if n >= 2:
                        dve.wait_ge(advanced, n - 1)
                    v.tensor_tensor(states[:, d, nxt].rearrange("p (h k) -> p h k", k=64),
                                    states[:, d, now].rearrange("p (h k) -> p h k", k=64), by,
                                    ALU.mult).then_inc(scaled, 1)
                    dve.wait_ge(scaled, 4 + n + 1)
                    v.tensor_tensor(states[:, d, nxt], states[:, d, nxt], acc[:, d], ALU.add).then_inc(advanced, 1)

    with ExitStack() as ctx:
        o = core.scope(nc, ctx, "sout")
        cum = o.sb("cum", [P, 2, 2, 8, P])
        seg = o.sb("seg", [P, 2, 8, P])
        tmp = o.sb("tmp", [P, 2, 512])
        intra = o.ps("intra", [P, 2, 512])
        inter = o.ps("inter", [P, 2, 2, 512])
        turned = o.ps("turned", [P, 2, 512])
        etok = s["etok"]
        loaded = [o.sem(f"loaded{i}") for i in range(2)]
        (diffed, exped, masked, y_ready, inter_ready, read, made, turned_ready, copied, stored, tmp_ready,
         clipped) = (
            o.sem(n) for n in ("diffed", "exped", "masked", "y_ready", "inter_ready", "read", "made",
                               "turned_ready", "copied", "stored", "tmp_ready", "clipped"))
        def turn(pe, c):
            pe.wait_ge(read, 2 * c + 2)
            if c >= 2:
                pe.wait_ge(copied, c - 1)
            for j in range(4):
                last = nc.tensor.transpose(turned[:, c % 2, j * P:(j + 1) * P],
                                           y_tok[:, c % 2, j * P:(j + 1) * P], core.ident[:])
            last.then_inc(turned_ready, 1)

        with nc.Block() as block:
            @block.sync
            def _(sp):
                for c in range(4):
                    if c >= 2:
                        sp.wait_ge(diffed, 2 * (c - 1))
                    for d in range(2):
                        sp.dma_start(cum[:, c % 2, d],
                                     spread(dram["cum"][32 * d + 8 * g:32 * d + 8 * g + 8, c * P:(c + 1) * P])
                                     ).then_inc(loaded[c % 2], 16)
                sp.wait_ge(copied, 4)
                sp.dma_start(rows(dram["y_ssm"][512 * g:512 * (g + 1)]), y[:]).then_inc(stored, 16)
                sp.wait_ge(stored, 16)

            @block.gpsimd
            def _(pool):
                for n in range(8):
                    c, d = n // 2, n % 2
                    pool.wait_ge(loaded[c % 2], 32 * (c // 2 + 1))
                    if n >= 2:
                        pool.wait_ge(y_ready, n - 1)
                    by = cum_tok[:, c, 32 * d + 8 * g:32 * d + 8 * g + 8].unsqueeze(2).broadcast_to([P, 8, P])
                    nc.gpsimd.tensor_tensor(seg[:, n % 2], by, cum[:, c % 2, d], ALU.subtract).then_inc(diffed, 1)

            @block.scalar
            def _(act):
                for n in range(8):
                    act.wait_ge(diffed, n + 1)
                    nc.scalar.activation(seg[:, n % 2], seg[:, n % 2], ACT.Relu).then_inc(clipped, 1)
                    act.wait_ge(clipped, n + 1)
                    nc.scalar.activation(seg[:, n % 2], seg[:, n % 2], ACT.Exp, scale=-1.0).then_inc(exped, 1)
                    if n % 2:
                        c = n // 2
                        if c:
                            act.wait_ge(turned_ready, c)
                            nc.scalar.activation(y[:, :, (c - 1) * P:c * P],
                                                 turned[:, (c - 1) % 2].rearrange("p (j t) -> p j t", t=P),
                                                 ACT.Copy).then_inc(copied, 1)
                act.wait_ge(turned_ready, 4)
                nc.scalar.activation(y[:, :, 3 * P:], turned[:, 1].rearrange("p (j t) -> p j t", t=P),
                                     ACT.Copy).then_inc(copied, 1)

            @block.vector
            def _(dve):
                v = nc.vector

                def mask(n):
                    c, d = n // 2, n % 2
                    dve.wait_ge(exped, n + 1)
                    v.tensor_tensor(seg[:, n % 2], seg[:, n % 2], cb[:, d, c:c + 1].broadcast_to([P, 8, P]),
                                    ALU.mult).then_inc(masked, 1)

                def out(c):
                    dve.wait_ge(inter_ready, c + 1)
                    for d in range(2):
                        if c:
                            dve.wait_ge(read, 2 * c)
                        by = etok[:, c, 32 * d + 8 * g:32 * d + 8 * g + 8].unsqueeze(2).broadcast_to([P, 8, 64])
                        v.tensor_tensor(tmp[:, d].rearrange("p (h k) -> p h k", k=64),
                                        inter[:, c % 2, d].rearrange("p (h k) -> p h k", k=64), by,
                                        ALU.mult).then_inc(tmp_ready, 1)
                    dve.wait_ge(tmp_ready, 2 * c + 2)
                    v.tensor_tensor(tmp[:, 0], tmp[:, 0], tmp[:, 1], ALU.add).then_inc(read, 1)
                    dve.wait_ge(read, 2 * c + 1)
                    dve.wait_ge(y_ready, 2 * c + 2)
                    v.tensor_tensor(y_tok[:, c % 2], tmp[:, 0], intra[:, c % 2], ALU.add).then_inc(read, 1)

                for c in range(4):
                    mask(2 * c)
                    mask(2 * c + 1)
                    if c >= 2:
                        dve.wait_ge(turned_ready, c - 1)
                    out(c)

            @block.tensor
            def _(pe):
                for c in range(4):
                    if c >= 2:
                        pe.wait_ge(read, 2 * (c - 1))
                    at = slice(c * P, (c + 1) * P)
                    for d in range(2):
                        last = nc.tensor.matmul(inter[:, c % 2, d], bc_[:, 1, at], states[:, d, c], start=True,
                                                stop=True)
                    last.then_inc(inter_ready, 1)
                    for d in range(2):
                        n = 2 * c + d
                        pe.wait_ge(masked, n + 1)
                        for h in range(8):
                            last = nc.tensor.matmul(intra[:, c % 2, h * 64:(h + 1) * 64], seg[:, n % 2, h],
                                                    xdt[:, d, c, h * 64:(h + 1) * 64], start=d == 0 and h == 0,
                                                    stop=d == 1 and h == 7, skip_group_check=True)
                        last.then_inc(y_ready, 1)
                    if c:
                        turn(pe, c - 1)
                turn(pe, 3)


def stage_ssm(nc, core):
    dram = core.dram
    with ExitStack() as ctx:
        o = core.scope(nc, ctx, "ssm")
        stage_ssm_context(nc, core)
        stage_centred_conv(nc, core, dram["z"][Z3["xbc"]:Z3["xbc"] + 3072], dram["xbc"], 24, T, 64)
        dt_tok, cum_tok, etok = (o.sb(n, [P, 4, 64]) for n in ("dt_tok", "cum_tok", "etok"))
        edges, ecum = o.sb("edges", [P, 64, 4]), o.sb("ecum", [P, 64, 4])
        stage_steps(nc, core, dram["z"][Z3["dt"]:Z3["dt"] + 64], T, P, dt_tok, cum_tok, cum_dram=dram["cum"],
                    edge_dram=dram["edge"])
        stage_load(nc, core, [(edges[:], spread(dram["edge"]))])
        with nc.Block() as block:
            @block.scalar
            def _(act):
                nc.scalar.activation(etok[:], cum_tok[:], ACT.Exp)
                nc.scalar.activation(ecum[:], edges[:], ACT.Exp)
        shapes = {"x": [P, 4, T], "bc": [P, 2, T], "x_tok": [P, 4, 512], "b_tok": [P, 4, P],
                  "xdt": [P, 2, 4, 512], "xw": [P, 2, 4, 512], "states": [P, 2, 4, 512], "cb": [P, 2, 4, P],
                  "y_tok": [P, 2, 512], "y": [P, 4, T], "dts": [P, 2, 4, 8]}
        tiles = {n: o.sb(n, shape) for n, shape in shapes.items()}
        tiles["etok"] = etok
        for g in range(4):
            stage_ssm_group(nc, core, g, tiles, dt_tok, cum_tok, ecum, edges)


def stage_ssm_out(nc, core, y):
    dram = core.dram
    with ExitStack() as ctx:
        o = core.scope(nc, ctx, "ssmout")
        rstd = o.sb("rstd", [P, 4, T])
        with ExitStack() as inner:
            s = core.scope(nc, inner, "gate")
            x, z = s.sb("x", [P, 2, 4, T]), s.sb("z", [P, 2, 4, T])
            step = s.sem("step")
            loaded = [s.sem(f"loaded{i}") for i in range(2)]
            gated = s.sem("gated")
            with nc.Block() as block:
                @block.sync
                def _(sp):
                    for g in range(4):
                        if g >= 2:
                            sp.wait_ge(gated, g - 1)
                        at = slice(512 * g, 512 * (g + 1))
                        sp.dma_start(y[:, 4 * g:4 * g + 4], rows(dram["y_ssm"][at])).then_inc(loaded[g % 2], 16)
                        sp.dma_start(x[:, g % 2], rows(dram["xbc"][at])).then_inc(loaded[g % 2], 16)
                        sp.dma_start(z[:, g % 2], rows(dram["z"][Z3["z"] + 512 * g:Z3["z"] + 512 * (g + 1)])
                                     ).then_inc(loaded[g % 2], 16)

                @block.vector
                def _(dve):
                    done = Steps(dve, step)
                    for g in range(4):
                        dve.wait_ge(loaded[g % 2], 48 * (g // 2 + 1))
                        for j in range(4):
                            n = 4 * g + j
                            done.mark(nc.vector.scalar_tensor_tensor(out=y[:, n], in0=x[:, g % 2, j],
                                                                     scalar=core.v("d_skip", n), in1=y[:, n],
                                                                     op0=ALU.mult, op1=ALU.add))
                        done.wait()
                        nc.vector.tensor_tensor(y[:, 4 * g:4 * g + 4], y[:, 4 * g:4 * g + 4], z[:, g % 2],
                                                ALU.mult).then_inc(gated, 1)
        stage_rstd(nc, core, y, rstd, 4, core.ones, 512, EPS)
        step = o.sem("step")
        with nc.Block() as block:
            @block.vector
            def _(dve):
                for n in range(SSM_TILES):
                    nc.vector.scalar_tensor_tensor(out=y[:, n], in0=y[:, n], scalar=core.v("ssm_norm_w", n),
                                                   in1=rstd[:, n // 4], op0=ALU.mult,
                                                   op1=ALU.mult).then_inc(step, 1)


def third_block(nc, core):
    dram = core.dram
    z, zc, gates = dram["z"], dram["zc"], dram["gates"]
    with ExitStack() as ctx:
        s = core.scope(nc, ctx, "third")
        mod = s.sb("mod", [P, 2, 48])
        stage_ada(nc, core, dram["w_ada_3"], core.v("c_3", 0, 16).rearrange("p (k m) -> p k m", m=2),
                  core.v("b_ada_3", 0, 48), mod)
        shift1, scale1, gate1, shift2, scale2, gate2 = (mod[:, 0, 8 * n:8 * n + 8] for n in range(6))
        with ExitStack() as inner:
            s1 = core.scope(nc, inner, "mixer")
            v_tok, v_ctx = s1.sb("v_tok", [P, 4, D]), s1.sb("v_ctx", [P, 2, D])
            with ExitStack() as deep:
                s2 = core.scope(nc, deep, "ctx")
                ctx_x, ctx_h = s2.sb("x", [P, DT, CTX]), s2.sb("h", [P, DT, CTX])
                stage_load(nc, core, [(ctx_x[:], rows(dram["ctxT"]))])
                stage_norm(nc, core, ctx_x, ctx_h, "norm1_w_3", (mod[:, 1, 8:16], mod[:, 1, 0:8]), toks=CTX)
                stage_rows(nc, core, [(dram["w3_qk"][2:4], zc[0:512], ACT.Copy),
                                      (dram["w3_xbc"][0:10], zc[512:3072], ACT.Copy)],
                           tails=[(dram["w3_lr"], zc[3072:3104]), (dram["w3_dt"], zc[3104:3168])],
                           toks=CTX, rhs=ctx_h)
                stage_tokens(nc, core, dram["w3_v"], v_ctx, toks=CTX, rhs=ctx_h)
            stage_norm(nc, core, core.x, core.h, "norm1_w_3", (scale1, shift1))
            stage_rows(nc, core,
                       [(dram["w3_qk"], z[0:1024], ACT.Copy), (dram["w3_xbc"], z[4096:7168], ACT.Copy),
                        (dram["w3_r"], z[1024:2048], ACT.Silu), (dram["w3_z"], z[2048:4096], ACT.Silu),
                        (dram["w3_g"], gates[0:2048], ACT.Sigmoid)],
                       tails=[(dram["w3_lr"], z[7168:7200]), (dram["w3_dt"], z[7200:7264])])
            stage_tokens(nc, core, dram["w3_v"], v_tok)
            y = s1.sb("y", [P, 8, T])
            stage_gla(nc, core, v_tok, v_ctx, y)
            stage_project(nc, core, dram["w_pa_3"], y, 8, core.h, gates=gates[0:D], first=True)
        stage_ssm(nc, core)
        with ExitStack() as inner:
            s1 = core.scope(nc, inner, "ssmy")
            y = s1.sb("y", [P, SSM_TILES, T])
            stage_ssm_out(nc, core, y)
            stage_project(nc, core, dram["w_pb_3"], y, SSM_TILES, core.h, gates=gates[D:2 * D])
        stage_project(nc, core, dram["w_out_3"], core.h, DT, core.x, scale=gate1)
        stage_norm(nc, core, core.x, core.h, "norm2_w_3", (scale2, shift2))
        stage_ffn(nc, core, dram["ffn_up_3"], dram["ffn_down_3"], scale=gate2)
    stage_norm(nc, core, core.x, core.x, "final_norm_w_3")



def stage_end(nc, core, out):
    with ExitStack() as ctx:
        s = core.scope(nc, ctx, "end")
        stored = s.sem("stored")
        with nc.Block() as block:
            @block.sync
            def _(sp):
                sp.dma_start(rows(out), core.x[:]).then_inc(stored, 16)
                sp.wait_ge(stored, 16)


def program(nc, dram, vec_at, vec_cols, out, blocks=(1, 2, 3)):
    with ExitStack() as ctx:
        core = Core(nc, ctx, dram, vec_at, vec_cols)
        stage_start(nc, core)
        if 1 in blocks:
            first_block(nc, core)
        if 2 in blocks:
            second_block(nc, core)
        if 3 in blocks:
            third_block(nc, core)
        stage_end(nc, core, out)




def tiled(w, cols):
    k, n = w.shape
    return np.ascontiguousarray(w.reshape(k // P, P, n // cols, cols).transpose(2, 1, 0, 3))


def up_pairs(gate, up):
    return np.ascontiguousarray(np.stack([tiled(gate, P), tiled(up, P)], axis=2))


def column(a):
    return a.reshape(-1, P).T


def taps(w):
    k, n = w.shape
    return w.reshape(k, n // P, P).transpose(2, 1, 0).reshape(P, -1)


def padded(a):
    out = np.zeros((P, a.shape[1]), a.dtype)
    out[:a.shape[0]] = a
    return out


def layout(i):
    a, v = {}, {}
    a["xT"] = np.ascontiguousarray(i["x"][0].T)
    w = i["w_in"][0]
    a["w_in_a"] = tiled(w[:, :4096], WCOLS)
    a["w_in_v"] = tiled(w[:, 4096:4608], 512)
    a["w_in_g"] = tiled(w[:, 4608:], WCOLS)
    a["sc_out"] = tiled(i["sc_out"][0], P)
    a["conf_out"] = tiled(i["conf_out"][0], P)
    a["diff_out"] = tiled(i["diff_out"][0], P)
    a["w_o"] = tiled(i["w_o"][0], P)
    a["pool_w"] = np.ascontiguousarray(
        i["pool_w"][0].reshape(4, P, 2, P).transpose(0, 2, 1, 3).reshape(8, P, 1, P))
    a["ffn_up"] = up_pairs(i["ffn_up"][0][:, :D_FF], i["ffn_up"][0][:, D_FF:])
    a["ffn_down"] = tiled(i["ffn_down"][0], P)
    for n in ("mix_norm", "pool_scale", "conf_conv_b", "conf_ln_g", "conf_ln_b", "ffn_norm", "diff_subln"):
        v[n] = column(i[n][0])
    for n in ("sc_conv", "conf_conv", "ffn_conv"):
        v[n] = taps(i[n][0])
    for n in ("q_norm", "k_norm"):
        v[n] = np.concatenate([i[n][0], i[n][0]]).reshape(P, 1)
    v["lam_q"] = padded(np.stack([i["lambda_q1"][0], i["lambda_q2"][0]], axis=1))
    v["lam_k"] = padded(np.stack([i["lambda_k1"][0], i["lambda_k2"][0]], axis=1))
    a["w_ada_2"] = tiled(i["w_ada_2"][0], 512)
    w = i["w_in_2"][0]
    a["w_in_2a"] = tiled(w[:, :2048], WCOLS)
    a["w_in_2b"] = tiled(w[:, 2064:3600], WCOLS)
    a["w_in_2g"] = tiled(w[:, 3888:], WCOLS)
    for n, (lo, hi) in enumerate(((2048, 2064), (3600, 3728), (3728, 3856), (3856, 3888))):
        a[f"w_in_2t{n}"] = tiled(w[:, lo:hi], hi - lo)[0]
    for n in ("w_branch_gdn_2", "w_branch_rwkv_2", "w_out_2"):
        a[n] = tiled(i[n][0], P)
    a["ffn_up_2"] = up_pairs(i["w_ffn_in_2"][0][:, :D_FF], i["w_ffn_in_2"][0][:, D_FF:])
    a["ffn_down_2"] = tiled(i["w_ffn_out_2"][0], P)
    for n in ("w2", "a2", "g2"):
        a[n] = np.ascontiguousarray(i[n + "_2"][0])
    v["c_2"] = column(i["c_2"][0])
    for n in ("b_ada_2", "norm1_w_2", "norm2_w_2"):
        v[n] = column(i[n][0])
    v["norm_f_w_2"] = column(i["norm_f_w_2"])
    v["conv_gdn"] = taps(i["conv_gdn_2"][0])
    v["conv_ffn_2"] = taps(i["conv_ffn_2"][0])
    v["onorm_gdn"] = np.concatenate([i["onorm_gdn_2"][0]] * 2).reshape(P, 1)
    heads = np.array([2 * j + q for _ in range(NC64) for q in range(2) for j in range(4)])
    v["a_log"] = padded(i["a_log_2"][0][heads].reshape(HN, 1))
    v["dt_bias"] = padded(i["dt_bias_2"][0][heads].reshape(HN, 1))
    mu = i["mu_rwkv_2"][0]
    v["mu_rkv"] = column(mu[:1536])
    v["mu_lo"] = np.concatenate([padded(mu[lo:hi].reshape(-1, 1)) for lo, hi in
                                 ((1536, 1600), (1600, 1664), (1664, 1792), (1792, 1824))], axis=1)
    for n in ("w0", "a0", "k_k", "k_a", "lnx_w", "lnx_b"):
        v[n] = column(i[n + "_2"][0])
    v["r_k"] = column(i["r_k_2"][0].reshape(-1))
    a["ctxT"] = np.ascontiguousarray(i["ctx_3"][0].T)
    a["w_ada_3"] = tiled(i["w_ada_3"][0], 512)
    w = i["w_in_3"][0]
    for n, (lo, hi) in {"qk": (0, 1024), "r": (2048, 3072), "z": (3104, 5152), "xbc": (5152, 8224),
                        "g": (8288, 10336)}.items():
        a["w3_" + n] = tiled(w[:, lo:hi], WCOLS)
    a["w3_v"] = tiled(w[:, 1024:2048], 512)
    a["w3_lr"] = tiled(w[:, 3072:3104], 32)[0]
    a["w3_dt"] = tiled(w[:, 8224:8288], 64)[0]
    for n in ("gla_up_f", "gla_up_b"):
        a[n] = np.ascontiguousarray(i[n + "_3"][0])
    for n in ("w_pa_3", "w_pb_3", "w_out_3"):
        a[n] = tiled(i[n][0], P)
    a["ffn_up_3"] = up_pairs(i["w_gate_3"][0], i["w_up_3"][0])
    a["ffn_down_3"] = tiled(i["w_down_3"][0], P)
    v["c_3"] = np.stack([column(i["c_3"][0]), column(i["c_ctx_3"])], axis=2).reshape(P, 16)
    for n in ("b_ada_3", "norm1_w_3", "norm2_w_3", "conv_b_3"):
        v[n] = column(i[n][0])
    v["final_norm_w_3"] = column(i["final_norm_w_3"])
    v["conv_w_3"] = taps(i["conv_w_3"][0])
    for n in ("gla_bias_f", "gla_bias_b", "gla_norm_w", "ssm_norm_w"):
        v[n] = column(i[n + "_3"][0])
    v["d_skip"] = column(np.repeat(i["d_skip_3"][0], 64))
    for n in ("dt_bias", "a_log"):
        v[n + "_3"] = padded(np.concatenate([i[n + "_f_3"][0], i[n + "_b_3"][0]]).reshape(64, 1))
    left = [np.array([[s // (2 << n) == t // (2 << n) and s // (1 << n) % 2 == 0 and t // (1 << n) % 2 == 1
                       for t in range(P)] for s in range(P)]) for n in range(GLA_LEVELS)]
    masks = [np.eye(P, dtype=bool)] + left + [m.T for m in left]
    a["masks"] = np.ascontiguousarray(np.stack(masks, axis=1).astype(np.int32))
    at, n = {}, 0
    for name, cols in v.items():
        at[name] = n
        n += cols.shape[1]
    a["vecs"] = np.ascontiguousarray(np.concatenate(list(v.values()), axis=1))
    return a, at


SCRATCH = {
    "z": (8192, T), "gates": (GATE_ROWS, T), "feat": (512 * len(F2), T), "hn": (3, HN, C64),
    "decay": (HN, C64, C64), "gram": (2 * HN, C64, C64), "inverse": (2 * HN, C64, C64),
    "zc": (3168, CTX), "xc": (2560, CTX), "xbc": (3072, T), "y_ssm": (2048, T), "cum": (64, T), "edge": (64, 4),
    "edge_c": (64, 1), "s0": (2, 4, P, 512),
}


def build(nc, arrays, at, blocks=(1, 2, 3)):
    dram = {n: nc.dram_tensor(f"in_{n}", a.shape, I32 if a.dtype == np.int32 else F32,
                              kind="ExternalInput").ap() for n, a in arrays.items()}
    for n, shape in SCRATCH.items():
        dram[n] = nc.dram_tensor(f"scratch_{n}", shape, F32).ap()
    out = nc.dram_tensor("out_T", (D, T), F32, kind="ExternalOutput").ap()
    program(nc, dram, at, arrays["vecs"].shape[1], out, blocks)


def kernel(**inputs):
    import concourse.bacc as _bacc
    from concourse.bass_utils import run_bass_kernel_spmd as _run

    arrays, at = layout({n: np.asarray(a) for n, a in inputs.items()})
    nc = _bacc.Bacc("TRN2", target_bir_lowering=False, num_devices=1)
    build(nc, arrays, at)
    r = _run(nc, [{f"in_{n}": a for n, a in arrays.items()}], core_ids=[0])
    return np.ascontiguousarray(r.results[0]["out_T"].T).reshape(1, T, D)
```

```python
import math
from contextlib import ExitStack

import numpy as np

import concourse.bass as bass
from concourse import mybir

F32 = mybir.dt.float32
F32R = mybir.dt.float32r
I32 = mybir.dt.int32
ALU = mybir.AluOpType
ACT = mybir.ActivationFunctionType
AX_X = mybir.AxisListType.X

P = 128
T = 512
D = 1024
DT = D // P
WCOLS = 256
EPS = 1e-6
D_FF = 2816
FT = D_FF // P
CTX = 256
C64 = 64
HN = 64
NC64 = T // C64
GATE_ROWS = 4096
LAM_INIT = 0.8 - 0.6 * math.exp(0.0)


class Steps:

    def __init__(self, eng, sem):
        self.eng, self.sem, self.n = eng, sem, 0

    def mark(self, ins):
        ins.then_inc(self.sem, 1)
        self.n += 1

    def wait(self):
        self.eng.wait_ge(self.sem, self.n)

    def __call__(self, ins):
        self.mark(ins)
        self.wait()


class Scope:

    def __init__(self, nc, ctx, name):
        self.nc, self.ctx, self.name = nc, ctx, name
        self.sems = []
        ctx.callback(self.close)

    def close(self):
        for sem in self.sems:
            self.nc.gpsimd.sem_clear(sem)
            self.nc.release_semaphore(sem)

    def sb(self, name, shape, dt=F32):
        return self.ctx.enter_context(self.nc.sbuf_tensor(f"{self.name}_{name}", shape, dt))

    def ps(self, name, shape):
        return self.ctx.enter_context(self.nc.psum_tensor(f"{self.name}_{name}", shape, F32))

    def sem(self, name):
        self.sems.append(self.nc.alloc_semaphore(f"{self.name}_{name}"))
        return self.sems[-1]


class Core:

    def __init__(self, nc, ctx, dram, vec_at, vec_cols):
        def sb(name, shape, dt=F32):
            return ctx.enter_context(nc.sbuf_tensor(name, shape, dt))

        self.dram, self.vec_at, self.count = dram, vec_at, 0
        self.vec = sb("vec", [P, vec_cols])
        self.ident = sb("ident", [P, P])
        self.ones = sb("ones", [P, P])
        self.halves = sb("halves", [P, P])
        self.x = sb("x_res", [P, DT, T])
        self.mod = sb("mod", [P, 3, 48])

    def v(self, name, k=0, n=1):
        at = self.vec_at[name] + k
        return self.vec[:, at:at + n]

    def scope(self, nc, ctx, name):
        self.count += 1
        return Scope(nc, ctx, f"{name}{self.count}")


def rows(ap):
    return ap.rearrange("(j p) t -> p j t", p=P)




def stage_start(nc, core):
    with ExitStack() as ctx:
        s = core.scope(nc, ctx, "start")
        loaded, made = s.sem("loaded"), s.sem("made")
        with nc.Block() as block:
            @block.sync
            def _(sp):
                sp.dma_start(core.vec[:], core.dram["vecs"]).then_inc(loaded, 16)
                sp.dma_start(core.x[:], rows(core.dram["xT"])).then_inc(loaded, 16)
                sp.wait_ge(loaded, 32)

            @block.gpsimd
            def _(pool):
                done = Steps(pool, made)
                done(nc.gpsimd.memset(core.ones[:], 1.0))
                done(nc.gpsimd.memset(core.halves[:], 0.0))
                done(nc.gpsimd.memset(core.halves[0:64, 0:64], 1.0))
                done(nc.gpsimd.memset(core.halves[64:128, 64:128], 1.0))
                done(nc.gpsimd.memset(core.ident[:], 0.0))
                done(nc.gpsimd.affine_select(out=core.ident[:], in_=core.ident[:], pattern=[[-1, P]],
                                             compare_op=ALU.not_equal, fill=1.0, base=0, channel_multiplier=1))


def stage_rstd(nc, core, src, dst, per, ones, count, eps, toks=T):
    n = src.shape[1]
    with ExitStack() as ctx:
        s = core.scope(nc, ctx, "rstd")
        sq = s.sb("sq", [P, n, toks])
        acc = s.ps("acc", [P, 4, 512])
        squared, summed, freed, inverted, step = (s.sem(x) for x in
                                                  ("squared", "summed", "freed", "inverted", "step"))
        with nc.Block() as block:
            @block.scalar
            def _(act):
                for k in range(n):
                    nc.scalar.activation(sq[:, k], src[:, k], ACT.Square).then_inc(squared, 1)
                for g in range(n // per):
                    act.wait_ge(inverted, g + 1)
                    nc.scalar.activation(dst[:, g], dst[:, g], ACT.Sqrt).then_inc(step, 1)

            @block.tensor
            def _(pe):
                for g in range(n // per):
                    if g >= 4:
                        pe.wait_ge(freed, g - 3)
                    for k in range(per):
                        pe.wait_ge(squared, g * per + k + 1)
                        last = nc.tensor.matmul(acc[:, g % 4, :toks], ones[:], sq[:, g * per + k],
                                                start=k == 0, stop=k == per - 1)
                    last.then_inc(summed, 1)

            @block.vector
            def _(dve):
                for g in range(n // per):
                    dve.wait_ge(summed, g + 1)
                    nc.vector.tensor_scalar(dst[:, g], acc[:, g % 4, :toks], 1.0 / count, eps,
                                            ALU.mult, ALU.add).then_inc(freed, 1)
                    dve.wait_ge(freed, g + 1)
                    nc.vector.reciprocal(dst[:, g], dst[:, g]).then_inc(inverted, 1)


def stage_centre(nc, core, src, per, ones, count):
    n = src.shape[1]
    with ExitStack() as ctx:
        s = core.scope(nc, ctx, "centre")
        mean = s.sb("mean", [P, 4, T])
        acc = s.ps("acc", [P, 4, 512])
        summed, freed, done = s.sem("summed"), s.sem("freed"), s.sem("done")
        with nc.Block() as block:
            @block.tensor
            def _(pe):
                for g in range(n // per):
                    if g >= 4:
                        pe.wait_ge(freed, g - 3)
                    for k in range(per):
                        last = nc.tensor.matmul(acc[:, g % 4, :], ones[:], src[:, g * per + k],
                                                start=k == 0, stop=k == per - 1)
                    last.then_inc(summed, 1)

            @block.vector
            def _(dve):
                for g in range(n // per):
                    dve.wait_ge(summed, g + 1)
                    nc.vector.tensor_scalar(mean[:, g % 4], acc[:, g % 4, :], 1.0 / count, None,
                                            ALU.mult).then_inc(freed, 1)
                    dve.wait_ge(freed, g + 1)
                    for k in range(per):
                        nc.vector.tensor_tensor(src[:, g * per + k], src[:, g * per + k], mean[:, g % 4],
                                                ALU.subtract).then_inc(done, 1)


def split_tiles(s, name, shape):
    return s.sb(f"{name}_hi", shape, F32R), s.sb(f"{name}_lo", shape, F32R)


def split_hi(nc, hi, src):
    return nc.scalar.activation(hi, src, ACT.Copy)


def split_lo(eng, lo, src, hi):
    return eng.tensor_tensor(lo, src, hi.bitcast(F32), ALU.subtract)


def product(nc, out, w, x, start, stop):
    (w_hi, w_lo), (x_hi, x_lo) = w, x
    nc.tensor.matmul(out, w_hi, x_hi, start=start, stop=False)
    nc.tensor.matmul(out, w_hi, x_lo, start=False, stop=False)
    return nc.tensor.matmul(out, w_lo, x_hi, start=False, stop=stop)


def span(eng, n, body):
    if n == 1:
        body(0)
    elif n > 1:
        with eng.Fori(0, n) as i:
            body(i)


def stage_norm(nc, core, src, gain, mod=None, toks=T, dst=None, parts=None):
    with ExitStack() as ctx:
        s = core.scope(nc, ctx, "norm")
        rstd = s.sb("rstd", [P, 1, toks])
        stage_rstd(nc, core, src, rstd, DT, core.ones, D, EPS, toks)
        full = s.sb("full", [P, DT])
        buf = s.sb("buf", [P, DT, toks]) if dst is None else dst
        ready, scaled, shifted, cut = (s.sem(n) for n in ("ready", "scaled", "shifted", "cut"))
        with nc.Block() as block:
            @block.vector
            def _(dve):
                g = core.v(gain, 0, DT)
                if mod is not None:
                    nc.vector.scalar_tensor_tensor(out=full[:], in0=mod[0], scalar=1.0, in1=g,
                                                   op0=ALU.add, op1=ALU.mult).then_inc(ready, 1)
                    dve.wait_ge(ready, 1)
                    g = full[:]
                for k in range(DT):
                    nc.vector.scalar_tensor_tensor(out=buf[:, k], in0=src[:, k], scalar=g[:, k:k + 1],
                                                   in1=rstd[:, 0], op0=ALU.mult,
                                                   op1=ALU.mult).then_inc(scaled, 1)
                if parts is not None:
                    for k in range(DT):
                        dve.wait_ge(cut, k + 1)
                        split_lo(nc.vector, parts[1][:, k], buf[:, k], parts[0][:, k]).then_inc(ready, 1)

            @block.scalar
            def _(act):
                for k in range(DT):
                    act.wait_ge(scaled, k + 1)
                    if mod is not None:
                        nc.scalar.activation(buf[:, k], buf[:, k], ACT.Identity,
                                             bias=mod[1][:, k:k + 1]).then_inc(shifted, 1)
                        act.wait_ge(shifted, k + 1)
                    if parts is not None:
                        split_hi(nc, parts[0][:, k], buf[:, k]).then_inc(cut, 1)


def stage_rows(nc, core, segments, rhs, tails=(), toks=T, beside=None):
    with ExitStack() as ctx:
        s = core.scope(nc, ctx, "rows")
        raw = s.sb("raw", [P, 2, DT, WCOLS])
        w_hi, w_lo = split_tiles(s, "w", [P, 2, DT, WCOLS])
        out = s.sb("out", [P, 2, 2, toks])
        acc = s.ps("acc", [P, 4, 512])
        loaded, cut_hi, cut_lo, made, copied, stored = (
            [s.sem(f"{n}{k}") for k in range(2)] for n in
            ("loaded", "cut_hi", "cut_lo", "made", "copied", "stored"))
        turns = [seg[0].shape[0] // 2 for seg in segments]
        base = [sum(turns[:n]) for n in range(len(turns))]
        total = sum(turns)
        if beside is not None:
            beside.open(s)

        def leading(act, k, i):
            act.wait_ge(loaded[k], i * 16 + 16)
            act.wait_ge(made[k], i * 2)
            split_hi(nc, w_hi[:, k], raw[:, k]).then_inc(cut_hi[k], 1)

        with nc.Block() as block:
            @block.sync
            def _(sp):
                for n, (wt, _, _) in enumerate(segments):
                    def turn(i):
                        for k in range(2):
                            if beside is not None:
                                beside.sync_turn(sp, n, i, k)
                            sp.wait_ge(cut_hi[k], i + base[n])
                            sp.wait_ge(cut_lo[k], i + base[n])
                            sp.dma_start(raw[:, k], wt[bass.ds(i * 2 + k, 1)].rearrange(
                                "a p k n -> p (a k) n")).then_inc(loaded[k], 16)
                    span(sp, turns[n], turn)

            @block.gpsimd
            def _(pool):
                def turn(i):
                    for k in range(2):
                        pool.wait_ge(cut_hi[k], i + 1)
                        split_lo(nc.gpsimd, w_lo[:, k], raw[:, k], w_hi[:, k]).then_inc(cut_lo[k], 1)
                span(pool, total, turn)

            @block.tensor
            def _(pe):
                for n in range(len(segments)):
                    def turn(i):
                        for k in range(2):
                            pe.wait_ge(cut_hi[k], i + base[n] + 1)
                            pe.wait_ge(cut_lo[k], i + base[n] + 1)
                            pe.wait_ge(copied[k], (i + base[n]) * 2)
                            for j in range(2):
                                at = slice(j * P, (j + 1) * P)
                                for c in range(DT):
                                    last = product(nc, acc[:, 2 * k + j, :toks],
                                                   (w_hi[:, k, c, at], w_lo[:, k, c, at]),
                                                   (rhs[0][:, c], rhs[1][:, c]), c == 0, c == DT - 1)
                                last.then_inc(made[k], 1)
                            if beside is not None:
                                beside.tensor_turn(pe, n, i, k)
                    span(pe, turns[n], turn)

            @block.scalar
            def _(act):
                leading(act, 0, 0)
                for n, (_, dst, func) in enumerate(segments):
                    def turn(i, last=False):
                        for k in range(2):
                            if not (last and k == 1):
                                leading(act, 1 - k, i + base[n] + k)
                            act.wait_ge(stored[k], (i + base[n]) * 16)
                            for j in range(2):
                                act.wait_ge(made[k], (i + base[n]) * 2 + j + 1)
                                nc.scalar.activation(out[:, k, j], acc[:, 2 * k + j, :toks],
                                                     func).then_inc(copied[k], 1)
                            act.wait_ge(copied[k], (i + base[n]) * 2 + 2)
                            act.dma_start(rows(dst[bass.ds(i * 2 * WCOLS + k * WCOLS, WCOLS), :]),
                                          out[:, k]).then_inc(stored[k], 16)
                    if n < len(segments) - 1:
                        span(act, turns[n], turn)
                    else:
                        span(act, turns[n] - 1, turn)
                        turn(turns[n] - 1, last=True)
                for k in range(2):
                    act.wait_ge(stored[k], 16 * total)

            if beside is not None:
                @block.vector
                def _(dve):
                    for n in range(len(segments)):
                        beside.vector_segment(dve, n, turns[n])
        if beside is not None:
            beside.close()
    if tails:
        tail_rows(nc, core, tails, rhs, toks)


def tail_rows(nc, core, tails, rhs, toks):
    with ExitStack() as ctx:
        s = core.scope(nc, ctx, "tails")
        n = len(tails)
        raw = s.sb("raw", [P, n, DT, P])
        w_hi, w_lo = split_tiles(s, "w", [P, n, DT, P])
        out = s.sb("out", [P, n, toks])
        acc = s.ps("acc", [P, n, 512])
        loaded, cut_hi, cut_lo, made, copied, stored = (
            s.sem(x) for x in ("loaded", "cut_hi", "cut_lo", "made", "copied", "stored"))
        wide = [wt.shape[2] for wt, _ in tails]
        with nc.Block() as block:
            @block.sync
            def _(sp):
                for m, (wt, _) in enumerate(tails):
                    sp.dma_start(raw[:, m, :, :wide[m]], wt).then_inc(loaded, 16)
                for m, (_, dst) in enumerate(tails):
                    sp.wait_ge(copied, m + 1)
                    sp.dma_start(dst, out[:wide[m], m]).then_inc(stored, 16)
                sp.wait_ge(stored, 16 * n)

            @block.scalar
            def _(act):
                act.wait_ge(loaded, 16 * n)
                for m in range(n):
                    split_hi(nc, w_hi[:, m, :, :wide[m]], raw[:, m, :, :wide[m]]).then_inc(cut_hi, 1)
                for m in range(n):
                    act.wait_ge(made, m + 1)
                    nc.scalar.activation(out[:wide[m], m], acc[:wide[m], m, :toks], ACT.Copy).then_inc(copied, 1)

            @block.vector
            def _(dve):
                for m in range(n):
                    dve.wait_ge(cut_hi, m + 1)
                    split_lo(nc.vector, w_lo[:, m, :, :wide[m]], raw[:, m, :, :wide[m]],
                             w_hi[:, m, :, :wide[m]]).then_inc(cut_lo, 1)

            @block.tensor
            def _(pe):
                for m in range(n):
                    pe.wait_ge(cut_hi, m + 1)
                    pe.wait_ge(cut_lo, m + 1)
                    for c in range(DT):
                        last = product(nc, acc[:wide[m], m, :toks],
                                       (w_hi[:, m, c, :wide[m]], w_lo[:, m, c, :wide[m]]),
                                       (rhs[0][:, c], rhs[1][:, c]), c == 0, c == DT - 1)
                    last.then_inc(made, 1)


def stage_tokens(nc, core, wt, rhs, dst, toks=T):
    chunks, per = wt.shape[0], toks // P
    with ExitStack() as ctx:
        s = core.scope(nc, ctx, "tokens")
        raw = s.sb("raw", [P, 2, DT, WCOLS])
        w_hi, w_lo = split_tiles(s, "w", [P, 2, DT, WCOLS])
        acc = s.ps("acc", [P, 4, 512])
        cut_hi, cut_lo, made, copied = (s.sem(x) for x in ("cut_hi", "cut_lo", "made", "copied"))
        loaded = [s.sem(f"loaded{n}") for n in range(2)]
        with nc.Block() as block:
            @block.sync
            def _(sp):
                for c in range(chunks):
                    if c >= 2:
                        sp.wait_ge(cut_lo, c - 1)
                    sp.dma_start(raw[:, c % 2], wt[c]).then_inc(loaded[c % 2], 16)

            @block.scalar
            def _(act):
                for c in range(chunks):
                    act.wait_ge(loaded[c % 2], 16 * (c // 2 + 1))
                    if c >= 2:
                        act.wait_ge(made, per * (c - 1))
                    split_hi(nc, w_hi[:, c % 2], raw[:, c % 2]).then_inc(cut_hi, 1)

            @block.gpsimd
            def _(pool):
                for c in range(chunks):
                    pool.wait_ge(cut_hi, c + 1)
                    split_lo(nc.gpsimd, w_lo[:, c % 2], raw[:, c % 2], w_hi[:, c % 2]).then_inc(cut_lo, 1)

            @block.tensor
            def _(pe):
                for n in range(chunks * per):
                    c, t = n // per, n % per
                    pe.wait_ge(cut_lo, c + 1)
                    if n >= 4:
                        pe.wait_ge(copied, n - 3)
                    at = slice(t * P, (t + 1) * P)
                    for k in range(DT):
                        last = product(nc, acc[:, n % 4, :WCOLS], (rhs[0][:, k, at], rhs[1][:, k, at]),
                                       (w_hi[:, c % 2, k], w_lo[:, c % 2, k]), k == 0, k == DT - 1)
                    last.then_inc(made, 1)

            @block.vector
            def _(dve):
                for n in range(chunks * per):
                    c, t = n // per, n % per
                    dve.wait_ge(made, n + 1)
                    nc.vector.tensor_copy(dst[:, t, c * WCOLS:(c + 1) * WCOLS], acc[:, n % 4, :WCOLS]
                                          ).then_inc(copied, 1)


def stage_project(nc, core, wt, kt, dst, y=None, parts=None, gates=None, first=False, scale=None,
                  groups=False):
    with ExitStack() as ctx:
        s = core.scope(nc, ctx, "project")
        n_in = 4 if groups else kt
        raw = s.sb("raw", [P, 2, kt, P])
        w_hi, w_lo = split_tiles(s, "w", [P, 2, kt, P])
        y_hi, y_lo = parts if y is None else split_tiles(s, "y", [P, n_in, T])
        gate = s.sb("gate", [P, 2, T]) if gates is not None else None
        part = s.sb("part", [P, 2, T]) if gates is not None else None
        acc = s.ps("acc", [P, 2, 512])
        y_hi_ready, y_lo_ready, cut_hi, cut_lo, made, freed, step = (
            s.sem(x) for x in ("y_hi_ready", "y_lo_ready", "cut_hi", "cut_lo", "made", "freed", "step"))
        loaded = [s.sem(f"loaded{n}") for n in range(2)]
        gate_loaded = [s.sem(f"gate_loaded{n}") for n in range(2)]
        with nc.Block() as block:
            @block.sync
            def _(sp):
                for m in range(DT):
                    if m >= 2:
                        sp.wait_ge(cut_lo, m - 1)
                    sp.dma_start(raw[:, m % 2], wt[m]).then_inc(loaded[m % 2], 16)
                    if gates is not None:
                        if m >= 2:
                            sp.wait_ge(freed, m - 1)
                        sp.dma_start(gate[:, m % 2], gates[m * P:(m + 1) * P]).then_inc(gate_loaded[m % 2], 16)

            @block.scalar
            def _(act):
                if y is not None:
                    for k in range(n_in):
                        split_hi(nc, y_hi[:, k], y[:, k]).then_inc(y_hi_ready, 1)
                for m in range(DT):
                    act.wait_ge(loaded[m % 2], 16 * (m // 2 + 1))
                    if m >= 2:
                        act.wait_ge(made, m - 1)
                    split_hi(nc, w_hi[:, m % 2], raw[:, m % 2]).then_inc(cut_hi, 1)

            @block.gpsimd
            def _(pool):
                for m in range(DT):
                    pool.wait_ge(cut_hi, m + 1)
                    split_lo(nc.gpsimd, w_lo[:, m % 2], raw[:, m % 2], w_hi[:, m % 2]).then_inc(cut_lo, 1)

            @block.tensor
            def _(pe):
                for m in range(DT):
                    pe.wait_ge(cut_lo, m + 1)
                    if m >= 2:
                        pe.wait_ge(freed, m - 1)
                    for k in range(kt):
                        x = m // 2 if groups else k
                        if y is not None and (m == 0 or groups):
                            pe.wait_ge(y_lo_ready, x + 1)
                        last = product(nc, acc[:, m % 2], (w_hi[:, m % 2, k], w_lo[:, m % 2, k]),
                                       (y_hi[:, x], y_lo[:, x]), k == 0, k == kt - 1)
                    last.then_inc(made, 1)

            @block.vector
            def _(dve):
                if y is not None:
                    for k in range(n_in):
                        dve.wait_ge(y_hi_ready, k + 1)
                        split_lo(nc.vector, y_lo[:, k], y[:, k], y_hi[:, k]).then_inc(y_lo_ready, 1)
                for m in range(DT):
                    by = 1.0 if scale is None else scale[:, m:m + 1]
                    dve.wait_ge(made, m + 1)
                    if gates is None:
                        nc.vector.scalar_tensor_tensor(out=dst[:, m], in0=acc[:, m % 2], scalar=by, in1=dst[:, m],
                                                       op0=ALU.mult, op1=ALU.add).then_inc(freed, 1)
                        continue
                    dve.wait_ge(gate_loaded[m % 2], 16 * (m // 2 + 1))
                    if not first and m >= 2:
                        dve.wait_ge(step, m - 1)
                    to = dst[:, m] if first else part[:, m % 2]
                    nc.vector.scalar_tensor_tensor(out=to, in0=acc[:, m % 2], scalar=by, in1=gate[:, m % 2],
                                                   op0=ALU.mult, op1=ALU.mult).then_inc(freed, 1)
                    if not first:
                        dve.wait_ge(freed, m + 1)
                        nc.vector.tensor_tensor(dst[:, m], dst[:, m], part[:, m % 2], ALU.add).then_inc(step, 1)


def stage_ffn(nc, core, gain, up, down, mod=None, conv=None, conv_up=False, scale=None):
    with ExitStack() as ctx:
        s0 = core.scope(nc, ctx, "ffn")
        mid_hi, mid_lo = split_tiles(s0, "mid", [P, FT, T])
        with ExitStack() as inner:
            s = core.scope(nc, inner, "up")
            h = split_tiles(s, "h", [P, DT, T])
            stage_norm(nc, core, core.x, gain, mod, parts=h)
            raw = s.sb("raw", [P, 2, DT, P])
            w_hi, w_lo = split_tiles(s, "w", [P, 2, 2, DT, P])
            gate = s.sb("gate", [P, 2, T])
            lift = s.sb("lift", [P, 2, T]) if conv_up else None
            acc = s.ps("acc", [P, 4, 512])
            loaded, cut_hi, cut_lo = ([s.sem(f"{n}{g}") for g in range(2)] for n in
                                      ("loaded", "cut_hi", "cut_lo"))
            made, tapped, convolved, gated, mixed, cut_mid, done_mid = (
                [s.sem(f"{n}{k}") for k in range(2)] for n in
                ("made", "tapped", "convolved", "gated", "mixed", "cut_mid", "done_mid"))
            sides = 2 if conv_up else 1
            turns = FT // 2

            def leading(act, i, k):
                for g in range(2):
                    act.wait_ge(loaded[g], i * 32 + 16 * (k + 1))
                    if g == 0:
                        act.wait_ge(made[k], i * 2)
                    split_hi(nc, w_hi[:, k, g], raw[:, g]).then_inc(cut_hi[g], 1)

            with nc.Block() as block:
                @block.sync
                def _(sp):
                    def turn(i):
                        for k in range(2):
                            for g in range(2):
                                sp.wait_ge(cut_lo[g], i * 2 + k)
                                sp.dma_start(raw[:, g], up[bass.ds(i * 2 + k, 1), :, g].rearrange(
                                    "a p k n -> p (a k) n")).then_inc(loaded[g], 16)
                    span(sp, turns, turn)

                @block.gpsimd
                def _(pool):
                    def turn(i):
                        for k in range(2):
                            for g in range(2):
                                pool.wait_ge(cut_hi[g], i * 2 + k + 1)
                                split_lo(nc.gpsimd, w_lo[:, k, g], raw[:, g], w_hi[:, k, g]
                                         ).then_inc(cut_lo[g], 1)
                    span(pool, turns, turn)

                @block.tensor
                def _(pe):
                    def turn(i):
                        for k in range(2):
                            for g in range(2):
                                pe.wait_ge(cut_lo[g], i * 2 + k + 1)
                                if g == 0:
                                    pe.wait_ge(mixed[k], i)
                                for c in range(DT):
                                    last = product(nc, acc[:, 2 * k + g], (w_hi[:, k, g, c], w_lo[:, k, g, c]),
                                                   (h[0][:, c], h[1][:, c]), c == 0, c == DT - 1)
                                last.then_inc(made[k], 1)
                    span(pe, turns, turn)

                @block.scalar
                def _(act):
                    leading(act, 0, 0)

                    def turn(i, last=False):
                        for k in range(2):
                            if not (last and k == 1):
                                leading(act, i + k, 1 - k)
                            act.wait_ge(done_mid[k], i)
                            if conv is None:
                                act.wait_ge(made[k], i * 2 + 1)
                                nc.scalar.activation(gate[:, k], acc[:, 2 * k], ACT.Silu).then_inc(gated[k], 1)
                            else:
                                for g in range(sides):
                                    act.wait_ge(made[k], i * 2 + g + 1)
                                    tap = conv[:, bass.ds(i * 6 + (3 * k + 2 + g * 3 * FT), 1)]
                                    nc.scalar.activation((gate, lift)[g][:, k], acc[:, 2 * k + g], ACT.Copy,
                                                         scale=tap).then_inc(tapped[k], 1)
                                act.wait_ge(convolved[k], i * (2 * sides) + 2)
                                nc.scalar.activation(gate[:, k], gate[:, k], ACT.Silu).then_inc(gated[k], 1)
                            act.wait_ge(mixed[k], i + 1)
                            nc.scalar.activation(mid_hi[:, bass.ds(i * 2 + k, 1), :], gate[:, k:k + 1],
                                                 ACT.Copy).then_inc(cut_mid[k], 1)
                    span(act, turns - 1, turn)
                    turn(turns - 1, last=True)

                @block.vector
                def _(dve):
                    def turn(i):
                        for k in range(2):
                            if conv is not None:
                                for g in range(sides):
                                    dve.wait_ge(tapped[k], i * sides + g + 1)
                                    buf = (gate, lift)[g]
                                    for lag in (1, 2):
                                        tap = conv[:, bass.ds(i * 6 + (3 * k + 2 - lag + g * 3 * FT), 1)]
                                        nc.vector.scalar_tensor_tensor(
                                            out=buf[:, k, lag:], in0=acc[:, 2 * k + g, :T - lag], scalar=tap,
                                            in1=buf[:, k, lag:], op0=ALU.mult, op1=ALU.add
                                        ).then_inc(convolved[k], 1)
                                        dve.wait_ge(convolved[k], i * (2 * sides) + (2 * g + lag))
                            dve.wait_ge(made[k], i * 2 + 2)
                            dve.wait_ge(gated[k], i + 1)
                            second = lift[:, k] if conv_up else acc[:, 2 * k + 1]
                            nc.vector.tensor_tensor(gate[:, k], gate[:, k], second, ALU.mult).then_inc(mixed[k], 1)
                            dve.wait_ge(cut_mid[k], i + 1)
                            nc.vector.tensor_tensor(
                                mid_lo[:, bass.ds(i * 2 + k, 1), :], gate[:, k:k + 1],
                                mid_hi[:, bass.ds(i * 2 + k, 1), :].bitcast(F32), ALU.subtract
                            ).then_inc(done_mid[k], 1)
                    span(dve, turns, turn)
        stage_project(nc, core, down, FT, core.x, parts=(mid_hi, mid_lo), scale=scale)


class Ada:

    COLS = 6 * D // 16
    TURNS = 8
    SETS = ((0,), (1, 2))

    def __init__(self, nc, core):
        self.nc, self.core = nc, core

    def open(self, s):
        nc, core = self.nc, self.core
        self.w = s.sb("ada_w", [P, 2, DT, self.COLS])
        self.sum = s.sb("ada_sum", [P, 2, 2, self.COLS])
        self.cond = s.sb("ada_cond", [P, DT, 3])
        self.acc = s.ps("ada_acc", [P, 3 * 48])
        self.loaded, self.summed, self.read = (
            [s.sem(f"ada_{n}{k}") for k in range(2)] for n in ("loaded", "summed", "read"))
        bent, self.added = s.sem("ada_bent"), s.sem("ada_added")
        with nc.Block() as block:
            @block.scalar
            def _(act):
                nc.scalar.activation(self.cond[:, :, 0:1], core.v("c_2", 0, DT).unsqueeze(2),
                                     ACT.Silu).then_inc(bent, 1)
                nc.scalar.activation(self.cond[:, :, 1:3],
                                     core.v("c_3", 0, 16).rearrange("p (k m) -> p k m", m=2),
                                     ACT.Silu).then_inc(bent, 1)

    def steps(self, n):
        per = [DT * len(sets) for sets in self.SETS]
        return self.TURNS * sum(per[:n]), per[n]

    def sync_turn(self, sp, n, i, k):
        before, per = self.steps(n)
        sp.wait_ge(self.summed[k], i * per + before)
        sp.dma_start(self.w[:, k], self.core.dram[("w_ada_2", "w_ada_3")[n]][bass.ds(i * 2 + k, 1)].rearrange(
            "a p k n -> p (a k) n")).then_inc(self.loaded[k], 16)

    def vector_segment(self, dve, n, turns):
        v = self.nc.vector
        before, per = self.steps(n)
        many = len(self.SETS[n])

        def turn(i):
            for k in range(2):
                dve.wait_ge(self.loaded[k], (i + self.TURNS * n) * 16 + 16)
                dve.wait_ge(self.read[k], i + self.TURNS * n)
                for c in range(DT):
                    for m, which in enumerate(self.SETS[n]):
                        at = self.sum[:, k, m]
                        by = self.cond[:, c, which:which + 1]
                        if c == 0:
                            v.tensor_scalar(at, self.w[:, k, c], by, None, ALU.mult).then_inc(self.summed[k], 1)
                        else:
                            dve.wait_ge(self.summed[k], i * per + (before + (c - 1) * many + m + 1))
                            v.scalar_tensor_tensor(out=at, in0=self.w[:, k, c], scalar=by, in1=at, op0=ALU.mult,
                                                   op1=ALU.add).then_inc(self.summed[k], 1)
        span(dve, turns, turn)

    def tensor_turn(self, pe, n, i, k):
        before, per = self.steps(n)
        pe.wait_ge(self.summed[k], i * per + (before + per))
        for m, which in enumerate(self.SETS[n]):
            for j in range(self.COLS // P):
                col = i * 6 + (3 * k + j + 48 * which)
                last = self.nc.tensor.matmul(self.acc[:, bass.ds(col, 1)], self.sum[:, k, m, j * P:(j + 1) * P],
                                             self.core.ones[:, 0:1], start=True, stop=True)
        last.then_inc(self.read[k], 1)

    def close(self):
        nc, core = self.nc, self.core
        with nc.Block() as block:
            @block.vector
            def _(dve):
                for which, bias in enumerate(("b_ada_2", "b_ada_3", "b_ada_3")):
                    nc.vector.tensor_tensor(core.mod[:, which], self.acc[:, 48 * which:48 * which + 48],
                                            core.v(bias, 0, 48), ALU.add).then_inc(self.added, 1)



Z1 = {"b": 0, "c": 512, "x": 1024, "pool": 1536, "conf": 2048, "q": 3072, "k": 3584}


def stage_short_conv(nc, core, z, y):
    with ExitStack() as ctx:
        s = core.scope(nc, ctx, "short")
        part = {n: s.sb(n, [P, 4, T]) for n in "bcx"}
        loaded, step = s.sem("loaded"), s.sem("step")
        with nc.Block() as block:
            @block.sync
            def _(sp):
                for n in "cxb":
                    sp.dma_start(part[n][:], rows(z[Z1[n]:Z1[n] + 512])).then_inc(loaded, 16)

            @block.vector
            def _(dve):
                done = Steps(dve, step)
                prod = part["c"]
                dve.wait_ge(loaded, 48)
                done(nc.vector.tensor_tensor(prod[:], prod[:], part["x"][:], ALU.mult))
                for j in range(4):
                    done.mark(nc.vector.tensor_scalar(y[:, j], prod[:, j], core.v("sc_conv", 3 * j + 2), None,
                                                      ALU.mult))
                done.wait()
                for lag in (1, 2):
                    for j in range(4):
                        done.mark(nc.vector.scalar_tensor_tensor(
                            out=y[:, j, lag:], in0=prod[:, j, :T - lag], scalar=core.v("sc_conv", 3 * j + 2 - lag),
                            in1=y[:, j, lag:], op0=ALU.mult, op1=ALU.add))
                    done.wait()
                done(nc.vector.tensor_tensor(y[:], y[:], part["b"][:], ALU.mult))


def stage_pool(nc, core, z, y):
    with ExitStack() as ctx:
        s = core.scope(nc, ctx, "pool")
        src = s.sb("src", [P, 4, T])
        even = s.sb("even", [P, 4, T])
        odd = s.sb("odd", [P, 4, T])
        inv = s.sb("inv", [P, 4, 16])
        loaded, step = s.sem("loaded"), s.sem("step")
        with nc.Block() as block:
            @block.sync
            def _(sp):
                sp.dma_start(src[:], rows(z[Z1["pool"]:Z1["pool"] + 512])).then_inc(loaded, 16)

            @block.vector
            def _(dve):
                done = Steps(dve, step)
                for g in range(4):
                    for t in range(2 << g):
                        done.mark(nc.vector.memset(inv[:, g, t:t + 1], 1.0 / (t + 1)))
                dve.wait_ge(loaded, 16)
                now = src
                for r in range(4):
                    nxt = even if r % 2 == 0 else odd
                    lag = 1 << r
                    done.mark(nc.vector.tensor_tensor(nxt[:, r:, lag:], now[:, r:, lag:], now[:, r:, :T - lag],
                                                      ALU.add))
                    done(nc.vector.tensor_copy(nxt[:, r:, :lag], now[:, r:, :lag]))
                    w = 2 << r
                    done.mark(nc.vector.scalar_tensor_tensor(out=y[:, r, w:], in0=nxt[:, r, w:], scalar=1.0 / w,
                                                             in1=src[:, r, w:], op0=ALU.mult, op1=ALU.subtract))
                    done(nc.vector.tensor_tensor(y[:, r, :w], nxt[:, r, :w], inv[:, r, :w], ALU.mult))
                    done(nc.vector.tensor_tensor(y[:, r, :w], y[:, r, :w], src[:, r, :w], ALU.subtract))
                    now = nxt


def stage_conformer(nc, core, z, y):
    taps = 31
    with ExitStack() as ctx:
        s = core.scope(nc, ctx, "conf")
        pad = s.sb("pad", [P, 4, taps - 1 + T])
        gate = s.sb("gate", [P, 4, T])
        loaded, sig, glu, step = s.sem("loaded"), s.sem("sig"), s.sem("glu"), s.sem("step")
        diag = s.sb("diag", [P, 4, P])
        acc = s.ps("acc", [P, 4, 512])
        diag_made, conv_done = s.sem("diag_made"), s.sem("conv_done")
        pe_taps = 14
        with nc.Block() as block:
            @block.sync
            def _(sp):
                at = Z1["conf"]
                sp.dma_start(pad[:, :, taps - 1:], rows(z[at:at + 512])).then_inc(loaded, 16)
                sp.dma_start(gate[:], rows(z[at + 512:at + 1024])).then_inc(loaded, 16)

            @block.scalar
            def _(act):
                act.wait_ge(loaded, 32)
                nc.scalar.activation(gate[:], gate[:], ACT.Sigmoid).then_inc(sig, 1)
                for n in range(4 * pe_taps):
                    if n >= 4:
                        act.wait_ge(conv_done, n - 3)
                    nc.scalar.activation(diag[:, n % 4], core.ident[:], ACT.Copy,
                                         scale=core.v("conf_conv", taps * (n // pe_taps) + n % pe_taps)
                                         ).then_inc(diag_made, 1)

            @block.tensor
            def _(pe):
                pe.wait_ge(glu, 1)
                for n in range(4 * pe_taps):
                    j, i = n // pe_taps, n % pe_taps
                    pe.wait_ge(diag_made, n + 1)
                    nc.tensor.matmul(acc[:, j], diag[:, n % 4], pad[:, j, i:i + T],
                                     start=i == 0, stop=i == pe_taps - 1).then_inc(conv_done, 1)

            @block.vector
            def _(dve):
                done = Steps(dve, step)
                done.mark(nc.vector.memset(pad[:, :, :taps - 1], 0.0))
                dve.wait_ge(sig, 1)
                nc.vector.tensor_tensor(pad[:, :, taps - 1:], pad[:, :, taps - 1:], gate[:],
                                        ALU.mult).then_inc(glu, 1)
                dve.wait_ge(glu, 1)
                done.wait()
                for j in range(4):
                    done.mark(nc.vector.tensor_scalar(y[:, j], pad[:, j, taps - 1:],
                                                      core.v("conf_conv", taps * j + taps - 1),
                                                      core.v("conf_conv_b", j), ALU.mult, ALU.add))
                for i in range(pe_taps, taps - 1):
                    done.wait()
                    for j in range(4):
                        done.mark(nc.vector.scalar_tensor_tensor(
                            out=y[:, j], in0=pad[:, j, i:i + T], scalar=core.v("conf_conv", taps * j + i),
                            in1=y[:, j], op0=ALU.mult, op1=ALU.add))
                done.wait()
                dve.wait_ge(conv_done, 4 * pe_taps)
                done(nc.vector.tensor_tensor(y[:], y[:], acc[:], ALU.add))
        stage_centre(nc, core, y, 4, core.ones, 512)
        rstd = gate[:, 0:1]
        stage_rstd(nc, core, y, rstd, 4, core.ones, 512, EPS)
        ready = s.sem("ready")
        with nc.Block() as block:
            @block.vector
            def _(dve):
                for j in range(4):
                    nc.vector.tensor_tensor(y[:, j], y[:, j], rstd[:, 0], ALU.mult).then_inc(ready, 1)

            @block.scalar
            def _(act):
                for j in range(4):
                    act.wait_ge(ready, j + 1)
                    nc.scalar.activation(y[:, j], y[:, j], ACT.Silu, bias=core.v("conf_ln_b", j),
                                         scale=core.v("conf_ln_g", j))


def stage_attention(nc, core, z, v_tok, y):
    with ExitStack() as ctx:
        s = core.scope(nc, ctx, "attn")
        q = s.sb("q", [P, 4, T])
        k = s.sb("k", [P, 4, T])
        rq = s.sb("rq", [P, 4, T])
        rk = s.sb("rk", [P, 4, T])
        loaded = s.sem("loaded")
        with nc.Block() as block:
            @block.sync
            def _(sp):
                sp.dma_start(q[:], rows(z[Z1["q"]:Z1["q"] + 512])).then_inc(loaded, 16)
                sp.dma_start(k[:], rows(z[Z1["k"]:Z1["k"] + 512])).then_inc(loaded, 16)
                sp.wait_ge(loaded, 32)
        stage_rstd(nc, core, q, rq, 1, core.halves, 64, EPS)
        stage_rstd(nc, core, k, rk, 1, core.halves, 64, EPS)
        with ExitStack() as inner:
            s = core.scope(nc, inner, "heads")
            mask = s.sb("mask", [P, P])
            probs = s.sb("probs", [P, 2, 2, T])
            attn = s.sb("attn", [P, 2, T])
            attn_t = s.sb("attn_t", [P, 2, 4, P])
            small = s.sb("small", [P, 2, 8])
            lam = s.sb("lam", [P, 8])
            scores = s.ps("scores", [P, 2, 2, 512])
            turned = s.ps("turned", [P, 2, 4, P])
            acc_o = s.ps("acc_o", [P, 2, 512])
            names = ("q_ready", "k_ready", "masked", "lam_in", "lam_sum", "lam_exp", "scored", "max_ready",
                     "exped", "mixed", "turned_ready", "turned_copied", "out_ready", "out_copied", "step", "made")
            (q_ready, k_ready, masked, lam_in, lam_sum, lam_exp, scored, max_ready, exped, mixed, turned_ready,
             turned_copied, out_ready, out_copied, step, made) = (s.sem(x) for x in names)
            units = [(h, b) for h in range(4) for b in range(4)]
            with nc.Block() as block:
                @block.gpsimd
                def _(pool):
                    nc.gpsimd.memset(mask[:], 0.0).then_inc(made, 1)
                    pool.wait_ge(made, 1)
                    nc.gpsimd.affine_select(out=mask[:], in_=mask[:], pattern=[[-1, P]], compare_op=ALU.is_ge,
                                            fill=-1e30, base=0, channel_multiplier=1).then_inc(made, 1)

                @block.tensor
                def _(pe):
                    pe.wait_ge(lam_in, 1)
                    nc.tensor.matmul(acc_o[:, 0, 0:2], core.ones[0:64, :], lam[0:64, 0:2], start=True,
                                     stop=True).then_inc(lam_sum, 1)
                    pe.wait_ge(q_ready, 4)
                    pe.wait_ge(k_ready, 4)

                    def score(n):
                        h, b = units[n]
                        if n >= 2:
                            pe.wait_ge(exped, 2 * (n - 1))
                        for m in range(2):
                            at = slice(64 * m, 64 * m + 64)
                            nc.tensor.matmul(scores[:, n % 2, m, :(b + 1) * P], q[at, h, b * P:(b + 1) * P],
                                             k[at, h, :(b + 1) * P], start=True, stop=True).then_inc(scored, 1)

                    def mix(n):
                        h, b = units[n]
                        pe.wait_ge(mixed, n + 1)
                        if n >= 2:
                            pe.wait_ge(turned_copied, n - 1)
                        for c in range(b + 1):
                            last = nc.tensor.transpose(turned[:, n % 2, c], attn[:, n % 2, c * P:(c + 1) * P],
                                                       core.ident[:])
                        last.then_inc(turned_ready, 1)
                        pe.wait_ge(turned_copied, n + 1)
                        if n >= 2:
                            pe.wait_ge(out_copied, n - 1)
                        for c in range(b + 1):
                            last = nc.tensor.matmul(acc_o[:, n % 2, :P], v_tok[:, c, h * P:(h + 1) * P],
                                                    attn_t[:, n % 2, c], start=c == 0, stop=c == b)
                        last.then_inc(out_ready, 1)

                    pe.wait_ge(lam_exp, 1)
                    score(0)
                    for n in range(len(units)):
                        if n + 1 < len(units):
                            score(n + 1)
                        mix(n)

                @block.scalar
                def _(act):
                    act.wait_ge(lam_sum, 1)
                    nc.scalar.activation(lam[:, 2:4], acc_o[:, 0, 0:2], ACT.Exp).then_inc(lam_exp, 1)
                    for n, (h, b) in enumerate(units):
                        if n >= 2:
                            act.wait_ge(mixed, n - 1)
                        for m in range(2):
                            act.wait_ge(max_ready, 2 * n + m + 1)
                            nc.scalar.activation(probs[:, n % 2, m, :(b + 1) * P], scores[:, n % 2, m, :(b + 1) * P],
                                                 ACT.Exp, scale=0.125, bias=small[:, n % 2, 2 + m:3 + m],
                                                 accum_out=small[:, n % 2, 4 + m:5 + m]).then_inc(exped, 1)

                @block.vector
                def _(dve):
                    done = Steps(dve, step)
                    nc.vector.tensor_tensor(lam[:, 0:2], core.v("lam_q", 0, 2), core.v("lam_k", 0, 2),
                                            ALU.mult).then_inc(lam_in, 1)
                    for h in range(4):
                        nc.vector.scalar_tensor_tensor(out=q[:, h], in0=q[:, h], scalar=core.v("q_norm"), in1=rq[:, h],
                                                       op0=ALU.mult, op1=ALU.mult).then_inc(q_ready, 1)
                        nc.vector.scalar_tensor_tensor(out=k[:, h], in0=k[:, h], scalar=core.v("k_norm"), in1=rk[:, h],
                                                       op0=ALU.mult, op1=ALU.mult).then_inc(k_ready, 1)
                    dve.wait_ge(lam_exp, 1)
                    done(nc.vector.tensor_tensor(lam[:, 4:5], lam[:, 3:4], lam[:, 2:3], ALU.subtract))
                    done(nc.vector.tensor_scalar(lam[:, 5:6], lam[:, 4:5], -LAM_INIT, None, ALU.add))
                    dve.wait_ge(made, 2)

                    def top(n):
                        h, b = units[n]
                        for m in range(2):
                            dve.wait_ge(scored, 2 * n + m + 1)
                            sc = scores[:, n % 2, m]
                            done(nc.vector.tensor_tensor(sc[:, b * P:(b + 1) * P], sc[:, b * P:(b + 1) * P], mask[:],
                                                         ALU.add))
                            done(nc.vector.reduce_max(small[:, n % 2, m:m + 1], sc[:, :(b + 1) * P], AX_X))
                            nc.vector.tensor_scalar(small[:, n % 2, 2 + m:3 + m], small[:, n % 2, m:m + 1], -0.125,
                                                    None, ALU.mult).then_inc(max_ready, 1)

                    top(0)
                    for n, (h, b) in enumerate(units):
                        if n + 1 < len(units):
                            top(n + 1)
                        w = (b + 1) * P
                        dve.wait_ge(exped, 2 * n + 2)
                        if n >= 2:
                            dve.wait_ge(turned_ready, n - 1)
                        inv = small[:, n % 2, 6:8]
                        done(nc.vector.reciprocal(inv, small[:, n % 2, 4:6]))
                        done(nc.vector.tensor_scalar(inv[:, 1:2], inv[:, 1:2], lam[:, 5:6], None, ALU.mult))
                        done(nc.vector.tensor_scalar(attn[:, n % 2, :w], probs[:, n % 2, 0, :w], inv[:, 0:1], None,
                                                     ALU.mult))
                        nc.vector.scalar_tensor_tensor(out=attn[:, n % 2, :w], in0=probs[:, n % 2, 1, :w],
                                                       scalar=inv[:, 1:2], in1=attn[:, n % 2, :w], op0=ALU.mult,
                                                       op1=ALU.add).then_inc(mixed, 1)
                        dve.wait_ge(turned_ready, n + 1)
                        if n >= 2:
                            dve.wait_ge(out_ready, n - 1)
                        nc.vector.tensor_copy(attn_t[:, n % 2, :b + 1], turned[:, n % 2, :b + 1]).then_inc(
                            turned_copied, 1)
                        dve.wait_ge(out_ready, n + 1)
                        nc.vector.tensor_copy(y[:, h, b * P:(b + 1) * P], acc_o[:, n % 2, :P]).then_inc(out_copied, 1)
        stage_rstd(nc, core, y, rq, 1, core.ones, P, EPS)
        s = core.scope(nc, ctx, "subln")
        with nc.Block() as block:
            @block.vector
            def _(dve):
                done = Steps(dve, s.sem("scaled"))
                for h in range(4):
                    done.mark(nc.vector.scalar_tensor_tensor(out=y[:, h], in0=y[:, h], scalar=core.v("diff_subln"),
                                                             in1=rq[:, h], op0=ALU.mult, op1=ALU.mult))
                done.wait()
                done(nc.vector.tensor_scalar(y[:], y[:], 1.0 - LAM_INIT, None, ALU.mult))


def first_rows(nc, core, v_tok):
    dram = core.dram
    with ExitStack() as ctx:
        h = split_tiles(core.scope(nc, ctx, "first_h"), "h", [P, DT, T])
        stage_norm(nc, core, core.x, "mix_norm", parts=h)
        stage_rows(nc, core, [(dram["w_in_a"], dram["z"][0:4096], ACT.Copy),
                              (dram["w_in_g"], dram["gates"], ACT.Sigmoid)], h, beside=Ada(nc, core))
        stage_tokens(nc, core, dram["w_in_v"], h, v_tok)


def first_block(nc, core):
    dram = core.dram
    z, g = dram["z"], dram["gates"]
    with ExitStack() as ctx:
        s = core.scope(nc, ctx, "first")
        v_tok = s.sb("v_tok", [P, 4, 512])
        first_rows(nc, core, v_tok)
        merged, y = s.sb("merged", [P, DT, T]), s.sb("y", [P, 4, T])
        stage_short_conv(nc, core, z, y)
        stage_project(nc, core, dram["sc_out"], 4, merged, y, gates=g[0:D], first=True)
        stage_pool(nc, core, z, y)
        stage_project(nc, core, dram["pool_w"], 1, merged, y, gates=g[D:2 * D], groups=True,
                      scale=core.v("pool_scale", 0, DT))
        stage_conformer(nc, core, z, y)
        stage_project(nc, core, dram["conf_out"], 4, merged, y, gates=g[2 * D:3 * D])
        stage_attention(nc, core, z, v_tok, y)
        stage_project(nc, core, dram["diff_out"], 4, merged, y, gates=g[3 * D:4 * D])
        stage_project(nc, core, dram["w_o"], DT, core.x, merged)
    stage_ffn(nc, core, "ffn_norm", dram["ffn_up"], dram["ffn_down"], conv=core.v("ffn_conv", 0, 6 * FT),
              conv_up=True)



def stage_softplus(nc, core, x, parts, n):
    with ExitStack() as ctx:
        s = core.scope(nc, ctx, "softplus")
        u, low, series = s.sb("u", [P, n]), s.sb("low", [P, n]), s.sb("series", [P, n])
        exped, negated, step = s.sem("exped"), s.sem("negated"), s.sem("step")
        with nc.Block() as block:
            @block.scalar
            def _(act):
                act.wait_ge(negated, 1)
                nc.scalar.activation(u[:parts], low[:parts], ACT.Exp).then_inc(exped, 1)

            @block.vector
            def _(dve):
                done = Steps(dve, step)
                v = nc.vector
                done(v.tensor_scalar(low[:parts], x[:parts], -1.0, None, ALU.mult))
                v.tensor_tensor(low[:parts], low[:parts], x[:parts], ALU.min).then_inc(negated, 1)
                dve.wait_ge(exped, 1)
                done(v.tensor_scalar(low[:parts], u[:parts], 2.0, None, ALU.add))
                done(v.reciprocal(low[:parts], low[:parts]))
                done(v.tensor_tensor(u[:parts], u[:parts], low[:parts], ALU.mult))
                done(v.tensor_tensor(low[:parts], u[:parts], u[:parts], ALU.mult))
                done(v.tensor_scalar(series[:parts], low[:parts], 2.0 / 15, 2.0 / 13, ALU.mult, ALU.add))
                for odd in (11, 9, 7, 5, 3, 1):
                    done(v.tensor_tensor(series[:parts], series[:parts], low[:parts], ALU.mult))
                    done(v.tensor_scalar(series[:parts], series[:parts], 2.0 / odd, None, ALU.add))
                done(v.tensor_tensor(series[:parts], series[:parts], u[:parts], ALU.mult))
                done(v.scalar_tensor_tensor(out=x[:parts], in0=x[:parts], scalar=0.0, in1=series[:parts],
                                            op0=ALU.max, op1=ALU.add))


F2 = {n: 512 * k for k, n in enumerate(
    ("q", "k", "qg", "kbg", "kd", "vb", "egc", "ra", "rb", "rk", "rr", "rv", "re", "bonus", "rg"))}
Z2 = {"q": 0, "k": 512, "v": 1024, "z": 1536, "pb": 2048, "ba": 3584, "lo": 3600, "glo": 3728}
UNIT = 8 * C64


def feat(core, name):
    at = F2[name]
    return rows(core.dram["feat"][at:at + 512])


def stage_gdn_gates(nc, core, decay_t, beta):
    z = core.dram["z"]
    with ExitStack() as ctx:
        s = core.scope(nc, ctx, "gates")
        g = s.sb("g", [HN, C64])
        keep = s.sb("keep", [HN, 2, C64])
        ones = s.sb("ones", [HN, C64])
        loaded, step0, fin = s.sem("loaded"), s.sem("step0"), s.sem("fin")
        by_unit = "(j q) (n c) -> n q j c"
        with nc.Block() as block:
            @block.sync
            def _(sp):
                for n in range(NC64):
                    for q in range(2):
                        at = n * 8 + q * 4
                        src = z[Z2["ba"]:Z2["ba"] + 8].rearrange(by_unit, q=2, c=C64)[n, q]
                        sp.dma_start(beta[at:at + 4], src).then_inc(loaded, 16)
                        src = z[Z2["ba"] + 8:Z2["ba"] + 16].rearrange(by_unit, q=2, c=C64)[n, q]
                        sp.dma_start(g[at:at + 4], src).then_inc(loaded, 16)
                sp.wait_ge(loaded, 512)

            @block.scalar
            def _(act):
                act.wait_ge(loaded, 512)
                nc.scalar.activation(beta[:], beta[:], ACT.Sigmoid)

            @block.vector
            def _(dve):
                dve.wait_ge(loaded, 512)
                nc.vector.tensor_scalar(g[:], g[:], core.v("dt_bias")[:HN], None, ALU.add)
        stage_softplus(nc, core, g, HN, C64)
        rate = s.sb("rate", [HN, 1])
        rate_ready, diff_ready, exp_done, summed, made, stored = (
            s.sem(x) for x in ("rate_ready", "diff_ready", "exp_done", "summed", "made", "stored"))
        hn = core.dram["hn"]
        with nc.Block() as block:
            @block.scalar
            def _(act):
                nc.scalar.activation(rate[:], core.v("a_log")[:HN], ACT.Exp).then_inc(rate_ready, 1)
                act.wait_ge(summed, 2)
                nc.scalar.activation(keep[:], keep[:], ACT.Exp).then_inc(exp_done, 1)
                act.wait_ge(diff_ready, 1)
                nc.scalar.activation(decay_t[:], decay_t[:], ACT.Exp).then_inc(exp_done, 1)
                act.wait_ge(exp_done, 1)
                act.dma_start(hn[0], beta[:]).then_inc(stored, 16)
                act.dma_start(hn[1:3].rearrange("a p c -> p a c"), keep[:]).then_inc(stored, 16)
                act.wait_ge(made, 1)
                act.dma_start(core.dram["decay"].rearrange("p s c -> p (s c)"),
                              decay_t[:].rearrange("p s c -> p (s c)")).then_inc(stored, 16)
                act.wait_ge(stored, 48)

            @block.vector
            def _(dve):
                done = Steps(dve, step0)
                v = nc.vector
                dve.wait_ge(rate_ready, 1)
                done.mark(v.memset(ones[:], 1.0))
                done(v.tensor_scalar(g[:], g[:], rate[:], -1.0, ALU.mult, ALU.mult))
                v.tensor_tensor_scan(keep[:, 0], ones[:], g[:], 0.0, ALU.mult, ALU.add).then_inc(summed, 1)
                dve.wait_ge(summed, 1)
                gc = g[:]
                done(v.tensor_copy(gc, keep[:, 0]))
                v.tensor_scalar(keep[:, 1], gc, gc[:, C64 - 1:C64], -1.0, ALU.subtract,
                                ALU.mult).then_inc(summed, 1)
                done(v.tensor_tensor(decay_t[:], gc.unsqueeze(1).broadcast_to([HN, C64, C64]),
                                     gc.unsqueeze(2).broadcast_to([HN, C64, C64]), ALU.subtract))
                v.tensor_scalar(decay_t[:], decay_t[:], 0.0, None, ALU.min).then_inc(diff_ready, 1)

            @block.gpsimd
            def _(pool):
                pool.wait_ge(exp_done, 2)
                nc.gpsimd.affine_select(out=decay_t[:], in_=decay_t[:], pattern=[[-1, C64], [1, C64]],
                                        compare_op=ALU.is_ge, fill=0.0, base=0,
                                        channel_multiplier=0).then_inc(made, 1)


def grams(nc, pe, out, lhs, rhs, n):
    at = slice(n * C64, (n + 1) * C64)
    for q in range(2):
        half = slice(64 * q, 64 * q + 64)
        for j in range(4):
            last = nc.tensor.matmul(out[:C64, q, j * C64:(j + 1) * C64], lhs[half, j, at], rhs[half, j, at],
                                    start=True, stop=True)
    return last


def stage_gram(nc, core, lhs, rhs, dst):
    with ExitStack() as ctx:
        s = core.scope(nc, ctx, "gram")
        out = s.sb("out", [C64, NC64, UNIT])
        acc = s.ps("acc", [P, 2, 2, 512])
        product, copied, stored = s.sem("product"), s.sem("copied"), s.sem("stored")
        with nc.Block() as block:
            @block.tensor
            def _(pe):
                for n in range(NC64):
                    if n >= 2:
                        pe.wait_ge(copied, n - 1)
                    grams(nc, pe, acc[:, n % 2], lhs, rhs, n).then_inc(product, 1)

            @block.vector
            def _(dve):
                for n in range(NC64):
                    dve.wait_ge(product, n + 1)
                    nc.vector.tensor_copy(out[:, n].rearrange("p (q c) -> p q c", q=2),
                                          acc[:C64, n % 2, :, :4 * C64]).then_inc(copied, 1)

            @block.sync
            def _(sp):
                for n in range(NC64):
                    sp.wait_ge(copied, n + 1)
                    sp.dma_start(dst[8 * n:8 * n + 8].rearrange("u i j -> i u j"),
                                 out[:, n].rearrange("p (u c) -> p u c", u=8)).then_inc(stored, 16)
                sp.wait_ge(stored, 16 * NC64)


def stage_gdn_prepare(nc, core, decay_t, beta):
    z = core.dram["z"]
    with ExitStack() as ctx:
        s = core.scope(nc, ctx, "gdn")
        raw = s.sb("raw", [P, 12, T])
        qkv = s.sb("qkv", [P, 12, T])
        loaded, step, conved = s.sem("loaded"), s.sem("step"), s.sem("conved")
        with nc.Block() as block:
            @block.sync
            def _(sp):
                sp.dma_start(raw[:], rows(z[0:1536])).then_inc(loaded, 16)

            @block.vector
            def _(dve):
                done = Steps(dve, step)
                dve.wait_ge(loaded, 16)
                for j in range(12):
                    done.mark(nc.vector.tensor_scalar(qkv[:, j], raw[:, j], core.v("conv_gdn", 4 * j + 3), None,
                                                      ALU.mult))
                for lag in (1, 2, 3):
                    done.wait()
                    for j in range(12):
                        ins = nc.vector.scalar_tensor_tensor(
                            out=qkv[:, j, lag:], in0=raw[:, j, :T - lag],
                            scalar=core.v("conv_gdn", 4 * j + 3 - lag), in1=qkv[:, j, lag:],
                            op0=ALU.mult, op1=ALU.add)
                        if lag < 3:
                            done.mark(ins)
                        else:
                            ins.then_inc(conved, 1)

            @block.scalar
            def _(act):
                for j in range(12):
                    act.wait_ge(conved, j + 1)
                    nc.scalar.activation(qkv[:, j], qkv[:, j], ACT.Silu)
        stage_rstd(nc, core, qkv[:, 0:8], raw[:, 0:8], 1, core.halves, 1.0, 1e-6)
        bcast = s.sb("bcast", [P, 3, 4, T])
        half, normed, scaled, stored, step2 = (s.sem(x) for x in ("half", "normed", "scaled", "stored", "step2"))
        spread = s.sem("spread")
        with nc.Block() as block:
            @block.sync
            def _(sp):
                for a in range(3):
                    for q in range(2):
                        for j in range(4):
                            src = core.dram["hn"][a].rearrange("(n q j) c -> q j n c", q=2, j=4)[q, j]
                            sp.dma_start(bcast[64 * q:64 * q + 64, a, j].rearrange("p (n c) -> p n c", c=C64),
                                         src.unsqueeze(0).broadcast_to([64, NC64, C64])).then_inc(spread, 16)
                sp.wait_ge(normed, 2)
                sp.dma_start(feat(core, "q"), qkv[:, 0:4]).then_inc(stored, 16)
                sp.dma_start(feat(core, "k"), qkv[:, 4:8]).then_inc(stored, 16)
                for n, (name, tile) in enumerate((("kd", raw[:, 0:4]), ("qg", raw[:, 4:8]), ("vb", raw[:, 8:12]),
                                                  ("kbg", bcast[:, 0]))):
                    sp.wait_ge(scaled, n + 1)
                    sp.dma_start(feat(core, name), tile).then_inc(stored, 16)
                sp.dma_start(feat(core, "egc"), bcast[:, 1]).then_inc(stored, 16)
                sp.wait_ge(stored, 16 * 7)

            @block.vector
            def _(dve):
                done = Steps(dve, step2)
                v = nc.vector
                v.scalar_tensor_tensor(out=qkv[:, 0:4], in0=qkv[:, 0:4], scalar=0.125, in1=raw[:, 0:4],
                                       op0=ALU.mult, op1=ALU.mult).then_inc(normed, 1)
                v.tensor_tensor(qkv[:, 4:8], qkv[:, 4:8], raw[:, 4:8], ALU.mult).then_inc(normed, 1)
                dve.wait_ge(normed, 2)
                dve.wait_ge(spread, 16 * 24)
                v.tensor_tensor(raw[:, 0:4], qkv[:, 4:8], bcast[:, 2], ALU.mult).then_inc(scaled, 1)
                v.tensor_tensor(raw[:, 4:8], qkv[:, 0:4], bcast[:, 1], ALU.mult).then_inc(scaled, 1)
                v.tensor_tensor(raw[:, 8:12], qkv[:, 8:12], bcast[:, 0], ALU.mult).then_inc(scaled, 1)
                dve.wait_ge(scaled, 3)
                done(v.tensor_tensor(bcast[:, 0], bcast[:, 0], bcast[:, 1], ALU.mult))
                v.tensor_tensor(bcast[:, 0], bcast[:, 0], qkv[:, 4:8], ALU.mult).then_inc(scaled, 1)
        stage_gram(nc, core, qkv[:, 4:8], qkv[:, 4:8], core.dram["gram"][0:HN])


def stage_rwkv_prepare(nc, core):
    z = core.dram["z"]
    with ExitStack() as ctx:
        s = core.scope(nc, ctx, "rwkv")
        r, k, v_ = (s.sb(n, [P, 4, T]) for n in ("r", "k", "v"))
        d = s.sb("d", [P, 4, T])
        lw, a, g = (s.sb(n, [P, 4, T]) for n in ("lw", "a", "g"))
        lo = s.sb("lo", [P, 4, T])
        low = s.sb("low", [P, 4, 512])
        acc = s.ps("acc", [P, 4, 512])
        loaded, step, mixed, bent, product, freed = (
            s.sem(x) for x in ("loaded", "step", "mixed", "bent", "product", "freed"))
        lows = ((0, 64), (1, 64), (2, P), (3, 32))
        with nc.Block() as block:
            @block.sync
            def _(sp):
                for n, at in ((0, 0), (1, 64)):
                    sp.dma_start(lo[:64, n], z[Z2["lo"] + at:Z2["lo"] + at + 64]).then_inc(loaded, 16)
                sp.dma_start(lo[:, 2], z[Z2["glo"]:Z2["glo"] + P]).then_inc(loaded, 16)
                sp.dma_start(lo[:32, 3], z[Z2["glo"] + P:Z2["glo"] + 160]).then_inc(loaded, 16)
                sp.dma_start(low[:64, 0], core.dram["w2"]).then_inc(loaded, 16)
                sp.dma_start(low[:64, 1], core.dram["a2"]).then_inc(loaded, 16)
                sp.dma_start(low[:, 2], core.dram["g2"][0:P]).then_inc(loaded, 16)
                sp.dma_start(low[:32, 3], core.dram["g2"][P:160]).then_inc(loaded, 16)
                for n, tile in enumerate((r, k, v_)):
                    at = Z2["pb"] + 512 * n
                    sp.dma_start(tile[:], rows(z[at:at + 512])).then_inc(loaded, 16)

            @block.vector
            def _(dve):
                done = Steps(dve, step)
                v = nc.vector
                dve.wait_ge(loaded, 16 * 11)
                for n, p in lows:
                    done.mark(v.tensor_tensor(d[:p, n, 1:], lo[:p, n, :T - 1], lo[:p, n, 1:], ALU.subtract))
                    done.mark(v.tensor_scalar(d[:p, n, 0:1], lo[:p, n, 0:1], -1.0, None, ALU.mult))
                done.wait()
                for n, p in lows:
                    v.scalar_tensor_tensor(out=lo[:p, n], in0=d[:p, n], scalar=core.v("mu_lo", n)[:p],
                                           in1=lo[:p, n], op0=ALU.mult, op1=ALU.add).then_inc(mixed, 1)
                dve.wait_ge(mixed, 4)
                for m, tile in enumerate((r, k, v_)):
                    done.mark(v.tensor_tensor(d[:, :, 1:], tile[:, :, :T - 1], tile[:, :, 1:], ALU.subtract))
                    done(v.tensor_scalar(d[:, :, 0:1], tile[:, :, 0:1], -1.0, None, ALU.mult))
                    for j in range(4):
                        done.mark(v.scalar_tensor_tensor(out=tile[:, j], in0=d[:, j],
                                                         scalar=core.v("mu_rkv", 4 * m + j), in1=tile[:, j],
                                                         op0=ALU.mult, op1=ALU.add))
                    done.wait()

            @block.scalar
            def _(act):
                act.wait_ge(mixed, 4)
                nc.scalar.activation(lo[:64, 0], lo[:64, 0], ACT.Tanh).then_inc(bent, 1)
                nc.scalar.activation(lo[:, 2], lo[:, 2], ACT.Sigmoid).then_inc(bent, 1)
                nc.scalar.activation(lo[:32, 3], lo[:32, 3], ACT.Sigmoid).then_inc(bent, 1)
                for n in range(12):
                    which, j = n // 4, n % 4
                    act.wait_ge(product, n + 1)
                    if which == 0:
                        ins = nc.scalar.activation(lw[:, j], acc[:, n % 4], ACT.Sigmoid, bias=core.v("w0", j))
                    elif which == 1:
                        ins = nc.scalar.activation(a[:, j], acc[:, n % 4], ACT.Sigmoid, bias=core.v("a0", j))
                    else:
                        ins = nc.scalar.activation(g[:, j], acc[:, n % 4], ACT.Copy)
                    ins.then_inc(freed, 1)

            @block.tensor
            def _(pe):
                pe.wait_ge(loaded, 16 * 11)
                pe.wait_ge(bent, 3)
                for n in range(12):
                    which, j = n // 4, n % 4
                    if n >= 4:
                        pe.wait_ge(freed, n - 3)
                    at = slice(j * P, (j + 1) * P)
                    if which < 2:
                        nc.tensor.matmul(acc[:, n % 4], low[:64, which, at], lo[:64, which], start=True,
                                         stop=True).then_inc(product, 1)
                    else:
                        nc.tensor.matmul(acc[:, n % 4], low[:, 2, at], lo[:, 2], start=True, stop=False)
                        nc.tensor.matmul(acc[:, n % 4], low[:32, 3, at], lo[:32, 3], start=False,
                                         stop=True).then_inc(product, 1)
        kk, rstd = lo, low
        s = core.scope(nc, ctx, "rwkv_kk")
        step = s.sem("step")
        with nc.Block() as block:
            @block.vector
            def _(dve):
                done = Steps(dve, step)
                v = nc.vector
                for j in range(4):
                    done.mark(v.tensor_scalar(kk[:, j], k[:, j], core.v("k_k", j), None, ALU.mult))
                    done.mark(v.tensor_scalar(d[:, j], a[:, j], -1.0, core.v("k_a", j), ALU.add, ALU.mult))
                done.wait()
                done(v.scalar_tensor_tensor(out=k[:], in0=d[:], scalar=1.0, in1=k[:], op0=ALU.add, op1=ALU.mult))
                done(v.tensor_scalar(lw[:], lw[:], -math.exp(-0.5), None, ALU.mult))
        stage_rstd(nc, core, kk, rstd, 1, core.halves, 1.0, 1e-6)
        s = core.scope(nc, ctx, "rwkv_scale")
        reset = s.sb("reset", [P, T])
        cw, e = s.sb("cw", [P, 4, T]), s.sb("e", [P, 4, T])
        step, summed, exped, ready, stored, sums = (
            s.sem(x) for x in ("step", "summed", "exped", "ready", "stored", "sums"))
        order = ("rv", "rg", "re", "rr", "rb", "rk", "ra", "bonus")
        tiles = {"rv": v_, "rg": g, "re": e, "rr": r, "rb": a, "rk": k, "ra": kk, "bonus": d}
        with nc.Block() as block:
            @block.vector
            def _(dve):
                done = Steps(dve, step)
                v = nc.vector
                done(v.memset(reset[:], 1.0))
                done(v.memset(reset[:].rearrange("p (n c) -> p n c", c=C64)[:, :, 0:1], 0.0))
                for j in range(4):
                    v.tensor_tensor_scan(cw[:, j], reset[:], lw[:, j], 0.0, ALU.mult, ALU.add).then_inc(summed, 1)
                dve.wait_ge(summed, 4)
                v.tensor_tensor(lw[:], cw[:], lw[:], ALU.subtract).then_inc(summed, 1)
                done(v.tensor_tensor(d[:], r[:], k[:], ALU.mult))
                for j in range(4):
                    v.tensor_scalar(d[:, j], d[:, j], core.v("r_k", j), None, ALU.mult).then_inc(ready, 1)
                done(v.tensor_tensor(kk[:], kk[:], rstd[:], ALU.mult))
                done(v.tensor_tensor(a[:], a[:], kk[:], ALU.mult))
                dve.wait_ge(exped, 3)
                v.tensor_tensor(r[:], r[:], e[:], ALU.mult).then_inc(ready, 1)
                v.tensor_tensor(a[:], a[:], cw[:], ALU.mult).then_inc(ready, 1)
                v.tensor_tensor(k[:], k[:], cw[:], ALU.mult).then_inc(ready, 1)
                v.scalar_tensor_tensor(out=kk[:], in0=kk[:], scalar=-1.0, in1=lw[:], op0=ALU.mult,
                                       op1=ALU.mult).then_inc(ready, 1)
                dve.wait_ge(sums, 4)
                v.tensor_tensor(d[:], acc[:], v_[:], ALU.mult).then_inc(ready, 1)

            @block.scalar
            def _(act):
                act.wait_ge(summed, 5)
                nc.scalar.activation(e[:], cw[:], ACT.Exp).then_inc(exped, 1)
                nc.scalar.activation(lw[:], lw[:], ACT.Exp).then_inc(exped, 1)
                act.wait_ge(exped, 2)
                nc.scalar.activation(cw[:], cw[:], ACT.Exp, scale=-1.0).then_inc(exped, 1)

            @block.tensor
            def _(pe):
                pe.wait_ge(ready, 4)
                for j in range(4):
                    nc.tensor.matmul(acc[:, j], core.halves[:], d[:, j], start=True, stop=True).then_inc(sums, 1)

            @block.sync
            def _(sp):
                for n, name in enumerate(order):
                    if n == 2:
                        sp.wait_ge(exped, 1)
                    if n >= 3:
                        sp.wait_ge(ready, 4 + n - 2)
                    sp.dma_start(feat(core, name), tiles[name][:]).then_inc(stored, 16)
                sp.wait_ge(stored, 16 * len(order))
        stage_gram(nc, core, kk, a, core.dram["gram"][HN:2 * HN])


class Inverse:

    def __init__(self, nc, core, decay_t, beta):
        self.nc, self.core, self.decay_t, self.beta = nc, core, decay_t, beta

    def open(self, s):
        self.m = s.sb("m", [P, C64, C64])
        self.inv = s.sb("inv", [P, C64, C64])
        self.prod = s.sb("prod", [P, C64, C64])
        self.loaded, self.step, self.stored = s.sem("m_loaded"), s.sem("inverse_step"), s.sem("inverse_stored")
        with self.nc.Block() as block:
            @block.sync
            def _(sp):
                sp.dma_start(self.m[:], self.core.dram["gram"]).then_inc(self.loaded, 16)
                sp.wait_ge(self.loaded, 16)

    def sync_turn(self, sp, n, i, k):
        pass

    def tensor_turn(self, pe, n, i, k):
        pass

    def vector_segment(self, dve, n, turns):
        m, inv, prod = self.m, self.inv, self.prod
        done = Steps(dve, self.step)
        v = self.nc.vector
        flat = inv[:].rearrange("p s c -> p (s c)")
        done(v.memset(flat, 0.0))
        done(v.memset(flat[:, ::C64 + 1], 1.0))
        low = m[:HN]
        done(v.tensor_tensor(low, low, self.decay_t[:].rearrange("p s c -> p c s"), ALU.mult))
        done(v.scalar_tensor_tensor(out=low, in0=low, scalar=-1.0,
                                    in1=self.beta[:].unsqueeze(2).broadcast_to([HN, C64, C64]),
                                    op0=ALU.mult, op1=ALU.mult))
        for i in range(1, C64):
            done(v.tensor_tensor(prod[:, :i, :i], inv[:, :i, :i],
                                 m[:, i:i + 1, :i].broadcast_to([P, i, i]), ALU.mult))
            done(v.tensor_reduce(inv[:, :i, i:i + 1], prod[:, :i, :i], AX_X, ALU.add))

    def close(self):
        with self.nc.Block() as block:
            @block.sync
            def _(sp):
                sp.dma_start(self.core.dram["inverse"], self.inv[:]).then_inc(self.stored, 16)
                sp.wait_ge(self.stored, 16)


def stage_to_tokens(nc, core, name, dst):
    with ExitStack() as ctx:
        s = core.scope(nc, ctx, "turn")
        src = s.sb("src", [P, 4, T])
        acc = s.ps("acc", [P, 4, 512])
        loaded, turned, copied = s.sem("loaded"), s.sem("turned"), s.sem("copied")
        with nc.Block() as block:
            @block.sync
            def _(sp):
                sp.dma_start(src[:], feat(core, name)).then_inc(loaded, 16)

            @block.tensor
            def _(pe):
                pe.wait_ge(loaded, 16)
                for n in range(NC64):
                    if n >= 4:
                        pe.wait_ge(copied, n - 3)
                    for j in range(4):
                        last = nc.tensor.transpose(acc[:C64, n % 4, j * P:(j + 1) * P],
                                                   src[:, j, n * C64:(n + 1) * C64], core.ident[:])
                    last.then_inc(turned, 1)

            @block.vector
            def _(dve):
                for n in range(NC64):
                    dve.wait_ge(turned, n + 1)
                    nc.vector.tensor_copy(dst[:, n].rearrange("p (q j c) -> p q j c", q=2, j=4),
                                          acc[:C64, n % 4].rearrange("p (j q c) -> p q j c", q=2, j=4)
                                          ).then_inc(copied, 1)


def stage_masked(nc, core, lhs, rhs, dst, weight=None, strict=False):
    with ExitStack() as ctx:
        s = core.scope(nc, ctx, "masked")
        acc = s.ps("acc", [P, 2, 2, 512])
        mask = s.sb("mask", [C64, C64])
        product, copied, made = s.sem("product"), s.sem("copied"), s.sem("made")
        with nc.Block() as block:
            @block.gpsimd
            def _(pool):
                if weight is None:
                    nc.gpsimd.memset(mask[:], 1.0).then_inc(made, 1)
                    pool.wait_ge(made, 1)
                    nc.gpsimd.affine_select(out=mask[:], in_=mask[:], pattern=[[1, C64]], compare_op=ALU.is_ge,
                                            fill=0.0, base=-1 if strict else 0,
                                            channel_multiplier=-1).then_inc(made, 1)

            @block.tensor
            def _(pe):
                for n in range(NC64):
                    if n >= 2:
                        pe.wait_ge(copied, n - 1)
                    grams(nc, pe, acc[:, n % 2], lhs, rhs, n).then_inc(product, 1)

            @block.vector
            def _(dve):
                if weight is None:
                    dve.wait_ge(made, 2)
                for n in range(NC64):
                    dve.wait_ge(product, n + 1)
                    if weight is None:
                        by = mask[:].unsqueeze(1).broadcast_to([C64, 8, C64]).rearrange("p (q j) c -> p q j c", q=2)
                    else:
                        by = weight[:, n].rearrange("p (q j c) -> p q j c", q=2, j=4)
                    nc.vector.tensor_tensor(dst[:, n].rearrange("p (q j c) -> p q j c", q=2, j=4),
                                            acc[:C64, n % 2, :, :4 * C64].rearrange("p q (j c) -> p q j c", c=C64),
                                            by, ALU.mult).then_inc(copied, 1)


def unit(tile, n, q, j):
    at = (q * 4 + j) * C64
    return tile[:, n, at:at + C64]


def by_unit(dram3):
    return dram3.rearrange("(n u) s c -> s n u c", u=8)


def stage_gdn_scan(nc, core, y):
    with ExitStack() as ctx:
        s = core.scope(nc, ctx, "gscan")
        q, kbg, egc = (s.sb(n, [P, 4, T]) for n in ("q", "kbg", "egc"))
        kd_tok, vb_tok, attn, inv = (s.sb(n, [C64, NC64, UNIT]) for n in ("kd_tok", "vb_tok", "attn", "inv"))
        loaded = s.sem("loaded")
        with nc.Block() as block:
            @block.sync
            def _(sp):
                sp.dma_start(q[:], feat(core, "q")).then_inc(loaded, 16)
                sp.dma_start(kbg[:], feat(core, "k")).then_inc(loaded, 16)
                sp.dma_start(egc[:], feat(core, "egc")).then_inc(loaded, 16)
                sp.dma_start(inv[:].rearrange("p n (u c) -> p n u c", c=C64),
                             by_unit(core.dram["decay"])).then_inc(loaded, 16)
                sp.wait_ge(loaded, 64)
        stage_masked(nc, core, kbg, q, attn, weight=inv)
        stage_to_tokens(nc, core, "kd", kd_tok)
        stage_to_tokens(nc, core, "vb", vb_tok)
        s = core.scope(nc, ctx, "gchunks")
        state = s.sb("state", [P, 4, C64])
        r, vn = s.sb("r", [C64, UNIT]), s.sb("vn", [C64, UNIT])
        ks = s.ps("ks", [P, 2, 512])
        tr = s.ps("tr", [P, 512])
        os_ = s.ps("os", [P, 2, 512])
        ov = s.ps("ov", [P, 512])
        up = s.ps("up", [P, 512])
        (loaded, ks_ready, r_ready, tr_ready, vn_ready, os_ready, ov_ready, up_ready, state_ready, o_copied,
         step) = (s.sem(x) for x in ("loaded", "ks_ready", "r_ready", "tr_ready", "vn_ready", "os_ready",
                                     "ov_ready", "up_ready", "state_ready", "o_copied", "step"))
        with nc.Block() as block:
            @block.sync
            def _(sp):
                sp.dma_start(q[:], feat(core, "qg")).then_inc(loaded, 16)
                sp.dma_start(kbg[:], feat(core, "kbg")).then_inc(loaded, 16)
                sp.dma_start(inv[:].rearrange("p n (u c) -> p n u c", c=C64),
                             by_unit(core.dram["inverse"][0:HN])).then_inc(loaded, 16)

            @block.tensor
            def _(pe):
                pe.wait_ge(loaded, 48)
                for n in range(NC64):
                    at = slice(n * C64, (n + 1) * C64)
                    pe.wait_ge(state_ready, n + 1)
                    for h in range(8):
                        c, j = h // 4, h % 4
                        half = slice(64 * c, 64 * c + 64)
                        last = nc.tensor.matmul(ks[:C64, c, j * C64:(j + 1) * C64], kbg[half, j, at],
                                                state[half, j], start=True, stop=True)
                    last.then_inc(ks_ready, 1)
                    if n:
                        pe.wait_ge(o_copied, n)
                    for h in range(8):
                        c, j = h // 4, h % 4
                        half = slice(64 * c, 64 * c + 64)
                        last = nc.tensor.matmul(os_[half, c, j * C64:(j + 1) * C64], state[half, j],
                                                q[half, j, at], start=True, stop=True)
                    last.then_inc(os_ready, 1)
                    pe.wait_ge(r_ready, n + 1)
                    for h in range(8):
                        c, j = h // 4, h % 4
                        last = nc.tensor.matmul(tr[:C64, h * C64:(h + 1) * C64], unit(inv, n, c, j),
                                                r[:, h * C64:(h + 1) * C64], start=True, stop=True)
                    last.then_inc(tr_ready, 1)
                    pe.wait_ge(vn_ready, n + 1)
                    for h in range(8):
                        c, j = h // 4, h % 4
                        half = slice(64 * c, 64 * c + 64)
                        last = nc.tensor.matmul(up[half, j * C64:(j + 1) * C64], unit(kd_tok, n, c, j),
                                                vn[:, h * C64:(h + 1) * C64], start=True, stop=True)
                    last.then_inc(up_ready, 1)
                    for h in range(8):
                        c, j = h // 4, h % 4
                        half = slice(64 * c, 64 * c + 64)
                        last = nc.tensor.matmul(ov[half, j * C64:(j + 1) * C64], vn[:, h * C64:(h + 1) * C64],
                                                unit(attn, n, c, j), start=True, stop=True)
                    last.then_inc(ov_ready, 1)

            @block.scalar
            def _(act):
                for n in range(NC64):
                    act.wait_ge(tr_ready, n + 1)
                    if n:
                        act.wait_ge(ov_ready, n)
                    nc.scalar.activation(vn[:], tr[:C64, :], ACT.Copy).then_inc(vn_ready, 1)

            @block.vector
            def _(dve):
                done = Steps(dve, step)
                v = nc.vector
                v.memset(state[:], 0.0).then_inc(state_ready, 1)
                for n in range(NC64):
                    dve.wait_ge(ks_ready, n + 1)
                    v.tensor_tensor(r[:].rearrange("p (q c) -> p q c", q=2),
                                    vb_tok[:, n].rearrange("p (q c) -> p q c", q=2), ks[:C64, :, :4 * C64],
                                    ALU.subtract).then_inc(r_ready, 1)
                    dve.wait_ge(os_ready, n + 1)
                    last = egc[:, :, n * C64 + C64 - 1:(n + 1) * C64]
                    done(v.tensor_tensor(state[:], state[:], last.broadcast_to([P, 4, C64]), ALU.mult))
                    dve.wait_ge(up_ready, n + 1)
                    v.tensor_tensor(state[:], state[:], up[:, :4 * C64].rearrange("p (j c) -> p j c", j=4),
                                    ALU.add).then_inc(state_ready, 1)
                    dst = y[:, :, n * C64:(n + 1) * C64]
                    for c in range(2):
                        half = slice(64 * c, 64 * c + 64)
                        done.mark(v.tensor_copy(dst[half], os_[half, c, :4 * C64].rearrange(
                            "p (j c) -> p j c", j=4)))
                    done.wait()
                    dve.wait_ge(ov_ready, n + 1)
                    v.tensor_tensor(dst, dst, ov[:, :4 * C64].rearrange("p (j c) -> p j c", j=4),
                                    ALU.add).then_inc(o_copied, 1)


def stage_rwkv_scan(nc, core, y):
    with ExitStack() as ctx:
        s = core.scope(nc, ctx, "rscan")
        ra, rr = s.sb("ra", [P, 4, T]), s.sb("rr", [P, 4, T])
        decay = s.sb("decay", [P, 4, NC64])
        b_tok, k_tok, v_tok, rb, rk, akv = (
            s.sb(n, [C64, NC64, UNIT]) for n in ("b_tok", "k_tok", "v_tok", "rb", "rk", "akv"))
        stage_to_tokens(nc, core, "rv", v_tok)
        with ExitStack() as inner:
            s1 = core.scope(nc, inner, "rmat")
            kb = s1.sb("kb", [P, 4, T])
            loaded, again, product, copied = (s1.sem(x) for x in ("loaded", "again", "product", "copied"))
            with nc.Block() as block:
                @block.sync
                def _(sp):
                    sp.dma_start(ra[:], feat(core, "ra")).then_inc(loaded, 16)
                    sp.dma_start(rr[:], feat(core, "rr")).then_inc(loaded, 16)
                    sp.dma_start(kb[:], feat(core, "rk")).then_inc(loaded, 16)
                    sp.wait_ge(loaded, 48)
            stage_masked(nc, core, kb, ra, b_tok, strict=True)
            stage_masked(nc, core, kb, rr, rk)
            acc = s1.ps("acc", [P, 2, 512])
            with nc.Block() as block:
                @block.sync
                def _(sp):
                    sp.dma_start(kb[:], feat(core, "rb")).then_inc(again, 16)
                    sp.wait_ge(again, 16)

                @block.tensor
                def _(pe):
                    for n in range(NC64):
                        if n >= 2:
                            pe.wait_ge(copied, n - 1)
                        for h in range(8):
                            at = slice(h * C64, (h + 1) * C64)
                            last = nc.tensor.matmul(acc[:C64, n % 2, at], b_tok[:, n, at], v_tok[:, n, at],
                                                    start=True, stop=True)
                        last.then_inc(product, 1)

                @block.vector
                def _(dve):
                    for n in range(NC64):
                        dve.wait_ge(product, n + 1)
                        nc.vector.tensor_copy(akv[:, n], acc[:C64, n % 2]).then_inc(copied, 1)
            stage_masked(nc, core, kb, rr, rb)
            last_loaded, picked = s1.sem("last_loaded"), s1.sem("picked")
            with nc.Block() as block:
                @block.sync
                def _(sp):
                    sp.dma_start(kb[:], feat(core, "re")).then_inc(last_loaded, 16)

                @block.vector
                def _(dve):
                    dve.wait_ge(last_loaded, 16)
                    nc.vector.tensor_copy(decay[:], kb[:].rearrange("p j (n c) -> p j n c", c=C64)[
                        :, :, :, C64 - 1]).then_inc(picked, 1)
        stage_to_tokens(nc, core, "rb", b_tok)
        stage_to_tokens(nc, core, "rk", k_tok)
        s = core.scope(nc, ctx, "rchunks")
        inv = s.sb("inv", [C64, NC64, UNIT])
        state = s.sb("state", [P, 4, C64])
        r, sa = s.sb("r", [C64, UNIT]), s.sb("sa", [C64, UNIT])
        as_ = s.ps("as", [P, 2, 512])
        tr = s.ps("tr", [P, 512])
        ys = s.ps("ys", [P, 2, 512])
        yv = s.ps("yv", [P, 512])
        up = s.ps("up", [P, 512])
        (loaded, as_ready, r_ready, tr_ready, sa_ready, ys_ready, yv_ready, up_ready, state_ready, y_copied,
         step) = (s.sem(x) for x in ("loaded", "as_ready", "r_ready", "tr_ready", "sa_ready", "ys_ready",
                                     "yv_ready", "up_ready", "state_ready", "y_copied", "step"))
        with nc.Block() as block:
            @block.sync
            def _(sp):
                sp.dma_start(inv[:].rearrange("p n (u c) -> p n u c", c=C64),
                             by_unit(core.dram["inverse"][HN:2 * HN])).then_inc(loaded, 16)

            @block.tensor
            def _(pe):
                pe.wait_ge(loaded, 16)
                for n in range(NC64):
                    at = slice(n * C64, (n + 1) * C64)
                    pe.wait_ge(state_ready, n + 1)
                    for h in range(8):
                        c, j = h // 4, h % 4
                        half = slice(64 * c, 64 * c + 64)
                        last = nc.tensor.matmul(as_[:C64, c, j * C64:(j + 1) * C64], ra[half, j, at],
                                                state[half, j], start=True, stop=True)
                    last.then_inc(as_ready, 1)
                    if n:
                        pe.wait_ge(y_copied, n)
                    for h in range(8):
                        c, j = h // 4, h % 4
                        half = slice(64 * c, 64 * c + 64)
                        last = nc.tensor.matmul(ys[half, c, j * C64:(j + 1) * C64], state[half, j],
                                                rr[half, j, at], start=True, stop=True)
                    last.then_inc(ys_ready, 1)
                    pe.wait_ge(r_ready, n + 1)
                    for h in range(8):
                        c, j = h // 4, h % 4
                        last = nc.tensor.matmul(tr[:C64, h * C64:(h + 1) * C64], unit(inv, n, c, j),
                                                r[:, h * C64:(h + 1) * C64], start=True, stop=True)
                    last.then_inc(tr_ready, 1)
                    pe.wait_ge(sa_ready, n + 1)
                    for h in range(8):
                        c, j = h // 4, h % 4
                        half = slice(64 * c, 64 * c + 64)
                        to = up[half, j * C64:(j + 1) * C64]
                        nc.tensor.matmul(to, unit(b_tok, n, c, j), sa[:, h * C64:(h + 1) * C64], start=True,
                                         stop=False)
                        last = nc.tensor.matmul(to, unit(k_tok, n, c, j), unit(v_tok, n, c, j), start=False,
                                                stop=True)
                    last.then_inc(up_ready, 1)
                    for h in range(8):
                        c, j = h // 4, h % 4
                        half = slice(64 * c, 64 * c + 64)
                        to = yv[half, j * C64:(j + 1) * C64]
                        nc.tensor.matmul(to, sa[:, h * C64:(h + 1) * C64], unit(rb, n, c, j), start=True,
                                         stop=False)
                        last = nc.tensor.matmul(to, unit(v_tok, n, c, j), unit(rk, n, c, j), start=False,
                                                stop=True)
                    last.then_inc(yv_ready, 1)

            @block.scalar
            def _(act):
                for n in range(NC64):
                    act.wait_ge(tr_ready, n + 1)
                    if n:
                        act.wait_ge(yv_ready, n)
                    nc.scalar.activation(sa[:], tr[:C64, :], ACT.Copy).then_inc(sa_ready, 1)

            @block.vector
            def _(dve):
                done = Steps(dve, step)
                v = nc.vector
                v.memset(state[:], 0.0).then_inc(state_ready, 1)
                for n in range(NC64):
                    dve.wait_ge(as_ready, n + 1)
                    v.tensor_tensor(r[:].rearrange("p (q c) -> p q c", q=2),
                                    akv[:, n].rearrange("p (q c) -> p q c", q=2), as_[:C64, :, :4 * C64],
                                    ALU.add).then_inc(r_ready, 1)
                    dve.wait_ge(ys_ready, n + 1)
                    dve.wait_ge(up_ready, n + 1)
                    done(v.tensor_tensor(state[:], state[:], up[:, :4 * C64].rearrange("p (j c) -> p j c", j=4),
                                         ALU.add))
                    v.tensor_tensor(state[:], state[:], decay[:, :, n:n + 1].broadcast_to([P, 4, C64]),
                                    ALU.mult).then_inc(state_ready, 1)
                    dst = y[:, :, n * C64:(n + 1) * C64]
                    for c in range(2):
                        half = slice(64 * c, 64 * c + 64)
                        done.mark(v.tensor_copy(dst[half], ys[half, c, :4 * C64].rearrange(
                            "p (j c) -> p j c", j=4)))
                    done.wait()
                    dve.wait_ge(yv_ready, n + 1)
                    v.tensor_tensor(dst, dst, yv[:, :4 * C64].rearrange("p (j c) -> p j c", j=4),
                                    ALU.add).then_inc(y_copied, 1)


def stage_gdn_out(nc, core, y):
    with ExitStack() as ctx:
        s = core.scope(nc, ctx, "gout")
        rstd, zt = s.sb("rstd", [P, 4, T]), s.sb("zt", [P, 4, T])
        loaded, bent, step = s.sem("loaded"), s.sem("bent"), s.sem("step")
        stage_rstd(nc, core, y, rstd, 1, core.halves, 64, EPS)
        with nc.Block() as block:
            @block.sync
            def _(sp):
                sp.dma_start(zt[:], rows(core.dram["z"][Z2["z"]:Z2["z"] + 512])).then_inc(loaded, 16)

            @block.scalar
            def _(act):
                act.wait_ge(loaded, 16)
                nc.scalar.activation(zt[:], zt[:], ACT.Silu).then_inc(bent, 1)

            @block.vector
            def _(dve):
                done = Steps(dve, step)
                done(nc.vector.scalar_tensor_tensor(out=y[:], in0=y[:], scalar=core.v("onorm_gdn"), in1=rstd[:],
                                                    op0=ALU.mult, op1=ALU.mult))
                dve.wait_ge(bent, 1)
                done(nc.vector.tensor_tensor(y[:], y[:], zt[:], ALU.mult))


def stage_rwkv_out(nc, core, y):
    with ExitStack() as ctx:
        s = core.scope(nc, ctx, "rout")
        rstd, bonus, g = (s.sb(n, [P, 4, T]) for n in ("rstd", "bonus", "g"))
        loaded, step = s.sem("loaded"), s.sem("step")
        stage_centre(nc, core, y, 1, core.halves, 64)
        stage_rstd(nc, core, y, rstd, 1, core.halves, 64, 64e-5)
        with nc.Block() as block:
            @block.sync
            def _(sp):
                sp.dma_start(bonus[:], feat(core, "bonus")).then_inc(loaded, 16)
                sp.dma_start(g[:], feat(core, "rg")).then_inc(loaded, 16)

            @block.vector
            def _(dve):
                done = Steps(dve, step)
                v = nc.vector
                for j in range(4):
                    done.mark(v.scalar_tensor_tensor(out=y[:, j], in0=y[:, j], scalar=core.v("lnx_w", j),
                                                     in1=rstd[:, j], op0=ALU.mult, op1=ALU.mult))
                done.wait()
                dve.wait_ge(loaded, 32)
                for j in range(4):
                    done.mark(v.scalar_tensor_tensor(out=y[:, j], in0=y[:, j], scalar=core.v("lnx_b", j),
                                                     in1=bonus[:, j], op0=ALU.add, op1=ALU.add))
                done.wait()
                done(v.tensor_tensor(y[:], y[:], g[:], ALU.mult))


def second_block(nc, core):
    dram = core.dram
    z, gates = dram["z"], dram["gates"]
    shift1, scale1, gate1, shift2, scale2, gate2 = (core.mod[:, 0, 8 * n:8 * n + 8] for n in range(6))
    with ExitStack() as ctx:
        s = core.scope(nc, ctx, "delta")
        h = split_tiles(s, "h", [P, DT, T])
        decay_t, beta = s.sb("decay_t", [HN, C64, C64]), s.sb("beta", [HN, C64])
        stage_norm(nc, core, core.x, "norm1_w_2", (scale1, shift1), parts=h)
        stage_rows(nc, core, [(dram["w_in_2a"], z[0:2048], ACT.Copy), (dram["w_in_2b"], z[2048:3584], ACT.Copy)],
                   h, tails=[(dram["w_in_2t0"], z[3584:3600]), (dram["w_in_2t1"], z[3600:3728]),
                             (dram["w_in_2t2"], z[3728:3856]), (dram["w_in_2t3"], z[3856:3888])])
        stage_gdn_gates(nc, core, decay_t, beta)
        stage_gdn_prepare(nc, core, decay_t, beta)
        stage_rwkv_prepare(nc, core)
        stage_rows(nc, core, [(dram["w_in_2g"], gates[0:2048], ACT.Sigmoid)], h,
                   beside=Inverse(nc, core, decay_t, beta))
    with ExitStack() as ctx:
        s = core.scope(nc, ctx, "second")
        merged, y = s.sb("merged", [P, DT, T]), s.sb("y", [P, 4, T])
        stage_gdn_scan(nc, core, y)
        stage_gdn_out(nc, core, y)
        stage_project(nc, core, dram["w_branch_gdn_2"], 4, merged, y, gates=gates[0:D], first=True)
        stage_rwkv_scan(nc, core, y)
        stage_rwkv_out(nc, core, y)
        stage_project(nc, core, dram["w_branch_rwkv_2"], 4, merged, y, gates=gates[D:2 * D])
        stage_project(nc, core, dram["w_out_2"], DT, core.x, merged, scale=gate1)
    stage_ffn(nc, core, "norm2_w_2", dram["ffn_up_2"], dram["ffn_down_2"], (scale2, shift2),
              conv=core.v("conv_ffn_2", 0, 3 * FT), scale=gate2)
    stage_norm(nc, core, core.x, "norm_f_w_2", dst=core.x)


Z3 = {"q": 0, "k": 512, "r": 1024, "z": 2048, "xbc": 4096, "lr": 7168, "dt": 7200}
ZC = {"k": 0, "xb": 512, "lr": 3072, "dt": 3104}
RANK = 16
GLA_LEVELS = 7
SSM_TILES = 16
SH = 32


def stage_log_gates(nc, core, lr, names, toks, chunk, b):
    with ExitStack() as ctx:
        s = core.scope(nc, ctx, "lgate")
        low = s.sb("low", [RANK, 2, toks])
        up = s.sb("up", [RANK, 2, 512])
        pre, e = s.sb("pre", [P, 4, toks]), s.sb("e", [P, 4, toks])
        reset = s.sb("reset", [P, 2, toks])
        acc = s.ps("acc", [P, 2, 4, 512])
        loaded, product, step, negated, logged, folded, acted = (
            s.sem(x) for x in ("loaded", "product", "step", "negated", "logged", "folded", "acted"))
        with nc.Block() as block:
            @block.sync
            def _(sp):
                for d in range(2):
                    sp.dma_start(low[:, d], lr[RANK * d:RANK * (d + 1)]).then_inc(loaded, 16)
                    sp.dma_start(up[:, d], core.dram[names[d]]).then_inc(loaded, 16)

            @block.tensor
            def _(pe):
                pe.wait_ge(loaded, 64)
                for d in range(2):
                    for j in range(4):
                        last = nc.tensor.matmul(acc[:, d, j, :toks], up[:, d, j * P:(j + 1) * P], low[:, d],
                                                start=True, stop=True)
                    last.then_inc(product, 1)

            @block.scalar
            def _(act):
                for d in range(2):
                    act.wait_ge(negated, d + 1)
                    nc.scalar.activation(e[:], e[:], ACT.Exp).then_inc(acted, 1)
                    act.wait_ge(acted, 2 * d + 1)
                    nc.scalar.activation(e[:], e[:], ACT.Ln, bias=1.0).then_inc(acted, 1)

            @block.vector
            def _(dve):
                done = Steps(dve, step)
                v = nc.vector
                edge = reset[:].rearrange("p d (n c) -> p d n c", c=chunk)
                done(v.memset(reset[:], 1.0))
                done.mark(v.memset(edge[:, 0, :, 0:1], 0.0))
                done(v.memset(edge[:, 1, :, chunk - 1:chunk], 0.0))
                for d in range(2):
                    dve.wait_ge(product, d + 1)
                    for j in range(4):
                        done.mark(v.tensor_scalar(pre[:, j], acc[:, d, j, :toks],
                                                  core.v(("gla_bias_f", "gla_bias_b")[d], j), None, ALU.add))
                    done.wait()
                    v.scalar_tensor_tensor(out=e[:], in0=pre[:], scalar=-1.0, in1=pre[:], op0=ALU.mult,
                                           op1=ALU.min).then_inc(negated, 1)
                    dve.wait_ge(acted, 2 * d + 2)
                    dve.wait_ge(negated, d + 1)
                    done(v.scalar_tensor_tensor(out=pre[:], in0=pre[:], scalar=0.0, in1=e[:], op0=ALU.min,
                                                op1=ALU.subtract))
                    done(v.tensor_scalar(pre[:], pre[:], 1.0 / 16, None, ALU.mult))
                    for j in range(4):
                        way = slice(None, None, -1) if d else slice(None)
                        done.mark(v.tensor_tensor_scan(b[:, d, j][:, way], reset[:, d][:, way], pre[:, j][:, way],
                                                       0.0, ALU.mult, ALU.add))
                    done.wait()


def stage_gla_context(nc, core, v_ctx, start):
    with ExitStack() as ctx:
        s = core.scope(nc, ctx, "gctx")
        b = s.sb("b", [P, 2, 4, CTX])
        stage_log_gates(nc, core, core.dram["zc"][ZC["lr"]:ZC["lr"] + 32], ("gla_up_f", "gla_up_b"), CTX, CTX, b)
        k = s.sb("k", [P, 4, CTX])
        k_tok = s.sb("k_tok", [P, 2, 2, 512])
        turned = s.ps("turned", [P, 2, 2, 512])
        acc = s.ps("acc", [P, 4, 512])
        loaded, diff, exped, weighted, turned_ready, copied, product, step, freed = (
            s.sem(x) for x in ("loaded", "diff", "exped", "weighted", "turned_ready", "copied", "product", "step",
                               "freed"))
        with nc.Block() as block:
            @block.sync
            def _(sp):
                sp.dma_start(k[:], rows(core.dram["zc"][ZC["k"]:ZC["k"] + 512])).then_inc(loaded, 16)

            @block.vector
            def _(dve):
                v = nc.vector
                for d in range(2):
                    at = 0 if d else CTX - 1
                    last = s.sb(f"last{d}", [P, 4, 1])
                    v.tensor_copy(last[:], b[:, d, :, at:at + 1]).then_inc(step, 1)
                    dve.wait_ge(step, d + 1)
                    v.tensor_tensor(b[:, d], last[:].broadcast_to([P, 4, CTX]), b[:, d],
                                    ALU.subtract).then_inc(diff, 1)
                dve.wait_ge(loaded, 16)
                for d in range(2):
                    dve.wait_ge(exped, d + 1)
                    v.tensor_tensor(b[:, d], b[:, d], k[:], ALU.mult).then_inc(weighted, 1)
                for d in range(2):
                    dve.wait_ge(turned_ready, d + 1)
                    v.tensor_copy(k_tok[:, d], turned[:, d]).then_inc(copied, 1)
                for n in range(8):
                    d, h = n // 4, n % 4
                    dve.wait_ge(product, n + 1)
                    v.tensor_copy(start[:, d, h], acc[:, n % 4, :256]).then_inc(freed, 1)

            @block.scalar
            def _(act):
                for d in range(2):
                    act.wait_ge(diff, d + 1)
                    nc.scalar.activation(b[:, d], b[:, d], ACT.Exp).then_inc(exped, 1)

            @block.tensor
            def _(pe):
                for d in range(2):
                    pe.wait_ge(weighted, d + 1)
                    for t in range(2):
                        for h in range(4):
                            last = nc.tensor.transpose(turned[:, d, t, h * P:(h + 1) * P],
                                                       b[:, d, h, t * P:(t + 1) * P], core.ident[:])
                    last.then_inc(turned_ready, 1)
                for n in range(8):
                    d, h = n // 4, n % 4
                    pe.wait_ge(copied, d + 1)
                    if n >= 4:
                        pe.wait_ge(freed, n - 3)
                    for t in range(2):
                        last = nc.tensor.matmul(acc[:, n % 4, :256], k_tok[:, d, t, h * P:(h + 1) * P],
                                                v_ctx[:, t, h * 256:(h + 1) * 256], start=t == 0, stop=t == 1)
                    last.then_inc(product, 1)


def stage_gla_levels(nc, core, q, k, b, attn):
    with ExitStack() as ctx:
        s = core.scope(nc, ctx, "levels")
        x = s.sb("x", [P, 2, 4, T])
        masks = s.sb("masks", [P, 2 * GLA_LEVELS + 1, P], I32)
        acc = s.ps("acc", [P, 2, 4, 512])
        loaded, diffed, exped, weighted, product, taken, cleared, doubled = (
            s.sem(n) for n in ("loaded", "diffed", "exped", "weighted", "product", "taken", "cleared", "doubled"))
        rounds = [(d, n) for d in range(2) for n in range(GLA_LEVELS)]

        def sides(n, tile):
            w = 2 << n
            both = tile.rearrange("p h (m w) -> p (h m) w", w=w)
            return both[:, :, :w // 2], both[:, :, w // 2:]

        with nc.Block() as block:
            @block.sync
            def _(sp):
                sp.dma_start(masks[:], core.dram["masks"]).then_inc(loaded, 16)

            @block.gpsimd
            def _(pool):
                for i, (d, n) in enumerate(rounds):
                    if i >= 2:
                        pool.wait_ge(product, i)
                    left, right = sides(n, x[:, i % 2])
                    bl, br = sides(n, b[:, d])
                    half = 1 << n
                    mid = br[:, :, 0:1] if d else bl[:, :, half - 1:half]
                    mid = mid.broadcast_to(list(bl.shape))
                    if d:
                        nc.gpsimd.tensor_tensor(left, bl, mid, ALU.subtract).then_inc(diffed, 1)
                        nc.gpsimd.tensor_tensor(right, mid, br, ALU.subtract).then_inc(diffed, 1)
                    else:
                        nc.gpsimd.tensor_tensor(left, mid, bl, ALU.subtract).then_inc(diffed, 1)
                        nc.gpsimd.tensor_tensor(right, br, mid, ALU.subtract).then_inc(diffed, 1)

            @block.scalar
            def _(act):
                for i in range(len(rounds)):
                    act.wait_ge(diffed, 2 * i + 2)
                    nc.scalar.activation(x[:, i % 2], x[:, i % 2], ACT.Exp).then_inc(exped, 1)

            @block.vector
            def _(dve):
                v = nc.vector

                def take(i):
                    for h in range(4):
                        dve.wait_ge(product, i + 1)
                        by = masks[:, i:i + 1].broadcast_to([P, 4, P])
                        src = acc[:, (i + 1) % 2, h].rearrange("p (c t) -> p c t", t=P)
                        if i == 0:
                            v.tensor_copy(attn[:, h], src).then_inc(cleared, 1)
                            dve.wait_ge(cleared, h + 1)
                            v.tensor_tensor(attn[:, h], attn[:, h], src, ALU.add).then_inc(taken, 1)
                        else:
                            v.copy_predicated(attn[:, h], by, src).then_inc(taken, 1)
                    dve.wait_ge(taken, 4 * i + 4)

                dve.wait_ge(loaded, 16)
                for i, (d, n) in enumerate(rounds):
                    dve.wait_ge(exped, i + 1)
                    left, right = sides(n, x[:, i % 2])
                    kl, kr = sides(n, k[:])
                    ql, qr = sides(n, q[:])
                    v.tensor_tensor(left, left, ql if d else kl, ALU.mult).then_inc(weighted, 1)
                    v.tensor_tensor(right, right, kr if d else qr, ALU.mult).then_inc(weighted, 1)
                    take(i)
                take(len(rounds))

            @block.tensor
            def _(pe):
                def products(i, lhs, rhs):
                    if i >= 2:
                        pe.wait_ge(taken, 4 * (i - 1))
                    for h in range(4):
                        for c in range(4):
                            at = slice(c * P, (c + 1) * P)
                            last = nc.tensor.matmul(acc[:, (i + 1) % 2, h, at], lhs[:, h, at], rhs[:, h, at],
                                                    start=True, stop=True)
                    last.then_inc(product, 1)

                products(0, k, q)
                for i in range(len(rounds)):
                    pe.wait_ge(weighted, 2 * i + 2)
                    products(i + 1, x[:, i % 2], x[:, i % 2])


def stage_gla_states(nc, core, q, k, b, v_tok, start, states):
    with ExitStack() as ctx:
        s = core.scope(nc, ctx, "gstate")
        kd = s.sb("kd", [P, 2, 4, T])
        edge = s.sb("edge", [P, 2, 4, 4])
        k_tok = s.sb("k_tok", [P, 2, 4, 512])
        turned = s.ps("turned", [P, 2, 512])
        acc = s.ps("acc", [P, 4, 512])
        (picked, diffed, exped, weighted, turned_ready, copied, product, advanced, scaled, step) = (
            s.sem(n) for n in ("picked", "diffed", "exped", "weighted", "turned_ready", "copied", "product",
                               "advanced", "scaled", "step"))
        with nc.Block() as block:
            @block.vector
            def _(dve):
                v = nc.vector
                for d in range(2):
                    at = 0 if d else P - 1
                    view = b[:, d].rearrange("p h (c t) -> p h c t", t=P)
                    v.tensor_copy(edge[:, d], view[:, :, :, at]).then_inc(picked, 1)
                    dve.wait_ge(picked, d + 1)
                    to = kd[:, d].rearrange("p h (c t) -> p h c t", t=P)
                    for h in range(4):
                        v.tensor_tensor(to[:, h], edge[:, d, h].unsqueeze(2).broadcast_to([P, 4, P]), view[:, h],
                                        ALU.subtract).then_inc(diffed, 1)
                for d in range(2):
                    dve.wait_ge(exped, 3 * d + 2)
                    v.tensor_tensor(kd[:, d], kd[:, d], k[:], ALU.mult).then_inc(weighted, 1)
                    dve.wait_ge(exped, 3 * d + 3)
                    v.tensor_tensor(b[:, d], b[:, d], q[:], ALU.mult).then_inc(scaled, 1)
                for n in range(8):
                    d, c = n // 4, n % 4
                    dve.wait_ge(turned_ready, n + 1)
                    v.tensor_copy(k_tok[:, d, c], turned[:, n % 2]).then_inc(copied, 1)
                v.tensor_copy(states[:, 0, :, 0], start[:, 0]).then_inc(step, 1)
                v.tensor_copy(states[:, 1, :, 3], start[:, 1]).then_inc(step, 1)
                dve.wait_ge(step, 2)
                for n in range(24):
                    i, d, h = n // 8, n // 4 % 2, n % 4
                    now, nxt = (3 - i, 2 - i) if d else (i, i + 1)
                    dve.wait_ge(product, n + 1)
                    if n >= 8:
                        dve.wait_ge(advanced, n - 7)
                    v.scalar_tensor_tensor(out=states[:, d, h, nxt], in0=states[:, d, h, now],
                                           scalar=edge[:, d, h, now:now + 1], in1=acc[:, n % 4, :256],
                                           op0=ALU.mult, op1=ALU.add).then_inc(advanced, 1)

            @block.scalar
            def _(act):
                for d in range(2):
                    act.wait_ge(diffed, 4 * d + 4)
                    nc.scalar.activation(edge[:, d], edge[:, d], ACT.Exp).then_inc(exped, 1)
                    nc.scalar.activation(kd[:, d], kd[:, d], ACT.Exp).then_inc(exped, 1)
                    nc.scalar.activation(b[:, d], b[:, d], ACT.Exp).then_inc(exped, 1)

            @block.tensor
            def _(pe):
                for n in range(8):
                    d, c = n // 4, n % 4
                    pe.wait_ge(weighted, d + 1)
                    if n >= 2:
                        pe.wait_ge(copied, n - 1)
                    for h in range(4):
                        last = nc.tensor.transpose(turned[:, n % 2, h * P:(h + 1) * P],
                                                   kd[:, d, h, c * P:(c + 1) * P], core.ident[:])
                    last.then_inc(turned_ready, 1)
                pe.wait_ge(copied, 8)
                for n in range(24):
                    i, d, h = n // 8, n // 4 % 2, n % 4
                    c = 3 - i if d else i
                    if n >= 4:
                        pe.wait_ge(advanced, n - 3)
                    nc.tensor.matmul(acc[:, n % 4, :256], k_tok[:, d, c, h * P:(h + 1) * P],
                                     v_tok[:, c, h * 256:(h + 1) * 256], start=True, stop=True
                                     ).then_inc(product, 1)


def stage_gla_out(nc, core, b, v_tok, states, attn, y):
    with ExitStack() as ctx:
        s = core.scope(nc, ctx, "glaout")
        with ExitStack() as inner:
            s1 = core.scope(nc, inner, "mix")
            acc = s1.ps("acc", [P, 8, 512])
            product, copied = s1.sem("product"), s1.sem("copied")
            with nc.Block() as block:
                @block.tensor
                def _(pe):
                    for n in range(8):
                        h, e = n // 2, n % 2
                        to = slice(h * 256 + e * P, h * 256 + (e + 1) * P)
                        for c in range(4):
                            at = slice(c * P, (c + 1) * P)
                            nc.tensor.matmul(acc[:, n, at], v_tok[:, c, to], attn[:, h, c], start=True, stop=False)
                            for d in range(2):
                                last = nc.tensor.matmul(acc[:, n, at], states[:, d, h, c, e * P:(e + 1) * P],
                                                        b[:, d, h, at], start=False, stop=d == 1)
                        last.then_inc(product, 1)

                @block.vector
                def _(dve):
                    for n in range(8):
                        dve.wait_ge(product, n + 1)
                        nc.vector.tensor_copy(y[:, n], acc[:, n]).then_inc(copied, 1)
        rstd = s.sb("rstd", [P, 4, T])
        stage_rstd(nc, core, y, rstd, 2, core.ones, 256, EPS)
        r = s.sb("r", [P, 8, T])
        loaded, step = s.sem("loaded"), s.sem("step")
        with nc.Block() as block:
            @block.sync
            def _(sp):
                sp.dma_start(r[:], rows(core.dram["z"][Z3["r"]:Z3["r"] + 1024])).then_inc(loaded, 16)

            @block.vector
            def _(dve):
                done = Steps(dve, step)
                for n in range(8):
                    done.mark(nc.vector.scalar_tensor_tensor(out=y[:, n], in0=y[:, n],
                                                             scalar=core.v("gla_norm_w", n % 2),
                                                             in1=rstd[:, n // 2], op0=ALU.mult, op1=ALU.mult))
                done.wait()
                dve.wait_ge(loaded, 16)
                done(nc.vector.tensor_tensor(y[:], y[:], r[:], ALU.mult))


def stage_load(nc, core, pairs):
    with ExitStack() as ctx:
        s = core.scope(nc, ctx, "load")
        loaded = s.sem("loaded")
        with nc.Block() as block:
            @block.sync
            def _(sp):
                for dst, src in pairs:
                    sp.dma_start(dst, src).then_inc(loaded, 16)
                sp.wait_ge(loaded, 16 * len(pairs))


def stage_gla(nc, core, v_tok, v_ctx, y):
    with ExitStack() as ctx:
        s = core.scope(nc, ctx, "gla")
        b = s.sb("b", [P, 2, 4, T])
        start = s.sb("start", [P, 2, 4, 256])
        states = s.sb("states", [P, 2, 4, 4, 256])
        attn = s.sb("attn", [P, 4, 4, P])
        stage_gla_context(nc, core, v_ctx, start)
        z = core.dram["z"]
        stage_log_gates(nc, core, z[Z3["lr"]:Z3["lr"] + 32], ("gla_up_f", "gla_up_b"), T, P, b)
        with ExitStack() as inner:
            s1 = core.scope(nc, inner, "qk")
            q, k = s1.sb("q", [P, 4, T]), s1.sb("k", [P, 4, T])
            scaled = s1.sem("scaled")
            stage_load(nc, core, [(q[:], rows(z[0:512])), (k[:], rows(z[512:1024]))])
            with nc.Block() as block:
                @block.vector
                def _(dve):
                    nc.vector.tensor_scalar(q[:], q[:], float(P) ** -0.5, None, ALU.mult).then_inc(scaled, 1)
            stage_gla_levels(nc, core, q, k, b, attn)
            stage_gla_states(nc, core, q, k, b, v_tok, start, states)
        stage_gla_out(nc, core, b, v_tok, states, attn, y)


def stage_centred_conv(nc, core, src, dst, tiles, toks, width):
    n = tiles // 4
    with ExitStack() as ctx:
        s = core.scope(nc, ctx, "cconv")
        raw, out = s.sb("raw", [P, 2, 4, toks]), s.sb("out", [P, 2, 4, toks])
        loaded, step, conved, bent = (s.sem(x) for x in ("loaded", "step", "conved", "bent"))
        stored = [s.sem(f"stored{i}") for i in range(2)]
        with nc.Block() as block:
            @block.sync
            def _(sp):
                for i in range(n):
                    if i >= 2:
                        sp.wait_ge(conved, 4 * (i - 1))
                    if i:
                        sp.wait_ge(loaded, 16 * i)
                    sp.dma_start(raw[:, i % 2], rows(src[512 * i:512 * (i + 1)])).then_inc(loaded, 16)

            @block.vector
            def _(dve):
                done = Steps(dve, step)
                for i in range(n):
                    dve.wait_ge(loaded, 16 * (i + 1))
                    if i >= 2:
                        dve.wait_ge(stored[i % 2], 16 * (i // 2))
                    for j in range(4):
                        done.mark(nc.vector.tensor_scalar(out[:, i % 2, j], raw[:, i % 2, j],
                                                          core.v("conv_w_3", 4 * (4 * i + j) + 2),
                                                          core.v("conv_b_3", 4 * i + j), ALU.mult, ALU.add))
                    done.wait()
                    for tap, lag in ((0, 2), (1, 1), (3, -1)):
                        for j in range(4):
                            a = raw[:, i % 2, j].rearrange("p (r w) -> p r w", w=width)
                            o = out[:, i % 2, j].rearrange("p (r w) -> p r w", w=width)
                            if lag > 0:
                                a, o = a[:, :, :width - lag], o[:, :, lag:]
                            else:
                                a, o = a[:, :, 1:], o[:, :, :width - 1]
                            ins = nc.vector.scalar_tensor_tensor(
                                out=o, in0=a, scalar=core.v("conv_w_3", 4 * (4 * i + j) + tap), in1=o,
                                op0=ALU.mult, op1=ALU.add)
                            if tap < 3:
                                done.mark(ins)
                            else:
                                ins.then_inc(conved, 1)
                        if tap < 3:
                            done.wait()

            @block.scalar
            def _(act):
                for i in range(n):
                    act.wait_ge(conved, 4 * (i + 1))
                    nc.scalar.activation(out[:, i % 2], out[:, i % 2], ACT.Silu).then_inc(bent, 1)
                    act.wait_ge(bent, i + 1)
                    act.dma_start(rows(dst[512 * i:512 * (i + 1)]), out[:, i % 2]).then_inc(stored[i % 2], 16)
                for i in range(min(n, 2)):
                    act.wait_ge(stored[i], 16 * ((n + 1 - i) // 2))


def stage_steps(nc, core, src, toks, chunk, dt_tok, cum_tok, cum_dram=None, edge_dram=None):
    n = toks // P
    with ExitStack() as ctx:
        s = core.scope(nc, ctx, "steps")
        dt, cum = s.sb("dt", [64, toks]), s.sb("cum", [64, toks])
        reset = s.sb("reset", [64, toks])
        rate = s.sb("rate", [64, 1])
        edges = s.sb("edges", [64, toks // chunk])
        acc = s.ps("acc", [P, 2, 512])
        rated, biased, step, summed, turned, copied, stored = (
            s.sem(x) for x in ("rated", "biased", "step", "summed", "turned", "copied", "stored"))
        stage_load(nc, core, [(dt[:], src)])
        with nc.Block() as block:
            @block.vector
            def _(dve):
                nc.vector.tensor_scalar(dt[:], dt[:], core.v("dt_bias_3")[:64], None, ALU.add).then_inc(biased, 1)
        stage_softplus(nc, core, dt, 64, toks)
        with nc.Block() as block:
            @block.scalar
            def _(act):
                nc.scalar.activation(rate[:], core.v("a_log_3")[:64], ACT.Exp).then_inc(rated, 1)

            @block.vector
            def _(dve):
                done = Steps(dve, step)
                v = nc.vector
                edge = reset[:].rearrange("p (n c) -> p n c", c=chunk)
                view = cum[:].rearrange("p (n c) -> p n c", c=chunk)
                done(v.memset(reset[:], 1.0))
                done.mark(v.memset(edge[:32, :, 0:1], 0.0))
                done.mark(v.memset(edge[32:64, :, chunk - 1:chunk], 0.0))
                dve.wait_ge(rated, 1)
                work = s.sb("work", [64, toks])
                done(v.tensor_scalar(work[:], dt[:], rate[:], -1.0, ALU.mult, ALU.mult))
                v.tensor_tensor_scan(cum[:32], reset[:32], work[:32], 0.0, ALU.mult, ALU.add).then_inc(summed, 1)
                v.tensor_tensor_scan(cum[32:64, ::-1], reset[32:64, ::-1], work[32:64, ::-1], 0.0, ALU.mult,
                                     ALU.add).then_inc(summed, 1)
                dve.wait_ge(summed, 2)
                v.tensor_copy(edges[:32], view[:32, :, chunk - 1]).then_inc(summed, 1)
                v.tensor_copy(edges[32:64], view[32:64, :, 0]).then_inc(summed, 1)
                dve.wait_ge(turned, 1)
                v.tensor_copy(dt_tok[:], acc[:, 0, :64 * n].rearrange("p (c h) -> p c h", h=64)
                              ).then_inc(copied, 1)
                v.tensor_copy(cum_tok[:], acc[:, 1, :64 * n].rearrange("p (c h) -> p c h", h=64)
                              ).then_inc(copied, 1)

            @block.tensor
            def _(pe):
                pe.wait_ge(summed, 2)
                for a, tile in enumerate((dt, cum)):
                    for c in range(n):
                        last = nc.tensor.transpose(acc[:, a, c * 64:(c + 1) * 64], tile[:, c * P:(c + 1) * P],
                                                   core.ident[:64, :64])
                last.then_inc(turned, 1)

            @block.sync
            def _(sp):
                sp.wait_ge(summed, 4)
                sp.dma_start(edge_dram, edges[:]).then_inc(stored, 16)
                if cum_dram is not None:
                    sp.dma_start(cum_dram, cum[:]).then_inc(stored, 16)
                sp.wait_ge(stored, 32 if cum_dram is not None else 16)


def spread(dram2, parts=P):
    shape = list(dram2.shape)
    return dram2.unsqueeze(0).broadcast_to([parts] + shape)


def stage_ssm_context(nc, core):
    dram = core.dram
    with ExitStack() as ctx:
        s = core.scope(nc, ctx, "sctx")
        dt_tok, cum_tok = s.sb("dt_tok", [P, 2, 64]), s.sb("cum_tok", [P, 2, 64])
        total = s.sb("total", [P, 64])
        stage_centred_conv(nc, core, dram["zc"][ZC["xb"]:ZC["xb"] + 2560], dram["xc"], 20, CTX, CTX)
        stage_steps(nc, core, dram["zc"][ZC["dt"]:ZC["dt"] + 64], CTX, CTX, dt_tok, cum_tok,
                    edge_dram=dram["edge_c"])
        w = s.sb("w", [P, 2, 64])
        x = s.sb("x", [P, 4, 5, CTX])
        x_tok = s.sb("x_tok", [P, 2, 2, 5 * P])
        xw = s.sb("xw", [P, 2, 2, 512])
        out = s.sb("out", [P, 2, 512])
        turned = s.ps("turned", [P, 2, 1024])
        acc = s.ps("acc", [P, 2, 512])
        (diffed, exped, ready, turned_ready, copied, weighted, product, saved) = (
            s.sem(n) for n in ("diffed", "exped", "ready", "turned_ready", "copied", "weighted", "product", "saved"))
        stored = s.sem("stored")
        stage_load(nc, core, [(total[:], spread(dram["edge_c"].rearrange("h a -> (h a)")))]
                   + [(x[:, g, :4], rows(dram["xc"][512 * g:512 * (g + 1)])) for g in range(4)]
                   + [(x[:, g, 4], dram["xc"][2048 + P * g:2048 + P * (g + 1)]) for g in range(4)])
        with nc.Block() as block:
            @block.vector
            def _(dve):
                v = nc.vector
                v.tensor_tensor(w[:], total[:].unsqueeze(1).broadcast_to([P, 2, 64]), cum_tok[:],
                                ALU.subtract).then_inc(diffed, 1)
                dve.wait_ge(exped, 1)
                v.tensor_tensor(w[:], w[:], dt_tok[:], ALU.mult).then_inc(ready, 1)
                dve.wait_ge(ready, 1)
                for g in range(4):
                    for t in range(2):
                        n = 2 * g + t
                        dve.wait_ge(turned_ready, n + 1)
                        v.tensor_copy(x_tok[:, g % 2, t], turned[:, t, :5 * P]).then_inc(copied, 1)
                    dve.wait_ge(copied, 2 * g + 2)
                    for d in range(2):
                        if g or d:
                            dve.wait_ge(product, 2 * g + d - 1 if 2 * g + d > 1 else 1)
                        for t in range(2):
                            by = w[:, t, 32 * d + 8 * g:32 * d + 8 * g + 8].unsqueeze(2).broadcast_to([P, 8, 64])
                            v.tensor_tensor(xw[:, d, t].rearrange("p (h c) -> p h c", c=64),
                                            x_tok[:, g % 2, t, :512].rearrange("p (h c) -> p h c", c=64), by,
                                            ALU.mult).then_inc(weighted, 1)

            @block.scalar
            def _(act):
                act.wait_ge(diffed, 1)
                nc.scalar.activation(w[:], w[:], ACT.Exp).then_inc(exped, 1)
                for n in range(8):
                    act.wait_ge(product, n + 1)
                    if n >= 2:
                        act.wait_ge(stored, 16 * (n - 1))
                    nc.scalar.activation(out[:, n % 2], acc[:, n % 2], ACT.Copy).then_inc(saved, 1)
                    act.wait_ge(saved, n + 1)
                    if n:
                        act.wait_ge(stored, 16 * n)
                    act.dma_start(dram["s0"][n % 2, n // 2], out[:, n % 2]).then_inc(stored, 16)
                act.wait_ge(stored, 128)

            @block.tensor
            def _(pe):
                for g in range(4):
                    for t in range(2):
                        if g:
                            pe.wait_ge(copied, 2 * g + t - 1)
                        for j in range(5):
                            last = nc.tensor.transpose(turned[:, t, j * P:(j + 1) * P],
                                                       x[:, g, j, t * P:(t + 1) * P], core.ident[:])
                        last.then_inc(turned_ready, 1)
                    for d in range(2):
                        n = 2 * g + d
                        pe.wait_ge(weighted, 2 * n + 2)
                        if n >= 2:
                            pe.wait_ge(saved, n - 1)
                        for t in range(2):
                            last = nc.tensor.matmul(acc[:, d], x_tok[:, g % 2, t, 512:], xw[:, d, t],
                                                    start=t == 0, stop=t == 1)
                        last.then_inc(product, 1)


def stage_ssm_group(nc, core, g, s, dt_tok, cum_tok, ecum, edges):
    dram = core.dram
    x, bc_ = s["x"], s["bc"]
    x_tok, b_tok = s["x_tok"], s["b_tok"]
    xdt, xw, states, cb, y_tok, y, dts = (s[n] for n in ("xdt", "xw", "states", "cb", "y_tok", "y", "dts"))
    with ExitStack() as ctx:
        o = core.scope(nc, ctx, "sprep")
        turned = o.ps("turned", [P, 2, 1024])
        gram = o.ps("gram", [P, 512])
        acc = o.ps("acc", [P, 2, 512])
        w = o.sb("w", [P, 2, 4, 8])
        heads = [slice(32 * d + 8 * g, 32 * d + 8 * g + 8) for d in range(2)]
        (loaded, turned_ready, copied, grammed, masked, diffed, exped, weighted, product, advanced, step,
         scaled) = (o.sem(n) for n in ("loaded", "turned_ready", "copied", "grammed", "masked", "diffed", "exped",
                                       "weighted", "product", "advanced", "step", "scaled"))
        with nc.Block() as block:
            @block.sync
            def _(sp):
                sp.dma_start(x[:], rows(dram["xbc"][512 * g:512 * (g + 1)])).then_inc(loaded, 16)
                sp.dma_start(bc_[:, 0], dram["xbc"][2048 + P * g:2048 + P * (g + 1)]).then_inc(loaded, 16)
                sp.dma_start(bc_[:, 1], dram["xbc"][2560 + P * g:2560 + P * (g + 1)]).then_inc(loaded, 16)
                sp.dma_start(states[:, 0, 0], dram["s0"][0, g]).then_inc(loaded, 16)
                sp.dma_start(states[:, 1, 3], dram["s0"][1, g]).then_inc(loaded, 16)

            @block.tensor
            def _(pe):
                pe.wait_ge(loaded, 80)
                for c in range(4):
                    at = slice(c * P, (c + 1) * P)
                    last = nc.tensor.matmul(gram[:, at], bc_[:, 0, at], bc_[:, 1, at], start=True, stop=True)
                last.then_inc(grammed, 1)
                for c in range(4):
                    at = slice(c * P, (c + 1) * P)
                    if c >= 2:
                        pe.wait_ge(copied, 2 * (c - 1))
                    for j in range(4):
                        nc.tensor.transpose(turned[:, c % 2, j * P:(j + 1) * P], x[:, j, at], core.ident[:])
                    nc.tensor.transpose(turned[:, c % 2, 512:640], bc_[:, 0, at],
                                        core.ident[:]).then_inc(turned_ready, 1)
                for n in range(6):
                    i, d = n // 2, n % 2
                    c = 3 - i if d else i
                    pe.wait_ge(weighted, 2)
                    if n >= 2:
                        pe.wait_ge(advanced, n - 1)
                    nc.tensor.matmul(acc[:, d], b_tok[:, c], xw[:, d, c], start=True, stop=True
                                     ).then_inc(product, 1)

            @block.scalar
            def _(act):
                for d in range(2):
                    act.wait_ge(diffed, d + 1)
                    nc.scalar.activation(w[:, d], w[:, d], ACT.Exp).then_inc(exped, 1)

            @block.gpsimd
            def _(pool):
                pool.wait_ge(masked, 2)
                for d in range(2):
                    nc.gpsimd.affine_select(out=cb[:, d], in_=cb[:, d],
                                            pattern=[[0, 4], [-1, P] if d else [1, P]], compare_op=ALU.is_ge,
                                            fill=0.0, base=0, channel_multiplier=1 if d else -1
                                            ).then_inc(step, 1)

            @block.vector
            def _(dve):
                v = nc.vector
                for d in range(2):
                    v.tensor_tensor(w[:, d], edges[:, heads[d], :].rearrange("p h c -> p c h"),
                                    cum_tok[:, :, heads[d]], ALU.subtract).then_inc(diffed, 1)
                dve.wait_ge(grammed, 1)
                for d in range(2):
                    v.tensor_copy(cb[:, d].rearrange("p c t -> p (c t)"), gram[:]).then_inc(masked, 1)
                for c in range(4):
                    dve.wait_ge(turned_ready, c + 1)
                    v.tensor_copy(x_tok[:, c], turned[:, c % 2, :512]).then_inc(copied, 1)
                    v.tensor_copy(b_tok[:, c], turned[:, c % 2, 512:640]).then_inc(copied, 1)
                dve.wait_ge(copied, 8)

                def by_head(dst, src, by):
                    return v.tensor_tensor(dst.rearrange("p c (h k) -> p (c h) k", k=64),
                                           src.rearrange("p c (h k) -> p (c h) k", k=64),
                                           by.unsqueeze(2).broadcast_to([P, 32, 64]), ALU.mult)

                for d in range(2):
                    small = dts[:, d]
                    v.tensor_copy(small, dt_tok[:, :, heads[d]]).then_inc(scaled, 1)
                    dve.wait_ge(scaled, 2 * d + 1)
                    by_head(xdt[:, d], x_tok[:], small.rearrange("p c h -> p (c h)")).then_inc(scaled, 1)
                    dve.wait_ge(exped, d + 1)
                    dve.wait_ge(scaled, 2 * d + 2)
                    by_head(xw[:, d], xdt[:, d], w[:, d].rearrange("p c h -> p (c h)")).then_inc(weighted, 1)
                for n in range(6):
                    i, d = n // 2, n % 2
                    now, nxt = (3 - i, 2 - i) if d else (i, i + 1)
                    dve.wait_ge(product, n + 1)
                    by = ecum[:, heads[d], now:now + 1].broadcast_to([P, 8, 64])
                    if n >= 2:
                        dve.wait_ge(advanced, n - 1)
                    v.tensor_tensor(states[:, d, nxt].rearrange("p (h k) -> p h k", k=64),
                                    states[:, d, now].rearrange("p (h k) -> p h k", k=64), by,
                                    ALU.mult).then_inc(scaled, 1)
                    dve.wait_ge(scaled, 4 + n + 1)
                    v.tensor_tensor(states[:, d, nxt], states[:, d, nxt], acc[:, d], ALU.add).then_inc(advanced, 1)

    with ExitStack() as ctx:
        o = core.scope(nc, ctx, "sout")
        cum = o.sb("cum", [P, 2, 2, 8, P])
        seg = o.sb("seg", [P, 2, 8, P])
        tmp = o.sb("tmp", [P, 2, 512])
        intra = o.ps("intra", [P, 2, 512])
        inter = o.ps("inter", [P, 2, 2, 512])
        turned = o.ps("turned", [P, 2, 512])
        etok = s["etok"]
        loaded = [o.sem(f"loaded{i}") for i in range(2)]
        (diffed, exped, masked, y_ready, inter_ready, read, made, turned_ready, copied, stored, tmp_ready,
         clipped) = (
            o.sem(n) for n in ("diffed", "exped", "masked", "y_ready", "inter_ready", "read", "made",
                               "turned_ready", "copied", "stored", "tmp_ready", "clipped"))
        def turn(pe, c):
            pe.wait_ge(read, 2 * c + 2)
            if c >= 2:
                pe.wait_ge(copied, c - 1)
            for j in range(4):
                last = nc.tensor.transpose(turned[:, c % 2, j * P:(j + 1) * P],
                                           y_tok[:, c % 2, j * P:(j + 1) * P], core.ident[:])
            last.then_inc(turned_ready, 1)

        with nc.Block() as block:
            @block.sync
            def _(sp):
                for c in range(4):
                    if c >= 2:
                        sp.wait_ge(diffed, 2 * (c - 1))
                    for d in range(2):
                        sp.dma_start(cum[:, c % 2, d],
                                     spread(dram["cum"][32 * d + 8 * g:32 * d + 8 * g + 8, c * P:(c + 1) * P])
                                     ).then_inc(loaded[c % 2], 16)
                sp.wait_ge(copied, 4)
                sp.dma_start(rows(dram["y_ssm"][512 * g:512 * (g + 1)]), y[:]).then_inc(stored, 16)
                sp.wait_ge(stored, 16)

            @block.gpsimd
            def _(pool):
                for n in range(8):
                    c, d = n // 2, n % 2
                    pool.wait_ge(loaded[c % 2], 32 * (c // 2 + 1))
                    if n >= 2:
                        pool.wait_ge(y_ready, n - 1)
                    by = cum_tok[:, c, 32 * d + 8 * g:32 * d + 8 * g + 8].unsqueeze(2).broadcast_to([P, 8, P])
                    nc.gpsimd.tensor_tensor(seg[:, n % 2], by, cum[:, c % 2, d], ALU.subtract).then_inc(diffed, 1)

            @block.scalar
            def _(act):
                for n in range(8):
                    act.wait_ge(diffed, n + 1)
                    nc.scalar.activation(seg[:, n % 2], seg[:, n % 2], ACT.Relu).then_inc(clipped, 1)
                    act.wait_ge(clipped, n + 1)
                    nc.scalar.activation(seg[:, n % 2], seg[:, n % 2], ACT.Exp, scale=-1.0).then_inc(exped, 1)
                    if n % 2:
                        c = n // 2
                        if c:
                            act.wait_ge(turned_ready, c)
                            nc.scalar.activation(y[:, :, (c - 1) * P:c * P],
                                                 turned[:, (c - 1) % 2].rearrange("p (j t) -> p j t", t=P),
                                                 ACT.Copy).then_inc(copied, 1)
                act.wait_ge(turned_ready, 4)
                nc.scalar.activation(y[:, :, 3 * P:], turned[:, 1].rearrange("p (j t) -> p j t", t=P),
                                     ACT.Copy).then_inc(copied, 1)

            @block.vector
            def _(dve):
                v = nc.vector

                def mask(n):
                    c, d = n // 2, n % 2
                    dve.wait_ge(exped, n + 1)
                    v.tensor_tensor(seg[:, n % 2], seg[:, n % 2], cb[:, d, c:c + 1].broadcast_to([P, 8, P]),
                                    ALU.mult).then_inc(masked, 1)

                def out(c):
                    dve.wait_ge(inter_ready, c + 1)
                    for d in range(2):
                        if c:
                            dve.wait_ge(read, 2 * c)
                        by = etok[:, c, 32 * d + 8 * g:32 * d + 8 * g + 8].unsqueeze(2).broadcast_to([P, 8, 64])
                        v.tensor_tensor(tmp[:, d].rearrange("p (h k) -> p h k", k=64),
                                        inter[:, c % 2, d].rearrange("p (h k) -> p h k", k=64), by,
                                        ALU.mult).then_inc(tmp_ready, 1)
                    dve.wait_ge(tmp_ready, 2 * c + 2)
                    v.tensor_tensor(tmp[:, 0], tmp[:, 0], tmp[:, 1], ALU.add).then_inc(read, 1)
                    dve.wait_ge(read, 2 * c + 1)
                    dve.wait_ge(y_ready, 2 * c + 2)
                    v.tensor_tensor(y_tok[:, c % 2], tmp[:, 0], intra[:, c % 2], ALU.add).then_inc(read, 1)

                for c in range(4):
                    mask(2 * c)
                    mask(2 * c + 1)
                    if c >= 2:
                        dve.wait_ge(turned_ready, c - 1)
                    out(c)

            @block.tensor
            def _(pe):
                for c in range(4):
                    if c >= 2:
                        pe.wait_ge(read, 2 * (c - 1))
                    at = slice(c * P, (c + 1) * P)
                    for d in range(2):
                        last = nc.tensor.matmul(inter[:, c % 2, d], bc_[:, 1, at], states[:, d, c], start=True,
                                                stop=True)
                    last.then_inc(inter_ready, 1)
                    for d in range(2):
                        n = 2 * c + d
                        pe.wait_ge(masked, n + 1)
                        for h in range(8):
                            last = nc.tensor.matmul(intra[:, c % 2, h * 64:(h + 1) * 64], seg[:, n % 2, h],
                                                    xdt[:, d, c, h * 64:(h + 1) * 64], start=d == 0 and h == 0,
                                                    stop=d == 1 and h == 7, skip_group_check=True)
                        last.then_inc(y_ready, 1)
                    if c:
                        turn(pe, c - 1)
                turn(pe, 3)


def stage_ssm(nc, core):
    dram = core.dram
    with ExitStack() as ctx:
        o = core.scope(nc, ctx, "ssm")
        stage_ssm_context(nc, core)
        stage_centred_conv(nc, core, dram["z"][Z3["xbc"]:Z3["xbc"] + 3072], dram["xbc"], 24, T, 64)
        dt_tok, cum_tok, etok = (o.sb(n, [P, 4, 64]) for n in ("dt_tok", "cum_tok", "etok"))
        edges, ecum = o.sb("edges", [P, 64, 4]), o.sb("ecum", [P, 64, 4])
        stage_steps(nc, core, dram["z"][Z3["dt"]:Z3["dt"] + 64], T, P, dt_tok, cum_tok, cum_dram=dram["cum"],
                    edge_dram=dram["edge"])
        stage_load(nc, core, [(edges[:], spread(dram["edge"]))])
        with nc.Block() as block:
            @block.scalar
            def _(act):
                nc.scalar.activation(etok[:], cum_tok[:], ACT.Exp)
                nc.scalar.activation(ecum[:], edges[:], ACT.Exp)
        shapes = {"x": [P, 4, T], "bc": [P, 2, T], "x_tok": [P, 4, 512], "b_tok": [P, 4, P],
                  "xdt": [P, 2, 4, 512], "xw": [P, 2, 4, 512], "states": [P, 2, 4, 512], "cb": [P, 2, 4, P],
                  "y_tok": [P, 2, 512], "y": [P, 4, T], "dts": [P, 2, 4, 8]}
        tiles = {n: o.sb(n, shape) for n, shape in shapes.items()}
        tiles["etok"] = etok
        for g in range(4):
            stage_ssm_group(nc, core, g, tiles, dt_tok, cum_tok, ecum, edges)


def stage_ssm_out(nc, core, y):
    dram = core.dram
    with ExitStack() as ctx:
        o = core.scope(nc, ctx, "ssmout")
        rstd = o.sb("rstd", [P, 4, T])
        with ExitStack() as inner:
            s = core.scope(nc, inner, "gate")
            x, z = s.sb("x", [P, 2, 4, T]), s.sb("z", [P, 2, 4, T])
            step = s.sem("step")
            loaded = [s.sem(f"loaded{i}") for i in range(2)]
            gated = s.sem("gated")
            with nc.Block() as block:
                @block.sync
                def _(sp):
                    for g in range(4):
                        if g >= 2:
                            sp.wait_ge(gated, g - 1)
                        at = slice(512 * g, 512 * (g + 1))
                        sp.dma_start(y[:, 4 * g:4 * g + 4], rows(dram["y_ssm"][at])).then_inc(loaded[g % 2], 16)
                        sp.dma_start(x[:, g % 2], rows(dram["xbc"][at])).then_inc(loaded[g % 2], 16)
                        sp.dma_start(z[:, g % 2], rows(dram["z"][Z3["z"] + 512 * g:Z3["z"] + 512 * (g + 1)])
                                     ).then_inc(loaded[g % 2], 16)

                @block.vector
                def _(dve):
                    done = Steps(dve, step)
                    for g in range(4):
                        dve.wait_ge(loaded[g % 2], 48 * (g // 2 + 1))
                        for j in range(4):
                            n = 4 * g + j
                            done.mark(nc.vector.scalar_tensor_tensor(out=y[:, n], in0=x[:, g % 2, j],
                                                                     scalar=core.v("d_skip", n), in1=y[:, n],
                                                                     op0=ALU.mult, op1=ALU.add))
                        done.wait()
                        nc.vector.tensor_tensor(y[:, 4 * g:4 * g + 4], y[:, 4 * g:4 * g + 4], z[:, g % 2],
                                                ALU.mult).then_inc(gated, 1)
        stage_rstd(nc, core, y, rstd, 4, core.ones, 512, EPS)
        step = o.sem("step")
        with nc.Block() as block:
            @block.vector
            def _(dve):
                for n in range(SSM_TILES):
                    nc.vector.scalar_tensor_tensor(out=y[:, n], in0=y[:, n], scalar=core.v("ssm_norm_w", n),
                                                   in1=rstd[:, n // 4], op0=ALU.mult,
                                                   op1=ALU.mult).then_inc(step, 1)


def third_block(nc, core):
    dram = core.dram
    z, zc, gates = dram["z"], dram["zc"], dram["gates"]
    mod, mod_ctx = core.mod[:, 1], core.mod[:, 2]
    shift1, scale1, gate1, shift2, scale2, gate2 = (mod[:, 8 * n:8 * n + 8] for n in range(6))
    with ExitStack() as ctx:
        merged = core.scope(nc, ctx, "third").sb("merged", [P, DT, T])
        with ExitStack() as inner:
            s1 = core.scope(nc, inner, "mixer")
            v_tok, v_ctx = s1.sb("v_tok", [P, 4, D]), s1.sb("v_ctx", [P, 2, D])
            with ExitStack() as deep:
                s2 = core.scope(nc, deep, "ctx")
                ctx_x, h = s2.sb("x", [P, DT, CTX]), split_tiles(s2, "h", [P, DT, CTX])
                stage_load(nc, core, [(ctx_x[:], rows(dram["ctxT"]))])
                stage_norm(nc, core, ctx_x, "norm1_w_3", (mod_ctx[:, 8:16], mod_ctx[:, 0:8]), toks=CTX, parts=h)
                stage_rows(nc, core, [(dram["w3_qk"][2:4], zc[0:512], ACT.Copy),
                                      (dram["w3_xbc"][0:10], zc[512:3072], ACT.Copy)], h,
                           tails=[(dram["w3_lr"], zc[3072:3104]), (dram["w3_dt"], zc[3104:3168])], toks=CTX)
                stage_tokens(nc, core, dram["w3_v"], h, v_ctx, toks=CTX)
            with ExitStack() as deep:
                h = split_tiles(core.scope(nc, deep, "third_h"), "h", [P, DT, T])
                stage_norm(nc, core, core.x, "norm1_w_3", (scale1, shift1), parts=h)
                stage_rows(nc, core,
                           [(dram["w3_qk"], z[0:1024], ACT.Copy), (dram["w3_xbc"], z[4096:7168], ACT.Copy),
                            (dram["w3_r"], z[1024:2048], ACT.Silu), (dram["w3_z"], z[2048:4096], ACT.Silu),
                            (dram["w3_g"], gates[0:2048], ACT.Sigmoid)], h,
                           tails=[(dram["w3_lr"], z[7168:7200]), (dram["w3_dt"], z[7200:7264])])
                stage_tokens(nc, core, dram["w3_v"], h, v_tok)
            y = s1.sb("y", [P, 8, T])
            stage_gla(nc, core, v_tok, v_ctx, y)
            stage_project(nc, core, dram["w_pa_3"], 8, merged, y, gates=gates[0:D], first=True)
        stage_ssm(nc, core)
        with ExitStack() as inner:
            y = core.scope(nc, inner, "ssmy").sb("y", [P, SSM_TILES, T])
            stage_ssm_out(nc, core, y)
            stage_project(nc, core, dram["w_pb_3"], SSM_TILES, merged, y, gates=gates[D:2 * D])
        stage_project(nc, core, dram["w_out_3"], DT, core.x, merged, scale=gate1)
    stage_ffn(nc, core, "norm2_w_3", dram["ffn_up_3"], dram["ffn_down_3"], (scale2, shift2), scale=gate2)
    stage_norm(nc, core, core.x, "final_norm_w_3", dst=core.x)



def stage_end(nc, core, out):
    with ExitStack() as ctx:
        s = core.scope(nc, ctx, "end")
        stored = s.sem("stored")
        with nc.Block() as block:
            @block.sync
            def _(sp):
                sp.dma_start(rows(out), core.x[:]).then_inc(stored, 16)
                sp.wait_ge(stored, 16)


def program(nc, dram, vec_at, vec_cols, out, blocks=(1, 2, 3)):
    with ExitStack() as ctx:
        core = Core(nc, ctx, dram, vec_at, vec_cols)
        stage_start(nc, core)
        if 1 in blocks:
            first_block(nc, core)
        if 2 in blocks:
            second_block(nc, core)
        if 3 in blocks:
            third_block(nc, core)
        stage_end(nc, core, out)




def tiled(w, cols):
    k, n = w.shape
    return np.ascontiguousarray(w.reshape(k // P, P, n // cols, cols).transpose(2, 1, 0, 3))


def up_pairs(gate, up):
    return np.ascontiguousarray(np.stack([tiled(gate, P), tiled(up, P)], axis=2))


def column(a):
    return a.reshape(-1, P).T


def taps(w):
    k, n = w.shape
    return w.reshape(k, n // P, P).transpose(2, 1, 0).reshape(P, -1)


def padded(a):
    out = np.zeros((P, a.shape[1]), a.dtype)
    out[:a.shape[0]] = a
    return out


def layout(i):
    a, v = {}, {}
    a["xT"] = np.ascontiguousarray(i["x"][0].T)
    w = i["w_in"][0]
    a["w_in_a"] = tiled(w[:, :4096], WCOLS)
    a["w_in_v"] = tiled(w[:, 4096:4608], WCOLS)
    a["w_in_g"] = tiled(w[:, 4608:], WCOLS)
    a["sc_out"] = tiled(i["sc_out"][0], P)
    a["conf_out"] = tiled(i["conf_out"][0], P)
    a["diff_out"] = tiled(i["diff_out"][0], P)
    a["w_o"] = tiled(i["w_o"][0], P)
    a["pool_w"] = np.ascontiguousarray(
        i["pool_w"][0].reshape(4, P, 2, P).transpose(0, 2, 1, 3).reshape(8, P, 1, P))
    a["ffn_up"] = up_pairs(i["ffn_up"][0][:, :D_FF], i["ffn_up"][0][:, D_FF:])
    a["ffn_down"] = tiled(i["ffn_down"][0], P)
    for n in ("mix_norm", "pool_scale", "conf_conv_b", "conf_ln_g", "conf_ln_b", "ffn_norm", "diff_subln"):
        v[n] = column(i[n][0])
    for n in ("sc_conv", "conf_conv", "ffn_conv"):
        v[n] = taps(i[n][0])
    for n in ("q_norm", "k_norm"):
        v[n] = np.concatenate([i[n][0], i[n][0]]).reshape(P, 1)
    v["lam_q"] = padded(np.stack([i["lambda_q1"][0], i["lambda_q2"][0]], axis=1))
    v["lam_k"] = padded(np.stack([i["lambda_k1"][0], i["lambda_k2"][0]], axis=1))
    a["w_ada_2"] = tiled(i["w_ada_2"][0], Ada.COLS)
    w = i["w_in_2"][0]
    a["w_in_2a"] = tiled(w[:, :2048], WCOLS)
    a["w_in_2b"] = tiled(w[:, 2064:3600], WCOLS)
    a["w_in_2g"] = tiled(w[:, 3888:], WCOLS)
    for n, (lo, hi) in enumerate(((2048, 2064), (3600, 3728), (3728, 3856), (3856, 3888))):
        a[f"w_in_2t{n}"] = tiled(w[:, lo:hi], hi - lo)[0]
    for n in ("w_branch_gdn_2", "w_branch_rwkv_2", "w_out_2"):
        a[n] = tiled(i[n][0], P)
    a["ffn_up_2"] = up_pairs(i["w_ffn_in_2"][0][:, :D_FF], i["w_ffn_in_2"][0][:, D_FF:])
    a["ffn_down_2"] = tiled(i["w_ffn_out_2"][0], P)
    for n in ("w2", "a2", "g2"):
        a[n] = np.ascontiguousarray(i[n + "_2"][0])
    v["c_2"] = column(i["c_2"][0])
    for n in ("b_ada_2", "norm1_w_2", "norm2_w_2"):
        v[n] = column(i[n][0])
    v["norm_f_w_2"] = column(i["norm_f_w_2"])
    v["conv_gdn"] = taps(i["conv_gdn_2"][0])
    v["conv_ffn_2"] = taps(i["conv_ffn_2"][0])
    v["onorm_gdn"] = np.concatenate([i["onorm_gdn_2"][0]] * 2).reshape(P, 1)
    heads = np.array([2 * j + q for _ in range(NC64) for q in range(2) for j in range(4)])
    v["a_log"] = padded(i["a_log_2"][0][heads].reshape(HN, 1))
    v["dt_bias"] = padded(i["dt_bias_2"][0][heads].reshape(HN, 1))
    mu = i["mu_rwkv_2"][0]
    v["mu_rkv"] = column(mu[:1536])
    v["mu_lo"] = np.concatenate([padded(mu[lo:hi].reshape(-1, 1)) for lo, hi in
                                 ((1536, 1600), (1600, 1664), (1664, 1792), (1792, 1824))], axis=1)
    for n in ("w0", "a0", "k_k", "k_a", "lnx_w", "lnx_b"):
        v[n] = column(i[n + "_2"][0])
    v["r_k"] = column(i["r_k_2"][0].reshape(-1))
    a["ctxT"] = np.ascontiguousarray(i["ctx_3"][0].T)
    a["w_ada_3"] = tiled(i["w_ada_3"][0], Ada.COLS)
    w = i["w_in_3"][0]
    for n, (lo, hi) in {"qk": (0, 1024), "r": (2048, 3072), "z": (3104, 5152), "xbc": (5152, 8224),
                        "g": (8288, 10336)}.items():
        a["w3_" + n] = tiled(w[:, lo:hi], WCOLS)
    a["w3_v"] = tiled(w[:, 1024:2048], WCOLS)
    a["w3_lr"] = tiled(w[:, 3072:3104], 32)[0]
    a["w3_dt"] = tiled(w[:, 8224:8288], 64)[0]
    for n in ("gla_up_f", "gla_up_b"):
        a[n] = np.ascontiguousarray(i[n + "_3"][0])
    for n in ("w_pa_3", "w_pb_3", "w_out_3"):
        a[n] = tiled(i[n][0], P)
    a["ffn_up_3"] = up_pairs(i["w_gate_3"][0], i["w_up_3"][0])
    a["ffn_down_3"] = tiled(i["w_down_3"][0], P)
    v["c_3"] = np.stack([column(i["c_3"][0]), column(i["c_ctx_3"])], axis=2).reshape(P, 16)
    for n in ("b_ada_3", "norm1_w_3", "norm2_w_3", "conv_b_3"):
        v[n] = column(i[n][0])
    v["final_norm_w_3"] = column(i["final_norm_w_3"])
    v["conv_w_3"] = taps(i["conv_w_3"][0])
    for n in ("gla_bias_f", "gla_bias_b", "gla_norm_w", "ssm_norm_w"):
        v[n] = column(i[n + "_3"][0])
    v["d_skip"] = column(np.repeat(i["d_skip_3"][0], 64))
    for n in ("dt_bias", "a_log"):
        v[n + "_3"] = padded(np.concatenate([i[n + "_f_3"][0], i[n + "_b_3"][0]]).reshape(64, 1))
    left = [np.array([[s // (2 << n) == t // (2 << n) and s // (1 << n) % 2 == 0 and t // (1 << n) % 2 == 1
                       for t in range(P)] for s in range(P)]) for n in range(GLA_LEVELS)]
    masks = [np.eye(P, dtype=bool)] + left + [m.T for m in left]
    a["masks"] = np.ascontiguousarray(np.stack(masks, axis=1).astype(np.int32))
    at, n = {}, 0
    for name, cols in v.items():
        at[name] = n
        n += cols.shape[1]
    a["vecs"] = np.ascontiguousarray(np.concatenate(list(v.values()), axis=1))
    return a, at


SCRATCH = {
    "z": (8192, T), "gates": (GATE_ROWS, T), "feat": (512 * len(F2), T), "hn": (3, HN, C64),
    "decay": (HN, C64, C64), "gram": (2 * HN, C64, C64), "inverse": (2 * HN, C64, C64),
    "zc": (3168, CTX), "xc": (2560, CTX), "xbc": (3072, T), "y_ssm": (2048, T), "cum": (64, T), "edge": (64, 4),
    "edge_c": (64, 1), "s0": (2, 4, P, 512),
}


def build(nc, arrays, at, blocks=(1, 2, 3)):
    dram = {n: nc.dram_tensor(f"in_{n}", a.shape, I32 if a.dtype == np.int32 else F32,
                              kind="ExternalInput").ap() for n, a in arrays.items()}
    for n, shape in SCRATCH.items():
        dram[n] = nc.dram_tensor(f"scratch_{n}", shape, F32).ap()
    out = nc.dram_tensor("out_T", (D, T), F32, kind="ExternalOutput").ap()
    program(nc, dram, at, arrays["vecs"].shape[1], out, blocks)


def kernel(**inputs):
    import concourse.bacc as _bacc
    from concourse.bass_utils import run_bass_kernel_spmd as _run

    arrays, at = layout({n: np.asarray(a) for n, a in inputs.items()})
    nc = _bacc.Bacc("TRN2", target_bir_lowering=False, num_devices=1)
    build(nc, arrays, at)
    r = _run(nc, [{f"in_{n}": a for n, a in arrays.items()}], core_ids=[0])
    return np.ascontiguousarray(r.results[0]["out_T"].T).reshape(1, T, D)
```

```python
import math
from contextlib import ExitStack

import numpy as np

import concourse.bass as bass
from concourse import mybir

F32 = mybir.dt.float32
F32R = mybir.dt.float32r
I32 = mybir.dt.int32
ALU = mybir.AluOpType
ACT = mybir.ActivationFunctionType
AX_X = mybir.AxisListType.X

P = 128
T = 512
D = 1024
DT = D // P
WCOLS = 256
EPS = 1e-6
D_FF = 2816
FT = D_FF // P
CTX = 256
C64 = 64
HN = 64
NC64 = T // C64
GATE_ROWS = 4096
CONF_TAPS = 31
LAM_INIT = 0.8 - 0.6 * math.exp(0.0)


class Steps:

    def __init__(self, eng, sem):
        self.eng, self.sem, self.n = eng, sem, 0

    def mark(self, ins):
        ins.then_inc(self.sem, 1)
        self.n += 1

    def wait(self):
        self.eng.wait_ge(self.sem, self.n)

    def __call__(self, ins):
        self.mark(ins)
        self.wait()


class Scope:

    def __init__(self, nc, ctx, name):
        self.nc, self.ctx, self.name = nc, ctx, name
        self.sems = []
        ctx.callback(self.close)

    def close(self):
        for sem in self.sems:
            self.nc.gpsimd.sem_clear(sem)
            self.nc.release_semaphore(sem)

    def sb(self, name, shape, dt=F32):
        return self.ctx.enter_context(self.nc.sbuf_tensor(f"{self.name}_{name}", shape, dt))

    def ps(self, name, shape):
        return self.ctx.enter_context(self.nc.psum_tensor(f"{self.name}_{name}", shape, F32))

    def sem(self, name):
        self.sems.append(self.nc.alloc_semaphore(f"{self.name}_{name}"))
        return self.sems[-1]


class Core:

    def __init__(self, nc, ctx, dram, vec_at, vec_cols):
        def sb(name, shape, dt=F32):
            return ctx.enter_context(nc.sbuf_tensor(name, shape, dt))

        self.dram, self.vec_at, self.count = dram, vec_at, 0
        self.vec = sb("vec", [P, vec_cols])
        self.ident = sb("ident", [P, P])
        self.ones = sb("ones", [P, P])
        self.halves = sb("halves", [P, P])
        self.pick = sb("pick", [P, 4, P])
        self.x = sb("x_res", [P, DT, T])
        self.mod = sb("mod", [P, 3, 48])

    def v(self, name, k=0, n=1):
        at = self.vec_at[name] + k
        return self.vec[:, at:at + n]

    def scope(self, nc, ctx, name):
        self.count += 1
        return Scope(nc, ctx, f"{name}{self.count}")


def rows(ap):
    return ap.rearrange("(j p) t -> p j t", p=P)




def stage_start(nc, core):
    with ExitStack() as ctx:
        s = core.scope(nc, ctx, "start")
        loaded, made = s.sem("loaded"), s.sem("made")
        with nc.Block() as block:
            @block.sync
            def _(sp):
                sp.dma_start(core.vec[:], core.dram["vecs"]).then_inc(loaded, 16)
                sp.dma_start(core.x[:], rows(core.dram["xT"])).then_inc(loaded, 16)
                sp.wait_ge(loaded, 32)

            @block.gpsimd
            def _(pool):
                done = Steps(pool, made)
                done(nc.gpsimd.memset(core.ones[:], 1.0))
                done(nc.gpsimd.memset(core.halves[:], 0.0))
                done(nc.gpsimd.memset(core.halves[0:64, 0:64], 1.0))
                done(nc.gpsimd.memset(core.halves[64:128, 64:128], 1.0))
                done(nc.gpsimd.memset(core.ident[:], 0.0))
                done(nc.gpsimd.affine_select(out=core.ident[:], in_=core.ident[:], pattern=[[-1, P]],
                                             compare_op=ALU.not_equal, fill=1.0, base=0, channel_multiplier=1))
                done(nc.gpsimd.tensor_copy(core.pick[:].rearrange("p q (s c) -> p (q s) c", s=2),
                                           core.ident[:, ::16].unsqueeze(2).broadcast_to([P, 8, 64])))


def stage_rstd(nc, core, src, dst, per, ones, count, eps, toks=T):
    n = src.shape[1]
    if n // per >= 4:
        return stage_group_rstd(nc, core, src, dst, per, ones, count, eps)
    with ExitStack() as ctx:
        s = core.scope(nc, ctx, "rstd")
        sq = s.sb("sq", [P, n, toks])
        acc = s.ps("acc", [P, 4, 512])
        squared, summed, freed, inverted, step = (s.sem(x) for x in
                                                  ("squared", "summed", "freed", "inverted", "step"))
        with nc.Block() as block:
            @block.scalar
            def _(act):
                for k in range(n):
                    nc.scalar.activation(sq[:, k], src[:, k], ACT.Square).then_inc(squared, 1)
                for g in range(n // per):
                    act.wait_ge(inverted, g + 1)
                    nc.scalar.activation(dst[:, g], dst[:, g], ACT.Sqrt).then_inc(step, 1)

            @block.tensor
            def _(pe):
                for g in range(n // per):
                    if g >= 4:
                        pe.wait_ge(freed, g - 3)
                    for k in range(per):
                        pe.wait_ge(squared, g * per + k + 1)
                        last = nc.tensor.matmul(acc[:, g % 4, :toks], ones[:], sq[:, g * per + k],
                                                start=k == 0, stop=k == per - 1)
                    last.then_inc(summed, 1)

            @block.vector
            def _(dve):
                for g in range(n // per):
                    dve.wait_ge(summed, g + 1)
                    nc.vector.tensor_scalar(dst[:, g], acc[:, g % 4, :toks], 1.0 / count, eps,
                                            ALU.mult, ALU.add).then_inc(freed, 1)
                    dve.wait_ge(freed, g + 1)
                    nc.vector.reciprocal(dst[:, g], dst[:, g]).then_inc(inverted, 1)


def stage_group_rstd(nc, core, src, dst, per, ones, count, eps):
    n = src.shape[1]
    groups, cut = n // per, T // 2
    with ExitStack() as ctx:
        s = core.scope(nc, ctx, "rstd")
        sq = s.sb("sq", [P, n, T])
        mean = s.sb("mean", [P, 2, T])
        banks = groups // 4
        acc = s.ps("acc", [P, banks, 512])
        wide = s.ps("wide", [P, 2, 512])
        squared, summed, scaled, inverted, rooted, spread, taken = (
            s.sem(x) for x in ("squared", "summed", "scaled", "inverted", "rooted", "spread", "taken"))
        steps = [(b, slice(half * cut, (half + 1) * cut)) for b in range(banks) for half in range(2)]
        with nc.Block() as block:
            @block.scalar
            def _(act):
                for k in range(n):
                    nc.scalar.activation(sq[:, k], src[:, k], ACT.Square).then_inc(squared, 1)
                for i, (b, at) in enumerate(steps):
                    act.wait_ge(inverted, i + 1)
                    nc.scalar.activation(mean[:, b, at], mean[:, b, at], ACT.Sqrt).then_inc(rooted, 1)

            @block.tensor
            def _(pe):
                for g in range(groups):
                    for k in range(per):
                        pe.wait_ge(squared, g * per + k + 1)
                        last = nc.tensor.matmul(acc[32 * (g % 4):32 * (g % 4) + 32, g // 4], ones[:, 48:80],
                                                sq[:, g * per + k], start=k == 0, stop=k == per - 1)
                    last.then_inc(summed, 1)
                for i, (b, at) in enumerate(steps):
                    pe.wait_ge(rooted, i + 1)
                    for q in range(4):
                        if 4 * i + q >= 2:
                            pe.wait_ge(taken, 4 * i + q - 1)
                        nc.tensor.matmul(wide[:, q % 2, :cut], core.pick[:, q], mean[:, b, at], start=True,
                                         stop=True).then_inc(spread, 1)

            @block.vector
            def _(dve):
                def take(i):
                    b, at = steps[i]
                    for q in range(4):
                        dve.wait_ge(spread, 4 * i + q + 1)
                        nc.vector.tensor_copy(dst[:, 4 * b + q, at], wide[:, q % 2, :cut]).then_inc(taken, 1)

                for i, (b, at) in enumerate(steps):
                    dve.wait_ge(summed, 4 * b + 4)
                    nc.vector.tensor_scalar(mean[:, b, at], acc[:, b, at], 1.0 / count, eps, ALU.mult,
                                            ALU.add).then_inc(scaled, 1)
                    dve.wait_ge(scaled, i + 1)
                    nc.vector.reciprocal(mean[:, b, at], mean[:, b, at]).then_inc(inverted, 1)
                    if i:
                        take(i - 1)
                take(len(steps) - 1)


def stage_centre(nc, core, src, per, ones, count):
    n = src.shape[1]
    with ExitStack() as ctx:
        s = core.scope(nc, ctx, "centre")
        mean = s.sb("mean", [P, 4, T])
        acc = s.ps("acc", [P, 4, 512])
        summed, freed, done = s.sem("summed"), s.sem("freed"), s.sem("done")
        with nc.Block() as block:
            @block.tensor
            def _(pe):
                for g in range(n // per):
                    if g >= 4:
                        pe.wait_ge(freed, g - 3)
                    for k in range(per):
                        last = nc.tensor.matmul(acc[:, g % 4, :], ones[:], src[:, g * per + k],
                                                start=k == 0, stop=k == per - 1)
                    last.then_inc(summed, 1)

            @block.vector
            def _(dve):
                for g in range(n // per):
                    dve.wait_ge(summed, g + 1)
                    nc.vector.tensor_scalar(mean[:, g % 4], acc[:, g % 4, :], 1.0 / count, None,
                                            ALU.mult).then_inc(freed, 1)
                    dve.wait_ge(freed, g + 1)
                    for k in range(per):
                        nc.vector.tensor_tensor(src[:, g * per + k], src[:, g * per + k], mean[:, g % 4],
                                                ALU.subtract).then_inc(done, 1)


def split_tiles(s, name, shape):
    return s.sb(f"{name}_hi", shape, F32R), s.sb(f"{name}_lo", shape, F32R)


def split_hi(nc, hi, src):
    return nc.scalar.activation(hi, src, ACT.Copy)


def split_lo(eng, lo, src, hi):
    return eng.tensor_tensor(lo, src, hi.bitcast(F32), ALU.subtract)


def product(nc, out, w, x, start, stop):
    (w_hi, w_lo), (x_hi, x_lo) = w, x
    nc.tensor.matmul(out, w_hi, x_hi, start=start, stop=False)
    nc.tensor.matmul(out, w_hi, x_lo, start=False, stop=False)
    return nc.tensor.matmul(out, w_lo, x_hi, start=False, stop=stop)


def span(eng, n, body):
    if n > 0:
        body(0)
    if n == 2:
        body(1)
    if n > 2:
        with eng.Fori(1, n) as i:
            body(i)


def free_after(eng, sem, count):
    if not (isinstance(count, int) and count == 0):
        eng.wait_ge(sem, count)


class Beside:

    def open(self, s):
        pass

    def sync_turn(self, sp, n, i, k):
        pass

    def tensor_turn(self, pe, n, i, k):
        pass

    def scalar_turn(self, act, n, i, k):
        pass

    def scalar_last(self, act):
        pass

    def vector_segment(self, dve, n, turns):
        pass

    def close(self):
        pass


def stage_norm(nc, core, src, gain, mod=None, toks=T, dst=None, parts=None, start=()):
    with ExitStack() as ctx:
        s = core.scope(nc, ctx, "norm")
        rstd = s.sb("rstd", [P, 1, toks])
        stage_rstd(nc, core, src, rstd, DT, core.ones, D, EPS, toks)
        full = s.sb("full", [P, DT])
        buf = s.sb("buf", [P, DT, toks]) if dst is None else dst
        ready, scaled, shifted, cut, lesser = (s.sem(n) for n in
                                               ("ready", "scaled", "shifted", "cut", "lesser"))
        with nc.Block() as block:
            @block.sync
            def _(sp):
                for to, at, sem in start:
                    sp.dma_start(to, at).then_inc(sem, 16)

            @block.vector
            def _(dve):
                g = core.v(gain, 0, DT)
                if mod is not None:
                    nc.vector.scalar_tensor_tensor(out=full[:], in0=mod[0], scalar=1.0, in1=g,
                                                   op0=ALU.add, op1=ALU.mult).then_inc(ready, 1)
                    dve.wait_ge(ready, 1)
                    g = full[:]
                for k in range(DT):
                    nc.vector.scalar_tensor_tensor(out=buf[:, k], in0=src[:, k], scalar=g[:, k:k + 1],
                                                   in1=rstd[:, 0], op0=ALU.mult,
                                                   op1=ALU.mult).then_inc(scaled, 1)
                    if mod is not None:
                        dve.wait_ge(scaled, k + 1)
                        nc.vector.tensor_scalar(buf[:, k], buf[:, k], mod[1][:, k:k + 1], None,
                                                ALU.add).then_inc(shifted, 1)

            if parts is not None:
                @block.scalar
                def _(act):
                    for k in range(DT):
                        act.wait_ge(scaled if mod is None else shifted, k + 1)
                        split_hi(nc, parts[0][:, k], buf[:, k]).then_inc(cut, 1)

                @block.gpsimd
                def _(pool):
                    for k in range(DT):
                        pool.wait_ge(cut, k + 1)
                        split_lo(nc.gpsimd, parts[1][:, k], buf[:, k], parts[0][:, k]).then_inc(lesser, 1)


def stage_rows(nc, core, segments, rhs, tails=(), beside=Beside()):
    with ExitStack() as ctx:
        s = core.scope(nc, ctx, "rows")
        raw = s.sb("raw", [P, 2, DT, WCOLS])
        w_hi, w_lo = split_tiles(s, "w", [P, 2, DT, WCOLS])
        out = s.sb("out", [P, 2, 2, T])
        acc = s.ps("acc", [P, 4, 512])
        halves = [slice(h * DT // 2, (h + 1) * DT // 2) for h in range(2)]
        loaded = [[s.sem(f"loaded{k}{h}") for h in range(2)] for k in range(2)]
        names = ["cut_hi", "cut_lo", "made", "copied", "stored"]
        cut_hi, cut_lo, made, copied, stored = ([s.sem(f"{n}{k}") for k in range(2)] for n in names)
        segments = [tuple(seg) + (rhs,) * (len(seg) == 3) for seg in segments]
        turns = [seg[0].shape[0] // 2 for seg in segments]
        base = [sum(turns[:n]) for n in range(len(turns))]
        total = sum(turns)
        beside.open(s)

        def leading(act, k, i):
            free_after(act, made[k], i * 2)
            for h, at in enumerate(halves):
                act.wait_ge(loaded[k][h], i * 16 + 16)
                split_hi(nc, w_hi[:, k, at], raw[:, k, at]).then_inc(cut_hi[k], 1)

        def products(pe, to, k, j, x, count):
            at = slice(j * P, (j + 1) * P)
            for c in range(DT):
                if j == 0 and c % (DT // 2) == 0:
                    pe.wait_ge(cut_lo[k], count * 2 + (c // (DT // 2) + 1))
                last = product(nc, to, (w_hi[:, k, c, at], w_lo[:, k, c, at]), (x[0][:, c], x[1][:, c]),
                               c == 0, c == DT - 1)
            return last

        with nc.Block() as block:
            @block.sync
            def _(sp):
                for n, (wt, *_) in enumerate(segments):
                    def turn(i):
                        for k in range(2):
                            beside.sync_turn(sp, n, i, k)
                            free_after(sp, cut_hi[k], (i + base[n]) * 2)
                            free_after(sp, cut_lo[k], (i + base[n]) * 2)
                            for h, at in enumerate(halves):
                                sp.dma_start(raw[:, k, at], wt[bass.ds(i * 2 + k, 1), :, at].rearrange(
                                    "a p k n -> p (a k) n")).then_inc(loaded[k][h], 16)
                    span(sp, turns[n], turn)

            @block.gpsimd
            def _(pool):
                def turn(i):
                    for k in range(2):
                        for h, at in enumerate(halves):
                            pool.wait_ge(cut_hi[k], i * 2 + (h + 1))
                            split_lo(nc.gpsimd, w_lo[:, k, at], raw[:, k, at], w_hi[:, k, at]
                                     ).then_inc(cut_lo[k], 1)
                span(pool, total, turn)

            @block.tensor
            def _(pe):
                for n, (_, _, _, x) in enumerate(segments):
                    def turn(i):
                        for k in range(2):
                            free_after(pe, copied[k], (i + base[n]) * 2)
                            for j in range(2):
                                products(pe, acc[:, 2 * k + j, :x[0].shape[-1]], k, j, x, i + base[n]
                                         ).then_inc(made[k], 1)
                            beside.tensor_turn(pe, n, i, k)
                    span(pe, turns[n], turn)

            @block.scalar
            def _(act):
                leading(act, 0, 0)
                for n, (_, dst, func, x) in enumerate(segments):
                    toks = x[0].shape[-1]

                    def turn(i, last=False):
                        for k in range(2):
                            if not (last and k == 1):
                                leading(act, 1 - k, i + base[n] + k)
                            at = bass.ds(i * 2 * WCOLS + k * WCOLS, WCOLS)
                            free_after(act, stored[k], (i + base[n]) * 16)
                            for j in range(2):
                                act.wait_ge(made[k], (i + base[n]) * 2 + j + 1)
                                nc.scalar.activation(out[:, k, j, :toks], acc[:, 2 * k + j, :toks],
                                                     func).then_inc(copied[k], 1)
                            act.wait_ge(copied[k], (i + base[n]) * 2 + 2)
                            act.dma_start(rows(dst[at, :]), out[:, k, :, :toks]).then_inc(stored[k], 16)
                            beside.scalar_turn(act, n, i, k)
                    if n < len(segments) - 1:
                        span(act, turns[n], turn)
                    else:
                        span(act, turns[n] - 1, turn)
                        turn(turns[n] - 1, last=True)
                for k in range(2):
                    act.wait_ge(stored[k], 16 * total)
                beside.scalar_last(act)

            @block.vector
            def _(dve):
                for n in range(len(segments)):
                    beside.vector_segment(dve, n, turns[n])
        beside.close()
    if tails:
        tail_rows(nc, core, tails)


def tail_rows(nc, core, tails):
    with ExitStack() as ctx:
        s = core.scope(nc, ctx, "tails")
        n = len(tails)
        raw = s.sb("raw", [P, n, DT, P])
        w_hi, w_lo = split_tiles(s, "w", [P, n, DT, P])
        out = s.sb("out", [P, n, T])
        acc = s.ps("acc", [P, n, 512])
        loaded, cut_hi, cut_lo, made, copied, stored = (
            s.sem(x) for x in ("loaded", "cut_hi", "cut_lo", "made", "copied", "stored"))
        wide = [wt.shape[2] for wt, _, _ in tails]
        toks = [rhs[0].shape[-1] for _, _, rhs in tails]
        with nc.Block() as block:
            @block.sync
            def _(sp):
                for m, (wt, _, _) in enumerate(tails):
                    sp.dma_start(raw[:, m, :, :wide[m]], wt).then_inc(loaded, 16)
                for m, (_, dst, _) in enumerate(tails):
                    sp.wait_ge(copied, m + 1)
                    sp.dma_start(dst, out[:wide[m], m, :toks[m]]).then_inc(stored, 16)
                sp.wait_ge(stored, 16 * n)

            @block.scalar
            def _(act):
                act.wait_ge(loaded, 16 * n)
                for m in range(n):
                    split_hi(nc, w_hi[:, m, :, :wide[m]], raw[:, m, :, :wide[m]]).then_inc(cut_hi, 1)
                for m in range(n):
                    act.wait_ge(made, m + 1)
                    nc.scalar.activation(out[:wide[m], m, :toks[m]], acc[:wide[m], m, :toks[m]],
                                         ACT.Copy).then_inc(copied, 1)

            @block.vector
            def _(dve):
                for m in range(n):
                    dve.wait_ge(cut_hi, m + 1)
                    split_lo(nc.vector, w_lo[:, m, :, :wide[m]], raw[:, m, :, :wide[m]],
                             w_hi[:, m, :, :wide[m]]).then_inc(cut_lo, 1)

            @block.tensor
            def _(pe):
                for m, (_, _, rhs) in enumerate(tails):
                    pe.wait_ge(cut_hi, m + 1)
                    pe.wait_ge(cut_lo, m + 1)
                    for c in range(DT):
                        last = product(nc, acc[:wide[m], m, :toks[m]],
                                       (w_hi[:, m, c, :wide[m]], w_lo[:, m, c, :wide[m]]),
                                       (rhs[0][:, c], rhs[1][:, c]), c == 0, c == DT - 1)
                    last.then_inc(made, 1)


def stage_tokens(nc, core, wt, pairs, start=()):
    chunks = wt.shape[0]
    tiles = [(rhs, dst, t) for rhs, dst in pairs for t in range(rhs[0].shape[-1] // P)]
    per = len(tiles)
    with ExitStack() as ctx:
        s = core.scope(nc, ctx, "tokens")
        raw = s.sb("raw", [P, 2, DT, WCOLS])
        w_hi, w_lo = split_tiles(s, "w", [P, 2, DT, WCOLS])
        acc = s.ps("acc", [P, 4, 512])
        halves = [slice(h * DT // 2, (h + 1) * DT // 2) for h in range(2)]
        cut_hi, cut_lo, made, copied = (s.sem(x) for x in ("cut_hi", "cut_lo", "made", "copied"))
        loaded = [[s.sem(f"loaded{n}{h}") for h in range(2)] for n in range(2)]
        with nc.Block() as block:
            @block.sync
            def _(sp):
                for c in range(chunks):
                    if c >= 2:
                        sp.wait_ge(cut_lo, 2 * (c - 1))
                    for h, at in enumerate(halves):
                        sp.dma_start(raw[:, c % 2, at], wt[c][:, at]).then_inc(loaded[c % 2][h], 16)
                for to, at, sem in start:
                    sp.dma_start(to, at).then_inc(sem, 16)

            @block.scalar
            def _(act):
                for c in range(chunks):
                    if c >= 2:
                        act.wait_ge(made, per * (c - 1))
                    for h, at in enumerate(halves):
                        act.wait_ge(loaded[c % 2][h], 16 * (c // 2 + 1))
                        split_hi(nc, w_hi[:, c % 2, at], raw[:, c % 2, at]).then_inc(cut_hi, 1)

            @block.gpsimd
            def _(pool):
                for c in range(chunks):
                    for h, at in enumerate(halves):
                        pool.wait_ge(cut_hi, 2 * c + h + 1)
                        split_lo(nc.gpsimd, w_lo[:, c % 2, at], raw[:, c % 2, at], w_hi[:, c % 2, at]
                                 ).then_inc(cut_lo, 1)

            @block.tensor
            def _(pe):
                for n in range(chunks * per):
                    c, (rhs, _, t) = n // per, tiles[n % per]
                    if n >= 4:
                        pe.wait_ge(copied, n - 3)
                    at = slice(t * P, (t + 1) * P)
                    for k in range(DT):
                        if k % (DT // 2) == 0:
                            pe.wait_ge(cut_lo, 2 * c + 2 * k // DT + 1)
                        last = product(nc, acc[:, n % 4, :WCOLS], (rhs[0][:, k, at], rhs[1][:, k, at]),
                                       (w_hi[:, c % 2, k], w_lo[:, c % 2, k]), k == 0, k == DT - 1)
                    last.then_inc(made, 1)

            @block.vector
            def _(dve):
                for n in range(chunks * per):
                    c, (_, dst, t) = n // per, tiles[n % per]
                    dve.wait_ge(made, n + 1)
                    nc.vector.tensor_copy(dst[:, t, c * WCOLS:(c + 1) * WCOLS], acc[:, n % 4, :WCOLS]
                                          ).then_inc(copied, 1)


def stage_project(nc, core, wt, kt, dst, y=None, parts=None, gates=None, first=False, scale=None,
                  groups=False):
    with ExitStack() as ctx:
        s = core.scope(nc, ctx, "project")
        n_in = 4 if groups else kt
        deep = 4 if kt <= DT else 2
        raw = s.sb("raw", [P, deep, kt, P])
        w_hi, w_lo = split_tiles(s, "w", [P, 2, kt, P])
        y_hi, y_lo = parts if y is None else split_tiles(s, "y", [P, n_in, T])
        gate = s.sb("gate", [P, 2, T]) if gates is not None else None
        part = s.sb("part", [P, 2, T]) if gates is not None else None
        acc = s.ps("acc", [P, 2, 512])
        y_hi_ready, y_lo_ready, cut_hi, cut_lo, made, freed, step = (
            s.sem(x) for x in ("y_hi_ready", "y_lo_ready", "cut_hi", "cut_lo", "made", "freed", "step"))
        pieces = 2 if kt > 1 else 1
        cuts = [slice(p * kt // pieces, (p + 1) * kt // pieces) for p in range(pieces)]
        loaded = [[s.sem(f"loaded{n}{p}") for p in range(pieces)] for n in range(deep)]
        gate_loaded = [s.sem(f"gate_loaded{n}") for n in range(2)]
        with nc.Block() as block:
            @block.sync
            def _(sp):
                for m in range(DT):
                    if m >= deep:
                        sp.wait_ge(cut_lo, pieces * (m - deep + 1))
                    for p, at in enumerate(cuts):
                        sp.dma_start(raw[:, m % deep, at], wt[m][:, at]).then_inc(loaded[m % deep][p], 16)
                    if gates is not None:
                        if m >= 2:
                            sp.wait_ge(freed, m - 1)
                        sp.dma_start(gate[:, m % 2], gates[m * P:(m + 1) * P]).then_inc(gate_loaded[m % 2], 16)

            @block.scalar
            def _(act):
                for m in range(DT):
                    if m >= 2:
                        act.wait_ge(made, m - 1)
                    for p, at in enumerate(cuts):
                        act.wait_ge(loaded[m % deep][p], 16 * (m // deep + 1))
                        split_hi(nc, w_hi[:, m % 2, at], raw[:, m % deep, at]).then_inc(cut_hi, 1)

            @block.gpsimd
            def _(pool):
                for m in range(DT):
                    for p, at in enumerate(cuts):
                        pool.wait_ge(cut_hi, pieces * m + p + 1)
                        split_lo(nc.gpsimd, w_lo[:, m % 2, at], raw[:, m % deep, at], w_hi[:, m % 2, at]
                                 ).then_inc(cut_lo, 1)

            @block.tensor
            def _(pe):
                for m in range(DT):
                    if m >= 2:
                        pe.wait_ge(freed, m - 1)
                    for k in range(kt):
                        for p, at in enumerate(cuts):
                            if k == at.start:
                                pe.wait_ge(cut_lo, pieces * m + p + 1)
                        x = m // 2 if groups else k
                        if y is not None and (m == 0 or groups):
                            pe.wait_ge(y_lo_ready, x + 1)
                        last = product(nc, acc[:, m % 2], (w_hi[:, m % 2, k], w_lo[:, m % 2, k]),
                                       (y_hi[:, x], y_lo[:, x]), k == 0, k == kt - 1)
                    last.then_inc(made, 1)

            @block.vector
            def _(dve):
                if y is not None:
                    for k in range(n_in):
                        nc.vector.tensor_copy(y_hi[:, k], y[:, k]).then_inc(y_hi_ready, 1)
                        dve.wait_ge(y_hi_ready, k + 1)
                        split_lo(nc.vector, y_lo[:, k], y[:, k], y_hi[:, k]).then_inc(y_lo_ready, 1)
                for m in range(DT):
                    by = 1.0 if scale is None else scale[:, m:m + 1]
                    dve.wait_ge(made, m + 1)
                    if gates is None:
                        nc.vector.scalar_tensor_tensor(out=dst[:, m], in0=acc[:, m % 2], scalar=by, in1=dst[:, m],
                                                       op0=ALU.mult, op1=ALU.add).then_inc(freed, 1)
                        continue
                    dve.wait_ge(gate_loaded[m % 2], 16 * (m // 2 + 1))
                    if not first and m >= 2:
                        dve.wait_ge(step, m - 1)
                    to = dst[:, m] if first else part[:, m % 2]
                    nc.vector.scalar_tensor_tensor(out=to, in0=acc[:, m % 2], scalar=by, in1=gate[:, m % 2],
                                                   op0=ALU.mult, op1=ALU.mult).then_inc(freed, 1)
                    if not first:
                        dve.wait_ge(freed, m + 1)
                        nc.vector.tensor_tensor(dst[:, m], dst[:, m], part[:, m % 2], ALU.add).then_inc(step, 1)


def stage_ffn(nc, core, gain, up, down, mod=None, conv=None, conv_up=False, scale=None):
    with ExitStack() as ctx:
        s0 = core.scope(nc, ctx, "ffn")
        mid_hi, mid_lo = split_tiles(s0, "mid", [P, FT, T])
        with ExitStack() as inner:
            s = core.scope(nc, inner, "up")
            h = split_tiles(s, "h", [P, DT, T])
            raw, loaded = s.sb("raw", [P, 2, DT, P]), [s.sem(f"loaded{g}") for g in range(2)]
            stage_norm(nc, core, core.x, gain, mod, parts=h,
                       start=[(raw[:, g], up[0, :, g], loaded[g]) for g in range(2)])
            w_hi, w_lo = split_tiles(s, "w", [P, 2, 2, DT, P])
            gate = s.sb("gate", [P, 2, T])
            lift = s.sb("lift", [P, 2, T]) if conv_up else None
            acc = s.ps("acc", [P, 4, 512])
            cut_hi, cut_lo = ([s.sem(f"{n}{g}") for g in range(2)] for n in ("cut_hi", "cut_lo"))
            made, tapped, convolved, gated, mixed, cut_mid, done_mid = (
                [s.sem(f"{n}{k}") for k in range(2)] for n in
                ("made", "tapped", "convolved", "gated", "mixed", "cut_mid", "done_mid"))
            sides = 2 if conv_up else 1
            turns = FT // 2

            def leading(act, i, k):
                for g in range(2):
                    act.wait_ge(loaded[g], i * 32 + 16 * (k + 1))
                    if g == 0:
                        free_after(act, made[k], i * 2)
                    split_hi(nc, w_hi[:, k, g], raw[:, g]).then_inc(cut_hi[g], 1)

            with nc.Block() as block:
                @block.sync
                def _(sp):
                    def turn(i):
                        for k in range(2):
                            for g in range(2):
                                if isinstance(i, int) and i + k == 0:
                                    continue
                                free_after(sp, cut_lo[g], i * 2 + k)
                                sp.dma_start(raw[:, g], up[bass.ds(i * 2 + k, 1), :, g].rearrange(
                                    "a p k n -> p (a k) n")).then_inc(loaded[g], 16)
                    span(sp, turns, turn)

                @block.gpsimd
                def _(pool):
                    def turn(i):
                        for k in range(2):
                            for g in range(2):
                                pool.wait_ge(cut_hi[g], i * 2 + k + 1)
                                split_lo(nc.gpsimd, w_lo[:, k, g], raw[:, g], w_hi[:, k, g]
                                         ).then_inc(cut_lo[g], 1)
                    span(pool, turns, turn)

                @block.tensor
                def _(pe):
                    def turn(i):
                        for k in range(2):
                            for g in range(2):
                                pe.wait_ge(cut_lo[g], i * 2 + k + 1)
                                if g == 0:
                                    free_after(pe, mixed[k], i)
                                for c in range(DT):
                                    last = product(nc, acc[:, 2 * k + g], (w_hi[:, k, g, c], w_lo[:, k, g, c]),
                                                   (h[0][:, c], h[1][:, c]), c == 0, c == DT - 1)
                                last.then_inc(made[k], 1)
                    span(pe, turns, turn)

                @block.scalar
                def _(act):
                    leading(act, 0, 0)

                    def turn(i, last=False):
                        for k in range(2):
                            if not (last and k == 1):
                                leading(act, i + k, 1 - k)
                            free_after(act, done_mid[k], i)
                            if conv is None:
                                act.wait_ge(made[k], i * 2 + 1)
                                nc.scalar.activation(gate[:, k], acc[:, 2 * k], ACT.Silu).then_inc(gated[k], 1)
                            else:
                                for g in range(sides):
                                    act.wait_ge(made[k], i * 2 + g + 1)
                                    tap = conv[:, bass.ds(i * 6 + (3 * k + 2 + g * 3 * FT), 1)]
                                    nc.scalar.activation((gate, lift)[g][:, k], acc[:, 2 * k + g], ACT.Copy,
                                                         scale=tap).then_inc(tapped[k], 1)
                                act.wait_ge(convolved[k], i * (2 * sides) + 2)
                                nc.scalar.activation(gate[:, k], gate[:, k], ACT.Silu).then_inc(gated[k], 1)
                            act.wait_ge(mixed[k], i + 1)
                            nc.scalar.activation(mid_hi[:, bass.ds(i * 2 + k, 1), :], gate[:, k:k + 1],
                                                 ACT.Copy).then_inc(cut_mid[k], 1)
                    span(act, turns - 1, turn)
                    turn(turns - 1, last=True)

                @block.vector
                def _(dve):
                    def turn(i):
                        for k in range(2):
                            if conv is not None:
                                for g in range(sides):
                                    dve.wait_ge(tapped[k], i * sides + g + 1)
                                    buf = (gate, lift)[g]
                                    for lag in (1, 2):
                                        tap = conv[:, bass.ds(i * 6 + (3 * k + 2 - lag + g * 3 * FT), 1)]
                                        nc.vector.scalar_tensor_tensor(
                                            out=buf[:, k, lag:], in0=acc[:, 2 * k + g, :T - lag], scalar=tap,
                                            in1=buf[:, k, lag:], op0=ALU.mult, op1=ALU.add
                                        ).then_inc(convolved[k], 1)
                                        dve.wait_ge(convolved[k], i * (2 * sides) + (2 * g + lag))
                            dve.wait_ge(made[k], i * 2 + 2)
                            dve.wait_ge(gated[k], i + 1)
                            second = lift[:, k] if conv_up else acc[:, 2 * k + 1]
                            nc.vector.tensor_tensor(gate[:, k], gate[:, k], second, ALU.mult).then_inc(mixed[k], 1)
                            dve.wait_ge(cut_mid[k], i + 1)
                            nc.vector.tensor_tensor(
                                mid_lo[:, bass.ds(i * 2 + k, 1), :], gate[:, k:k + 1],
                                mid_hi[:, bass.ds(i * 2 + k, 1), :].bitcast(F32), ALU.subtract
                            ).then_inc(done_mid[k], 1)
                    span(dve, turns, turn)
        stage_project(nc, core, down, FT, core.x, parts=(mid_hi, mid_lo), scale=scale)


class Ada(Beside):

    COLS = 6 * D // 16
    TURNS = 8
    SETS = ((0,), (1, 2))

    def __init__(self, nc, core):
        self.nc, self.core = nc, core

    def open(self, s):
        nc, core = self.nc, self.core
        self.w = s.sb("ada_w", [P, 2, DT, self.COLS])
        self.sum = s.sb("ada_sum", [P, 2, 2, self.COLS])
        self.cond = s.sb("ada_cond", [P, DT, 3])
        self.acc = s.ps("ada_acc", [P, 3 * 48])
        self.loaded, self.summed, self.read = (
            [s.sem(f"ada_{n}{k}") for k in range(2)] for n in ("loaded", "summed", "read"))
        bent, self.added = s.sem("ada_bent"), s.sem("ada_added")
        with nc.Block() as block:
            @block.scalar
            def _(act):
                nc.scalar.activation(self.cond[:, :, 0:1], core.v("c_2", 0, DT).unsqueeze(2),
                                     ACT.Silu).then_inc(bent, 1)
                nc.scalar.activation(self.cond[:, :, 1:3],
                                     core.v("c_3", 0, 16).rearrange("p (k m) -> p k m", m=2),
                                     ACT.Silu).then_inc(bent, 1)

    def steps(self, n):
        per = [DT * len(sets) for sets in self.SETS]
        return self.TURNS * sum(per[:n]), per[n]

    def sync_turn(self, sp, n, i, k):
        before, per = self.steps(n)
        free_after(sp, self.summed[k], i * per + before)
        sp.dma_start(self.w[:, k], self.core.dram[("w_ada_2", "w_ada_3")[n]][bass.ds(i * 2 + k, 1)].rearrange(
            "a p k n -> p (a k) n")).then_inc(self.loaded[k], 16)

    def vector_segment(self, dve, n, turns):
        v = self.nc.vector
        before, per = self.steps(n)
        many = len(self.SETS[n])

        def turn(i):
            for k in range(2):
                dve.wait_ge(self.loaded[k], (i + self.TURNS * n) * 16 + 16)
                free_after(dve, self.read[k], i + self.TURNS * n)
                for c in range(DT):
                    for m, which in enumerate(self.SETS[n]):
                        at = self.sum[:, k, m]
                        by = self.cond[:, c, which:which + 1]
                        if c == 0:
                            v.tensor_scalar(at, self.w[:, k, c], by, None, ALU.mult).then_inc(self.summed[k], 1)
                        else:
                            dve.wait_ge(self.summed[k], i * per + (before + (c - 1) * many + m + 1))
                            v.scalar_tensor_tensor(out=at, in0=self.w[:, k, c], scalar=by, in1=at, op0=ALU.mult,
                                                   op1=ALU.add).then_inc(self.summed[k], 1)
        span(dve, turns, turn)

    def tensor_turn(self, pe, n, i, k):
        before, per = self.steps(n)
        pe.wait_ge(self.summed[k], i * per + (before + per))
        for m, which in enumerate(self.SETS[n]):
            for j in range(self.COLS // P):
                col = i * 6 + (3 * k + j + 48 * which)
                last = self.nc.tensor.matmul(self.acc[:, bass.ds(col, 1)], self.sum[:, k, m, j * P:(j + 1) * P],
                                             self.core.ones[:, 0:1], start=True, stop=True)
        last.then_inc(self.read[k], 1)

    def close(self):
        nc, core = self.nc, self.core
        with nc.Block() as block:
            @block.vector
            def _(dve):
                for which, bias in enumerate(("b_ada_2", "b_ada_3", "b_ada_3")):
                    nc.vector.tensor_tensor(core.mod[:, which], self.acc[:, 48 * which:48 * which + 48],
                                            core.v(bias, 0, 48), ALU.add).then_inc(self.added, 1)



Z1 = {"b": 0, "c": 512, "x": 1024, "pool": 1536, "conf": 2048, "q": 3072, "k": 3584}


def stage_short_conv(nc, core, part, loaded, y):
    with ExitStack() as ctx:
        s = core.scope(nc, ctx, "short")
        step = s.sem("step")
        with nc.Block() as block:
            @block.vector
            def _(dve):
                done = Steps(dve, step)
                prod = part["c"]
                dve.wait_ge(loaded, 48)
                done(nc.vector.tensor_tensor(prod[:], prod[:], part["x"][:], ALU.mult))
                for j in range(4):
                    done.mark(nc.vector.tensor_scalar(y[:, j], prod[:, j], core.v("sc_conv", 3 * j + 2), None,
                                                      ALU.mult))
                done.wait()
                for lag in (1, 2):
                    for j in range(4):
                        done.mark(nc.vector.scalar_tensor_tensor(
                            out=y[:, j, lag:], in0=prod[:, j, :T - lag], scalar=core.v("sc_conv", 3 * j + 2 - lag),
                            in1=y[:, j, lag:], op0=ALU.mult, op1=ALU.add))
                    done.wait()
                done(nc.vector.tensor_tensor(y[:], y[:], part["b"][:], ALU.mult))


def stage_pool(nc, core, src, loaded, y):
    with ExitStack() as ctx:
        s = core.scope(nc, ctx, "pool")
        even = s.sb("even", [P, 4, T])
        odd = s.sb("odd", [P, 4, T])
        inv = s.sb("inv", [P, 4, 16])
        step = s.sem("step")
        with nc.Block() as block:
            @block.vector
            def _(dve):
                done = Steps(dve, step)
                for g in range(4):
                    for t in range(2 << g):
                        done.mark(nc.vector.memset(inv[:, g, t:t + 1], 1.0 / (t + 1)))
                dve.wait_ge(loaded, 16)
                now = src
                for r in range(4):
                    nxt = even if r % 2 == 0 else odd
                    lag = 1 << r
                    done.mark(nc.vector.tensor_tensor(nxt[:, r:, lag:], now[:, r:, lag:], now[:, r:, :T - lag],
                                                      ALU.add))
                    done(nc.vector.tensor_copy(nxt[:, r:, :lag], now[:, r:, :lag]))
                    w = 2 << r
                    done.mark(nc.vector.scalar_tensor_tensor(out=y[:, r, w:], in0=nxt[:, r, w:], scalar=1.0 / w,
                                                             in1=src[:, r, w:], op0=ALU.mult, op1=ALU.subtract))
                    done(nc.vector.tensor_tensor(y[:, r, :w], nxt[:, r, :w], inv[:, r, :w], ALU.mult))
                    done(nc.vector.tensor_tensor(y[:, r, :w], y[:, r, :w], src[:, r, :w], ALU.subtract))
                    now = nxt


def stage_conformer(nc, core, pad, gate, loaded, y):
    taps = CONF_TAPS
    with ExitStack() as ctx:
        s = core.scope(nc, ctx, "conf")
        sig, glu, step = s.sem("sig"), s.sem("glu"), s.sem("step")
        diag = s.sb("diag", [P, 4, P])
        acc = s.ps("acc", [P, 4, 512])
        diag_made, conv_done = s.sem("diag_made"), s.sem("conv_done")
        pe_taps = 14
        with nc.Block() as block:
            @block.scalar
            def _(act):
                act.wait_ge(loaded, 32)
                nc.scalar.activation(gate[:], gate[:], ACT.Sigmoid).then_inc(sig, 1)
                for n in range(4 * pe_taps):
                    if n >= 4:
                        act.wait_ge(conv_done, n - 3)
                    nc.scalar.activation(diag[:, n % 4], core.ident[:], ACT.Copy,
                                         scale=core.v("conf_conv", taps * (n // pe_taps) + n % pe_taps)
                                         ).then_inc(diag_made, 1)

            @block.tensor
            def _(pe):
                pe.wait_ge(glu, 1)
                for n in range(4 * pe_taps):
                    j, i = n // pe_taps, n % pe_taps
                    pe.wait_ge(diag_made, n + 1)
                    nc.tensor.matmul(acc[:, j], diag[:, n % 4], pad[:, j, i:i + T],
                                     start=i == 0, stop=i == pe_taps - 1).then_inc(conv_done, 1)

            @block.vector
            def _(dve):
                done = Steps(dve, step)
                done.mark(nc.vector.memset(pad[:, :, :taps - 1], 0.0))
                dve.wait_ge(sig, 1)
                nc.vector.tensor_tensor(pad[:, :, taps - 1:], pad[:, :, taps - 1:], gate[:],
                                        ALU.mult).then_inc(glu, 1)
                dve.wait_ge(glu, 1)
                done.wait()
                for j in range(4):
                    done.mark(nc.vector.tensor_scalar(y[:, j], pad[:, j, taps - 1:],
                                                      core.v("conf_conv", taps * j + taps - 1),
                                                      core.v("conf_conv_b", j), ALU.mult, ALU.add))
                for i in range(pe_taps, taps - 1):
                    done.wait()
                    for j in range(4):
                        done.mark(nc.vector.scalar_tensor_tensor(
                            out=y[:, j], in0=pad[:, j, i:i + T], scalar=core.v("conf_conv", taps * j + i),
                            in1=y[:, j], op0=ALU.mult, op1=ALU.add))
                done.wait()
                dve.wait_ge(conv_done, 4 * pe_taps)
                done(nc.vector.tensor_tensor(y[:], y[:], acc[:], ALU.add))
        stage_centre(nc, core, y, 4, core.ones, 512)
        rstd = gate[:, 0:1]
        stage_rstd(nc, core, y, rstd, 4, core.ones, 512, EPS)
        ready = s.sem("ready")
        with nc.Block() as block:
            @block.vector
            def _(dve):
                for j in range(4):
                    nc.vector.tensor_tensor(y[:, j], y[:, j], rstd[:, 0], ALU.mult).then_inc(ready, 1)

            @block.scalar
            def _(act):
                for j in range(4):
                    act.wait_ge(ready, j + 1)
                    nc.scalar.activation(y[:, j], y[:, j], ACT.Silu, bias=core.v("conf_ln_b", j),
                                         scale=core.v("conf_ln_g", j))


def stage_attention(nc, core, q, k, loaded, v_tok, y):
    with ExitStack() as ctx:
        s = core.scope(nc, ctx, "attn")
        rq = s.sb("rq", [P, 4, T])
        rk = s.sb("rk", [P, 4, T])
        stage_load(nc, core, [], earlier=(loaded, 2))
        stage_rstd(nc, core, q, rq, 1, core.halves, 64, EPS)
        stage_rstd(nc, core, k, rk, 1, core.halves, 64, EPS)
        with ExitStack() as inner:
            s = core.scope(nc, inner, "heads")
            mask = s.sb("mask", [P, P])
            probs = s.sb("probs", [P, 2, 2, T])
            attn = s.sb("attn", [P, 2, T])
            attn_t = s.sb("attn_t", [P, 2, 4, P])
            small = s.sb("small", [P, 2, 8])
            lam = s.sb("lam", [P, 8])
            scores = s.ps("scores", [P, 2, 2, 512])
            turned = s.ps("turned", [P, 2, 4, P])
            acc_o = s.ps("acc_o", [P, 2, 512])
            names = ("q_ready", "k_ready", "masked", "lam_in", "lam_sum", "lam_exp", "scored", "max_ready",
                     "exped", "mixed", "turned_ready", "turned_copied", "out_ready", "out_copied", "step", "made")
            (q_ready, k_ready, masked, lam_in, lam_sum, lam_exp, scored, max_ready, exped, mixed, turned_ready,
             turned_copied, out_ready, out_copied, step, made) = (s.sem(x) for x in names)
            units = [(h, b) for h in range(4) for b in range(4)]
            with nc.Block() as block:
                @block.gpsimd
                def _(pool):
                    nc.gpsimd.memset(mask[:], 0.0).then_inc(made, 1)
                    pool.wait_ge(made, 1)
                    nc.gpsimd.affine_select(out=mask[:], in_=mask[:], pattern=[[-1, P]], compare_op=ALU.is_ge,
                                            fill=-1e30, base=0, channel_multiplier=1).then_inc(made, 1)

                @block.tensor
                def _(pe):
                    pe.wait_ge(lam_in, 1)
                    nc.tensor.matmul(acc_o[:, 0, 0:2], core.ones[0:64, :], lam[0:64, 0:2], start=True,
                                     stop=True).then_inc(lam_sum, 1)
                    pe.wait_ge(q_ready, 4)
                    pe.wait_ge(k_ready, 4)

                    def score(n):
                        h, b = units[n]
                        if n >= 2:
                            pe.wait_ge(exped, 2 * (n - 1))
                        for m in range(2):
                            at = slice(64 * m, 64 * m + 64)
                            nc.tensor.matmul(scores[:, n % 2, m, :(b + 1) * P], q[at, h, b * P:(b + 1) * P],
                                             k[at, h, :(b + 1) * P], start=True, stop=True).then_inc(scored, 1)

                    def turn(n):
                        h, b = units[n]
                        pe.wait_ge(mixed, n + 1)
                        if n >= 2:
                            pe.wait_ge(turned_copied, n - 1)
                        for c in range(b + 1):
                            last = nc.tensor.transpose(turned[:, n % 2, c], attn[:, n % 2, c * P:(c + 1) * P],
                                                       core.ident[:])
                        last.then_inc(turned_ready, 1)

                    def out(n):
                        h, b = units[n]
                        pe.wait_ge(turned_copied, n + 1)
                        if n >= 2:
                            pe.wait_ge(out_copied, n - 1)
                        for c in range(b + 1):
                            last = nc.tensor.matmul(acc_o[:, n % 2, :P], v_tok[:, c, h * P:(h + 1) * P],
                                                    attn_t[:, n % 2, c], start=c == 0, stop=c == b)
                        last.then_inc(out_ready, 1)

                    pe.wait_ge(lam_exp, 1)
                    score(0)
                    score(1)
                    for n in range(len(units)):
                        turn(n)
                        if n + 2 < len(units):
                            score(n + 2)
                        out(n)

                @block.scalar
                def _(act):
                    act.wait_ge(lam_sum, 1)
                    nc.scalar.activation(lam[:, 2:4], acc_o[:, 0, 0:2], ACT.Exp).then_inc(lam_exp, 1)

                    def exps(n):
                        h, b = units[n]
                        if n >= 2:
                            act.wait_ge(mixed, n - 1)
                        for m in range(2):
                            act.wait_ge(max_ready, 2 * n + m + 1)
                            nc.scalar.activation(probs[:, n % 2, m, :(b + 1) * P], scores[:, n % 2, m, :(b + 1) * P],
                                                 ACT.Exp, scale=0.125, bias=small[:, n % 2, 2 + m:3 + m],
                                                 accum_out=small[:, n % 2, 4 + m:5 + m]).then_inc(exped, 1)

                    exps(0)
                    for n, (h, b) in enumerate(units):
                        if n + 1 < len(units):
                            exps(n + 1)
                        act.wait_ge(turned_ready, n + 1)
                        if n >= 2:
                            act.wait_ge(out_ready, n - 1)
                        nc.scalar.activation(attn_t[:, n % 2, :b + 1], turned[:, n % 2, :b + 1], ACT.Copy
                                             ).then_inc(turned_copied, 1)
                        act.wait_ge(out_ready, n + 1)
                        nc.scalar.activation(y[:, h, b * P:(b + 1) * P], acc_o[:, n % 2, :P], ACT.Copy
                                             ).then_inc(out_copied, 1)

                @block.vector
                def _(dve):
                    done = Steps(dve, step)
                    nc.vector.tensor_tensor(lam[:, 0:2], core.v("lam_q", 0, 2), core.v("lam_k", 0, 2),
                                            ALU.mult).then_inc(lam_in, 1)
                    for h in range(4):
                        nc.vector.scalar_tensor_tensor(out=q[:, h], in0=q[:, h], scalar=core.v("q_norm"), in1=rq[:, h],
                                                       op0=ALU.mult, op1=ALU.mult).then_inc(q_ready, 1)
                        nc.vector.scalar_tensor_tensor(out=k[:, h], in0=k[:, h], scalar=core.v("k_norm"), in1=rk[:, h],
                                                       op0=ALU.mult, op1=ALU.mult).then_inc(k_ready, 1)
                    dve.wait_ge(lam_exp, 1)
                    done(nc.vector.tensor_tensor(lam[:, 4:5], lam[:, 3:4], lam[:, 2:3], ALU.subtract))
                    done(nc.vector.tensor_scalar(lam[:, 5:6], lam[:, 4:5], -LAM_INIT, None, ALU.add))
                    dve.wait_ge(made, 2)

                    def top(n):
                        h, b = units[n]
                        for m in range(2):
                            dve.wait_ge(scored, 2 * n + m + 1)
                            sc = scores[:, n % 2, m]
                            done(nc.vector.tensor_tensor(sc[:, b * P:(b + 1) * P], sc[:, b * P:(b + 1) * P], mask[:],
                                                         ALU.add))
                            done(nc.vector.reduce_max(small[:, n % 2, m:m + 1], sc[:, :(b + 1) * P], AX_X))
                            nc.vector.tensor_scalar(small[:, n % 2, 2 + m:3 + m], small[:, n % 2, m:m + 1], -0.125,
                                                    None, ALU.mult).then_inc(max_ready, 1)

                    top(0)
                    for n, (h, b) in enumerate(units):
                        if n + 1 < len(units):
                            top(n + 1)
                        w = (b + 1) * P
                        dve.wait_ge(exped, 2 * n + 2)
                        if n >= 2:
                            dve.wait_ge(turned_ready, n - 1)
                        inv = small[:, n % 2, 6:8]
                        done(nc.vector.reciprocal(inv, small[:, n % 2, 4:6]))
                        done(nc.vector.tensor_scalar(inv[:, 1:2], inv[:, 1:2], lam[:, 5:6], None, ALU.mult))
                        done(nc.vector.tensor_scalar(attn[:, n % 2, :w], probs[:, n % 2, 0, :w], inv[:, 0:1], None,
                                                     ALU.mult))
                        nc.vector.scalar_tensor_tensor(out=attn[:, n % 2, :w], in0=probs[:, n % 2, 1, :w],
                                                       scalar=inv[:, 1:2], in1=attn[:, n % 2, :w], op0=ALU.mult,
                                                       op1=ALU.add).then_inc(mixed, 1)
        stage_rstd(nc, core, y, rq, 1, core.ones, P, EPS)
        s = core.scope(nc, ctx, "subln")
        with nc.Block() as block:
            @block.vector
            def _(dve):
                done = Steps(dve, s.sem("scaled"))
                for h in range(4):
                    done.mark(nc.vector.scalar_tensor_tensor(out=y[:, h], in0=y[:, h], scalar=core.v("diff_subln"),
                                                             in1=rq[:, h], op0=ALU.mult, op1=ALU.mult))
                done.wait()
                done(nc.vector.tensor_scalar(y[:], y[:], 1.0 - LAM_INIT, None, ALU.mult))


class MixerInputs:

    def __init__(self, core, s):
        z = core.dram["z"]
        self.short = {n: s.sb(f"short_{n}", [P, 4, T]) for n in "cxb"}
        self.pool = s.sb("pool_src", [P, 4, T])
        self.pad, self.gate = s.sb("pad", [P, 4, CONF_TAPS - 1 + T]), s.sb("gate", [P, 4, T])
        self.short_loaded, self.pool_loaded, self.conf_loaded = (
            s.sem(n) for n in ("short_loaded", "pool_loaded", "conf_loaded"))
        self.loads = [(self.short[n][:], Z1[n], self.short_loaded) for n in "cxb"] + [
            (self.pool[:], Z1["pool"], self.pool_loaded),
            (self.pad[:, :, CONF_TAPS - 1:], Z1["conf"], self.conf_loaded),
            (self.gate[:], Z1["conf"] + 512, self.conf_loaded)]
        self.loads = [(dst, rows(z[at:at + 512]), sem) for dst, at, sem in self.loads]


def first_rows(nc, core, v_tok, inputs):
    dram = core.dram
    with ExitStack() as ctx:
        h = split_tiles(core.scope(nc, ctx, "first_h"), "h", [P, DT, T])
        stage_norm(nc, core, core.x, "mix_norm", parts=h)
        stage_rows(nc, core, [(dram["w_in_a"], dram["z"][0:4096], ACT.Copy),
                              (dram["w_in_g"], dram["gates"], ACT.Sigmoid)], h, beside=Ada(nc, core))
        stage_tokens(nc, core, dram["w_in_v"], [(h, v_tok)], start=inputs.loads)


def first_block(nc, core):
    dram = core.dram
    z, g = dram["z"], dram["gates"]
    with ExitStack() as ctx:
        s = core.scope(nc, ctx, "first")
        v_tok, inputs = s.sb("v_tok", [P, 4, 512]), MixerInputs(core, s)
        first_rows(nc, core, v_tok, inputs)
        q, k, qk_loaded = s.sb("q", [P, 4, T]), s.sb("k", [P, 4, T]), s.sem("qk_loaded")
        stage_load(nc, core, [], start=[(q[:], rows(z[Z1["q"]:Z1["q"] + 512])),
                                        (k[:], rows(z[Z1["k"]:Z1["k"] + 512]))], started=qk_loaded)
        merged, y = s.sb("merged", [P, DT, T]), s.sb("y", [P, 4, T])
        stage_short_conv(nc, core, inputs.short, inputs.short_loaded, y)
        stage_project(nc, core, dram["sc_out"], 4, merged, y, gates=g[0:D], first=True)
        stage_pool(nc, core, inputs.pool, inputs.pool_loaded, y)
        stage_project(nc, core, dram["pool_w"], 1, merged, y, gates=g[D:2 * D], groups=True,
                      scale=core.v("pool_scale", 0, DT))
        stage_conformer(nc, core, inputs.pad, inputs.gate, inputs.conf_loaded, y)
        stage_project(nc, core, dram["conf_out"], 4, merged, y, gates=g[2 * D:3 * D])
        stage_attention(nc, core, q, k, qk_loaded, v_tok, y)
        stage_project(nc, core, dram["diff_out"], 4, merged, y, gates=g[3 * D:4 * D])
        stage_project(nc, core, dram["w_o"], DT, core.x, merged)
    stage_ffn(nc, core, "ffn_norm", dram["ffn_up"], dram["ffn_down"], conv=core.v("ffn_conv", 0, 6 * FT),
              conv_up=True)



def stage_softplus(nc, core, x, parts, n):
    with ExitStack() as ctx:
        s = core.scope(nc, ctx, "softplus")
        u, low, series = s.sb("u", [P, n]), s.sb("low", [P, n]), s.sb("series", [P, n])
        exped, negated, step = s.sem("exped"), s.sem("negated"), s.sem("step")
        with nc.Block() as block:
            @block.scalar
            def _(act):
                act.wait_ge(negated, 1)
                nc.scalar.activation(u[:parts], low[:parts], ACT.Exp).then_inc(exped, 1)

            @block.vector
            def _(dve):
                done = Steps(dve, step)
                v = nc.vector
                done(v.tensor_scalar(low[:parts], x[:parts], -1.0, None, ALU.mult))
                v.tensor_tensor(low[:parts], low[:parts], x[:parts], ALU.min).then_inc(negated, 1)
                dve.wait_ge(exped, 1)
                done(v.tensor_scalar(low[:parts], u[:parts], 2.0, None, ALU.add))
                done(v.reciprocal(low[:parts], low[:parts]))
                done(v.tensor_tensor(u[:parts], u[:parts], low[:parts], ALU.mult))
                done(v.tensor_tensor(low[:parts], u[:parts], u[:parts], ALU.mult))
                done(v.tensor_scalar(series[:parts], low[:parts], 2.0 / 15, 2.0 / 13, ALU.mult, ALU.add))
                for odd in (11, 9, 7, 5, 3, 1):
                    done(v.tensor_tensor(series[:parts], series[:parts], low[:parts], ALU.mult))
                    done(v.tensor_scalar(series[:parts], series[:parts], 2.0 / odd, None, ALU.add))
                done(v.tensor_tensor(series[:parts], series[:parts], u[:parts], ALU.mult))
                done(v.scalar_tensor_tensor(out=x[:parts], in0=x[:parts], scalar=0.0, in1=series[:parts],
                                            op0=ALU.max, op1=ALU.add))


F2 = {n: 512 * k for k, n in enumerate(
    ("q", "k", "qg", "kbg", "kd", "vb", "egc", "ra", "rb", "rk", "rr", "rv", "re", "bonus", "rg"))}
Z2 = {"q": 0, "k": 512, "v": 1024, "z": 1536, "pb": 2048, "ba": 3584, "lo": 3600, "glo": 3728}
UNIT = 8 * C64


def feat(core, name):
    at = F2[name]
    return rows(core.dram["feat"][at:at + 512])


def stage_gdn_gates(nc, core, decay_t, beta):
    z = core.dram["z"]
    with ExitStack() as ctx:
        s = core.scope(nc, ctx, "gates")
        g = s.sb("g", [HN, C64])
        keep = s.sb("keep", [HN, 2, C64])
        ones = s.sb("ones", [HN, C64])
        loaded, step0, fin = s.sem("loaded"), s.sem("step0"), s.sem("fin")
        by_unit = "(j q) (n c) -> n q j c"
        with nc.Block() as block:
            @block.sync
            def _(sp):
                for n in range(NC64):
                    for q in range(2):
                        at = n * 8 + q * 4
                        src = z[Z2["ba"]:Z2["ba"] + 8].rearrange(by_unit, q=2, c=C64)[n, q]
                        sp.dma_start(beta[at:at + 4], src).then_inc(loaded, 16)
                        src = z[Z2["ba"] + 8:Z2["ba"] + 16].rearrange(by_unit, q=2, c=C64)[n, q]
                        sp.dma_start(g[at:at + 4], src).then_inc(loaded, 16)
                sp.wait_ge(loaded, 512)

            @block.scalar
            def _(act):
                act.wait_ge(loaded, 512)
                nc.scalar.activation(beta[:], beta[:], ACT.Sigmoid)

            @block.vector
            def _(dve):
                dve.wait_ge(loaded, 512)
                nc.vector.tensor_scalar(g[:], g[:], core.v("dt_bias")[:HN], None, ALU.add)
        stage_softplus(nc, core, g, HN, C64)
        rate = s.sb("rate", [HN, 1])
        rate_ready, diff_ready, exp_done, summed, made, stored = (
            s.sem(x) for x in ("rate_ready", "diff_ready", "exp_done", "summed", "made", "stored"))
        hn = core.dram["hn"]
        with nc.Block() as block:
            @block.scalar
            def _(act):
                nc.scalar.activation(rate[:], core.v("a_log")[:HN], ACT.Exp).then_inc(rate_ready, 1)
                act.wait_ge(summed, 2)
                nc.scalar.activation(keep[:], keep[:], ACT.Exp).then_inc(exp_done, 1)
                act.wait_ge(diff_ready, 1)
                nc.scalar.activation(decay_t[:], decay_t[:], ACT.Exp).then_inc(exp_done, 1)
                act.wait_ge(exp_done, 1)
                act.dma_start(hn[0], beta[:]).then_inc(stored, 16)
                act.dma_start(hn[1:3].rearrange("a p c -> p a c"), keep[:]).then_inc(stored, 16)
                act.wait_ge(made, 1)
                act.dma_start(core.dram["decay"].rearrange("p s c -> p (s c)"),
                              decay_t[:].rearrange("p s c -> p (s c)")).then_inc(stored, 16)
                act.wait_ge(stored, 48)

            @block.vector
            def _(dve):
                done = Steps(dve, step0)
                v = nc.vector
                dve.wait_ge(rate_ready, 1)
                done.mark(v.memset(ones[:], 1.0))
                done(v.tensor_scalar(g[:], g[:], rate[:], -1.0, ALU.mult, ALU.mult))
                v.tensor_tensor_scan(keep[:, 0], ones[:], g[:], 0.0, ALU.mult, ALU.add).then_inc(summed, 1)
                dve.wait_ge(summed, 1)
                gc = g[:]
                done(v.tensor_copy(gc, keep[:, 0]))
                v.tensor_scalar(keep[:, 1], gc, gc[:, C64 - 1:C64], -1.0, ALU.subtract,
                                ALU.mult).then_inc(summed, 1)
                done(v.tensor_tensor(decay_t[:], gc.unsqueeze(1).broadcast_to([HN, C64, C64]),
                                     gc.unsqueeze(2).broadcast_to([HN, C64, C64]), ALU.subtract))
                v.tensor_scalar(decay_t[:], decay_t[:], 0.0, None, ALU.min).then_inc(diff_ready, 1)

            @block.gpsimd
            def _(pool):
                pool.wait_ge(exp_done, 2)
                nc.gpsimd.affine_select(out=decay_t[:], in_=decay_t[:], pattern=[[-1, C64], [1, C64]],
                                        compare_op=ALU.is_ge, fill=0.0, base=0,
                                        channel_multiplier=0).then_inc(made, 1)


def grams(nc, pe, out, lhs, rhs, n):
    at = slice(n * C64, (n + 1) * C64)
    for q in range(2):
        half = slice(64 * q, 64 * q + 64)
        for j in range(4):
            last = nc.tensor.matmul(out[:C64, q, j * C64:(j + 1) * C64], lhs[half, j, at], rhs[half, j, at],
                                    start=True, stop=True)
    return last


def stage_gram(nc, core, lhs, rhs, dst):
    with ExitStack() as ctx:
        s = core.scope(nc, ctx, "gram")
        out = s.sb("out", [C64, NC64, UNIT])
        acc = s.ps("acc", [P, 2, 2, 512])
        product, copied, stored = s.sem("product"), s.sem("copied"), s.sem("stored")
        with nc.Block() as block:
            @block.tensor
            def _(pe):
                for n in range(NC64):
                    if n >= 2:
                        pe.wait_ge(copied, n - 1)
                    grams(nc, pe, acc[:, n % 2], lhs, rhs, n).then_inc(product, 1)

            @block.vector
            def _(dve):
                for n in range(NC64):
                    dve.wait_ge(product, n + 1)
                    nc.vector.tensor_copy(out[:, n].rearrange("p (q c) -> p q c", q=2),
                                          acc[:C64, n % 2, :, :4 * C64]).then_inc(copied, 1)

            @block.sync
            def _(sp):
                for n in range(NC64):
                    sp.wait_ge(copied, n + 1)
                    sp.dma_start(dst[8 * n:8 * n + 8].rearrange("u i j -> i u j"),
                                 out[:, n].rearrange("p (u c) -> p u c", u=8)).then_inc(stored, 16)
                sp.wait_ge(stored, 16 * NC64)


def stage_gdn_prepare(nc, core, decay_t, beta):
    z = core.dram["z"]
    with ExitStack() as ctx:
        s = core.scope(nc, ctx, "gdn")
        raw = s.sb("raw", [P, 12, T])
        qkv = s.sb("qkv", [P, 12, T])
        bcast = s.sb("bcast", [P, 3, 4, T])
        step, conved, spread = s.sem("step"), s.sem("conved"), s.sem("spread")
        loaded = [s.sem(f"loaded{part}") for part in range(3)]
        with nc.Block() as block:
            @block.sync
            def _(sp):
                for part in range(3):
                    sp.dma_start(raw[:, 4 * part:4 * part + 4], rows(z[512 * part:512 * part + 512])
                                 ).then_inc(loaded[part], 16)
                for a in range(3):
                    for q in range(2):
                        for j in range(4):
                            src = core.dram["hn"][a].rearrange("(n q j) c -> q j n c", q=2, j=4)[q, j]
                            sp.dma_start(bcast[64 * q:64 * q + 64, a, j].rearrange("p (n c) -> p n c", c=C64),
                                         src.unsqueeze(0).broadcast_to([64, NC64, C64])).then_inc(spread, 16)
                sp.wait_ge(spread, 16 * 24)

            @block.vector
            def _(dve):
                done = Steps(dve, step)
                for part in range(3):
                    tiles = range(4 * part, 4 * part + 4)
                    dve.wait_ge(loaded[part], 16)
                    for j in tiles:
                        done.mark(nc.vector.tensor_scalar(qkv[:, j], raw[:, j], core.v("conv_gdn", 4 * j + 3),
                                                          None, ALU.mult))
                    for lag in (1, 2, 3):
                        done.wait()
                        for j in tiles:
                            ins = nc.vector.scalar_tensor_tensor(
                                out=qkv[:, j, lag:], in0=raw[:, j, :T - lag],
                                scalar=core.v("conv_gdn", 4 * j + 3 - lag), in1=qkv[:, j, lag:],
                                op0=ALU.mult, op1=ALU.add)
                            if lag < 3:
                                done.mark(ins)
                            else:
                                ins.then_inc(conved, 1)

            @block.scalar
            def _(act):
                for j in range(12):
                    act.wait_ge(conved, j + 1)
                    nc.scalar.activation(qkv[:, j], qkv[:, j], ACT.Silu)
        stage_rstd(nc, core, qkv[:, 0:8], raw[:, 0:8], 1, core.halves, 1.0, 1e-6)
        half, normed, scaled, stored, step2 = (s.sem(x) for x in ("half", "normed", "scaled", "stored", "step2"))
        with nc.Block() as block:
            @block.sync
            def _(sp):
                sp.wait_ge(normed, 2)
                sp.dma_start(feat(core, "q"), qkv[:, 0:4]).then_inc(stored, 16)
                sp.dma_start(feat(core, "k"), qkv[:, 4:8]).then_inc(stored, 16)
                for n, (name, tile) in enumerate((("kd", raw[:, 0:4]), ("qg", raw[:, 4:8]), ("vb", raw[:, 8:12]),
                                                  ("kbg", bcast[:, 0]))):
                    sp.wait_ge(scaled, n + 1)
                    sp.dma_start(feat(core, name), tile).then_inc(stored, 16)
                sp.dma_start(feat(core, "egc"), bcast[:, 1]).then_inc(stored, 16)
                sp.wait_ge(stored, 16 * 7)

            @block.vector
            def _(dve):
                done = Steps(dve, step2)
                v = nc.vector
                v.scalar_tensor_tensor(out=qkv[:, 0:4], in0=qkv[:, 0:4], scalar=0.125, in1=raw[:, 0:4],
                                       op0=ALU.mult, op1=ALU.mult).then_inc(normed, 1)
                v.tensor_tensor(qkv[:, 4:8], qkv[:, 4:8], raw[:, 4:8], ALU.mult).then_inc(normed, 1)
                dve.wait_ge(normed, 2)
                v.tensor_tensor(raw[:, 0:4], qkv[:, 4:8], bcast[:, 2], ALU.mult).then_inc(scaled, 1)
                v.tensor_tensor(raw[:, 4:8], qkv[:, 0:4], bcast[:, 1], ALU.mult).then_inc(scaled, 1)
                v.tensor_tensor(raw[:, 8:12], qkv[:, 8:12], bcast[:, 0], ALU.mult).then_inc(scaled, 1)
                dve.wait_ge(scaled, 3)
                done(v.tensor_tensor(bcast[:, 0], bcast[:, 0], bcast[:, 1], ALU.mult))
                v.tensor_tensor(bcast[:, 0], bcast[:, 0], qkv[:, 4:8], ALU.mult).then_inc(scaled, 1)
        stage_gram(nc, core, qkv[:, 4:8], qkv[:, 4:8], core.dram["gram"][0:HN])


def stage_rwkv_prepare(nc, core):
    z = core.dram["z"]
    with ExitStack() as ctx:
        s = core.scope(nc, ctx, "rwkv")
        r, k, v_ = (s.sb(n, [P, 4, T]) for n in ("r", "k", "v"))
        d = s.sb("d", [P, 4, T])
        lw, a, g = (s.sb(n, [P, 4, T]) for n in ("lw", "a", "g"))
        lo = s.sb("lo", [P, 4, T])
        low = s.sb("low", [P, 4, 512])
        acc = s.ps("acc", [P, 4, 512])
        loaded, step, mixed, bent, product, freed = (
            s.sem(x) for x in ("loaded", "step", "mixed", "bent", "product", "freed"))
        rkv_loaded = [s.sem(f"rkv_loaded{n}") for n in range(3)]
        lows = ((0, 64), (1, 64), (2, P), (3, 32))
        with nc.Block() as block:
            @block.sync
            def _(sp):
                for n, at in ((0, 0), (1, 64)):
                    sp.dma_start(lo[:64, n], z[Z2["lo"] + at:Z2["lo"] + at + 64]).then_inc(loaded, 16)
                sp.dma_start(lo[:, 2], z[Z2["glo"]:Z2["glo"] + P]).then_inc(loaded, 16)
                sp.dma_start(lo[:32, 3], z[Z2["glo"] + P:Z2["glo"] + 160]).then_inc(loaded, 16)
                sp.dma_start(low[:64, 0], core.dram["w2"]).then_inc(loaded, 16)
                sp.dma_start(low[:64, 1], core.dram["a2"]).then_inc(loaded, 16)
                sp.dma_start(low[:, 2], core.dram["g2"][0:P]).then_inc(loaded, 16)
                sp.dma_start(low[:32, 3], core.dram["g2"][P:160]).then_inc(loaded, 16)
                for n, tile in enumerate((r, k, v_)):
                    at = Z2["pb"] + 512 * n
                    sp.dma_start(tile[:], rows(z[at:at + 512])).then_inc(rkv_loaded[n], 16)

            @block.vector
            def _(dve):
                done = Steps(dve, step)
                v = nc.vector
                dve.wait_ge(loaded, 16 * 8)
                for n, p in lows:
                    done.mark(v.tensor_tensor(d[:p, n, 1:], lo[:p, n, :T - 1], lo[:p, n, 1:], ALU.subtract))
                    done.mark(v.tensor_scalar(d[:p, n, 0:1], lo[:p, n, 0:1], -1.0, None, ALU.mult))
                done.wait()
                for n, p in lows:
                    v.scalar_tensor_tensor(out=lo[:p, n], in0=d[:p, n], scalar=core.v("mu_lo", n)[:p],
                                           in1=lo[:p, n], op0=ALU.mult, op1=ALU.add).then_inc(mixed, 1)
                dve.wait_ge(mixed, 4)
                for m, tile in enumerate((r, k, v_)):
                    dve.wait_ge(rkv_loaded[m], 16)
                    done.mark(v.tensor_tensor(d[:, :, 1:], tile[:, :, :T - 1], tile[:, :, 1:], ALU.subtract))
                    done(v.tensor_scalar(d[:, :, 0:1], tile[:, :, 0:1], -1.0, None, ALU.mult))
                    for j in range(4):
                        done.mark(v.scalar_tensor_tensor(out=tile[:, j], in0=d[:, j],
                                                         scalar=core.v("mu_rkv", 4 * m + j), in1=tile[:, j],
                                                         op0=ALU.mult, op1=ALU.add))
                    done.wait()

            @block.scalar
            def _(act):
                act.wait_ge(mixed, 4)
                nc.scalar.activation(lo[:64, 0], lo[:64, 0], ACT.Tanh).then_inc(bent, 1)
                nc.scalar.activation(lo[:, 2], lo[:, 2], ACT.Sigmoid).then_inc(bent, 1)
                nc.scalar.activation(lo[:32, 3], lo[:32, 3], ACT.Sigmoid).then_inc(bent, 1)
                for n in range(12):
                    which, j = n // 4, n % 4
                    act.wait_ge(product, n + 1)
                    if which == 0:
                        ins = nc.scalar.activation(lw[:, j], acc[:, n % 4], ACT.Sigmoid, bias=core.v("w0", j))
                    elif which == 1:
                        ins = nc.scalar.activation(a[:, j], acc[:, n % 4], ACT.Sigmoid, bias=core.v("a0", j))
                    else:
                        ins = nc.scalar.activation(g[:, j], acc[:, n % 4], ACT.Copy)
                    ins.then_inc(freed, 1)

            @block.tensor
            def _(pe):
                pe.wait_ge(loaded, 16 * 8)
                pe.wait_ge(bent, 3)
                for n in range(12):
                    which, j = n // 4, n % 4
                    if n >= 4:
                        pe.wait_ge(freed, n - 3)
                    at = slice(j * P, (j + 1) * P)
                    if which < 2:
                        nc.tensor.matmul(acc[:, n % 4], low[:64, which, at], lo[:64, which], start=True,
                                         stop=True).then_inc(product, 1)
                    else:
                        nc.tensor.matmul(acc[:, n % 4], low[:, 2, at], lo[:, 2], start=True, stop=False)
                        nc.tensor.matmul(acc[:, n % 4], low[:32, 3, at], lo[:32, 3], start=False,
                                         stop=True).then_inc(product, 1)
        kk, rstd = lo, low
        s = core.scope(nc, ctx, "rwkv_kk")
        step = s.sem("step")
        with nc.Block() as block:
            @block.vector
            def _(dve):
                done = Steps(dve, step)
                v = nc.vector
                for j in range(4):
                    done.mark(v.tensor_scalar(kk[:, j], k[:, j], core.v("k_k", j), None, ALU.mult))
                    done.mark(v.tensor_scalar(d[:, j], a[:, j], -1.0, core.v("k_a", j), ALU.add, ALU.mult))
                done.wait()
                done(v.scalar_tensor_tensor(out=k[:], in0=d[:], scalar=1.0, in1=k[:], op0=ALU.add, op1=ALU.mult))
                done(v.tensor_scalar(lw[:], lw[:], -math.exp(-0.5), None, ALU.mult))
        stage_rstd(nc, core, kk, rstd, 1, core.halves, 1.0, 1e-6)
        s = core.scope(nc, ctx, "rwkv_scale")
        reset = s.sb("reset", [P, T])
        cw, e = s.sb("cw", [P, 4, T]), s.sb("e", [P, 4, T])
        step, summed, exped, ready, stored, sums = (
            s.sem(x) for x in ("step", "summed", "exped", "ready", "stored", "sums"))
        order = ("rv", "rg", "re", "rr", "rb", "rk", "ra", "bonus")
        tiles = {"rv": v_, "rg": g, "re": e, "rr": r, "rb": a, "rk": k, "ra": kk, "bonus": d}
        with nc.Block() as block:
            @block.vector
            def _(dve):
                done = Steps(dve, step)
                v = nc.vector
                done(v.memset(reset[:], 1.0))
                done(v.memset(reset[:].rearrange("p (n c) -> p n c", c=C64)[:, :, 0:1], 0.0))
                for j in range(4):
                    v.tensor_tensor_scan(cw[:, j], reset[:], lw[:, j], 0.0, ALU.mult, ALU.add).then_inc(summed, 1)
                dve.wait_ge(summed, 4)
                v.tensor_tensor(lw[:], cw[:], lw[:], ALU.subtract).then_inc(summed, 1)
                done(v.tensor_tensor(d[:], r[:], k[:], ALU.mult))
                for j in range(4):
                    v.tensor_scalar(d[:, j], d[:, j], core.v("r_k", j), None, ALU.mult).then_inc(ready, 1)
                done(v.tensor_tensor(kk[:], kk[:], rstd[:], ALU.mult))
                done(v.tensor_tensor(a[:], a[:], kk[:], ALU.mult))
                dve.wait_ge(exped, 3)
                v.tensor_tensor(r[:], r[:], e[:], ALU.mult).then_inc(ready, 1)
                v.tensor_tensor(a[:], a[:], cw[:], ALU.mult).then_inc(ready, 1)
                v.tensor_tensor(k[:], k[:], cw[:], ALU.mult).then_inc(ready, 1)
                v.scalar_tensor_tensor(out=kk[:], in0=kk[:], scalar=-1.0, in1=lw[:], op0=ALU.mult,
                                       op1=ALU.mult).then_inc(ready, 1)
                dve.wait_ge(sums, 4)
                v.tensor_tensor(d[:], acc[:], v_[:], ALU.mult).then_inc(ready, 1)

            @block.scalar
            def _(act):
                act.wait_ge(summed, 5)
                nc.scalar.activation(e[:], cw[:], ACT.Exp).then_inc(exped, 1)
                nc.scalar.activation(lw[:], lw[:], ACT.Exp).then_inc(exped, 1)
                act.wait_ge(exped, 2)
                nc.scalar.activation(cw[:], cw[:], ACT.Exp, scale=-1.0).then_inc(exped, 1)

            @block.tensor
            def _(pe):
                pe.wait_ge(ready, 4)
                for j in range(4):
                    nc.tensor.matmul(acc[:, j], core.halves[:], d[:, j], start=True, stop=True).then_inc(sums, 1)

            @block.sync
            def _(sp):
                for n, name in enumerate(order):
                    if n == 2:
                        sp.wait_ge(exped, 1)
                    if n >= 3:
                        sp.wait_ge(ready, 4 + n - 2)
                    sp.dma_start(feat(core, name), tiles[name][:]).then_inc(stored, 16)
                sp.wait_ge(stored, 16 * len(order))
        stage_gram(nc, core, kk, a, core.dram["gram"][HN:2 * HN])


class Inverse(Beside):

    def __init__(self, nc, core, decay, beta):
        self.nc, self.core, self.beta = nc, core, beta
        self.decay_t, self.prod = decay[:HN], decay

    def open(self, s):
        self.m = s.sb("m", [P, C64, C64])
        self.inv = s.sb("inv", [P, C64, C64])
        self.loaded, self.step, self.stored = (s.sem(f"inverse_{n}") for n in ("loaded", "step", "stored"))
        with self.nc.Block() as block:
            @block.sync
            def _(sp):
                sp.dma_start(self.m[:], self.core.dram["gram"]).then_inc(self.loaded, 16)
                sp.wait_ge(self.loaded, 16)

    def vector_segment(self, dve, n, turns):
        if n:
            return
        m, inv, prod = self.m, self.inv, self.prod
        done = Steps(dve, self.step)
        v = self.nc.vector
        flat = inv[:].rearrange("p s c -> p (s c)")
        done(v.memset(flat, 0.0))
        done(v.memset(flat[:, ::C64 + 1], 1.0))
        low = m[:HN]
        done(v.tensor_tensor(low, low, self.decay_t.rearrange("p s c -> p c s"), ALU.mult))
        done(v.scalar_tensor_tensor(out=low, in0=low, scalar=-1.0,
                                    in1=self.beta[:].unsqueeze(2).broadcast_to([HN, C64, C64]),
                                    op0=ALU.mult, op1=ALU.mult))
        for i in range(1, C64):
            done(v.tensor_tensor(prod[:, :i, :i], inv[:, :i, :i],
                                 m[:, i:i + 1, :i].broadcast_to([P, i, i]), ALU.mult))
            done(v.tensor_reduce(inv[:, :i, i:i + 1], prod[:, :i, :i], AX_X, ALU.add))

    def close(self):
        with self.nc.Block() as block:
            @block.sync
            def _(sp):
                sp.dma_start(self.core.dram["inverse"], self.inv[:]).then_inc(self.stored, 16)
                sp.wait_ge(self.stored, 16)


def stage_to_tokens(nc, core, pairs, ahead=()):
    with ExitStack() as ctx:
        s = core.scope(nc, ctx, "turn")
        src = s.sb("src", [P, len(pairs), 4, T])
        acc = s.ps("acc", [P, 4, 512])
        turned, copied, ahead_loaded = s.sem("turned"), s.sem("copied"), s.sem("ahead_loaded")
        loaded = [s.sem(f"loaded{m}") for m in range(len(pairs))]
        steps = [(m, n) for m in range(len(pairs)) for n in range(NC64)]
        with nc.Block() as block:
            @block.sync
            def _(sp):
                for m, (name, _) in enumerate(pairs):
                    sp.dma_start(src[:, m], feat(core, name)).then_inc(loaded[m], 16)
                for to, at in ahead:
                    sp.dma_start(to, at).then_inc(ahead_loaded, 16)
                if ahead:
                    sp.wait_ge(ahead_loaded, 16 * len(ahead))

            @block.tensor
            def _(pe):
                for i, (m, n) in enumerate(steps):
                    pe.wait_ge(loaded[m], 16)
                    if i >= 4:
                        pe.wait_ge(copied, i - 3)
                    for j in range(4):
                        last = nc.tensor.transpose(acc[:C64, i % 4, j * P:(j + 1) * P],
                                                   src[:, m, j, n * C64:(n + 1) * C64], core.ident[:])
                    last.then_inc(turned, 1)

            @block.vector
            def _(dve):
                for i, (m, n) in enumerate(steps):
                    dve.wait_ge(turned, i + 1)
                    nc.vector.tensor_copy(pairs[m][1][:, n].rearrange("p (q j c) -> p q j c", q=2, j=4),
                                          acc[:C64, i % 4].rearrange("p (j q c) -> p q j c", q=2, j=4)
                                          ).then_inc(copied, 1)


def stage_masked(nc, core, lhs, rhs, dst, weight=None, strict=False):
    with ExitStack() as ctx:
        s = core.scope(nc, ctx, "masked")
        acc = s.ps("acc", [P, 2, 2, 512])
        mask = s.sb("mask", [C64, C64])
        product, copied, made = s.sem("product"), s.sem("copied"), s.sem("made")
        with nc.Block() as block:
            @block.gpsimd
            def _(pool):
                if weight is None:
                    nc.gpsimd.memset(mask[:], 1.0).then_inc(made, 1)
                    pool.wait_ge(made, 1)
                    nc.gpsimd.affine_select(out=mask[:], in_=mask[:], pattern=[[1, C64]], compare_op=ALU.is_ge,
                                            fill=0.0, base=-1 if strict else 0,
                                            channel_multiplier=-1).then_inc(made, 1)

            @block.tensor
            def _(pe):
                for n in range(NC64):
                    if n >= 2:
                        pe.wait_ge(copied, n - 1)
                    grams(nc, pe, acc[:, n % 2], lhs, rhs, n).then_inc(product, 1)

            @block.vector
            def _(dve):
                if weight is None:
                    dve.wait_ge(made, 2)
                for n in range(NC64):
                    dve.wait_ge(product, n + 1)
                    if weight is None:
                        by = mask[:].unsqueeze(1).broadcast_to([C64, 8, C64]).rearrange("p (q j) c -> p q j c", q=2)
                    else:
                        by = weight[:, n].rearrange("p (q j c) -> p q j c", q=2, j=4)
                    nc.vector.tensor_tensor(dst[:, n].rearrange("p (q j c) -> p q j c", q=2, j=4),
                                            acc[:C64, n % 2, :, :4 * C64].rearrange("p q (j c) -> p q j c", c=C64),
                                            by, ALU.mult).then_inc(copied, 1)


def unit(tile, n, q, j):
    at = (q * 4 + j) * C64
    return tile[:, n, at:at + C64]


def by_unit(dram3):
    return dram3.rearrange("(n u) s c -> s n u c", u=8)


def stage_gdn_scan(nc, core, y):
    with ExitStack() as ctx:
        s = core.scope(nc, ctx, "gscan")
        q, kbg, egc = (s.sb(n, [P, 4, T]) for n in ("q", "kbg", "egc"))
        kd_tok, vb_tok, attn, inv = (s.sb(n, [C64, NC64, UNIT]) for n in ("kd_tok", "vb_tok", "attn", "inv"))
        by_chunk = inv[:].rearrange("p n (u c) -> p n u c", c=C64)
        stage_to_tokens(nc, core, [("kd", kd_tok)], [
            (q[:], feat(core, "q")), (kbg[:], feat(core, "k")), (by_chunk, by_unit(core.dram["decay"])),
            (egc[:], feat(core, "egc"))])
        stage_masked(nc, core, kbg, q, attn, weight=inv)
        stage_to_tokens(nc, core, [("vb", vb_tok)], [
            (q[:], feat(core, "qg")), (kbg[:], feat(core, "kbg")),
            (by_chunk, by_unit(core.dram["inverse"][0:HN]))])
        s = core.scope(nc, ctx, "gchunks")
        state = s.sb("state", [P, 4, C64])
        r, vn = s.sb("r", [C64, UNIT]), s.sb("vn", [C64, UNIT])
        ks = s.ps("ks", [P, 2, 512])
        tr = s.ps("tr", [P, 512])
        os_ = s.ps("os", [P, 2, 512])
        ov = s.ps("ov", [P, 512])
        up = s.ps("up", [P, 512])
        (ks_ready, r_ready, tr_ready, vn_ready, os_ready, ov_ready, up_ready, state_ready, o_copied,
         step) = (s.sem(x) for x in ("ks_ready", "r_ready", "tr_ready", "vn_ready", "os_ready",
                                     "ov_ready", "up_ready", "state_ready", "o_copied", "step"))
        with nc.Block() as block:
            @block.tensor
            def _(pe):
                for n in range(NC64):
                    at = slice(n * C64, (n + 1) * C64)
                    pe.wait_ge(state_ready, n + 1)
                    for h in range(8):
                        c, j = h // 4, h % 4
                        half = slice(64 * c, 64 * c + 64)
                        last = nc.tensor.matmul(ks[:C64, c, j * C64:(j + 1) * C64], kbg[half, j, at],
                                                state[half, j], start=True, stop=True)
                    last.then_inc(ks_ready, 1)
                    if n:
                        pe.wait_ge(o_copied, n)
                    for h in range(8):
                        c, j = h // 4, h % 4
                        half = slice(64 * c, 64 * c + 64)
                        last = nc.tensor.matmul(os_[half, c, j * C64:(j + 1) * C64], state[half, j],
                                                q[half, j, at], start=True, stop=True)
                    last.then_inc(os_ready, 1)
                    pe.wait_ge(r_ready, n + 1)
                    for h in range(8):
                        c, j = h // 4, h % 4
                        last = nc.tensor.matmul(tr[:C64, h * C64:(h + 1) * C64], unit(inv, n, c, j),
                                                r[:, h * C64:(h + 1) * C64], start=True, stop=True)
                    last.then_inc(tr_ready, 1)
                    pe.wait_ge(vn_ready, n + 1)
                    for h in range(8):
                        c, j = h // 4, h % 4
                        half = slice(64 * c, 64 * c + 64)
                        last = nc.tensor.matmul(up[half, j * C64:(j + 1) * C64], unit(kd_tok, n, c, j),
                                                vn[:, h * C64:(h + 1) * C64], start=True, stop=True)
                    last.then_inc(up_ready, 1)
                    for h in range(8):
                        c, j = h // 4, h % 4
                        half = slice(64 * c, 64 * c + 64)
                        last = nc.tensor.matmul(ov[half, j * C64:(j + 1) * C64], vn[:, h * C64:(h + 1) * C64],
                                                unit(attn, n, c, j), start=True, stop=True)
                    last.then_inc(ov_ready, 1)

            @block.scalar
            def _(act):
                for n in range(NC64):
                    act.wait_ge(tr_ready, n + 1)
                    if n:
                        act.wait_ge(ov_ready, n)
                    nc.scalar.activation(vn[:], tr[:C64, :], ACT.Copy).then_inc(vn_ready, 1)

            @block.vector
            def _(dve):
                done = Steps(dve, step)
                v = nc.vector
                v.memset(state[:], 0.0).then_inc(state_ready, 1)
                for n in range(NC64):
                    dve.wait_ge(ks_ready, n + 1)
                    v.tensor_tensor(r[:].rearrange("p (q c) -> p q c", q=2),
                                    vb_tok[:, n].rearrange("p (q c) -> p q c", q=2), ks[:C64, :, :4 * C64],
                                    ALU.subtract).then_inc(r_ready, 1)
                    dve.wait_ge(os_ready, n + 1)
                    last = egc[:, :, n * C64 + C64 - 1:(n + 1) * C64]
                    done(v.tensor_tensor(state[:], state[:], last.broadcast_to([P, 4, C64]), ALU.mult))
                    dve.wait_ge(up_ready, n + 1)
                    v.tensor_tensor(state[:], state[:], up[:, :4 * C64].rearrange("p (j c) -> p j c", j=4),
                                    ALU.add).then_inc(state_ready, 1)
                    dst = y[:, :, n * C64:(n + 1) * C64]
                    for c in range(2):
                        half = slice(64 * c, 64 * c + 64)
                        done.mark(v.tensor_copy(dst[half], os_[half, c, :4 * C64].rearrange(
                            "p (j c) -> p j c", j=4)))
                    done.wait()
                    dve.wait_ge(ov_ready, n + 1)
                    v.tensor_tensor(dst, dst, ov[:, :4 * C64].rearrange("p (j c) -> p j c", j=4),
                                    ALU.add).then_inc(o_copied, 1)


def stage_rwkv_scan(nc, core, y):
    with ExitStack() as ctx:
        s = core.scope(nc, ctx, "rscan")
        ra, rr = s.sb("ra", [P, 4, T]), s.sb("rr", [P, 4, T])
        decay = s.sb("decay", [P, 4, NC64])
        b_tok, k_tok, v_tok, rb, rk, akv = (
            s.sb(n, [C64, NC64, UNIT]) for n in ("b_tok", "k_tok", "v_tok", "rb", "rk", "akv"))
        inv = s.sb("inv", [C64, NC64, UNIT])
        with ExitStack() as inner:
            s1 = core.scope(nc, inner, "rmat")
            kb, end = s1.sb("kb", [P, 4, T]), s1.sb("end", [P, 4, T])
            again, product, copied = (s1.sem(x) for x in ("again", "product", "copied"))
            stage_to_tokens(nc, core, [("rv", v_tok)], [
                (ra[:], feat(core, "ra")), (kb[:], feat(core, "rk")), (rr[:], feat(core, "rr"))])
            stage_masked(nc, core, kb, ra, b_tok, strict=True)
            stage_masked(nc, core, kb, rr, rk)
            acc = s1.ps("acc", [P, 2, 512])
            with nc.Block() as block:
                @block.sync
                def _(sp):
                    sp.dma_start(kb[:], feat(core, "rb")).then_inc(again, 16)
                    sp.dma_start(end[:], feat(core, "re")).then_inc(again, 16)
                    sp.wait_ge(again, 32)

                @block.tensor
                def _(pe):
                    for n in range(NC64):
                        if n >= 2:
                            pe.wait_ge(copied, n - 1)
                        for h in range(8):
                            at = slice(h * C64, (h + 1) * C64)
                            last = nc.tensor.matmul(acc[:C64, n % 2, at], b_tok[:, n, at], v_tok[:, n, at],
                                                    start=True, stop=True)
                        last.then_inc(product, 1)

                @block.vector
                def _(dve):
                    for n in range(NC64):
                        dve.wait_ge(product, n + 1)
                        nc.vector.tensor_copy(akv[:, n], acc[:C64, n % 2]).then_inc(copied, 1)
            stage_masked(nc, core, kb, rr, rb)
            picked = s1.sem("picked")
            with nc.Block() as block:
                @block.vector
                def _(dve):
                    nc.vector.tensor_copy(decay[:], end[:].rearrange("p j (n c) -> p j n c", c=C64)[
                        :, :, :, C64 - 1]).then_inc(picked, 1)
        stage_to_tokens(nc, core, [("rb", b_tok), ("rk", k_tok)], [
            (inv[:].rearrange("p n (u c) -> p n u c", c=C64), by_unit(core.dram["inverse"][HN:2 * HN]))])
        s = core.scope(nc, ctx, "rchunks")
        state = s.sb("state", [P, 4, C64])
        r, sa = s.sb("r", [C64, UNIT]), s.sb("sa", [C64, UNIT])
        as_ = s.ps("as", [P, 2, 512])
        tr = s.ps("tr", [P, 512])
        ys = s.ps("ys", [P, 2, 512])
        yv = s.ps("yv", [P, 512])
        up = s.ps("up", [P, 512])
        (as_ready, r_ready, tr_ready, sa_ready, ys_ready, yv_ready, up_ready, state_ready, y_copied,
         step) = (s.sem(x) for x in ("as_ready", "r_ready", "tr_ready", "sa_ready", "ys_ready",
                                     "yv_ready", "up_ready", "state_ready", "y_copied", "step"))
        with nc.Block() as block:
            @block.tensor
            def _(pe):
                for n in range(NC64):
                    at = slice(n * C64, (n + 1) * C64)
                    pe.wait_ge(state_ready, n + 1)
                    for h in range(8):
                        c, j = h // 4, h % 4
                        half = slice(64 * c, 64 * c + 64)
                        last = nc.tensor.matmul(as_[:C64, c, j * C64:(j + 1) * C64], ra[half, j, at],
                                                state[half, j], start=True, stop=True)
                    last.then_inc(as_ready, 1)
                    if n:
                        pe.wait_ge(y_copied, n)
                    for h in range(8):
                        c, j = h // 4, h % 4
                        half = slice(64 * c, 64 * c + 64)
                        last = nc.tensor.matmul(ys[half, c, j * C64:(j + 1) * C64], state[half, j],
                                                rr[half, j, at], start=True, stop=True)
                    last.then_inc(ys_ready, 1)
                    pe.wait_ge(r_ready, n + 1)
                    for h in range(8):
                        c, j = h // 4, h % 4
                        last = nc.tensor.matmul(tr[:C64, h * C64:(h + 1) * C64], unit(inv, n, c, j),
                                                r[:, h * C64:(h + 1) * C64], start=True, stop=True)
                    last.then_inc(tr_ready, 1)
                    pe.wait_ge(sa_ready, n + 1)
                    for h in range(8):
                        c, j = h // 4, h % 4
                        half = slice(64 * c, 64 * c + 64)
                        to = up[half, j * C64:(j + 1) * C64]
                        nc.tensor.matmul(to, unit(b_tok, n, c, j), sa[:, h * C64:(h + 1) * C64], start=True,
                                         stop=False)
                        last = nc.tensor.matmul(to, unit(k_tok, n, c, j), unit(v_tok, n, c, j), start=False,
                                                stop=True)
                    last.then_inc(up_ready, 1)
                    for h in range(8):
                        c, j = h // 4, h % 4
                        half = slice(64 * c, 64 * c + 64)
                        to = yv[half, j * C64:(j + 1) * C64]
                        nc.tensor.matmul(to, sa[:, h * C64:(h + 1) * C64], unit(rb, n, c, j), start=True,
                                         stop=False)
                        last = nc.tensor.matmul(to, unit(v_tok, n, c, j), unit(rk, n, c, j), start=False,
                                                stop=True)
                    last.then_inc(yv_ready, 1)

            @block.scalar
            def _(act):
                for n in range(NC64):
                    act.wait_ge(tr_ready, n + 1)
                    if n:
                        act.wait_ge(yv_ready, n)
                    nc.scalar.activation(sa[:], tr[:C64, :], ACT.Copy).then_inc(sa_ready, 1)

            @block.vector
            def _(dve):
                done = Steps(dve, step)
                v = nc.vector
                v.memset(state[:], 0.0).then_inc(state_ready, 1)
                for n in range(NC64):
                    dve.wait_ge(as_ready, n + 1)
                    v.tensor_tensor(r[:].rearrange("p (q c) -> p q c", q=2),
                                    akv[:, n].rearrange("p (q c) -> p q c", q=2), as_[:C64, :, :4 * C64],
                                    ALU.add).then_inc(r_ready, 1)
                    dve.wait_ge(ys_ready, n + 1)
                    dve.wait_ge(up_ready, n + 1)
                    done(v.tensor_tensor(state[:], state[:], up[:, :4 * C64].rearrange("p (j c) -> p j c", j=4),
                                         ALU.add))
                    v.tensor_tensor(state[:], state[:], decay[:, :, n:n + 1].broadcast_to([P, 4, C64]),
                                    ALU.mult).then_inc(state_ready, 1)
                    dst = y[:, :, n * C64:(n + 1) * C64]
                    for c in range(2):
                        half = slice(64 * c, 64 * c + 64)
                        done.mark(v.tensor_copy(dst[half], ys[half, c, :4 * C64].rearrange(
                            "p (j c) -> p j c", j=4)))
                    done.wait()
                    dve.wait_ge(yv_ready, n + 1)
                    v.tensor_tensor(dst, dst, yv[:, :4 * C64].rearrange("p (j c) -> p j c", j=4),
                                    ALU.add).then_inc(y_copied, 1)


def stage_gdn_out(nc, core, y):
    with ExitStack() as ctx:
        s = core.scope(nc, ctx, "gout")
        rstd, zt = s.sb("rstd", [P, 4, T]), s.sb("zt", [P, 4, T])
        loaded, bent, step = s.sem("loaded"), s.sem("bent"), s.sem("step")
        stage_rstd(nc, core, y, rstd, 1, core.halves, 64, EPS)
        with nc.Block() as block:
            @block.sync
            def _(sp):
                sp.dma_start(zt[:], rows(core.dram["z"][Z2["z"]:Z2["z"] + 512])).then_inc(loaded, 16)

            @block.scalar
            def _(act):
                act.wait_ge(loaded, 16)
                nc.scalar.activation(zt[:], zt[:], ACT.Silu).then_inc(bent, 1)

            @block.vector
            def _(dve):
                done = Steps(dve, step)
                done(nc.vector.scalar_tensor_tensor(out=y[:], in0=y[:], scalar=core.v("onorm_gdn"), in1=rstd[:],
                                                    op0=ALU.mult, op1=ALU.mult))
                dve.wait_ge(bent, 1)
                done(nc.vector.tensor_tensor(y[:], y[:], zt[:], ALU.mult))


def stage_rwkv_out(nc, core, y):
    with ExitStack() as ctx:
        s = core.scope(nc, ctx, "rout")
        rstd, bonus, g = (s.sb(n, [P, 4, T]) for n in ("rstd", "bonus", "g"))
        loaded, step = s.sem("loaded"), s.sem("step")
        stage_centre(nc, core, y, 1, core.halves, 64)
        stage_rstd(nc, core, y, rstd, 1, core.halves, 64, 64e-5)
        with nc.Block() as block:
            @block.sync
            def _(sp):
                sp.dma_start(bonus[:], feat(core, "bonus")).then_inc(loaded, 16)
                sp.dma_start(g[:], feat(core, "rg")).then_inc(loaded, 16)

            @block.vector
            def _(dve):
                done = Steps(dve, step)
                v = nc.vector
                for j in range(4):
                    done.mark(v.scalar_tensor_tensor(out=y[:, j], in0=y[:, j], scalar=core.v("lnx_w", j),
                                                     in1=rstd[:, j], op0=ALU.mult, op1=ALU.mult))
                done.wait()
                dve.wait_ge(loaded, 32)
                for j in range(4):
                    done.mark(v.scalar_tensor_tensor(out=y[:, j], in0=y[:, j], scalar=core.v("lnx_b", j),
                                                     in1=bonus[:, j], op0=ALU.add, op1=ALU.add))
                done.wait()
                done(v.tensor_tensor(y[:], y[:], g[:], ALU.mult))


def second_block(nc, core):
    dram = core.dram
    z, gates = dram["z"], dram["gates"]
    shift1, scale1, gate1, shift2, scale2, gate2 = (core.mod[:, 0, 8 * n:8 * n + 8] for n in range(6))
    with ExitStack() as ctx:
        s = core.scope(nc, ctx, "delta")
        h = split_tiles(s, "h", [P, DT, T])
        decay, beta = s.sb("decay", [P, C64, C64]), s.sb("beta", [HN, C64])
        decay_t = decay[:HN]
        stage_norm(nc, core, core.x, "norm1_w_2", (scale1, shift1), parts=h)
        stage_rows(nc, core, [(dram["w_in_2a"], z[0:2048], ACT.Copy), (dram["w_in_2b"], z[2048:3584], ACT.Copy)],
                   h, tails=[(dram["w_in_2t0"], z[3584:3600], h), (dram["w_in_2t1"], z[3600:3728], h),
                             (dram["w_in_2t2"], z[3728:3856], h), (dram["w_in_2t3"], z[3856:3888], h)])
        stage_gdn_gates(nc, core, decay_t, beta)
        stage_gdn_prepare(nc, core, decay_t, beta)
        stage_rwkv_prepare(nc, core)
        h_ctx = split_tiles(core.scope(nc, ctx, "ctx_h"), "h", [P, DT, CTX])
        with ExitStack() as source:
            ctx_x = core.scope(nc, source, "ctx_x").sb("x", [P, DT, CTX])
            stage_load(nc, core, [(ctx_x[:], rows(dram["ctxT"]))])
            stage_norm(nc, core, ctx_x, "norm1_w_3", (core.mod[:, 2, 8:16], core.mod[:, 2, 0:8]), toks=CTX,
                       parts=h_ctx)
        zc = dram["zc"]
        stage_rows(nc, core, [(dram["w_in_2g"], gates[0:2048], ACT.Sigmoid),
                              (dram["w3_qk"][2:4], zc[0:512], ACT.Copy, h_ctx),
                              (dram["w3_xbc"][0:10], zc[512:3072], ACT.Copy, h_ctx)], h,
                   tails=[(dram["w3_lr"], zc[3072:3104], h_ctx), (dram["w3_dt"], zc[3104:3168], h_ctx)],
                   beside=Inverse(nc, core, decay, beta))
        with ExitStack() as context:
            s2 = core.scope(nc, context, "v_ctx")
            v_ctx, stored = s2.sb("v", [P, 2, D]), s2.sem("stored")
            stage_tokens(nc, core, dram["w3_v"], [(h_ctx, v_ctx)])
            with nc.Block() as block:
                @block.sync
                def _(sp):
                    sp.dma_start(dram["v_ctx"], v_ctx[:]).then_inc(stored, 16)
                    sp.wait_ge(stored, 16)
    with ExitStack() as ctx:
        s = core.scope(nc, ctx, "second")
        merged, y = s.sb("merged", [P, DT, T]), s.sb("y", [P, 4, T])
        stage_gdn_scan(nc, core, y)
        stage_gdn_out(nc, core, y)
        stage_project(nc, core, dram["w_branch_gdn_2"], 4, merged, y, gates=gates[0:D], first=True)
        stage_rwkv_scan(nc, core, y)
        stage_rwkv_out(nc, core, y)
        stage_project(nc, core, dram["w_branch_rwkv_2"], 4, merged, y, gates=gates[D:2 * D])
        stage_project(nc, core, dram["w_out_2"], DT, core.x, merged, scale=gate1)
    stage_ffn(nc, core, "norm2_w_2", dram["ffn_up_2"], dram["ffn_down_2"], (scale2, shift2),
              conv=core.v("conv_ffn_2", 0, 3 * FT), scale=gate2)
    stage_norm(nc, core, core.x, "norm_f_w_2", dst=core.x)


Z3 = {"q": 0, "k": 512, "r": 1024, "z": 2048, "xbc": 4096, "lr": 7168, "dt": 7200}
ZC = {"k": 0, "xb": 512, "lr": 3072, "dt": 3104}
RANK = 16
GLA_LEVELS = 7
SSM_TILES = 16
SH = 32


def stage_log_gates(nc, core, lr, names, toks, chunk, b):
    with ExitStack() as ctx:
        s = core.scope(nc, ctx, "lgate")
        low = s.sb("low", [RANK, 2, toks])
        up = s.sb("up", [RANK, 2, 512])
        pre, e = s.sb("pre", [P, 4, toks]), s.sb("e", [P, 4, toks])
        reset = s.sb("reset", [P, 2, toks])
        acc = s.ps("acc", [P, 2, 4, 512])
        loaded, product, step, negated, logged, folded, acted = (
            s.sem(x) for x in ("loaded", "product", "step", "negated", "logged", "folded", "acted"))
        with nc.Block() as block:
            @block.sync
            def _(sp):
                for d in range(2):
                    sp.dma_start(low[:, d], lr[RANK * d:RANK * (d + 1)]).then_inc(loaded, 16)
                    sp.dma_start(up[:, d], core.dram[names[d]]).then_inc(loaded, 16)

            @block.tensor
            def _(pe):
                pe.wait_ge(loaded, 64)
                for d in range(2):
                    for j in range(4):
                        last = nc.tensor.matmul(acc[:, d, j, :toks], up[:, d, j * P:(j + 1) * P], low[:, d],
                                                start=True, stop=True)
                    last.then_inc(product, 1)

            @block.scalar
            def _(act):
                for d in range(2):
                    act.wait_ge(negated, d + 1)
                    nc.scalar.activation(e[:], e[:], ACT.Exp).then_inc(acted, 1)
                    act.wait_ge(acted, 2 * d + 1)
                    nc.scalar.activation(e[:], e[:], ACT.Ln, bias=1.0).then_inc(acted, 1)

            @block.vector
            def _(dve):
                done = Steps(dve, step)
                v = nc.vector
                edge = reset[:].rearrange("p d (n c) -> p d n c", c=chunk)
                done(v.memset(reset[:], 1.0))
                done.mark(v.memset(edge[:, 0, :, 0:1], 0.0))
                done(v.memset(edge[:, 1, :, chunk - 1:chunk], 0.0))
                for d in range(2):
                    dve.wait_ge(product, d + 1)
                    for j in range(4):
                        done.mark(v.tensor_scalar(pre[:, j], acc[:, d, j, :toks],
                                                  core.v(("gla_bias_f", "gla_bias_b")[d], j), None, ALU.add))
                    done.wait()
                    v.scalar_tensor_tensor(out=e[:], in0=pre[:], scalar=-1.0, in1=pre[:], op0=ALU.mult,
                                           op1=ALU.min).then_inc(negated, 1)
                    dve.wait_ge(acted, 2 * d + 2)
                    dve.wait_ge(negated, d + 1)
                    done(v.scalar_tensor_tensor(out=pre[:], in0=pre[:], scalar=0.0, in1=e[:], op0=ALU.min,
                                                op1=ALU.subtract))
                    done(v.tensor_scalar(pre[:], pre[:], 1.0 / 16, None, ALU.mult))
                    for j in range(4):
                        way = slice(None, None, -1) if d else slice(None)
                        done.mark(v.tensor_tensor_scan(b[:, d, j][:, way], reset[:, d][:, way], pre[:, j][:, way],
                                                       0.0, ALU.mult, ALU.add))
                    done.wait()


def stage_gla_context(nc, core, start):
    with ExitStack() as ctx:
        s = core.scope(nc, ctx, "gctx")
        b = s.sb("b", [P, 2, 4, CTX])
        stage_log_gates(nc, core, core.dram["zc"][ZC["lr"]:ZC["lr"] + 32], ("gla_up_f", "gla_up_b"), CTX, CTX, b)
        k, v_ctx = s.sb("k", [P, 4, CTX]), s.sb("v", [P, 2, D])
        k_tok = s.sb("k_tok", [P, 2, 2, 512])
        turned = s.ps("turned", [P, 2, 2, 512])
        acc = s.ps("acc", [P, 4, 512])
        loaded, diff, exped, weighted, turned_ready, copied, product, step, freed = (
            s.sem(x) for x in ("loaded", "diff", "exped", "weighted", "turned_ready", "copied", "product", "step",
                               "freed"))
        with nc.Block() as block:
            @block.sync
            def _(sp):
                sp.dma_start(k[:], rows(core.dram["zc"][ZC["k"]:ZC["k"] + 512])).then_inc(loaded, 16)
                sp.dma_start(v_ctx[:], core.dram["v_ctx"]).then_inc(loaded, 16)

            @block.vector
            def _(dve):
                v = nc.vector
                for d in range(2):
                    at = 0 if d else CTX - 1
                    last = s.sb(f"last{d}", [P, 4, 1])
                    v.tensor_copy(last[:], b[:, d, :, at:at + 1]).then_inc(step, 1)
                    dve.wait_ge(step, d + 1)
                    v.tensor_tensor(b[:, d], last[:].broadcast_to([P, 4, CTX]), b[:, d],
                                    ALU.subtract).then_inc(diff, 1)
                dve.wait_ge(loaded, 32)
                for d in range(2):
                    dve.wait_ge(exped, d + 1)
                    v.tensor_tensor(b[:, d], b[:, d], k[:], ALU.mult).then_inc(weighted, 1)
                for d in range(2):
                    dve.wait_ge(turned_ready, d + 1)
                    v.tensor_copy(k_tok[:, d], turned[:, d]).then_inc(copied, 1)
                for n in range(8):
                    d, h = n // 4, n % 4
                    dve.wait_ge(product, n + 1)
                    v.tensor_copy(start[:, d, h], acc[:, n % 4, :256]).then_inc(freed, 1)

            @block.scalar
            def _(act):
                for d in range(2):
                    act.wait_ge(diff, d + 1)
                    nc.scalar.activation(b[:, d], b[:, d], ACT.Exp).then_inc(exped, 1)

            @block.tensor
            def _(pe):
                for d in range(2):
                    pe.wait_ge(weighted, d + 1)
                    for t in range(2):
                        for h in range(4):
                            last = nc.tensor.transpose(turned[:, d, t, h * P:(h + 1) * P],
                                                       b[:, d, h, t * P:(t + 1) * P], core.ident[:])
                    last.then_inc(turned_ready, 1)
                for n in range(8):
                    d, h = n // 4, n % 4
                    pe.wait_ge(copied, d + 1)
                    if n >= 4:
                        pe.wait_ge(freed, n - 3)
                    for t in range(2):
                        last = nc.tensor.matmul(acc[:, n % 4, :256], k_tok[:, d, t, h * P:(h + 1) * P],
                                                v_ctx[:, t, h * 256:(h + 1) * 256], start=t == 0, stop=t == 1)
                    last.then_inc(product, 1)


def stage_gla_levels(nc, core, q, k, b, attn):
    with ExitStack() as ctx:
        s = core.scope(nc, ctx, "levels")
        x = s.sb("x", [P, 3, 4, T])
        masks = s.sb("masks", [P, 2 * GLA_LEVELS + 1, P], I32)
        acc = s.ps("acc", [P, 2, 4, 512])
        loaded, diffed, exped, weighted, product, taken, cleared, doubled = (
            s.sem(n) for n in ("loaded", "diffed", "exped", "weighted", "product", "taken", "cleared", "doubled"))
        rounds = [(d, n) for d in range(2) for n in range(GLA_LEVELS)]

        def sides(n, tile):
            w = 2 << n
            both = tile.rearrange("p h (m w) -> p (h m) w", w=w)
            return both[:, :, :w // 2], both[:, :, w // 2:]

        with nc.Block() as block:
            @block.sync
            def _(sp):
                sp.dma_start(masks[:], core.dram["masks"]).then_inc(loaded, 16)

            @block.gpsimd
            def _(pool):
                for i, (d, n) in enumerate(rounds):
                    if i >= 3:
                        pool.wait_ge(product, i - 1)
                    left, right = sides(n, x[:, i % 3])
                    bl, br = sides(n, b[:, d])
                    half = 1 << n
                    mid = br[:, :, 0:1] if d else bl[:, :, half - 1:half]
                    mid = mid.broadcast_to(list(bl.shape))
                    if d:
                        nc.gpsimd.tensor_tensor(left, bl, mid, ALU.subtract).then_inc(diffed, 1)
                        nc.gpsimd.tensor_tensor(right, mid, br, ALU.subtract).then_inc(diffed, 1)
                    else:
                        nc.gpsimd.tensor_tensor(left, mid, bl, ALU.subtract).then_inc(diffed, 1)
                        nc.gpsimd.tensor_tensor(right, br, mid, ALU.subtract).then_inc(diffed, 1)

            @block.scalar
            def _(act):
                for i in range(len(rounds)):
                    act.wait_ge(diffed, 2 * i + 2)
                    nc.scalar.activation(x[:, i % 3], x[:, i % 3], ACT.Exp).then_inc(exped, 1)

            @block.vector
            def _(dve):
                v = nc.vector

                def take(i):
                    for h in range(4):
                        dve.wait_ge(product, i + 1)
                        by = masks[:, i:i + 1].broadcast_to([P, 4, P])
                        src = acc[:, (i + 1) % 2, h].rearrange("p (c t) -> p c t", t=P)
                        if i == 0:
                            v.tensor_copy(attn[:, h], src).then_inc(cleared, 1)
                            dve.wait_ge(cleared, h + 1)
                            v.tensor_tensor(attn[:, h], attn[:, h], src, ALU.add).then_inc(taken, 1)
                        else:
                            v.copy_predicated(attn[:, h], by, src).then_inc(taken, 1)
                    dve.wait_ge(taken, 4 * i + 4)

                dve.wait_ge(loaded, 16)
                for i, (d, n) in enumerate(rounds):
                    dve.wait_ge(exped, i + 1)
                    left, right = sides(n, x[:, i % 3])
                    kl, kr = sides(n, k[:])
                    ql, qr = sides(n, q[:])
                    v.tensor_tensor(left, left, ql if d else kl, ALU.mult).then_inc(weighted, 1)
                    v.tensor_tensor(right, right, kr if d else qr, ALU.mult).then_inc(weighted, 1)
                    take(i)
                take(len(rounds))

            @block.tensor
            def _(pe):
                def products(i, lhs, rhs):
                    if i >= 2:
                        pe.wait_ge(taken, 4 * (i - 1))
                    for h in range(4):
                        for c in range(4):
                            at = slice(c * P, (c + 1) * P)
                            last = nc.tensor.matmul(acc[:, (i + 1) % 2, h, at], lhs[:, h, at], rhs[:, h, at],
                                                    start=True, stop=True)
                    last.then_inc(product, 1)

                products(0, k, q)
                for i in range(len(rounds)):
                    pe.wait_ge(weighted, 2 * i + 2)
                    products(i + 1, x[:, i % 3], x[:, i % 3])


def stage_gla_states(nc, core, q, k, b, v_tok, start, states):
    with ExitStack() as ctx:
        s = core.scope(nc, ctx, "gstate")
        kd = s.sb("kd", [P, 2, 4, T])
        edge = s.sb("edge", [P, 2, 4, 4])
        k_tok = s.sb("k_tok", [P, 2, 4, 512])
        turned = s.ps("turned", [P, 2, 512])
        acc = s.ps("acc", [P, 4, 512])
        (picked, diffed, exped, weighted, turned_ready, copied, product, advanced, scaled, step) = (
            s.sem(n) for n in ("picked", "diffed", "exped", "weighted", "turned_ready", "copied", "product",
                               "advanced", "scaled", "step"))
        with nc.Block() as block:
            @block.vector
            def _(dve):
                v = nc.vector
                for d in range(2):
                    at = 0 if d else P - 1
                    view = b[:, d].rearrange("p h (c t) -> p h c t", t=P)
                    v.tensor_copy(edge[:, d], view[:, :, :, at]).then_inc(picked, 1)
                    dve.wait_ge(picked, d + 1)
                    to = kd[:, d].rearrange("p h (c t) -> p h c t", t=P)
                    for h in range(4):
                        v.tensor_tensor(to[:, h], edge[:, d, h].unsqueeze(2).broadcast_to([P, 4, P]), view[:, h],
                                        ALU.subtract).then_inc(diffed, 1)
                for d in range(2):
                    dve.wait_ge(exped, 3 * d + 2)
                    v.tensor_tensor(kd[:, d], kd[:, d], k[:], ALU.mult).then_inc(weighted, 1)
                    dve.wait_ge(exped, 3 * d + 3)
                    v.tensor_tensor(b[:, d], b[:, d], q[:], ALU.mult).then_inc(scaled, 1)
                for n in range(8):
                    d, c = n // 4, n % 4
                    dve.wait_ge(turned_ready, n + 1)
                    v.tensor_copy(k_tok[:, d, c], turned[:, n % 2]).then_inc(copied, 1)
                v.tensor_copy(states[:, 0, :, 0], start[:, 0]).then_inc(step, 1)
                v.tensor_copy(states[:, 1, :, 3], start[:, 1]).then_inc(step, 1)
                dve.wait_ge(step, 2)
                for n in range(24):
                    i, d, h = n // 8, n // 4 % 2, n % 4
                    now, nxt = (3 - i, 2 - i) if d else (i, i + 1)
                    dve.wait_ge(product, n + 1)
                    if n >= 8:
                        dve.wait_ge(advanced, n - 7)
                    v.scalar_tensor_tensor(out=states[:, d, h, nxt], in0=states[:, d, h, now],
                                           scalar=edge[:, d, h, now:now + 1], in1=acc[:, n % 4, :256],
                                           op0=ALU.mult, op1=ALU.add).then_inc(advanced, 1)

            @block.scalar
            def _(act):
                for d in range(2):
                    act.wait_ge(diffed, 4 * d + 4)
                    nc.scalar.activation(edge[:, d], edge[:, d], ACT.Exp).then_inc(exped, 1)
                    nc.scalar.activation(kd[:, d], kd[:, d], ACT.Exp).then_inc(exped, 1)
                    nc.scalar.activation(b[:, d], b[:, d], ACT.Exp).then_inc(exped, 1)

            @block.tensor
            def _(pe):
                for n in range(8):
                    d, c = n // 4, n % 4
                    pe.wait_ge(weighted, d + 1)
                    if n >= 2:
                        pe.wait_ge(copied, n - 1)
                    for h in range(4):
                        last = nc.tensor.transpose(turned[:, n % 2, h * P:(h + 1) * P],
                                                   kd[:, d, h, c * P:(c + 1) * P], core.ident[:])
                    last.then_inc(turned_ready, 1)
                pe.wait_ge(copied, 8)
                for n in range(24):
                    i, d, h = n // 8, n // 4 % 2, n % 4
                    c = 3 - i if d else i
                    if n >= 4:
                        pe.wait_ge(advanced, n - 3)
                    nc.tensor.matmul(acc[:, n % 4, :256], k_tok[:, d, c, h * P:(h + 1) * P],
                                     v_tok[:, c, h * 256:(h + 1) * 256], start=True, stop=True
                                     ).then_inc(product, 1)


def stage_gla_out(nc, core, b, v_tok, states, attn, y):
    with ExitStack() as ctx:
        s = core.scope(nc, ctx, "glaout")
        r, loaded = s.sb("r", [P, 8, T]), s.sem("loaded")
        with ExitStack() as inner:
            s1 = core.scope(nc, inner, "mix")
            acc = s1.ps("acc", [P, 8, 512])
            product, copied = s1.sem("product"), s1.sem("copied")
            with nc.Block() as block:
                @block.sync
                def _(sp):
                    sp.dma_start(r[:], rows(core.dram["z"][Z3["r"]:Z3["r"] + 1024])).then_inc(loaded, 16)

                @block.tensor
                def _(pe):
                    for n in range(8):
                        h, e = n // 2, n % 2
                        to = slice(h * 256 + e * P, h * 256 + (e + 1) * P)
                        for c in range(4):
                            at = slice(c * P, (c + 1) * P)
                            nc.tensor.matmul(acc[:, n, at], v_tok[:, c, to], attn[:, h, c], start=True, stop=False)
                            for d in range(2):
                                last = nc.tensor.matmul(acc[:, n, at], states[:, d, h, c, e * P:(e + 1) * P],
                                                        b[:, d, h, at], start=False, stop=d == 1)
                        last.then_inc(product, 1)

                @block.vector
                def _(dve):
                    for n in range(8):
                        dve.wait_ge(product, n + 1)
                        nc.vector.tensor_copy(y[:, n], acc[:, n]).then_inc(copied, 1)
        rstd = s.sb("rstd", [P, 4, T])
        stage_rstd(nc, core, y, rstd, 2, core.ones, 256, EPS)
        step = s.sem("step")
        with nc.Block() as block:
            @block.vector
            def _(dve):
                done = Steps(dve, step)
                for n in range(8):
                    done.mark(nc.vector.scalar_tensor_tensor(out=y[:, n], in0=y[:, n],
                                                             scalar=core.v("gla_norm_w", n % 2),
                                                             in1=rstd[:, n // 2], op0=ALU.mult, op1=ALU.mult))
                done.wait()
                dve.wait_ge(loaded, 16)
                done(nc.vector.tensor_tensor(y[:], y[:], r[:], ALU.mult))


def stage_load(nc, core, pairs, start=(), started=None, earlier=None):
    with ExitStack() as ctx:
        s = core.scope(nc, ctx, "load")
        loaded = s.sem("loaded")
        with nc.Block() as block:
            @block.sync
            def _(sp):
                for dst, src in pairs:
                    sp.dma_start(dst, src).then_inc(loaded, 16)
                for dst, src in start:
                    sp.dma_start(dst, src).then_inc(started, 16)
                if pairs:
                    sp.wait_ge(loaded, 16 * len(pairs))
                if earlier is not None:
                    sp.wait_ge(earlier[0], 16 * earlier[1])


def stage_gla(nc, core, v_tok, y):
    with ExitStack() as ctx:
        s = core.scope(nc, ctx, "gla")
        b = s.sb("b", [P, 2, 4, T])
        start = s.sb("start", [P, 2, 4, 256])
        states = s.sb("states", [P, 2, 4, 4, 256])
        attn = s.sb("attn", [P, 4, 4, P])
        z = core.dram["z"]
        q, k, qk_loaded = s.sb("q", [P, 4, T]), s.sb("k", [P, 4, T]), s.sem("qk_loaded")
        stage_load(nc, core, [], start=[(q[:], rows(z[0:512])), (k[:], rows(z[512:1024]))], started=qk_loaded)
        stage_gla_context(nc, core, start)
        stage_log_gates(nc, core, z[Z3["lr"]:Z3["lr"] + 32], ("gla_up_f", "gla_up_b"), T, P, b)
        stage_load(nc, core, [], earlier=(qk_loaded, 2))
        scaled = s.sem("scaled")
        with nc.Block() as block:
            @block.vector
            def _(dve):
                nc.vector.tensor_scalar(q[:], q[:], float(P) ** -0.5, None, ALU.mult).then_inc(scaled, 1)
        stage_gla_levels(nc, core, q, k, b, attn)
        stage_gla_states(nc, core, q, k, b, v_tok, start, states)
        stage_gla_out(nc, core, b, v_tok, states, attn, y)


class CentredConvs(Beside):

    def __init__(self, nc, core):
        self.nc, self.core = nc, core
        dram = core.dram
        self.parts = [
            dict(src=dram["z"][Z3["xbc"]:Z3["xbc"] + 3072], dst=dram["xbc"], toks=T, width=64, slots=(2, 2)),
            dict(src=dram["zc"][ZC["xb"]:ZC["xb"] + 2560], dst=dram["xc"], toks=CTX, width=CTX, slots=(3, 2))]
        tiles = [part["src"].shape[0] // P for part in self.parts]
        self.turns = [n // sum(part["slots"]) for n, part in zip(tiles, self.parts)]

    def open(self, s):
        self.raw, self.out = s.sb("conv_raw", [P, 2, 2 * T]), s.sb("conv_out", [P, 2, 2 * T])
        self.loaded, self.stepped, self.bent, self.stored = (
            [s.sem(f"conv_{n}{k}") for k in range(2)] for n in ("loaded", "stepped", "bent", "stored"))

    def at(self, n, i, k):
        slots = self.parts[n]["slots"]
        before = sum(self.turns[:n])
        steps = sum(4 * self.parts[m]["slots"][k] * self.turns[m] for m in range(n))
        return slots[k], i * sum(slots) + k * slots[0], i + before, i * (4 * slots[k]) + steps

    def view(self, buf, n, k):
        toks, many = self.parts[n]["toks"], self.parts[n]["slots"][k]
        return buf[:, k, :many * toks].rearrange("p (j t) -> p j t", t=toks)

    def sync_turn(self, sp, n, i, k):
        many, tile, turn, steps = self.at(n, i, k)
        free_after(sp, self.stepped[k], steps)
        sp.dma_start(self.view(self.raw, n, k), rows(self.parts[n]["src"][bass.ds(tile * P, many * P), :])
                     ).then_inc(self.loaded[k], 16)

    def scalar_turn(self, act, n, i, k):
        many, tile, turn, steps = self.at(n, i, k)
        out = self.view(self.out, n, k)
        act.wait_ge(self.stepped[k], steps + 4 * many)
        self.nc.scalar.activation(out, out, ACT.Silu).then_inc(self.bent[k], 1)
        act.wait_ge(self.bent[k], turn + 1)
        act.dma_start(rows(self.parts[n]["dst"][bass.ds(tile * P, many * P), :]), out
                      ).then_inc(self.stored[k], 16)

    def scalar_last(self, act):
        for k in range(2):
            act.wait_ge(self.stored[k], 16 * sum(self.turns))

    def vector_segment(self, dve, n, turns):
        v, width = self.nc.vector, self.parts[n]["width"]

        def column(name, per, tile, j, tap=0):
            at = self.core.vec_at[name] + per * j + tap
            return self.core.vec[:, bass.ds(tile * per + at, 1)]

        def turn_(i):
            for k in range(2):
                many, tile, turn, steps = self.at(n, i, k)
                raw, out = self.view(self.raw, n, k), self.view(self.out, n, k)
                dve.wait_ge(self.loaded[k], turn * 16 + 16)
                free_after(dve, self.stored[k], turn * 16)
                for j in range(many):
                    v.tensor_scalar(out[:, j], raw[:, j], column("conv_w_3", 4, tile, j, 2),
                                    column("conv_b_3", 1, tile, j), ALU.mult, ALU.add
                                    ).then_inc(self.stepped[k], 1)
                for r, (tap, lag) in enumerate(((0, 2), (1, 1), (3, -1))):
                    for j in range(many):
                        dve.wait_ge(self.stepped[k], steps + (many * r + j + 1))
                        a = raw[:, j].rearrange("p (r w) -> p r w", w=width)
                        o = out[:, j].rearrange("p (r w) -> p r w", w=width)
                        if lag > 0:
                            a, o = a[:, :, :width - lag], o[:, :, lag:]
                        else:
                            a, o = a[:, :, 1:], o[:, :, :width - 1]
                        v.scalar_tensor_tensor(out=o, in0=a, scalar=column("conv_w_3", 4, tile, j, tap), in1=o,
                                               op0=ALU.mult, op1=ALU.add).then_inc(self.stepped[k], 1)
        span(dve, turns, turn_)


def stage_steps(nc, core, src, toks, chunk, dt_tok, cum_tok, cum_dram=None, edge_dram=None, start=(),
                started=None):
    n = toks // P
    with ExitStack() as ctx:
        s = core.scope(nc, ctx, "steps")
        dt, cum = s.sb("dt", [64, toks]), s.sb("cum", [64, toks])
        reset = s.sb("reset", [64, toks])
        rate = s.sb("rate", [64, 1])
        edges = s.sb("edges", [64, toks // chunk])
        acc = s.ps("acc", [P, 2, 512])
        rated, biased, step, summed, turned, copied, stored = (
            s.sem(x) for x in ("rated", "biased", "step", "summed", "turned", "copied", "stored"))
        stage_load(nc, core, [(dt[:], src)], start, started)
        with nc.Block() as block:
            @block.vector
            def _(dve):
                nc.vector.tensor_scalar(dt[:], dt[:], core.v("dt_bias_3")[:64], None, ALU.add).then_inc(biased, 1)
        stage_softplus(nc, core, dt, 64, toks)
        with nc.Block() as block:
            @block.scalar
            def _(act):
                nc.scalar.activation(rate[:], core.v("a_log_3")[:64], ACT.Exp).then_inc(rated, 1)

            @block.vector
            def _(dve):
                done = Steps(dve, step)
                v = nc.vector
                edge = reset[:].rearrange("p (n c) -> p n c", c=chunk)
                view = cum[:].rearrange("p (n c) -> p n c", c=chunk)
                done(v.memset(reset[:], 1.0))
                done.mark(v.memset(edge[:32, :, 0:1], 0.0))
                done.mark(v.memset(edge[32:64, :, chunk - 1:chunk], 0.0))
                dve.wait_ge(rated, 1)
                work = s.sb("work", [64, toks])
                done(v.tensor_scalar(work[:], dt[:], rate[:], -1.0, ALU.mult, ALU.mult))
                v.tensor_tensor_scan(cum[:32], reset[:32], work[:32], 0.0, ALU.mult, ALU.add).then_inc(summed, 1)
                v.tensor_tensor_scan(cum[32:64, ::-1], reset[32:64, ::-1], work[32:64, ::-1], 0.0, ALU.mult,
                                     ALU.add).then_inc(summed, 1)
                dve.wait_ge(summed, 2)
                v.tensor_copy(edges[:32], view[:32, :, chunk - 1]).then_inc(summed, 1)
                v.tensor_copy(edges[32:64], view[32:64, :, 0]).then_inc(summed, 1)
                dve.wait_ge(turned, 1)
                v.tensor_copy(dt_tok[:], acc[:, 0, :64 * n].rearrange("p (c h) -> p c h", h=64)
                              ).then_inc(copied, 1)
                v.tensor_copy(cum_tok[:], acc[:, 1, :64 * n].rearrange("p (c h) -> p c h", h=64)
                              ).then_inc(copied, 1)

            @block.tensor
            def _(pe):
                pe.wait_ge(summed, 2)
                for a, tile in enumerate((dt, cum)):
                    for c in range(n):
                        last = nc.tensor.transpose(acc[:, a, c * 64:(c + 1) * 64], tile[:, c * P:(c + 1) * P],
                                                   core.ident[:64, :64])
                last.then_inc(turned, 1)

            @block.sync
            def _(sp):
                sp.wait_ge(summed, 4)
                sp.dma_start(edge_dram, edges[:]).then_inc(stored, 16)
                if cum_dram is not None:
                    sp.dma_start(cum_dram, cum[:]).then_inc(stored, 16)
                sp.wait_ge(stored, 32 if cum_dram is not None else 16)


def spread(dram2, parts=P):
    shape = list(dram2.shape)
    return dram2.unsqueeze(0).broadcast_to([parts] + shape)


def stage_ssm_context(nc, core):
    dram = core.dram
    with ExitStack() as ctx:
        s = core.scope(nc, ctx, "sctx")
        dt_tok, cum_tok = s.sb("dt_tok", [P, 2, 64]), s.sb("cum_tok", [P, 2, 64])
        total = s.sb("total", [P, 64])
        x, x_loaded = s.sb("x", [P, 4, 5, CTX]), s.sem("x_loaded")
        x_parts = ([(x[:, g, :4], rows(dram["xc"][512 * g:512 * (g + 1)])) for g in range(4)]
                   + [(x[:, g, 4], dram["xc"][2048 + P * g:2048 + P * (g + 1)]) for g in range(4)])
        stage_steps(nc, core, dram["zc"][ZC["dt"]:ZC["dt"] + 64], CTX, CTX, dt_tok, cum_tok,
                    edge_dram=dram["edge_c"], start=x_parts, started=x_loaded)
        w = s.sb("w", [P, 2, 64])
        x_tok = s.sb("x_tok", [P, 2, 2, 5 * P])
        xw = s.sb("xw", [P, 2, 2, 512])
        out = s.sb("out", [P, 2, 512])
        turned = s.ps("turned", [P, 2, 1024])
        acc = s.ps("acc", [P, 2, 512])
        (diffed, exped, ready, turned_ready, copied, weighted, product, saved) = (
            s.sem(n) for n in ("diffed", "exped", "ready", "turned_ready", "copied", "weighted", "product", "saved"))
        stored = s.sem("stored")
        stage_load(nc, core, [(total[:], spread(dram["edge_c"].rearrange("h a -> (h a)")))],
                   earlier=(x_loaded, len(x_parts)))
        with nc.Block() as block:
            @block.vector
            def _(dve):
                v = nc.vector
                v.tensor_tensor(w[:], total[:].unsqueeze(1).broadcast_to([P, 2, 64]), cum_tok[:],
                                ALU.subtract).then_inc(diffed, 1)
                dve.wait_ge(exped, 1)
                v.tensor_tensor(w[:], w[:], dt_tok[:], ALU.mult).then_inc(ready, 1)
                dve.wait_ge(ready, 1)
                for g in range(4):
                    for t in range(2):
                        n = 2 * g + t
                        dve.wait_ge(turned_ready, n + 1)
                        v.tensor_copy(x_tok[:, g % 2, t], turned[:, t, :5 * P]).then_inc(copied, 1)
                    dve.wait_ge(copied, 2 * g + 2)
                    for d in range(2):
                        if g or d:
                            dve.wait_ge(product, 2 * g + d - 1 if 2 * g + d > 1 else 1)
                        for t in range(2):
                            by = w[:, t, 32 * d + 8 * g:32 * d + 8 * g + 8].unsqueeze(2).broadcast_to([P, 8, 64])
                            v.tensor_tensor(xw[:, d, t].rearrange("p (h c) -> p h c", c=64),
                                            x_tok[:, g % 2, t, :512].rearrange("p (h c) -> p h c", c=64), by,
                                            ALU.mult).then_inc(weighted, 1)

            @block.scalar
            def _(act):
                act.wait_ge(diffed, 1)
                nc.scalar.activation(w[:], w[:], ACT.Exp).then_inc(exped, 1)
                for n in range(8):
                    act.wait_ge(product, n + 1)
                    if n >= 2:
                        act.wait_ge(stored, 16 * (n - 1))
                    nc.scalar.activation(out[:, n % 2], acc[:, n % 2], ACT.Copy).then_inc(saved, 1)
                    act.wait_ge(saved, n + 1)
                    if n:
                        act.wait_ge(stored, 16 * n)
                    act.dma_start(dram["s0"][n % 2, n // 2], out[:, n % 2]).then_inc(stored, 16)
                act.wait_ge(stored, 128)

            @block.tensor
            def _(pe):
                for g in range(4):
                    for t in range(2):
                        if g:
                            pe.wait_ge(copied, 2 * g + t - 1)
                        for j in range(5):
                            last = nc.tensor.transpose(turned[:, t, j * P:(j + 1) * P],
                                                       x[:, g, j, t * P:(t + 1) * P], core.ident[:])
                        last.then_inc(turned_ready, 1)
                    for d in range(2):
                        n = 2 * g + d
                        pe.wait_ge(weighted, 2 * n + 2)
                        if n >= 2:
                            pe.wait_ge(saved, n - 1)
                        for t in range(2):
                            last = nc.tensor.matmul(acc[:, d], x_tok[:, g % 2, t, 512:], xw[:, d, t],
                                                    start=t == 0, stop=t == 1)
                        last.then_inc(product, 1)


def load_ssm_group(core, sp, g, s, inputs_loaded):
    dram = core.dram
    bc_, states = s["bc"][:, g % 2], s["states"][:, g % 2]
    for dst, src in ((s["x"][:], rows(dram["xbc"][512 * g:512 * (g + 1)])),
                     (bc_[:, 0], dram["xbc"][2048 + P * g:2048 + P * (g + 1)]),
                     (bc_[:, 1], dram["xbc"][2560 + P * g:2560 + P * (g + 1)]),
                     (states[:, 0, 0], dram["s0"][0, g]), (states[:, 1, 3], dram["s0"][1, g])):
        sp.dma_start(dst, src).then_inc(inputs_loaded, 16)


def load_cum(core, sp, g, c, s, cum_loaded):
    for d in range(2):
        sp.dma_start(s["cum"][:, c % 2, d],
                     spread(core.dram["cum"][32 * d + 8 * g:32 * d + 8 * g + 8, c * P:(c + 1) * P])
                     ).then_inc(cum_loaded[c % 2], 16)


def ssm_difference(nc, pool, g, n, s, cum_tok, sems):
    c, d = n // 2, n % 2
    pool.wait_ge(sems["cum_loaded"][c % 2], 64 * g + 32 * (c // 2 + 1))
    by = cum_tok[:, c, 32 * d + 8 * g:32 * d + 8 * g + 8].unsqueeze(2).broadcast_to([P, 8, P])
    nc.gpsimd.tensor_tensor(s["seg"][:, n % 4], by, s["cum"][:, c % 2, d], ALU.subtract
                            ).then_inc(sems["diffed"], 1)


def ssm_decay(nc, act, g, n, s, sems):
    seg = s["seg"][:, n % 4]
    act.wait_ge(sems["diffed"], 8 * g + n + 1)
    nc.scalar.activation(seg, seg, ACT.Relu).then_inc(sems["clipped"], 1)
    act.wait_ge(sems["clipped"], 8 * g + n + 1)
    nc.scalar.activation(seg, seg, ACT.Exp, scale=-1.0).then_inc(sems["exped"], 1)


def stage_ssm_group(nc, core, g, s, dt_tok, cum_tok, ecum, edges, sems):
    dram = core.dram
    x, bc_ = s["x"], s["bc"][:, g % 2]
    x_tok, b_tok = s["x_tok"], s["b_tok"]
    xdt, xw, cb, y_tok, y, dts, cum = (s[n] for n in ("xdt", "xw", "cb", "y_tok", "y", "dts", "cum"))
    states = s["states"][:, g % 2]
    inputs_loaded, cum_loaded, seg = sems["inputs_loaded"], sems["cum_loaded"], s["seg"]
    with ExitStack() as ctx:
        o = core.scope(nc, ctx, "sprep")
        turned = o.ps("turned", [P, 2, 1024])
        gram = o.ps("gram", [P, 512])
        acc = o.ps("acc", [P, 2, 512])
        w = o.sb("w", [P, 2, 4, 8])
        heads = [slice(32 * d + 8 * g, 32 * d + 8 * g + 8) for d in range(2)]
        (turned_ready, copied, grammed, masked, diffed, exped, product, advanced, step,
         scaled) = (o.sem(n) for n in ("turned_ready", "copied", "grammed", "masked", "diffed", "exped",
                                       "product", "advanced", "step", "scaled"))
        weighted = [o.sem(f"weighted{d}") for d in range(2)]

        def by_head(eng, dst, src, by):
            return eng.tensor_tensor(dst.rearrange("p c (h k) -> p (c h) k", k=64),
                                     src.rearrange("p c (h k) -> p (c h) k", k=64),
                                     by.unsqueeze(2).broadcast_to([P, 32, 64]), ALU.mult)

        with nc.Block() as block:
            @block.sync
            def _(sp):
                if g == 0:
                    load_ssm_group(core, sp, g, s, inputs_loaded)
                for c in range(2):
                    load_cum(core, sp, g, c, s, cum_loaded)

            @block.tensor
            def _(pe):
                pe.wait_ge(inputs_loaded, 80 * (g + 1))
                for c in range(4):
                    at = slice(c * P, (c + 1) * P)
                    last = nc.tensor.matmul(gram[:, at], bc_[:, 0, at], bc_[:, 1, at], start=True, stop=True)
                last.then_inc(grammed, 1)
                for c in range(4):
                    at = slice(c * P, (c + 1) * P)
                    if c >= 2:
                        pe.wait_ge(copied, 2 * (c - 1))
                    for j in range(4):
                        nc.tensor.transpose(turned[:, c % 2, j * P:(j + 1) * P], x[:, j, at], core.ident[:])
                    nc.tensor.transpose(turned[:, c % 2, 512:640], bc_[:, 0, at],
                                        core.ident[:]).then_inc(turned_ready, 1)
                for n in range(6):
                    i, d = n // 2, n % 2
                    c = 3 - i if d else i
                    pe.wait_ge(weighted[d], 1)
                    if n >= 2:
                        pe.wait_ge(advanced, n - 1)
                    nc.tensor.matmul(acc[:, d], b_tok[:, c], xw[:, d, c], start=True, stop=True
                                     ).then_inc(product, 1)

            @block.scalar
            def _(act):
                for d in range(2):
                    act.wait_ge(diffed, d + 1)
                    nc.scalar.activation(w[:, d], w[:, d], ACT.Exp).then_inc(exped, 1)
                for n in range(4):
                    ssm_decay(nc, act, g, n, s, sems)

            @block.gpsimd
            def _(pool):
                pool.wait_ge(masked, 2)
                for d in range(2):
                    nc.gpsimd.affine_select(out=cb[:, d], in_=cb[:, d],
                                            pattern=[[0, 4], [-1, P] if d else [1, P]], compare_op=ALU.is_ge,
                                            fill=0.0, base=0, channel_multiplier=1 if d else -1
                                            ).then_inc(step, 1)
                pool.wait_ge(exped, 1)
                pool.wait_ge(scaled, 2)
                by_head(nc.gpsimd, xw[:, 0], xdt[:, 0], w[:, 0].rearrange("p c h -> p (c h)")
                        ).then_inc(weighted[0], 1)
                for n in range(4):
                    ssm_difference(nc, pool, g, n, s, cum_tok, sems)

            @block.vector
            def _(dve):
                v = nc.vector
                for d in range(2):
                    v.tensor_tensor(w[:, d], edges[:, heads[d], :].rearrange("p h c -> p c h"),
                                    cum_tok[:, :, heads[d]], ALU.subtract).then_inc(diffed, 1)
                dve.wait_ge(grammed, 1)
                for d in range(2):
                    v.tensor_copy(cb[:, d].rearrange("p c t -> p (c t)"), gram[:]).then_inc(masked, 1)
                for c in range(4):
                    dve.wait_ge(turned_ready, c + 1)
                    v.tensor_copy(x_tok[:, c], turned[:, c % 2, :512]).then_inc(copied, 1)
                    v.tensor_copy(b_tok[:, c], turned[:, c % 2, 512:640]).then_inc(copied, 1)
                dve.wait_ge(copied, 8)

                for d in range(2):
                    small = dts[:, d]
                    v.tensor_copy(small, dt_tok[:, :, heads[d]]).then_inc(scaled, 1)
                    dve.wait_ge(scaled, 2 * d + 1)
                    by_head(v, xdt[:, d], x_tok[:], small.rearrange("p c h -> p (c h)")).then_inc(scaled, 1)
                dve.wait_ge(exped, 2)
                dve.wait_ge(scaled, 4)
                by_head(v, xw[:, 1], xdt[:, 1], w[:, 1].rearrange("p c h -> p (c h)")).then_inc(weighted[1], 1)
                for n in range(6):
                    i, d = n // 2, n % 2
                    now, nxt = (3 - i, 2 - i) if d else (i, i + 1)
                    dve.wait_ge(product, n + 1)
                    by = ecum[:, heads[d], now:now + 1].broadcast_to([P, 8, 64])
                    if n >= 2:
                        dve.wait_ge(advanced, n - 1)
                    v.tensor_tensor(states[:, d, nxt].rearrange("p (h k) -> p h k", k=64),
                                    states[:, d, now].rearrange("p (h k) -> p h k", k=64), by,
                                    ALU.mult).then_inc(scaled, 1)
                    dve.wait_ge(scaled, 4 + n + 1)
                    v.tensor_tensor(states[:, d, nxt], states[:, d, nxt], acc[:, d], ALU.add).then_inc(advanced, 1)

    with ExitStack() as ctx:
        o = core.scope(nc, ctx, "sout")
        tmp = o.sb("tmp", [P, 2, 512])
        intra = o.ps("intra", [P, 2, 512])
        inter = o.ps("inter", [P, 2, 2, 512])
        turned = o.ps("turned", [P, 2, 512])
        etok = s["etok"]
        diffed, exped, y_stored = sems["diffed"], sems["exped"], sems["y_stored"]
        masked, y_ready, inter_ready, read, turned_ready, copied, tmp_ready = (
            o.sem(n) for n in ("masked", "y_ready", "inter_ready", "read", "turned_ready", "copied", "tmp_ready"))

        def turn(pe, c):
            pe.wait_ge(read, 2 * c + 2)
            if c >= 2:
                pe.wait_ge(copied, c - 1)
            for j in range(4):
                last = nc.tensor.transpose(turned[:, c % 2, j * P:(j + 1) * P],
                                           y_tok[:, c % 2, j * P:(j + 1) * P], core.ident[:])
            last.then_inc(turned_ready, 1)

        with nc.Block() as block:
            @block.sync
            def _(sp):
                if g < 3:
                    load_ssm_group(core, sp, g + 1, s, inputs_loaded)
                for c in (2, 3):
                    sp.wait_ge(diffed, 8 * g + 2 * (c - 1))
                    load_cum(core, sp, g, c, s, cum_loaded)
                sp.wait_ge(copied, 4)
                sp.dma_start(rows(dram["y_ssm"][512 * g:512 * (g + 1)]), y[:]).then_inc(y_stored, 16)
                if g == 3:
                    sp.wait_ge(y_stored, 64)

            @block.gpsimd
            def _(pool):
                for n in range(4, 8):
                    pool.wait_ge(y_ready, n - 3)
                    ssm_difference(nc, pool, g, n, s, cum_tok, sems)

            @block.scalar
            def _(act):
                def copy_out(c):
                    act.wait_ge(turned_ready, c + 1)
                    nc.scalar.activation(y[:, :, c * P:(c + 1) * P],
                                         turned[:, c % 2].rearrange("p (j t) -> p j t", t=P),
                                         ACT.Copy).then_inc(copied, 1)

                if g:
                    act.wait_ge(y_stored, 16 * g)
                for n in range(4, 8):
                    ssm_decay(nc, act, g, n, s, sems)
                    if n % 2:
                        copy_out((n - 5) // 2)
                copy_out(2)
                copy_out(3)

            @block.vector
            def _(dve):
                v = nc.vector

                def mask(n):
                    c, d = n // 2, n % 2
                    dve.wait_ge(exped, 8 * g + n + 1)
                    v.tensor_tensor(seg[:, n % 4], seg[:, n % 4], cb[:, d, c:c + 1].broadcast_to([P, 8, P]),
                                    ALU.mult).then_inc(masked, 1)

                def out(c):
                    dve.wait_ge(inter_ready, c + 1)
                    for d in range(2):
                        if c:
                            dve.wait_ge(read, 2 * c)
                        by = etok[:, c, 32 * d + 8 * g:32 * d + 8 * g + 8].unsqueeze(2).broadcast_to([P, 8, 64])
                        v.tensor_tensor(tmp[:, d].rearrange("p (h k) -> p h k", k=64),
                                        inter[:, c % 2, d].rearrange("p (h k) -> p h k", k=64), by,
                                        ALU.mult).then_inc(tmp_ready, 1)
                    dve.wait_ge(tmp_ready, 2 * c + 2)
                    v.tensor_tensor(tmp[:, 0], tmp[:, 0], tmp[:, 1], ALU.add).then_inc(read, 1)
                    dve.wait_ge(read, 2 * c + 1)
                    dve.wait_ge(y_ready, 2 * c + 2)
                    v.tensor_tensor(y_tok[:, c % 2], tmp[:, 0], intra[:, c % 2], ALU.add).then_inc(read, 1)

                mask(0)
                mask(1)
                for c in range(4):
                    if c < 3:
                        mask(2 * c + 2)
                        mask(2 * c + 3)
                    if c >= 2:
                        dve.wait_ge(turned_ready, c - 1)
                    out(c)

            @block.tensor
            def _(pe):
                for c in range(4):
                    if c >= 2:
                        pe.wait_ge(read, 2 * (c - 1))
                    at = slice(c * P, (c + 1) * P)
                    for d in range(2):
                        last = nc.tensor.matmul(inter[:, c % 2, d], bc_[:, 1, at], states[:, d, c], start=True,
                                                stop=True)
                    last.then_inc(inter_ready, 1)
                    for d in range(2):
                        n = 2 * c + d
                        pe.wait_ge(masked, n + 1)
                        for h in range(8):
                            last = nc.tensor.matmul(intra[:, c % 2, h * 64:(h + 1) * 64], seg[:, n % 4, h],
                                                    xdt[:, d, c, h * 64:(h + 1) * 64], start=d == 0 and h == 0,
                                                    stop=d == 1 and h == 7, skip_group_check=True)
                        last.then_inc(y_ready, 1)
                    if c:
                        turn(pe, c - 1)
                turn(pe, 3)


def stage_ssm(nc, core):
    dram = core.dram
    with ExitStack() as ctx:
        o = core.scope(nc, ctx, "ssm")
        stage_ssm_context(nc, core)
        dt_tok, cum_tok, etok = (o.sb(n, [P, 4, 64]) for n in ("dt_tok", "cum_tok", "etok"))
        edges, ecum = o.sb("edges", [P, 64, 4]), o.sb("ecum", [P, 64, 4])
        stage_steps(nc, core, dram["z"][Z3["dt"]:Z3["dt"] + 64], T, P, dt_tok, cum_tok, cum_dram=dram["cum"],
                    edge_dram=dram["edge"])
        stage_load(nc, core, [(edges[:], spread(dram["edge"]))])
        with nc.Block() as block:
            @block.scalar
            def _(act):
                nc.scalar.activation(etok[:], cum_tok[:], ACT.Exp)
                nc.scalar.activation(ecum[:], edges[:], ACT.Exp)
        shapes = {"x": [P, 4, T], "bc": [P, 2, 2, T], "x_tok": [P, 4, 512], "b_tok": [P, 4, P],
                  "xdt": [P, 2, 4, 512], "xw": [P, 2, 4, 512], "states": [P, 2, 2, 4, 512], "cb": [P, 2, 4, P],
                  "y_tok": [P, 2, 512], "y": [P, 4, T], "dts": [P, 2, 4, 8], "cum": [P, 2, 2, 8, P],
                  "seg": [P, 4, 8, P]}
        tiles = {n: o.sb(n, shape) for n, shape in shapes.items()}
        tiles["etok"] = etok
        sems = {n: o.sem(n) for n in ("inputs_loaded", "diffed", "clipped", "exped", "y_stored")}
        sems["cum_loaded"] = [o.sem(f"cum_loaded{i}") for i in range(2)]
        for g in range(4):
            stage_ssm_group(nc, core, g, tiles, dt_tok, cum_tok, ecum, edges, sems)


def stage_ssm_out(nc, core, y):
    dram = core.dram
    with ExitStack() as ctx:
        o = core.scope(nc, ctx, "ssmout")
        rstd = o.sb("rstd", [P, 4, T])
        with ExitStack() as inner:
            s = core.scope(nc, inner, "gate")
            x, z = s.sb("x", [P, 2, 4, T]), s.sb("z", [P, 2, 4, T])
            step = s.sem("step")
            loaded = [s.sem(f"loaded{i}") for i in range(2)]
            gated = s.sem("gated")
            with nc.Block() as block:
                @block.sync
                def _(sp):
                    for g in range(4):
                        if g >= 2:
                            sp.wait_ge(gated, g - 1)
                        at = slice(512 * g, 512 * (g + 1))
                        sp.dma_start(y[:, 4 * g:4 * g + 4], rows(dram["y_ssm"][at])).then_inc(loaded[g % 2], 16)
                        sp.dma_start(x[:, g % 2], rows(dram["xbc"][at])).then_inc(loaded[g % 2], 16)
                        sp.dma_start(z[:, g % 2], rows(dram["z"][Z3["z"] + 512 * g:Z3["z"] + 512 * (g + 1)])
                                     ).then_inc(loaded[g % 2], 16)

                @block.vector
                def _(dve):
                    done = Steps(dve, step)
                    for g in range(4):
                        dve.wait_ge(loaded[g % 2], 48 * (g // 2 + 1))
                        for j in range(4):
                            n = 4 * g + j
                            done.mark(nc.vector.scalar_tensor_tensor(out=y[:, n], in0=x[:, g % 2, j],
                                                                     scalar=core.v("d_skip", n), in1=y[:, n],
                                                                     op0=ALU.mult, op1=ALU.add))
                        done.wait()
                        nc.vector.tensor_tensor(y[:, 4 * g:4 * g + 4], y[:, 4 * g:4 * g + 4], z[:, g % 2],
                                                ALU.mult).then_inc(gated, 1)
        stage_rstd(nc, core, y, rstd, 4, core.ones, 512, EPS)
        step = o.sem("step")
        with nc.Block() as block:
            @block.vector
            def _(dve):
                for n in range(SSM_TILES):
                    nc.vector.scalar_tensor_tensor(out=y[:, n], in0=y[:, n], scalar=core.v("ssm_norm_w", n),
                                                   in1=rstd[:, n // 4], op0=ALU.mult,
                                                   op1=ALU.mult).then_inc(step, 1)


def third_block(nc, core):
    dram = core.dram
    z, gates = dram["z"], dram["gates"]
    mod = core.mod[:, 1]
    shift1, scale1, gate1, shift2, scale2, gate2 = (mod[:, 8 * n:8 * n + 8] for n in range(6))
    with ExitStack() as ctx:
        merged = core.scope(nc, ctx, "third").sb("merged", [P, DT, T])
        with ExitStack() as inner:
            s1 = core.scope(nc, inner, "mixer")
            v_tok = s1.sb("v_tok", [P, 4, D])
            with ExitStack() as deep:
                h = split_tiles(core.scope(nc, deep, "third_h"), "h", [P, DT, T])
                stage_norm(nc, core, core.x, "norm1_w_3", (scale1, shift1), parts=h)
                stage_rows(nc, core, [(dram["w3_qk"], z[0:1024], ACT.Copy),
                                      (dram["w3_xbc"], z[4096:7168], ACT.Copy)], h,
                           tails=[(dram["w3_lr"], z[7168:7200], h), (dram["w3_dt"], z[7200:7264], h)])
                stage_tokens(nc, core, dram["w3_v"], [(h, v_tok)])
                stage_rows(nc, core, [(dram["w3_rz"], z[1024:4096], ACT.Silu),
                                      (dram["w3_g"], gates[0:2048], ACT.Sigmoid)], h,
                           beside=CentredConvs(nc, core))
            y = s1.sb("y", [P, 8, T])
            stage_gla(nc, core, v_tok, y)
            stage_project(nc, core, dram["w_pa_3"], 8, merged, y, gates=gates[0:D], first=True)
        stage_ssm(nc, core)
        with ExitStack() as inner:
            y = core.scope(nc, inner, "ssmy").sb("y", [P, SSM_TILES, T])
            stage_ssm_out(nc, core, y)
            stage_project(nc, core, dram["w_pb_3"], SSM_TILES, merged, y, gates=gates[D:2 * D])
        stage_project(nc, core, dram["w_out_3"], DT, core.x, merged, scale=gate1)
    stage_ffn(nc, core, "norm2_w_3", dram["ffn_up_3"], dram["ffn_down_3"], (scale2, shift2), scale=gate2)
    stage_norm(nc, core, core.x, "final_norm_w_3", dst=core.x)



def stage_end(nc, core, out):
    with ExitStack() as ctx:
        s = core.scope(nc, ctx, "end")
        stored = s.sem("stored")
        with nc.Block() as block:
            @block.sync
            def _(sp):
                sp.dma_start(rows(out), core.x[:]).then_inc(stored, 16)
                sp.wait_ge(stored, 16)


def program(nc, dram, vec_at, vec_cols, out, blocks=(1, 2, 3)):
    with ExitStack() as ctx:
        core = Core(nc, ctx, dram, vec_at, vec_cols)
        stage_start(nc, core)
        if 1 in blocks:
            first_block(nc, core)
        if 2 in blocks:
            second_block(nc, core)
        if 3 in blocks:
            third_block(nc, core)
        stage_end(nc, core, out)




def tiled(w, cols):
    k, n = w.shape
    return np.ascontiguousarray(w.reshape(k // P, P, n // cols, cols).transpose(2, 1, 0, 3))


def up_pairs(gate, up):
    return np.ascontiguousarray(np.stack([tiled(gate, P), tiled(up, P)], axis=2))


def column(a):
    return a.reshape(-1, P).T


def taps(w):
    k, n = w.shape
    return w.reshape(k, n // P, P).transpose(2, 1, 0).reshape(P, -1)


def padded(a):
    out = np.zeros((P, a.shape[1]), a.dtype)
    out[:a.shape[0]] = a
    return out


def layout(i):
    a, v = {}, {}
    a["xT"] = np.ascontiguousarray(i["x"][0].T)
    w = i["w_in"][0]
    a["w_in_a"] = tiled(w[:, :4096], WCOLS)
    a["w_in_v"] = tiled(w[:, 4096:4608], WCOLS)
    a["w_in_g"] = tiled(w[:, 4608:], WCOLS)
    a["sc_out"] = tiled(i["sc_out"][0], P)
    a["conf_out"] = tiled(i["conf_out"][0], P)
    a["diff_out"] = tiled(i["diff_out"][0], P)
    a["w_o"] = tiled(i["w_o"][0], P)
    a["pool_w"] = np.ascontiguousarray(
        i["pool_w"][0].reshape(4, P, 2, P).transpose(0, 2, 1, 3).reshape(8, P, 1, P))
    a["ffn_up"] = up_pairs(i["ffn_up"][0][:, :D_FF], i["ffn_up"][0][:, D_FF:])
    a["ffn_down"] = tiled(i["ffn_down"][0], P)
    for n in ("mix_norm", "pool_scale", "conf_conv_b", "conf_ln_g", "conf_ln_b", "ffn_norm", "diff_subln"):
        v[n] = column(i[n][0])
    for n in ("sc_conv", "conf_conv", "ffn_conv"):
        v[n] = taps(i[n][0])
    for n in ("q_norm", "k_norm"):
        v[n] = np.concatenate([i[n][0], i[n][0]]).reshape(P, 1)
    v["lam_q"] = padded(np.stack([i["lambda_q1"][0], i["lambda_q2"][0]], axis=1))
    v["lam_k"] = padded(np.stack([i["lambda_k1"][0], i["lambda_k2"][0]], axis=1))
    a["w_ada_2"] = tiled(i["w_ada_2"][0], Ada.COLS)
    w = i["w_in_2"][0]
    a["w_in_2a"] = tiled(w[:, :2048], WCOLS)
    a["w_in_2b"] = tiled(w[:, 2064:3600], WCOLS)
    a["w_in_2g"] = tiled(w[:, 3888:], WCOLS)
    for n, (lo, hi) in enumerate(((2048, 2064), (3600, 3728), (3728, 3856), (3856, 3888))):
        a[f"w_in_2t{n}"] = tiled(w[:, lo:hi], hi - lo)[0]
    for n in ("w_branch_gdn_2", "w_branch_rwkv_2", "w_out_2"):
        a[n] = tiled(i[n][0], P)
    a["ffn_up_2"] = up_pairs(i["w_ffn_in_2"][0][:, :D_FF], i["w_ffn_in_2"][0][:, D_FF:])
    a["ffn_down_2"] = tiled(i["w_ffn_out_2"][0], P)
    for n in ("w2", "a2", "g2"):
        a[n] = np.ascontiguousarray(i[n + "_2"][0])
    v["c_2"] = column(i["c_2"][0])
    for n in ("b_ada_2", "norm1_w_2", "norm2_w_2"):
        v[n] = column(i[n][0])
    v["norm_f_w_2"] = column(i["norm_f_w_2"])
    v["conv_gdn"] = taps(i["conv_gdn_2"][0])
    v["conv_ffn_2"] = taps(i["conv_ffn_2"][0])
    v["onorm_gdn"] = np.concatenate([i["onorm_gdn_2"][0]] * 2).reshape(P, 1)
    heads = np.array([2 * j + q for _ in range(NC64) for q in range(2) for j in range(4)])
    v["a_log"] = padded(i["a_log_2"][0][heads].reshape(HN, 1))
    v["dt_bias"] = padded(i["dt_bias_2"][0][heads].reshape(HN, 1))
    mu = i["mu_rwkv_2"][0]
    v["mu_rkv"] = column(mu[:1536])
    v["mu_lo"] = np.concatenate([padded(mu[lo:hi].reshape(-1, 1)) for lo, hi in
                                 ((1536, 1600), (1600, 1664), (1664, 1792), (1792, 1824))], axis=1)
    for n in ("w0", "a0", "k_k", "k_a", "lnx_w", "lnx_b"):
        v[n] = column(i[n + "_2"][0])
    v["r_k"] = column(i["r_k_2"][0].reshape(-1))
    a["ctxT"] = np.ascontiguousarray(i["ctx_3"][0].T)
    a["w_ada_3"] = tiled(i["w_ada_3"][0], Ada.COLS)
    w = i["w_in_3"][0]
    for n, (lo, hi) in {"qk": (0, 1024), "xbc": (5152, 8224),
                        "g": (8288, 10336)}.items():
        a["w3_" + n] = tiled(w[:, lo:hi], WCOLS)
    a["w3_rz"] = tiled(np.concatenate([w[:, 2048:3072], w[:, 3104:5152]], axis=1), WCOLS)
    a["w3_v"] = tiled(w[:, 1024:2048], WCOLS)
    a["w3_lr"] = tiled(w[:, 3072:3104], 32)[0]
    a["w3_dt"] = tiled(w[:, 8224:8288], 64)[0]
    for n in ("gla_up_f", "gla_up_b"):
        a[n] = np.ascontiguousarray(i[n + "_3"][0])
    for n in ("w_pa_3", "w_pb_3", "w_out_3"):
        a[n] = tiled(i[n][0], P)
    a["ffn_up_3"] = up_pairs(i["w_gate_3"][0], i["w_up_3"][0])
    a["ffn_down_3"] = tiled(i["w_down_3"][0], P)
    v["c_3"] = np.stack([column(i["c_3"][0]), column(i["c_ctx_3"])], axis=2).reshape(P, 16)
    for n in ("b_ada_3", "norm1_w_3", "norm2_w_3", "conv_b_3"):
        v[n] = column(i[n][0])
    v["final_norm_w_3"] = column(i["final_norm_w_3"])
    v["conv_w_3"] = taps(i["conv_w_3"][0])
    for n in ("gla_bias_f", "gla_bias_b", "gla_norm_w", "ssm_norm_w"):
        v[n] = column(i[n + "_3"][0])
    v["d_skip"] = column(np.repeat(i["d_skip_3"][0], 64))
    for n in ("dt_bias", "a_log"):
        v[n + "_3"] = padded(np.concatenate([i[n + "_f_3"][0], i[n + "_b_3"][0]]).reshape(64, 1))
    left = [np.array([[s // (2 << n) == t // (2 << n) and s // (1 << n) % 2 == 0 and t // (1 << n) % 2 == 1
                       for t in range(P)] for s in range(P)]) for n in range(GLA_LEVELS)]
    masks = [np.eye(P, dtype=bool)] + left + [m.T for m in left]
    a["masks"] = np.ascontiguousarray(np.stack(masks, axis=1).astype(np.int32))
    at, n = {}, 0
    for name, cols in v.items():
        at[name] = n
        n += cols.shape[1]
    a["vecs"] = np.ascontiguousarray(np.concatenate(list(v.values()), axis=1))
    return a, at


SCRATCH = {
    "z": (8192, T), "gates": (GATE_ROWS, T), "feat": (512 * len(F2), T), "hn": (3, HN, C64),
    "decay": (HN, C64, C64), "gram": (2 * HN, C64, C64), "inverse": (2 * HN, C64, C64),
    "zc": (3168, CTX), "xc": (2560, CTX), "xbc": (3072, T), "y_ssm": (2048, T), "cum": (64, T), "edge": (64, 4),
    "edge_c": (64, 1), "s0": (2, 4, P, 512),
    "v_ctx": (P, 2, D),
}


def build(nc, arrays, at, blocks=(1, 2, 3)):
    dram = {n: nc.dram_tensor(f"in_{n}", a.shape, I32 if a.dtype == np.int32 else F32,
                              kind="ExternalInput").ap() for n, a in arrays.items()}
    for n, shape in SCRATCH.items():
        dram[n] = nc.dram_tensor(f"scratch_{n}", shape, F32).ap()
    out = nc.dram_tensor("out_T", (D, T), F32, kind="ExternalOutput").ap()
    program(nc, dram, at, arrays["vecs"].shape[1], out, blocks)


def kernel(**inputs):
    import concourse.bacc as _bacc
    from concourse.bass_utils import run_bass_kernel_spmd as _run

    arrays, at = layout({n: np.asarray(a) for n, a in inputs.items()})
    nc = _bacc.Bacc("TRN2", target_bir_lowering=False, num_devices=1)
    build(nc, arrays, at)
    r = _run(nc, [{f"in_{n}": a for n, a in arrays.items()}], core_ids=[0])
    return np.ascontiguousarray(r.results[0]["out_T"].T).reshape(1, T, D)
```
